# Optimizing a Trainium2 kernel written in Bass

```python
import jax, jax.numpy as jnp
from jax import lax
import numpy as np

D_MODEL = 1024
BATCH = 1
SEQ = 256
DEPTH = 2

CHUNK = 64
PE_DIM = 256
EPS = 1e-6
M_HEADS = 4
M_DK = 256
M_DV = 256
M_QK = M_HEADS * M_DK
M_V = M_HEADS * M_DV
CONV_K = 4
R_HEADS = 4
R_DK = 256
R_DV = 512
R_QK = R_HEADS * R_DK
R_V = R_HEADS * R_DV
ROPE_BASE = 10000.0
D_FF = 4 * D_MODEL
IN_SIZES = (M_QK, M_QK, M_V, M_V, M_HEADS, M_HEADS, R_QK, R_QK, R_V, R_V, D_MODEL, D_MODEL)
N_IN = M_QK * 2 + M_V * 2 + M_HEADS * 2 + R_QK * 2 + R_V * 2 + D_MODEL * 2
F_GATE_OFFSET = M_QK * 2 + M_V * 2 + M_HEADS


def split_cols(z):
    outs = []
    off = 0
    for s in IN_SIZES:
        outs.append(z[..., off:off + s])
        off += s
    return outs

def rmsnorm(x, g):
    xf = x.astype(jnp.float32)
    y = xf * lax.rsqrt(jnp.mean(xf * xf, axis=-1, keepdims=True) + EPS)
    return (y * g.astype(jnp.float32)).astype(x.dtype)

def head_layernorm(y, g, n_heads):
    B, S, W = y.shape
    yf = y.astype(jnp.float32).reshape(B, S, n_heads, W // n_heads)
    mu = jnp.mean(yf, axis=-1, keepdims=True)
    var = jnp.mean(jnp.square(yf - mu), axis=-1, keepdims=True)
    yn = ((yf - mu) * lax.rsqrt(var + EPS)).reshape(B, S, W)
    return yn * g.astype(jnp.float32)

def causal_conv(u, w, b):
    S = u.shape[1]
    up = jnp.pad(u, ((0, 0), (CONV_K - 1, 0), (0, 0)))
    out = b
    for j in range(CONV_K):
        out = out + up[:, j:j + S, :] * w[j]
    return out

def rope(x, cos, sin):
    half = x.shape[-1] // 2
    x1, x2 = x[..., :half], x[..., half:]
    return jnp.concatenate([x1 * cos - x2 * sin, x1 * sin + x2 * cos], axis=-1)

def to_chunks(x, n_heads):
    B, S, W = x.shape
    return x.reshape(B, S // CHUNK, CHUNK, n_heads, W // n_heads).transpose(1, 0, 3, 2, 4)

def gates_to_chunks(g):
    B, S, H = g.shape
    return g.reshape(B, S // CHUNK, CHUNK, H).transpose(1, 0, 3, 2)

def from_chunks(y):
    NC, B, H, L, d = y.shape
    return y.transpose(1, 0, 3, 2, 4).reshape(B, NC * L, H * d)

def mlstm_chunkwise(q, k, v, li, lf):
    NC, B, H, L, dk = q.shape
    dv = v.shape[-1]
    causal = jnp.tril(jnp.ones((L, L), dtype=bool))

    def step(carry, inp):
        C, n, m = carry
        qc, kc, vc, lic, lfc = inp
        b = jnp.cumsum(lfc, axis=-1)
        log_intra = b[..., :, None] - b[..., None, :] + lic[..., None, :]
        log_intra = jnp.where(causal, log_intra, -jnp.inf)
        log_inter = b + m[..., None]
        m_t = jnp.maximum(log_inter, jnp.max(log_intra, axis=-1))
        d_intra = jnp.exp(log_intra - m_t[..., None])
        d_inter = jnp.exp(log_inter - m_t)
        s = jnp.einsum('bhtd,bhsd->bhts', qc, kc) * d_intra
        num = jnp.einsum('bhts,bhsv->bhtv', s, vc) + d_inter[..., None] * jnp.einsum('bhtd,bhdv->bhtv', qc, C)
        den = jnp.sum(s, axis=-1) + d_inter * jnp.einsum('bhtd,bhd->bht', qc, n)
        h = num / jnp.maximum(jnp.abs(den), jnp.exp(-m_t))[..., None]
        b_end = b[..., -1]
        log_w = b_end[..., None] - b + lic
        m_new = jnp.maximum(b_end + m, jnp.max(log_w, axis=-1))
        w = jnp.exp(log_w - m_new[..., None])
        decay = jnp.exp(b_end + m - m_new)
        C = decay[..., None, None] * C + jnp.einsum('bhsd,bhsv->bhdv', kc * w[..., None], vc)
        n = decay[..., None] * n + jnp.einsum('bhs,bhsd->bhd', w, kc)
        return (C, n, m_new), h

    init = (jnp.zeros((B, H, dk, dv), jnp.float32), jnp.zeros((B, H, dk), jnp.float32),
            jnp.zeros((B, H), jnp.float32))
    _, hs = lax.scan(step, init, (q, k, v, li, lf))
    return hs

def retention_chunkwise(q, k, v, log_gamma):
    NC, B, H, L, dk = q.shape
    dv = v.shape[-1]
    pos = jnp.arange(L, dtype=jnp.float32)
    diff = pos[:, None] - pos[None, :]
    lg = log_gamma[:, None, None]
    intra = jnp.where(diff >= 0, jnp.exp(jnp.maximum(diff, 0.0) * lg), 0.0)
    inter = jnp.exp((pos + 1.0) * log_gamma[:, None])
    kdec = jnp.exp((L - 1.0 - pos) * log_gamma[:, None])
    cdec = jnp.exp(L * log_gamma)

    def step(R, inp):
        qc, kc, vc = inp
        s = jnp.einsum('bhtd,bhsd->bhts', qc, kc) * intra
        y = jnp.einsum('bhts,bhsv->bhtv', s, vc) + jnp.einsum('bhtd,bhdv->bhtv', qc, R) * inter[..., None]
        R = cdec[:, None, None] * R + jnp.einsum('bhsd,bhsv->bhdv', kc * kdec[..., None], vc)
        return R, y

    _, ys = lax.scan(step, jnp.zeros((B, H, dk, dv), jnp.float32), (q, k, v))
    return ys

def first_inputs(seed: int = 0) -> dict:
    key = jax.random.key(seed)
    ks = jax.random.split(key, 24)
    f32 = jnp.float32

    def nrm(k, shape, scale):
        return jax.random.normal(k, shape, f32) * scale

    def gain(k, shape):
        return 1.0 + 0.05 * jax.random.normal(k, shape, f32)

    b_in = nrm(ks[4], (DEPTH, N_IN), 0.02)
    f_bias = jnp.linspace(3.0, 6.0, M_HEADS, dtype=f32)[None, :] + nrm(ks[5], (DEPTH, M_HEADS), 0.1)
    b_in = b_in.at[:, F_GATE_OFFSET:F_GATE_OFFSET + M_HEADS].set(f_bias)
    return {
        "x": nrm(ks[0], (BATCH, SEQ, D_MODEL), 1.0),
        "p": nrm(ks[1], (DEPTH, BATCH, SEQ, PE_DIM), 1.0),
        "norm1_g": gain(ks[2], (DEPTH, D_MODEL)),
        "w_in": nrm(ks[3], (DEPTH, D_MODEL, N_IN), D_MODEL ** -0.5),
        "b_in": b_in,
        "conv_w": nrm(ks[6], (DEPTH, CONV_K, 2 * M_QK), CONV_K ** -0.5),
        "conv_b": nrm(ks[7], (DEPTH, 2 * M_QK), 0.02),
        "m_norm_g": gain(ks[8], (DEPTH, M_V)),
        "r_norm_g": gain(ks[9], (DEPTH, R_V)),
        "w_bm": nrm(ks[10], (DEPTH, M_V, D_MODEL), M_V ** -0.5),
        "w_br": nrm(ks[11], (DEPTH, R_V, D_MODEL), R_V ** -0.5),
        "w_out": nrm(ks[12], (DEPTH, D_MODEL, D_MODEL), D_MODEL ** -0.5),
        "norm2_g": gain(ks[13], (DEPTH, D_MODEL)),
        "w_ff1": nrm(ks[14], (DEPTH, D_MODEL, D_FF), D_MODEL ** -0.5),
        "b_ff1": nrm(ks[15], (DEPTH, D_FF), 0.02),
        "w_ff2": nrm(ks[16], (DEPTH, D_FF, D_MODEL), D_FF ** -0.5),
        "b_ff2": nrm(ks[17], (DEPTH, D_MODEL), 0.02),
        "norm3_g": gain(ks[18], (DEPTH, D_MODEL)),
        "w_pe_gate": nrm(ks[19], (DEPTH, D_MODEL, D_MODEL), D_MODEL ** -0.5),
        "w_pe": nrm(ks[20], (DEPTH, PE_DIM, D_MODEL), PE_DIM ** -0.5),
        "final_g": gain(ks[21], (D_MODEL,)),
    }

def first_block(x, p, norm1_g, w_in, b_in, conv_w, conv_b, m_norm_g, r_norm_g, w_bm, w_br,
              w_out, norm2_g, w_ff1, b_ff1, w_ff2, b_ff2, norm3_g, w_pe_gate, w_pe, final_g):
    B, S, _ = x.shape
    dt = x.dtype
    f32 = jnp.float32
    pos = jnp.arange(S, dtype=f32)
    inv_freq = ROPE_BASE ** (-jnp.arange(0, R_DK, 2, dtype=f32) / R_DK)
    ang = pos[:, None] * inv_freq[None, :]
    cos = jnp.cos(ang)[:, None, :]
    sin = jnp.sin(ang)[:, None, :]
    log_gamma = jnp.log(1.0 - jnp.exp2(-5.0 - jnp.arange(R_HEADS, dtype=f32)))

    for i in range(DEPTH):
        h = rmsnorm(x, norm1_g[i])
        z = h @ w_in[i] + b_in[i]
        _, _, mv, mo, mi, mf, rq, rk, rv, rg, gm, gr = split_cols(z)
        qk = jax.nn.silu(causal_conv(z[..., :2 * M_QK], conv_w[i], conv_b[i]))
        mq = qk[..., :M_QK] * (M_DK ** -0.5)
        mk = qk[..., M_QK:]

        hm = mlstm_chunkwise(
            to_chunks(mq.astype(f32), M_HEADS), to_chunks(mk.astype(f32), M_HEADS),
            to_chunks(mv.astype(f32), M_HEADS),
            gates_to_chunks(mi.astype(f32)), gates_to_chunks(jax.nn.log_sigmoid(mf.astype(f32))))
        hm = from_chunks(hm)
        y_m = (jax.nn.sigmoid(mo.astype(f32)) * head_layernorm(hm, m_norm_g[i], M_HEADS)).astype(dt)

        rq4 = rope(rq.astype(f32).reshape(B, S, R_HEADS, R_DK), cos, sin)
        rk4 = rope(rk.astype(f32).reshape(B, S, R_HEADS, R_DK), cos, sin) * (R_DK ** -0.5)
        hr = retention_chunkwise(
            to_chunks(rq4.reshape(B, S, R_QK), R_HEADS), to_chunks(rk4.reshape(B, S, R_QK), R_HEADS),
            to_chunks(rv.astype(f32), R_HEADS), log_gamma)
        hr = from_chunks(hr)
        y_r = (jax.nn.silu(rg.astype(f32)) * head_layernorm(hr, r_norm_g[i], R_HEADS)).astype(dt)

        merged = jax.nn.sigmoid(gm) * (y_m @ w_bm[i]) + jax.nn.sigmoid(gr) * (y_r @ w_br[i])
        x = x + merged @ w_out[i]

        h2 = rmsnorm(x, norm2_g[i])
        x = x + jnp.square(jax.nn.relu(h2 @ w_ff1[i] + b_ff1[i])) @ w_ff2[i] + b_ff2[i]

        h3 = rmsnorm(x, norm3_g[i])
        x = x + jax.nn.sigmoid(h3 @ w_pe_gate[i]) * (p[i] @ w_pe[i])

    return rmsnorm(x, final_g)


GLA_HEADS = 4
GLA_VW = D_MODEL // 2
GLA_DV = GLA_VW // GLA_HEADS
GLA_KW = GLA_VW // 2
GLA_DK = GLA_KW // GLA_HEADS
GLA_LORA = 16
GLA_TAU = 16.0
GLA_CHUNK = 64
RWKV_W = D_MODEL - GLA_VW
RWKV_HEAD = 64
RWKV_HEADS = RWKV_W // RWKV_HEAD
RWKV_W_LORA = 32
RWKV_A_LORA = 32
RWKV_G_LORA = 96
RWKV_LNX_EPS = 64e-5
ATT_HEADS = 8
ATT_HEAD = D_MODEL // ATT_HEADS
IDX_HEADS = 8
IDX_DIM = 64
TOPK_MAX = 256
Q_BLOCK = 128
ROPE_THETA = 10000.0
NEG = -1e30
PEER_HEADS = 8
PEER_DKEY = 128
PEER_NKEYS = 128
PEER_N_EXPERTS = PEER_NKEYS * PEER_NKEYS
PEER_TOPK = 16
PEER_TOKEN_BLOCK = 128
DN_ALPHA = (2 * DEPTH) ** 0.25
DN_BETA = (8 * DEPTH) ** -0.25
LN_EPS = 1e-5
N_EVEN = (DEPTH + 1) // 2
N_ODD = DEPTH // 2

GLA_SPLITS = (GLA_KW, GLA_KW, GLA_VW, GLA_VW, GLA_LORA)
RWKV_SPLITS = (RWKV_W, RWKV_W, RWKV_W, RWKV_W_LORA, RWKV_A_LORA, RWKV_G_LORA)
GLA_IN = sum(GLA_SPLITS)
RWKV_IN = sum(RWKV_SPLITS)
EVEN_IN = GLA_IN + RWKV_IN
ODD_SPLITS = (ATT_HEADS * ATT_HEAD, ATT_HEAD, ATT_HEAD, IDX_HEADS * IDX_DIM, IDX_DIM, IDX_HEADS)
ODD_IN = sum(ODD_SPLITS)


F32 = jnp.float32

def _split(t, sizes):
    cuts = [int(c) for c in np.cumsum(sizes)[:-1]]
    return jnp.split(t, cuts, axis=-1)

def layer_norm(x, g, b):
    xf = x.astype(F32)
    mu = xf.mean(-1, keepdims=True)
    var = jnp.square(xf - mu).mean(-1, keepdims=True)
    return ((xf - mu) * lax.rsqrt(var + LN_EPS) * g + b).astype(x.dtype)

def rope_tables(T, dim):
    inv = ROPE_THETA ** (-jnp.arange(0, dim, 2, dtype=F32) / dim)
    ang = jnp.arange(T, dtype=F32)[:, None] * inv[None, :]
    return jnp.cos(ang), jnp.sin(ang)

def apply_rope(x, cos, sin):
    x1, x2 = jnp.split(x, 2, axis=-1)
    return jnp.concatenate([x1 * cos - x2 * sin, x2 * cos + x1 * sin], -1).astype(x.dtype)

def gla_chunked(q, k, v, log_a):
    B, T, H, dk = q.shape
    dv = v.shape[-1]
    C = GLA_CHUNK
    n = T // C

    def chunks(t):
        return t.astype(F32).reshape(B, n, C, H, -1).transpose(0, 3, 1, 2, 4)

    q, k, v, la = chunks(q) * dk ** -0.5, chunks(k), chunks(v), chunks(log_a)
    b = jnp.cumsum(la, axis=3)
    b_last = b[:, :, :, -1:, :]
    q_in = q * jnp.exp(b)
    k_in = k * jnp.exp(-b)
    k_out = k * jnp.exp(b_last - b)
    causal = jnp.tril(jnp.ones((C, C), dtype=bool))
    A = jnp.where(causal, jnp.einsum('bhnid,bhnjd->bhnij', q_in, k_in), 0.0)
    o = jnp.einsum('bhnij,bhnje->bhnie', A, v)
    kv = jnp.einsum('bhnjd,bhnje->bhnde', k_out, v)
    dec = jnp.exp(b_last[:, :, :, 0, :])

    def step(S, inp):
        dec_n, kv_n = inp
        return dec_n[..., None] * S + kv_n, S

    S0 = jnp.zeros((B, H, dk, dv), F32)
    _, S_prev = lax.scan(step, S0, (jnp.moveaxis(dec, 2, 0), jnp.moveaxis(kv, 2, 0)))
    S_prev = jnp.moveaxis(S_prev, 0, 2)
    o = o + jnp.einsum('bhnid,bhnde->bhnie', q_in, S_prev)
    return o.transpose(0, 2, 3, 1, 4).reshape(B, T, H, dv)

def rwkv7_scan(r, w, k, v, a, b):
    B, T, H, N = r.shape

    def step(S, inp):
        r_t, w_t, k_t, v_t, a_t, b_t = inp
        sa = jnp.einsum('bhij,bhj->bhi', S, a_t)
        S = S * w_t[:, :, None, :] + sa[..., None] * b_t[:, :, None, :] + v_t[..., None] * k_t[:, :, None, :]
        return S, jnp.einsum('bhij,bhj->bhi', S, r_t)

    xs = tuple(jnp.moveaxis(t.astype(F32), 1, 0) for t in (r, w, k, v, a, b))
    _, y = lax.scan(step, jnp.zeros((B, H, N, N), F32), xs)
    return jnp.moveaxis(y, 0, 1)

def even_mixer(x, w_in, gla_a_w2, gla_a_b, gla_norm_g, rwkv_mu, rwkv_w0, rwkv_w2, rwkv_a0, rwkv_a2,
               rwkv_g2, rwkv_k_k, rwkv_k_a, rwkv_r_k, rwkv_lnx_g, rwkv_lnx_b, w_out):
    B, T, _ = x.shape

    def heads(t, h):
        return t.reshape(B, T, h, -1)

    p = x @ w_in
    gla_p, rw_p = p[..., :GLA_IN], p[..., GLA_IN:]
    gq, gk, gv, gg, gal = _split(gla_p, GLA_SPLITS)
    log_a = jax.nn.log_sigmoid((gal @ gla_a_w2 + gla_a_b).astype(F32)) / GLA_TAU
    o = gla_chunked(heads(gq, GLA_HEADS), heads(gk, GLA_HEADS), heads(gv, GLA_HEADS), heads(log_a, GLA_HEADS))
    o = o * lax.rsqrt(jnp.mean(jnp.square(o), -1, keepdims=True) + LN_EPS) * gla_norm_g
    gla_out = (o.reshape(B, T, GLA_VW) * jax.nn.silu(gg.astype(F32))).astype(x.dtype)
    prev = jnp.pad(rw_p, ((0, 0), (1, 0), (0, 0)))[:, :-1]
    rw_p = rw_p + (prev - rw_p) * rwkv_mu
    r, k, v, wl, al, gl = _split(rw_p, RWKV_SPLITS)
    w_log = -jax.nn.softplus(-(rwkv_w0 + jnp.tanh(wl) @ rwkv_w2).astype(F32)) - 0.5
    decay = jnp.exp(-jnp.exp(w_log))
    a = jax.nn.sigmoid((rwkv_a0 + al @ rwkv_a2).astype(F32))
    g = jax.nn.sigmoid(gl) @ rwkv_g2
    kk = heads((k * rwkv_k_k).astype(F32), RWKV_HEADS)
    kk = kk / jnp.maximum(jnp.sqrt(jnp.sum(jnp.square(kk), -1, keepdims=True)), 1e-12)
    k = k * (1.0 + (a - 1.0) * rwkv_k_a)
    a_h = heads(a, RWKV_HEADS)
    r_h, k_h, v_h = heads(r, RWKV_HEADS), heads(k, RWKV_HEADS), heads(v, RWKV_HEADS)
    y = rwkv7_scan(r_h, heads(decay, RWKV_HEADS), k_h, v_h, -kk, kk * a_h)
    mu = y.mean(-1, keepdims=True)
    var = jnp.square(y - mu).mean(-1, keepdims=True)
    y = (y - mu) * lax.rsqrt(var + RWKV_LNX_EPS) * rwkv_lnx_g.reshape(RWKV_HEADS, RWKV_HEAD) \
        + rwkv_lnx_b.reshape(RWKV_HEADS, RWKV_HEAD)
    bonus = jnp.sum((r_h * k_h * rwkv_r_k).astype(F32), -1, keepdims=True) * v_h.astype(F32)
    rwkv_out = ((y + bonus).reshape(B, T, RWKV_W) * g.astype(F32)).astype(x.dtype)
    return jnp.concatenate([gla_out, rwkv_out], -1) @ w_out

def dsa_mixer(x, w_in, w_out):
    B, T, _ = x.shape
    q, k, v, qi, ki, wi = _split(x @ w_in, ODD_SPLITS)
    q = q.reshape(B, T, ATT_HEADS, ATT_HEAD)
    qi = qi.reshape(B, T, IDX_HEADS, IDX_DIM)
    cos_a, sin_a = rope_tables(T, ATT_HEAD)
    cos_i, sin_i = rope_tables(T, IDX_DIM)
    q = apply_rope(q, cos_a[:, None], sin_a[:, None])
    k = apply_rope(k, cos_a, sin_a)
    qi = apply_rope(qi, cos_i[:, None], sin_i[:, None])
    ki = apply_rope(ki, cos_i, sin_i)
    wi = wi.astype(F32) * (IDX_HEADS ** -0.5 * IDX_DIM ** -0.5)
    n_sel = min(TOPK_MAX, T // 4)
    key_pos = jnp.arange(T)
    gather = jax.vmap(lambda tab, ids: tab[ids])

    def block(start):
        qb = lax.dynamic_slice_in_dim(q, start, Q_BLOCK, axis=1)
        qib = lax.dynamic_slice_in_dim(qi, start, Q_BLOCK, axis=1)
        wib = lax.dynamic_slice_in_dim(wi, start, Q_BLOCK, axis=1)
        q_pos = start + jnp.arange(Q_BLOCK)
        s = jax.nn.relu(jnp.einsum('bqhd,bsd->bqhs', qib, ki).astype(F32))
        score = jnp.einsum('bqh,bqhs->bqs', wib, s)
        score = jnp.where(key_pos[None, None, :] <= q_pos[None, :, None], score, NEG)
        _, sel = lax.top_k(score, n_sel)
        valid = sel <= q_pos[None, :, None]
        ks, vs = gather(k, sel), gather(v, sel)
        logit = jnp.einsum('bqhd,bqkd->bqhk', qb, ks).astype(F32) * ATT_HEAD ** -0.5
        logit = jnp.where(valid[:, :, None, :], logit, NEG)
        pr = jax.nn.softmax(logit, axis=-1).astype(vs.dtype)
        return jnp.einsum('bqhk,bqkd->bqhd', pr, vs)

    starts = jnp.arange(T // Q_BLOCK, dtype=jnp.int32) * Q_BLOCK
    o = lax.map(block, starts)
    o = jnp.moveaxis(o, 0, 1).reshape(B, T, ATT_HEADS * ATT_HEAD)
    return o @ w_out

def peer_ffn(x, w_q, sub_keys, exp_u, exp_v):
    B, T, D = x.shape
    q = (x @ w_q).reshape(B, T, PEER_HEADS, 2, PEER_DKEY // 2)
    s = jnp.einsum('bthcd,hcnd->bthcn', q, sub_keys).astype(F32)
    top_s, top_i = lax.top_k(s, PEER_TOPK)
    cand_s = (top_s[..., 0, :, None] + top_s[..., 1, None, :]).reshape(B, T, PEER_HEADS, -1)
    cand_i = (top_i[..., 0, :, None] * PEER_NKEYS + top_i[..., 1, None, :]).reshape(B, T, PEER_HEADS, -1)
    best_s, pos = lax.top_k(cand_s, PEER_TOPK)
    idx = jnp.take_along_axis(cand_i, pos, axis=-1)
    gate = jax.nn.softmax(best_s, axis=-1)
    nb = (B * T) // PEER_TOKEN_BLOCK
    hk = PEER_HEADS * PEER_TOPK
    xs = (x.reshape(nb, PEER_TOKEN_BLOCK, D), idx.reshape(nb, PEER_TOKEN_BLOCK, hk),
          gate.reshape(nb, PEER_TOKEN_BLOCK, hk))

    def block(args):
        xb, ib, gb = args
        h = jax.nn.gelu(jnp.einsum('md,mkd->mk', xb, exp_u[ib]).astype(F32), approximate=False)
        coef = (gb * h).astype(xb.dtype)
        return jnp.einsum('mk,mkd->md', coef, exp_v[ib])

    return lax.map(block, xs).reshape(B, T, D)

def second_inputs(seed: int = 0) -> dict:
    key = jax.random.key(seed)
    ks = iter(jax.random.split(key, 32))

    def nrm(shape, scale):
        return jax.random.normal(next(ks), shape, F32) * scale

    E, O, L, D = N_EVEN, N_ODD, DEPTH, D_MODEL
    return {
        'x': nrm((BATCH, SEQ, D), 1.0),
        'even_w_in': nrm((E, D, EVEN_IN), D ** -0.5),
        'gla_a_w2': nrm((E, GLA_LORA, GLA_KW), GLA_LORA ** -0.5),
        'gla_a_b': nrm((E, GLA_KW), 0.1),
        'gla_norm_g': 1.0 + nrm((E, GLA_DV), 0.05),
        'rwkv_mu': jax.random.uniform(next(ks), (E, RWKV_IN), F32, 0.0, 1.0),
        'rwkv_w0': jax.random.uniform(next(ks), (E, RWKV_W), F32, -6.5, -1.5),
        'rwkv_w2': nrm((E, RWKV_W_LORA, RWKV_W), 0.1 * RWKV_W_LORA ** -0.5),
        'rwkv_a0': nrm((E, RWKV_W), 0.1),
        'rwkv_a2': nrm((E, RWKV_A_LORA, RWKV_W), 0.5 * RWKV_A_LORA ** -0.5),
        'rwkv_g2': nrm((E, RWKV_G_LORA, RWKV_W), 2.0 * RWKV_G_LORA ** -0.5),
        'rwkv_k_k': 0.85 + nrm((E, RWKV_W), 0.05),
        'rwkv_k_a': 1.0 + nrm((E, RWKV_W), 0.05),
        'rwkv_r_k': nrm((E, RWKV_HEADS, RWKV_HEAD), 0.1),
        'rwkv_lnx_g': 1.0 + nrm((E, RWKV_W), 0.05),
        'rwkv_lnx_b': nrm((E, RWKV_W), 0.02),
        'even_w_out': nrm((E, D, D), DN_BETA * D ** -0.5),
        'odd_w_in': nrm((O, D, ODD_IN), D ** -0.5),
        'odd_w_out': nrm((O, D, D), DN_BETA * D ** -0.5),
        'mix_ln_g': 1.0 + nrm((L, D), 0.05),
        'mix_ln_b': nrm((L, D), 0.02),
        'peer_w_q': nrm((L, D, PEER_HEADS * PEER_DKEY), D ** -0.5),
        'peer_sub_keys': nrm((L, PEER_HEADS, 2, PEER_NKEYS, PEER_DKEY // 2), (PEER_DKEY // 2) ** -0.5),
        'peer_u': nrm((L, PEER_N_EXPERTS, D), D ** -0.5),
        'peer_v': nrm((L, PEER_N_EXPERTS, D), DN_BETA * PEER_HEADS ** -0.5),
        'ffn_ln_g': 1.0 + nrm((L, D), 0.05),
        'ffn_ln_b': nrm((L, D), 0.02),
    }

def second_block(x, even_w_in, gla_a_w2, gla_a_b, gla_norm_g, rwkv_mu, rwkv_w0, rwkv_w2, rwkv_a0, rwkv_a2,
              rwkv_g2, rwkv_k_k, rwkv_k_a, rwkv_r_k, rwkv_lnx_g, rwkv_lnx_b, even_w_out, odd_w_in,
              odd_w_out, mix_ln_g, mix_ln_b, peer_w_q, peer_sub_keys, peer_u, peer_v, ffn_ln_g, ffn_ln_b):
    for layer in range(DEPTH):
        i = layer // 2
        if layer % 2 == 0:
            mix = even_mixer(x, even_w_in[i], gla_a_w2[i], gla_a_b[i], gla_norm_g[i], rwkv_mu[i], rwkv_w0[i],
                             rwkv_w2[i], rwkv_a0[i], rwkv_a2[i], rwkv_g2[i], rwkv_k_k[i], rwkv_k_a[i],
                             rwkv_r_k[i], rwkv_lnx_g[i], rwkv_lnx_b[i], even_w_out[i])
        else:
            mix = dsa_mixer(x, odd_w_in[i], odd_w_out[i])
        x = layer_norm(DN_ALPHA * x + mix, mix_ln_g[layer], mix_ln_b[layer])
        ffn = peer_ffn(x, peer_w_q[layer], peer_sub_keys[layer], peer_u[layer], peer_v[layer])
        x = layer_norm(DN_ALPHA * x + ffn, ffn_ln_g[layer], ffn_ln_b[layer])
    return x


def setup_inputs(seed=0):
    out = dict(first_inputs(seed))
    for name, value in second_inputs(seed + 1).items():
        if name != "x":
            out[name + "_2"] = value
    return out


def reference(
    x, p, norm1_g, w_in, b_in, conv_w, conv_b, m_norm_g, r_norm_g, w_bm, w_br, w_out, norm2_g,
    w_ff1, b_ff1, w_ff2, b_ff2, norm3_g, w_pe_gate, w_pe, final_g, even_w_in_2, gla_a_w2_2,
    gla_a_b_2, gla_norm_g_2, rwkv_mu_2, rwkv_w0_2, rwkv_w2_2, rwkv_a0_2, rwkv_a2_2, rwkv_g2_2,
    rwkv_k_k_2, rwkv_k_a_2, rwkv_r_k_2, rwkv_lnx_g_2, rwkv_lnx_b_2, even_w_out_2, odd_w_in_2,
    odd_w_out_2, mix_ln_g_2, mix_ln_b_2, peer_w_q_2, peer_sub_keys_2, peer_u_2, peer_v_2,
    ffn_ln_g_2, ffn_ln_b_2,
):
    x = first_block(
        x, p, norm1_g, w_in, b_in, conv_w, conv_b, m_norm_g, r_norm_g, w_bm, w_br, w_out,
        norm2_g, w_ff1, b_ff1, w_ff2, b_ff2, norm3_g, w_pe_gate, w_pe, final_g,
    )
    return second_block(
        x, even_w_in_2, gla_a_w2_2, gla_a_b_2, gla_norm_g_2, rwkv_mu_2, rwkv_w0_2, rwkv_w2_2,
        rwkv_a0_2, rwkv_a2_2, rwkv_g2_2, rwkv_k_k_2, rwkv_k_a_2, rwkv_r_k_2, rwkv_lnx_g_2,
        rwkv_lnx_b_2, even_w_out_2, odd_w_in_2, odd_w_out_2, mix_ln_g_2, mix_ln_b_2, peer_w_q_2,
        peer_sub_keys_2, peer_u_2, peer_v_2, ffn_ln_g_2, ffn_ln_b_2,
    )


_drawn_inputs = setup_inputs


def setup_inputs(seed=0):
    import zlib

    import numpy as np

    out = dict(_drawn_inputs(seed))
    spreads = {}
    factors = {'conv_b': 5.812,
     'norm3_g': 3.933,
     'gla_a_b_2': 4.439,
     'gla_norm_g_2': 4.668,
     'rwkv_w2_2': 8.0,
     'rwkv_a0_2': 3.334,
     'rwkv_lnx_g_2': 2.856,
     'rwkv_lnx_b_2': 5.013}
    for name, (base, spread) in spreads.items():
        noise = np.random.default_rng([zlib.crc32(name.encode()), seed]).standard_normal(out[name].shape)
        drawn = base * np.exp(spread * noise) if base else spread * noise
        out[name] = __import__('jax').numpy.asarray(drawn.astype(out[name].dtype))
    for name, factor in factors.items():
        out[name] = (out[name] * factor).astype(out[name].dtype)
    return out
```

```python
from contextlib import ExitStack

import numpy as np
import concourse.bass as bass
from concourse import mybir

F32 = mybir.dt.float32
F32R = mybir.dt.float32r
U32 = mybir.dt.uint32
ALU = mybir.AluOpType
ACT = mybir.ActivationFunctionType
AXX = mybir.AxisListType.X

P = 128
D = 1024
S = 256
TT = S // P
KD = D // P
LAYERS = 2
CW = 512
KB = 4
TW = KB * CW
RAW = 4
SPLIT = 2
EPS = 1e-6
HEADS = 4
MDV = 256
RDV = 512
NEG = 1e30

ORDER_A = [("mqk", 4, 2), ("mv", 2, 2), ("mo", 2, 2), ("gm", 2, 2), ("bm", 2, 2), ("rqk", 4, 2), ("rv", 4, 2),
           ("rg", 4, 2), ("gr", 2, 2), ("br", 2, 4), ("out", 2, 2), ("ffa1", 4, 2), ("ffa2", 2, 4),
           ("ffb1", 4, 2), ("ffb2", 2, 4), ("peg", 2, 2)]
CHUNK, TILE = {}, {}
_c = _t = 0
for _name, _n, _per in ORDER_A:
    for _i in range(_n):
        CHUNK[_name, _i] = _c
        TILE[_name, _i] = _t
        _c, _t = _c + 1, _t + _per
CHUNKS_A, TILES_A = _c, _t
PER_CHUNK = {_name: _per for _name, _n, _per in ORDER_A}
assert CHUNKS_A % 2 == 0 and TILES_A % RAW == 0

BY_ACT = ("mqk", "rqk", "ffa1", "ffb1")
TAKEN = []
for _name, _n, _ in ORDER_A:
    for _i in range(_n):
        TAKEN.append((_name in BY_ACT, 1 + sum(a == (_name in BY_ACT) for a, _ in TAKEN)))

ROW_OF = {}
ROW_CHUNK = []
for _name, _n, _gains in (("mv", 2, 0), ("mo", 2, 1), ("gm", 2, 0), ("rv", 4, 0), ("rg", 4, 1), ("gr", 2, 0), ("ffb2", 2, 0)):
    for _i in range(_n):
        ROW_OF[_name, _i] = len(ROW_CHUNK)
        ROW_CHUNK += [CHUNK[_name, _i]] * (1 + _gains)
ROWS_A = len(ROW_CHUNK)
RROW = 4
assert ROWS_A % RROW == 0

COL = {}
_c = 0
for _name, _n in (("norm1", 8), ("norm2", 8), ("norm3", 8), ("bmqk", 16), ("brqk", 16), ("convw", 64), ("convb", 16),
                  ("bff1", 32), ("gatew", 64)):
    COL[_name] = _c
    _c += _n
COLS_A = _c

T_H, T_YM, T_YR, T_MG, T_H2, T_H3, T_ALL = 0, 4, 8, 16, 20, 24, 28

CONST_A = {}
_c = 0
for _name, _n in (("cum", P), ("ones", P), ("mask", P), ("decay", HEADS * 384), ("cos", S), ("sin", S), ("headsel", HEADS * P),
                  ("eps", 1), ("one", 1)):
    CONST_A[_name] = (_c, _n)
    _c += _n
CONSTS_A = _c
CHUNK_T = 64
LEVELS = 6
CONST_B = {}
_c = 0
for _name, _n in (("same_head", P), ("strict_upto", 2 * P), ("diag2", 2 * P), ("levels", LEVELS * P), ("keep", S), ("half", 2),
                  ("iota", P), ("causal", TT * S), ("cos128", TT * 64), ("sin128", TT * 64), ("cos64", TT * 32), ("sin64", TT * 32),
                  ("ln_eps", 1), ("lnx_eps", 1), ("one", 1)):
    CONST_B[_name] = (_c, _n)
    _c += _n
CONSTS_B = _c

B0 = LAYERS * TILES_A
EVEN, EVEN_OUT, ODD, ODD_OUT = 0, 12, 148, 156
PEER_Q, PEER_UV = (16, 160), (20, 164)
TILES_B = 292
ALPHA = (2 * LAYERS) ** 0.25
LN_EPS, LNX_EPS = 1e-5, 64e-5
GH, GDK, GDV = 4, 64, 128
RH, RN = 8, 64
EW = 512
AH, AD = 8, 128
IH, ID = 8, 64
SELECT = 64
KEYS, PH, PK = 128, 8, 16
JH = KEYS // 2
PAIRS = JH // 2
GT = 4
HOT = 4
GROUPS = S // GT

ECOL = {}
_c = 0
for _name, _n in (("mu_side", 2), ("mu", 12), ("gla_a_b", 2), ("w0", 4), ("a0", 4), ("k_k", 4), ("k_a", 4), ("r_k", 4)):
    ECOL[_name] = _c
    _c += _n
ECOLS = _c

ORDER_B = [("gqk", EVEN, 1, "act"), ("gv", EVEN + 2, 1, "act"), ("gg", EVEN + 4, 1, "act"), ("r", EVEN + 6, 1, "act"),
           ("k", EVEN + 8, 1, "act"), ("v", EVEN + 10, 1, "act"), ("eout", EVEN_OUT, 2, "dve"), ("pq0", PEER_Q[0], 2, "act"),
           ("oq", ODD, 2, "dve"), ("oqi", ODD + 4, 1, "dve"), ("okv", ODD + 6, 1, "dve"), ("oout", ODD_OUT, 2, "dve"),
           ("pq1", PEER_Q[1], 2, "act")]
CHUNK_B, TILE_B, READ_B = {}, {}, []
for _name, _t, _n, _by in ORDER_B:
    for _i in range(_n):
        CHUNK_B[_name, _i] = len(READ_B)
        TILE_B[_name, _i] = _t + 2 * _i
        READ_B.append((_by, 1 + sum(b == _by for b, _ in READ_B)))

LORA = 1024
G2, W2 = (slice(0, 96), slice(0, EW)), (slice(96, 128), slice(0, EW))
GA2, A2 = (slice(0, 32), slice(EW, EW + 256)), (slice(32, 64), slice(EW, 2 * EW))
EROW = {"gla_g": slice(0, GDV), "lnx_g": slice(GDV, GDV + EW), "lnx_b": slice(GDV + EW, GDV + 2 * EW)}
EROWS = GDV + 2 * EW
HALVES = tuple(slice(t * P, (t + 1) * P) for t in range(TT))
FT = EW // P
GP = GH // 2
CH = P // CHUNK_T


def steps(*names):
    return {name: i + 1 for i, name in enumerate(names)}


EVEN_PE = steps("side", "la", "w", "a", "g", "scores", "keys", "kv", "o")
EVEN_ACT = steps("side", "gates", "lnexp", "w", "a", "decays", "keys", "square", "std")
EVEN_DVE = steps("side", "la", "cumsum", "decayed", "scores", "states", "gla")
RW_PE = steps("bonus", "kk", "nat0", "nat1", "nat2", "nat3", "lb", "lk", "x0", "d0", "x1", "d1", "x2", "d2", "x3", "d3", "x4", "d4",
              "x5", "d5", "z", "wv", "ta", "u0", "s0", "u1", "s1", "y")
RW_ACT = steps("decays", "norm", "nat0", "nat1", "nat2", "nat3", "ta", "std")
RW_DVE = steps("cumsum", "square", "bonus", "tilde", "lb", "lk", "x0", "d0", "x1", "d1", "x2", "d2", "x3", "d3", "x4", "d4", "x5", "d5",
               "z", "wv", "u0", "s0", "u1", "s1", "stats", "out")
ODD_PE = steps("qt", "it", "index0", "index1", "logits0", "pt0", "o0", "logits1", "pt1", "o1")
ODD_ACT = steps("qt", "it", "index0", "index1", "exp0", "pt0", "exp1", "pt1")
ODD_DVE = steps("rope", "kib", "index0", "index1", "logits0", "probs0", "logits1", "probs1")


class Order:

    def __init__(self, eng, own):
        self.eng, self.own, self.count = eng, own, {}

    def __call__(self, ins, signal=None):
        s = self.own if signal is None else signal
        self.count[s] = self.count.get(s, 0) + 1
        ins.then_inc(s, 1)
        self.eng.wait_ge(s, self.count[s])

    def also(self, ins):
        self.count[self.own] = self.count.get(self.own, 0) + 1
        ins.then_inc(self.own, 1)

    def settle(self):
        self.eng.wait_ge(self.own, self.count[self.own])


class Common:

    def __init__(self, nc, ctx, weights):
        def sb(name, shape, dt=F32):
            return ctx.enter_context(nc.sbuf_tensor(name, shape, dt))

        def sem(name):
            return ctx.enter_context(nc.semaphore(name))

        self.weights = weights
        self.raw = sb("raw", [P, RAW, TW])
        self.w_hi = sb("w_hi", [P, SPLIT, TW], F32R)
        self.w_lo = sb("w_lo", [P, SPLIT, TW], F32R)
        self.x = sb("x", [P, TT, D])
        self.act_hi = sb("act_hi", [P, KD, S], F32R)
        self.act_lo = sb("act_lo", [P, KD, S], F32R)
        self.ident_sb = sb("ident_sb", [P, P])
        self.ident = self.ident_sb[:, :]
        self.psum = [ctx.enter_context(nc.psum_tensor(f"bank{b}", [P, CW], F32)) for b in range(8)]
        self.raw_loaded = [sem(f"raw_loaded{r}") for r in range(RAW)]
        self.hi_ready = sem("hi_ready")
        self.lo_ready = sem("lo_ready")
        self.tile_used = sem("tile_used")
        self.x_ready = sem("x_ready")
        self.out_stored = sem("out_stored")


def first_block(nc, ctx, m, x_in, rows, cols, bgate, p_t, w_pe, final_row, identity, consts_a):
    raw, w_hi, w_lo, x, act_hi, act_lo, ident, psum = m.raw, m.w_hi, m.w_lo, m.x, m.act_hi, m.act_lo, m.ident, m.psum
    raw_loaded, hi_ready, lo_ready, tile_used, x_ready = m.raw_loaded, m.hi_ready, m.lo_ready, m.tile_used, m.x_ready

    def sb(name, shape, dt=F32, stack=ctx):
        return stack.enter_context(nc.sbuf_tensor(name, shape, dt))

    def sem(name):
        return ctx.enter_context(nc.semaphore(name))

    memory = ExitStack()
    const_a = sb("const_a", [P, CONSTS_A], F32, memory)

    def cst(name):
        first, n = CONST_A[name]
        return const_a[:, first:first + n]

    eps = cst("eps")
    attention = memory.enter_context(ExitStack())
    qk_t = sb("qk_t", [P, 16, S], F32, attention)
    val = sb("val", [P, TT, HEADS * (RDV + 2)], F32, attention)
    attention.close()
    mix_hi = sb("mix_hi", [P, 16, S], F32R, memory)
    mix_lo = sb("mix_lo", [P, 16, S], F32R, memory)
    pad = sb("pad", [P, 64], F32, memory)
    y = sb("y", [P, TT, HEADS * RDV], F32, memory)
    merged = sb("merged", [P, TT, D], F32, memory)
    gate = sb("gate", [P, TT, D], F32, memory)
    row = sb("row", [P, RROW, CW], F32, memory)
    col = sb("col", [P, COLS_A], F32, memory)
    bgate_row = sb("bgate_row", [P, 8], F32, memory)
    shifted = sb("shifted", [P, 4, S + 3], F32, memory)
    conv = sb("conv", [P, 4, S], F32, memory)
    pre = sb("pre", [P, TT, CW], F32, memory)
    decayed = sb("decayed", [P, HEADS, 3, P], F32, memory)
    weighed = sb("weighed", [P, 2, 3 * P], F32, memory)
    junk = sb("junk", [P, D], F32, memory)
    gw_hi = sb("gw_hi", [P, KD, 8], F32R, memory)
    gw_lo = sb("gw_lo", [P, KD, 8], F32R, memory)
    gz = sb("gz", [P, TT, 8], F32, memory)
    gl = sb("gl", [P, 4, TT, HEADS], F32, memory)
    gi = sb("gi", [P, TT, HEADS], F32, memory)
    grow = sb("grow", [HEADS, S], F32, memory)
    mrow = sb("mrow", [HEADS, S], F32, memory)
    floor = sb("floor", [P, TT, HEADS], F32, memory)
    ssq = sb("ssq", [P, TT], F32, memory)
    rstd = sb("rstd", [P, TT], F32, memory)
    st6 = sb("st6", [P, 6], F32, memory)
    stats = sb("stats", [P, TT, HEADS, 2], F32, memory)
    hstd = sb("hstd", [P, TT, HEADS], F32, memory)
    den = sb("den", [P, 2], F32, memory)
    wpe_sb = y[:, :, :].rearrange("p t n -> p (t n)")[:, 0:2 * D].rearrange("p (k n) -> p k n", k=2)
    pt_sb = y[:, :, :].rearrange("p t n -> p (t n)")[:, 2 * D:2 * D + 2 * S].rearrange("p (k n) -> p k n", k=2)
    val_m = val[:, :, 0:HEADS * (MDV + 1)].rearrange("p t (h n) -> p t h n", h=HEADS)
    val_r = val[:, :, 0:HEADS * RDV]

    const_loaded = sem("const_loaded")
    x_loaded = sem("x_loaded")
    layer_left = sem("layer_left")
    layer_open = sem("layer_open")
    cleared = sem("cleared")
    final_loaded = sem("final_loaded")
    final_std = sem("final_std")
    col_loaded = sem("col_loaded")
    row_loaded = [sem(f"row_loaded{r}") for r in range(RROW)]
    pe_loaded = sem("pe_loaded")

    per_layer = []

    def lsem(name):
        per_layer.append(sem(name))
        return per_layer[-1]

    act_step = lsem("act_step")
    dve_step = lsem("dve_step")
    read_act = lsem("read_act")
    read_dve = lsem("read_dve")
    std_ready = lsem("std_ready")
    xn_ready = lsem("xn_ready")
    trans_done = lsem("trans_done")
    t_hi = lsem("t_hi")
    t_lo = lsem("t_lo")
    gw_split = lsem("gw_split")
    gate_mm = lsem("gate_mm")
    gz_ready = lsem("gz_ready")
    lnf_ready = lsem("lnf_ready")
    lf_ready = lsem("lf_ready")
    gi_ready = lsem("gi_ready")
    m_ready = lsem("m_ready")
    fm_ready = lsem("fm_ready")
    mmask_ready = lsem("mmask_ready")
    decay_ready = lsem("decay_ready")
    floor_ready = lsem("floor_ready")
    conv_done = lsem("conv_done")
    mqk_ready = lsem("mqk_ready")
    rqk_ready = lsem("rqk_ready")
    score_done = lsem("score_done")
    weighed_ready = lsem("weighed_ready")
    y_done = lsem("y_done")
    my_read = lsem("my_read")
    ry_read = lsem("ry_read")
    stats_ready = lsem("stats_ready")
    hstd_ready = lsem("hstd_ready")
    gated = lsem("gated")
    y_ready = lsem("y_ready")
    merged_ready = lsem("merged_ready")
    relu_ready = lsem("relu_ready")
    sq_ready = lsem("sq_ready")
    ff_hi = lsem("ff_hi")
    ff_lo = lsem("ff_lo")
    pe_mm = lsem("pe_mm")

    def wait_read(eng, c):
        by_act, count = TAKEN[c]
        eng.wait_ge(read_act if by_act else read_dve, count)

    with nc.Block() as block:

        @block.sync
        def _(sp):
            for r in range(RAW):
                sp.dma_start(raw[:, r, :], m.weights[r]).then_inc(raw_loaded[r], 16)
            with sp.Fori(1, LAYERS * TILES_A // RAW + 1) as n:
                for r in range(RAW):
                    sp.wait_ge(lo_ready, n * RAW + (r - RAW + 1))
                    sp.dma_start(raw[:, r, :], m.weights[n * RAW + r]).then_inc(raw_loaded[r], 16)

        @block.gpsimd
        def _(pool):
            pool.dma_start(ident, identity).then_inc(const_loaded, 16)
            pool.dma_start(const_a[:, :], consts_a).then_inc(const_loaded, 16)
            pool.dma_start(x[:, :, :], x_in).then_inc(x_loaded, 16)
            with pool.Fori(0, LAYERS) as layer:
                pool.dma_start(col[:, :], cols[layer]).then_inc(col_loaded, 16)
                pool.dma_start(bgate_row[:, :], bgate[layer].partition_broadcast(P)).then_inc(col_loaded, 16)
                for r in range(ROWS_A):
                    if r >= RROW:
                        wait_read(pool, ROW_CHUNK[r - RROW])
                    if r == ROW_OF["ffb2", 0]:
                        pool.wait_ge(t_lo, T_MG)
                        pool.dma_start(wpe_sb, w_pe[layer]).then_inc(pe_loaded, 16)
                        pool.dma_start(pt_sb, p_t[layer]).then_inc(pe_loaded, 16)
                    pool.dma_start(row[:, r % RROW, :], rows[layer, r].partition_broadcast(P)).then_inc(row_loaded[r % RROW], 16)
                pool.wait_ge(layer_left, layer * 3 + 3)
                pool.sem_inc(cleared, 1)
                for s in per_layer:
                    pool.sem_clear(s)
                pool.sem_inc(layer_open, 1)
            pool.dma_start(row[:, 0:2, :].rearrange("p a n -> p (a n)"), final_row.partition_broadcast(P)).then_inc(final_loaded, 16)

        def row_slot(name, i, k=0):
            r = ROW_OF[name, i] + k
            return row[:, r % RROW, :], row_loaded[r % RROW], 16 * (r // RROW + 1)

        @block.tensor
        def _(pe):
            def mm3(dst, lh, ll, rh, rl, first, last):
                nc.tensor.matmul(dst, lh, rh, start=first, stop=False)
                nc.tensor.matmul(dst, lh, rl, start=False, stop=False)
                return nc.tensor.matmul(dst, ll, rh, start=False, stop=last)

            def natural(base, k0, c, per, hi, lo):
                for j in range(per):
                    k = k0 + j
                    pe.wait_ge(lo_ready, base + (k + 1))
                    for kk in range(KB):
                        ki = j * KB + kk
                        for t in range(TT):
                            ts = slice(t * P, (t + 1) * P)
                            ws = slice(kk * CW, (kk + 1) * CW)
                            last = mm3(psum[2 * (c % 2) + t][:, :], hi[:, ki, ts], lo[:, ki, ts], w_hi[:, k % SPLIT, ws],
                                       w_lo[:, k % SPLIT, ws], ki == 0, ki == per * KB - 1)
                    last.then_inc(tile_used, 1)

            def featured(base, k0, c, hi, lo):
                for j in range(2):
                    k = k0 + j
                    pe.wait_ge(lo_ready, base + (k + 1))
                    for f in range(4):
                        for kk in range(KB):
                            ki = j * KB + kk
                            ws = slice(kk * CW + f * P, kk * CW + (f + 1) * P)
                            dst = psum[2 * (c % 2) + f // 2][:, (f % 2) * S:(f % 2 + 1) * S]
                            wh, wl = w_hi[:, k % SPLIT, ws], w_lo[:, k % SPLIT, ws]
                            nc.tensor.matmul(dst, wh, hi[:, ki, :], start=ki == 0 and f % 2 == 0, stop=False)
                            nc.tensor.matmul(dst, wh, lo[:, ki, :], start=False, stop=False)
                            last = nc.tensor.matmul(dst, wl, hi[:, ki, :], start=False, stop=ki == KD - 1 and f % 2 == 1)
                    last.then_inc(tile_used, 1)

            def transposes(src, blocks):
                for b in range(blocks // 2):
                    for k in (2 * b, 2 * b + 1):
                        for t in range(TT):
                            last = nc.tensor.transpose(psum[4 + b][:, (k % 2) * S + t * P:(k % 2) * S + (t + 1) * P],
                                                       src(k, t), ident)
                    last.then_inc(trans_done, 1)

            pe.wait_ge(const_loaded, 32)
            with pe.Fori(0, LAYERS) as layer:
                base = layer * TILES_A

                def bank_free(c):
                    if c >= 2:
                        wait_read(pe, c - 2)

                def nat(name, i, hi, lo):
                    bank_free(CHUNK[name, i])
                    natural(base, TILE[name, i], CHUNK[name, i], PER_CHUNK[name], hi, lo)

                def feat(name, i, hi, lo):
                    bank_free(CHUNK[name, i])
                    featured(base, TILE[name, i], CHUNK[name, i], hi, lo)

                def normed(i):
                    pe.wait_ge(xn_ready, 2 * (i + 1))
                    transposes(lambda k, t: gate[:, t, k * P:(k + 1) * P], KD)

                normed(0)
                pe.wait_ge(t_lo, T_YM)
                pe.wait_ge(gw_split, 2)
                for t in range(TT):
                    for k in range(KD):
                        ts = slice(t * P, (t + 1) * P)
                        last = mm3(psum[6][:, t * 8:t * 8 + 8], act_hi[:, k, ts], act_lo[:, k, ts], gw_hi[:, k, :],
                                   gw_lo[:, k, :], k == 0, k == KD - 1)
                last.then_inc(gate_mm, 1)
                feat("mqk", 0, act_hi, act_lo)
                pe.wait_ge(lf_ready, 1)
                lf = gl[:, 2, :, :]
                nc.tensor.matmul(psum[7][:, 0:HEADS], cst("cum"), lf[:, 0, :], start=True, stop=True)
                nc.tensor.matmul(psum[7][:, HEADS:2 * HEADS], cst("ones"), lf[:, 0, :], start=True, stop=False)
                nc.tensor.matmul(psum[7][:, HEADS:2 * HEADS], cst("cum"), lf[:, 1, :], start=False, stop=True).then_inc(gate_mm, 1)
                feat("mqk", 1, act_hi, act_lo)
                pe.wait_ge(gi_ready, 1)
                for t in range(TT):
                    last = nc.tensor.transpose(psum[6][0:HEADS, t * P:(t + 1) * P], gi[:, t, :], ident)
                last.then_inc(gate_mm, 1)
                feat("mqk", 2, act_hi, act_lo)
                pe.wait_ge(m_ready, 1)
                for t in range(TT):
                    last = nc.tensor.transpose(psum[7][:, 8 + t * HEADS:8 + (t + 1) * HEADS], mrow[:, t * P:(t + 1) * P],
                                               ident[0:HEADS, 0:HEADS])
                last.then_inc(gate_mm, 1)
                for h in range(HEADS):
                    sel = cst("headsel")[0:HEADS, h * P:(h + 1) * P]
                    last = nc.tensor.matmul(psum[4 + h // 2][:, (h % 2) * S:(h % 2 + 1) * S], sel, mrow[:, :], start=True, stop=True)
                last.then_inc(gate_mm, 1)
                feat("mqk", 3, act_hi, act_lo)
                nat("mv", 0, act_hi, act_lo)
                nat("mv", 1, act_hi, act_lo)

                def attend(h0, width, values, qk_ready, v_chunk, y_read):
                    def outputs(h):
                        pe.wait_ge(weighed_ready, h0 + h + 1)
                        if h >= 1:
                            pe.wait_ge(y_read, h)
                        if h == 0:
                            wait_read(pe, v_chunk)
                        w = weighed[:, h % 2, :]
                        nc.tensor.matmul(psum[6][:, 0:width], w[:, 0:P], values(0, h), start=True, stop=True)
                        nc.tensor.matmul(psum[7][:, 0:width], w[:, P:2 * P], values(0, h), start=True, stop=False)
                        nc.tensor.matmul(psum[7][:, 0:width], w[:, 2 * P:3 * P], values(1, h), start=False, stop=True).then_inc(y_done, 1)

                    pe.wait_ge(qk_ready, 4)
                    for h in range(HEADS):
                        if h >= 2:
                            pe.wait_ge(weighed_ready, h0 + h - 1)
                        bank = psum[4 + h % 2]
                        for d in range(2):
                            nc.tensor.matmul(bank[:, 0:S], qk_t[:, 8 + 2 * h + d, 0:P], qk_t[:, 2 * h + d, :], start=d == 0, stop=d == 1)
                        for d in range(2):
                            last = nc.tensor.matmul(bank[:, S:S + P], qk_t[:, 8 + 2 * h + d, P:S], qk_t[:, 2 * h + d, P:S],
                                                    start=d == 0, stop=d == 1)
                        last.then_inc(score_done, 1)
                        if h >= 1:
                            outputs(h - 1)
                    outputs(HEADS - 1)

                pe.wait_ge(mmask_ready, HEADS)
                attend(0, MDV + 1, lambda t, h: val_m[:, t, h, :], mqk_ready, CHUNK["mv", 1], my_read)
                nat("mo", 0, act_hi, act_lo)
                nat("mo", 1, act_hi, act_lo)
                pe.wait_ge(y_ready, 2)
                transposes(lambda k, t: y[:, t, k * P:(k + 1) * P], KD)
                nat("gm", 0, act_hi, act_lo)
                nat("gm", 1, act_hi, act_lo)
                pe.wait_ge(t_lo, T_YR)
                nat("bm", 0, mix_hi, mix_lo)
                nat("bm", 1, mix_hi, mix_lo)
                for i in range(4):
                    feat("rqk", i, act_hi, act_lo)
                for i in range(4):
                    nat("rv", i, act_hi, act_lo)
                attend(HEADS, RDV, lambda t, h: val_r[:, t, h * RDV:(h + 1) * RDV], rqk_ready, CHUNK["rv", 3], ry_read)
                for i in range(4):
                    nat("rg", i, act_hi, act_lo)
                pe.wait_ge(y_ready, 6)
                transposes(lambda k, t: y[:, t, k * P:(k + 1) * P], KD)
                nat("gr", 0, act_hi, act_lo)
                nat("gr", 1, act_hi, act_lo)
                pe.wait_ge(t_lo, T_YR + 4)
                transposes(lambda k, t: y[:, t, D + k * P:D + (k + 1) * P], KD)
                pe.wait_ge(t_lo, T_MG)
                nat("br", 0, mix_hi, mix_lo)
                nat("br", 1, mix_hi, mix_lo)
                pe.wait_ge(merged_ready, 2)
                transposes(lambda k, t: merged[:, t, k * P:(k + 1) * P], KD)
                pe.wait_ge(t_lo, T_H2)
                nat("out", 0, mix_hi, mix_lo)
                nat("out", 1, mix_hi, mix_lo)
                normed(1)
                pe.wait_ge(t_lo, T_H3)
                for half, (one, two) in enumerate((("ffa1", "ffa2"), ("ffb1", "ffb2"))):
                    for i in range(4):
                        feat(one, i, act_hi, act_lo)
                    pe.wait_ge(ff_lo, 4 * half + 4)
                    for i in range(2):
                        nat(two, i, mix_hi, mix_lo)
                normed(2)
                pe.wait_ge(t_lo, T_ALL)
                pe.wait_ge(pe_loaded, layer * 32 + 32)
                for i in range(2):
                    for t in range(TT):
                        for k in range(2):
                            last = nc.tensor.matmul(psum[4 + 2 * i + t][:, :], pt_sb[:, k, t * P:(t + 1) * P],
                                                    wpe_sb[:, k, i * CW:(i + 1) * CW], start=k == 0, stop=k == 1)
                last.then_inc(pe_mm, 1)
                nat("peg", 0, act_hi, act_lo)
                nat("peg", 1, act_hi, act_lo)
                wait_read(pe, CHUNKS_A - 1)
                pe.sem_inc(layer_left, 1)
                pe.wait_ge(layer_open, layer + 1)

        @block.scalar
        def _(act):
            def split_hi(base, k, free=True):
                act.wait_ge(raw_loaded[k % RAW], base * (16 // RAW) + 16 * (k // RAW + 1))
                if free:
                    act.wait_ge(tile_used, base + (k - 1))
                nc.scalar.activation(w_hi[:, k % SPLIT, :], raw[:, k % RAW, :], ACT.Copy).then_inc(hi_ready, 1)

            for k in range(SPLIT):
                split_hi(0, k, free=False)
            act.wait_ge(const_loaded, 32)
            act.wait_ge(x_loaded, 16)
            with act.Fori(0, LAYERS) as layer:
                base = layer * TILES_A
                do = Order(act, act_step)

                def stream(name, i):
                    for j in range(PER_CHUNK[name]):
                        split_hi(base, TILE[name, i] + j + SPLIT)

                def taken(name, i):
                    act.wait_ge(tile_used, base + (TILE[name, i] + PER_CHUNK[name]))

                def norm(i, c):
                    if c is not None:
                        wait_read(act, c)
                    for t in range(TT):
                        do(nc.scalar.activation(junk[:, :], x[:, t, :], ACT.Square, accum_out=ssq[:, t:t + 1]))
                    do(nc.scalar.activation(rstd[:, :], ssq[:, :], ACT.Sqrt, bias=eps, scale=1.0 / D), std_ready)
                    g0 = COL[f"norm{i + 1}"]
                    first = (T_H, T_H2, T_H3)[i]
                    for b in range(KD // 2):
                        act.wait_ge(trans_done, first + b + 1)
                        for k in (2 * b, 2 * b + 1):
                            ins = nc.scalar.activation(act_hi[:, k, :], psum[4 + b][:, (k % 2) * S:(k % 2 + 1) * S], ACT.Copy,
                                                       scale=col[:, g0 + k:g0 + k + 1])
                            do(ins, t_hi if k % 2 else None)

                def mixed(first, k0):
                    for b in range(KD // 2):
                        act.wait_ge(trans_done, first + b + 1)
                        do(nc.scalar.activation(mix_hi[:, k0 + 2 * b:k0 + 2 * b + 2, :].rearrange("p k s -> p (k s)"),
                                                psum[4 + b][:, :], ACT.Copy), t_hi)

                act.wait_ge(col_loaded, layer * 32 + 32)
                do(nc.scalar.activation(gw_hi[:, :, :].rearrange("p k n -> p (k n)"), col[:, COL["gatew"]:COL["gatew"] + 64], ACT.Copy), gw_split)
                norm(0, None)
                act.wait_ge(gz_ready, 1)
                do(nc.scalar.activation(gl[:, 0, :, :], gz[:, :, 4:8], ACT.Abs))
                do(nc.scalar.activation(gl[:, 0, :, :], gl[:, 0, :, :], ACT.Exp, scale=-1.0))
                do(nc.scalar.activation(gl[:, 1, :, :], gl[:, 0, :, :], ACT.Ln, bias=cst("one")), lnf_ready)

                def biased(name, i, bias):
                    taken(name, i)
                    for f in range(4):
                        n = bias + 4 * i + f
                        do(nc.scalar.activation(shifted[:, f, 3:], psum[2 * (CHUNK[name, i] % 2) + f // 2][:, (f % 2) * S:(f % 2 + 1) * S],
                                                ACT.Identity, bias=col[:, n:n + 1]), read_act if f == 3 else None)

                def silu(i):
                    act.wait_ge(conv_done, i + 1)
                    do(nc.scalar.activation(qk_t[:, 4 * i:4 * i + 4, :], conv[:, :, :], ACT.Silu), mqk_ready)

                for i in range(4):
                    stream("mqk", i)
                    if i >= 1:
                        act.wait_ge(conv_done, i)
                    biased("mqk", i, COL["bmqk"])
                    if i >= 1:
                        silu(i - 1)
                act.wait_ge(fm_ready, 1)
                do(nc.scalar.activation(floor[:, :, :], gl[:, 0, :, :], ACT.Exp, scale=-1.0), floor_ready)
                for h in range(HEADS):
                    act.wait_ge(mmask_ready, h + 1)
                    do(nc.scalar.activation(decayed[:, h, 0:2, :], decayed[:, h, 0:2, :], ACT.Exp, bias=gi[:, 0, h:h + 1], scale=-1.0))
                    do(nc.scalar.activation(decayed[:, h, 2, :], decayed[:, h, 2, :], ACT.Exp, bias=gi[:, 1, h:h + 1], scale=-1.0), decay_ready)
                stream("mv", 0)
                silu(3)
                stream("mv", 1)

                def head_std(n):
                    act.wait_ge(stats_ready, n)
                    do(nc.scalar.activation(hstd[:, :, :], stats[:, :, :, 1], ACT.Sqrt, bias=eps), hstd_ready)

                head_std(1)

                def gates(name, i, func, dst):
                    stream(name, i)
                    wait_read(act, CHUNK[name, i])
                    do(nc.scalar.activation(dst, pre[:, :, :], func), gated)

                for i in range(2):
                    gates("mo", i, ACT.Sigmoid, pre[:, :, :])
                mixed(T_YM, 0)
                for i in range(2):
                    gates("gm", i, ACT.Sigmoid, gate[:, :, i * CW:(i + 1) * CW])
                for i in range(2):
                    stream("bm", i)
                for i in range(4):
                    stream("rqk", i)
                    if i >= 1:
                        act.wait_ge(rqk_ready, i)
                    biased("rqk", i, COL["brqk"])
                for i in range(4):
                    stream("rv", i)
                for h in range(HEADS):
                    act.wait_ge(y_done, HEADS + h + 1)
                    for t in range(TT):
                        do(nc.scalar.activation(y[:, t, h * RDV:(h + 1) * RDV], psum[6 + t][:, :], ACT.Copy), ry_read if t == 1 else None)
                head_std(2)
                for i in range(4):
                    gates("rg", i, ACT.Silu, pre[:, :, :])
                mixed(T_YR, 0)
                for i in range(2):
                    gates("gr", i, ACT.Sigmoid, gate[:, :, i * CW:(i + 1) * CW])
                mixed(T_YR + 4, KD)
                for i in range(2):
                    stream("br", i)
                mixed(T_MG, 0)
                for i in range(2):
                    stream("out", i)
                norm(1, CHUNK["out", 1])
                for half, (one, two) in enumerate((("ffa1", "ffa2"), ("ffb1", "ffb2"))):
                    for i in range(4):
                        stream(one, i)
                        taken(one, i)
                        if 4 * half + i >= 1:
                            act.wait_ge(ff_lo, 4 * half + i)
                        for f in range(4):
                            n = COL["bff1"] + 16 * half + 4 * i + f
                            do(nc.scalar.activation(conv[:, f, :], psum[2 * (CHUNK[one, i] % 2) + f // 2][:, (f % 2) * S:(f % 2 + 1) * S],
                                                    ACT.Relu, bias=col[:, n:n + 1]), read_act if f == 3 else None)
                        act.wait_ge(sq_ready, 4 * half + i + 1)
                        do(nc.scalar.activation(mix_hi[:, 4 * i:4 * i + 4, :], conv[:, :, :], ACT.Copy), ff_hi)
                    for i in range(2):
                        stream(two, i)
                norm(2, CHUNK["ffb2", 1])
                for i in range(2):
                    stream("peg", i)
                    taken("peg", i)
                    c = CHUNK["peg", i]
                    for t in range(TT):
                        do(nc.scalar.activation(gate[:, t, i * CW:(i + 1) * CW], psum[2 * (c % 2) + t][:, :], ACT.Sigmoid), gated if t else None)
                act.sem_inc(layer_left, 1)
                act.wait_ge(layer_open, layer + 1)
            do = Order(act, act_step)
            for t in range(TT):
                do(nc.scalar.activation(junk[:, :], x[:, t, :], ACT.Square, accum_out=ssq[:, t:t + 1]))
            do(nc.scalar.activation(rstd[:, :], ssq[:, :], ACT.Sqrt, bias=eps, scale=1.0 / D), final_std)

        @block.vector
        def _(dve):
            def split_lo(base, k):
                dve.wait_ge(hi_ready, base + (k + 1))
                nc.vector.tensor_tensor(w_lo[:, k % SPLIT, :], raw[:, k % RAW, :], w_hi[:, k % SPLIT, :].bitcast(F32), ALU.subtract).then_inc(lo_ready, 1)

            for k in range(SPLIT):
                split_lo(0, k)
            dve.wait_ge(const_loaded, 32)
            dve.wait_ge(x_loaded, 16)
            with dve.Fori(0, LAYERS) as layer:
                base = layer * TILES_A
                do = Order(dve, dve_step)
                V = nc.vector

                def stream(name, i):
                    for j in range(PER_CHUNK[name]):
                        split_lo(base, TILE[name, i] + j + SPLIT)

                def taken(name, i):
                    dve.wait_ge(tile_used, base + (TILE[name, i] + PER_CHUNK[name]))

                def row_of(name, i, k=0):
                    ap, s, n = row_slot(name, i, k)
                    dve.wait_ge(s, layer * (16 * ROWS_A // RROW) + n)
                    return ap

                def norm(i):
                    dve.wait_ge(std_ready, i + 1)
                    do(V.reciprocal(rstd[:, :], rstd[:, :]))
                    for t in range(TT):
                        do(V.tensor_scalar(gate[:, t, :], x[:, t, :], rstd[:, t:t + 1], None, ALU.mult), xn_ready)
                    g0 = COL[f"norm{i + 1}"]
                    first = (T_H, T_H2, T_H3)[i]
                    for b in range(KD // 2):
                        dve.wait_ge(t_hi, first + b + 1)
                        for k in (2 * b, 2 * b + 1):
                            do(V.scalar_tensor_tensor(out=act_lo[:, k, :], in0=psum[4 + b][:, (k % 2) * S:(k % 2 + 1) * S],
                                                      scalar=col[:, g0 + k:g0 + k + 1], in1=act_hi[:, k, :].bitcast(F32),
                                                      op0=ALU.mult, op1=ALU.subtract), t_lo if k % 2 else None)

                def mixed(first, k0):
                    for b in range(KD // 2):
                        dve.wait_ge(t_hi, first + b + 1)
                        ks = slice(k0 + 2 * b, k0 + 2 * b + 2)
                        do(V.tensor_tensor(mix_lo[:, ks, :].rearrange("p k s -> p (k s)"), psum[4 + b][:, :],
                                           mix_hi[:, ks, :].rearrange("p k s -> p (k s)").bitcast(F32), ALU.subtract), t_lo)

                dve.wait_ge(col_loaded, layer * 32 + 32)
                dve.wait_ge(gw_split, 1)
                do(V.memset(shifted[:, :, 0:3], 0.0))
                do(V.memset(val_m[:, :, :, MDV:MDV + 1], 1.0))
                gwl = V.tensor_tensor(gw_lo[:, :, :].rearrange("p k n -> p (k n)"), col[:, COL["gatew"]:COL["gatew"] + 64],
                                      gw_hi[:, :, :].rearrange("p k n -> p (k n)").bitcast(F32), ALU.subtract)
                gwl.then_inc(gw_split, 1)
                norm(0)
                dve.wait_ge(gate_mm, 1)
                for t in range(TT):
                    do(V.tensor_tensor(gz[:, t, :], psum[6][:, t * 8:t * 8 + 8], bgate_row[:, :], ALU.add), gz_ready if t else None)
                dve.wait_ge(lnf_ready, 1)
                do(V.scalar_tensor_tensor(out=gl[:, 2, :, :], in0=gz[:, :, 4:8], scalar=0.0, in1=gl[:, 1, :, :], op0=ALU.min, op1=ALU.subtract), lf_ready)

                def convolve(i):
                    wait_read(dve, CHUNK["mqk", i])
                    if i >= 1:
                        dve.wait_ge(mqk_ready, i)
                    for j in range(4):
                        for f in range(4):
                            w = COL["convw"] + 16 * j + 4 * i + f
                            b = COL["convb"] + 4 * i + f
                            if j == 0:
                                ins = V.tensor_scalar(conv[:, f, :], shifted[:, f, 0:S], col[:, w:w + 1], col[:, b:b + 1], ALU.mult, ALU.add)
                            else:
                                ins = V.scalar_tensor_tensor(out=conv[:, f, :], in0=shifted[:, f, j:j + S], scalar=col[:, w:w + 1],
                                                             in1=conv[:, f, :], op0=ALU.mult, op1=ALU.add)
                            do(ins, conv_done if j == 3 and f == 3 else None)

                stream("mqk", 0)
                convolve(0)
                dve.wait_ge(gate_mm, 2)
                do(V.tensor_copy(gl[:, 3, :, :].rearrange("p t h -> p (t h)"), psum[7][:, 0:2 * HEADS]))
                do(V.tensor_tensor(gi[:, :, :], gz[:, :, 0:4], gl[:, 3, :, :], ALU.subtract), gi_ready)
                stream("mqk", 1)
                convolve(1)
                dve.wait_ge(gate_mm, 3)
                do(V.tensor_copy(grow[:, :], psum[6][0:HEADS, 0:S]))
                do(V.tensor_tensor_scan(mrow[:, :], grow[:, :], grow[:, :], 0.0, ALU.max, ALU.max), m_ready)
                stream("mqk", 2)
                convolve(2)
                dve.wait_ge(gate_mm, 4)
                do(V.tensor_tensor(gl[:, 0, :, :].rearrange("p t h -> p (t h)"), gl[:, 3, :, :].rearrange("p t h -> p (t h)"),
                                   psum[7][:, 8:8 + 2 * HEADS], ALU.add), fm_ready)
                dve.wait_ge(gate_mm, 5)
                for h in range(HEADS):
                    m = psum[4 + h // 2][:, (h % 2) * S:(h % 2 + 1) * S]
                    for b, t, masked in ((0, 0, 1), (1, 1, 0), (2, 1, 1)):
                        dst, src = decayed[:, h, b, :], m[:, t * P:(t + 1) * P]
                        ins = V.tensor_tensor(dst, src, cst("mask"), ALU.add) if masked else V.tensor_copy(dst, src)
                        do(ins, mmask_ready if b == 2 else None)
                stream("mqk", 3)
                convolve(3)
                for i in range(2):
                    stream("mv", i)
                    taken("mv", i)
                    r = row_of("mv", i)
                    for t in range(TT):
                        do(V.tensor_tensor(val_m[:, t, 2 * i:2 * i + 2, 0:MDV], psum[2 * (CHUNK["mv", i] % 2) + t][:, :].rearrange("p (h n) -> p h n", h=2),
                                           r.rearrange("p (h n) -> p h n", h=2), ALU.add), read_dve if t else None)

                def weigh(h0, h, scale, weights_of):
                    dve.wait_ge(score_done, h0 + h + 1)
                    if h >= 2:
                        dve.wait_ge(y_done, h0 + h - 1)
                    do(V.scalar_tensor_tensor(out=weighed[:, h % 2, :], in0=psum[4 + h % 2][:, 0:3 * P], scalar=scale, in1=weights_of(h),
                                              op0=ALU.mult, op1=ALU.mult), weighed_ready)

                def statistics(src, t, h):
                    do(V.bn_stats(st6[:, :], src))
                    do(V.bn_aggr(stats[:, t, h, :], st6[:, :]), stats_ready if (t, h) == (TT - 1, HEADS - 1) else None)

                def head_norm(n, width):
                    dve.wait_ge(hstd_ready, n)
                    do(V.reciprocal(hstd[:, :, :], hstd[:, :, :]))
                    for h in range(HEADS):
                        for t in range(TT):
                            ys = y[:, t, h * width:(h + 1) * width]
                            do(V.tensor_scalar(ys, ys, stats[:, t, h, 0:1], hstd[:, t, h:h + 1], ALU.subtract, ALU.mult))

                def m_output(h):
                    dve.wait_ge(y_done, h + 1)
                    for t in range(TT):
                        total = psum[6 + t][:, MDV:MDV + 1]
                        do(V.scalar_tensor_tensor(out=den[:, 0:1], in0=total, scalar=-1.0, in1=floor[:, t, h:h + 1], op0=ALU.mult, op1=ALU.max))
                        do(V.tensor_tensor(den[:, 0:1], den[:, 0:1], total, ALU.max))
                        do(V.reciprocal(den[:, 1:2], den[:, 0:1]))
                        do(V.tensor_scalar(y[:, t, h * MDV:(h + 1) * MDV], psum[6 + t][:, 0:MDV], den[:, 1:2], None, ALU.mult), my_read if t else None)
                        statistics(y[:, t, h * MDV:(h + 1) * MDV], t, h)

                dve.wait_ge(floor_ready, 1)
                for h in range(HEADS):
                    dve.wait_ge(decay_ready, h + 1)
                    weigh(0, h, MDV ** -0.5, lambda h: decayed[:, h, :, :].rearrange("p b s -> p (b s)"))
                    if h >= 1:
                        m_output(h - 1)
                m_output(HEADS - 1)
                head_norm(1, MDV)

                def gate_in(name, i, c0=None):
                    taken(name, i)
                    r = row_of(name, i)
                    for t in range(TT):
                        do(V.tensor_tensor(pre[:, t, :], psum[2 * (CHUNK[name, i] % 2) + t][:, :], r, ALU.add), read_dve if t else None)

                def gated_mixer(name, n, ready0):
                    for i in range(n):
                        stream(name, i)
                        g = row_of(name, i, 1)
                        for t in range(TT):
                            ys = y[:, t, i * CW:(i + 1) * CW]
                            do(V.tensor_tensor(ys, ys, g, ALU.mult))
                        gate_in(name, i)
                        dve.wait_ge(gated, ready0 + i + 1)
                        for t in range(TT):
                            ys = y[:, t, i * CW:(i + 1) * CW]
                            do(V.tensor_tensor(ys, ys, pre[:, t, :], ALU.mult), y_ready if t else None)

                gated_mixer("mo", 2, 0)
                mixed(T_YM, 0)
                for i in range(2):
                    stream("gm", i)
                    if i:
                        dve.wait_ge(gated, 2 + i)
                    gate_in("gm", i)
                for i in range(2):
                    stream("bm", i)
                    taken("bm", i)
                    dve.wait_ge(gated, 4)
                    for t in range(TT):
                        cs = slice(i * CW, (i + 1) * CW)
                        do(V.tensor_tensor(merged[:, t, cs], psum[2 * (CHUNK["bm", i] % 2) + t][:, :], gate[:, t, cs], ALU.mult), read_dve if t else None)

                def rotate(i):
                    wait_read(dve, CHUNK["rqk", i])
                    for a in range(2):
                        x1, x2 = shifted[:, 2 * a, 3:], shifted[:, 2 * a + 1, 3:]
                        o1, o2 = qk_t[:, 4 * i + 2 * a, :], qk_t[:, 4 * i + 2 * a + 1, :]
                        do(V.tensor_tensor(o1, x1, cst("cos"), ALU.mult))
                        do(V.tensor_tensor(o2, x1, cst("sin"), ALU.mult))
                        do(V.tensor_tensor(conv[:, 0, :], x2, cst("sin"), ALU.mult))
                        do(V.tensor_tensor(conv[:, 1, :], x2, cst("cos"), ALU.mult))
                        do(V.tensor_tensor(o1, o1, conv[:, 0, :], ALU.subtract))
                        do(V.tensor_tensor(o2, o2, conv[:, 1, :], ALU.add), rqk_ready if a else None)

                for i in range(4):
                    stream("rqk", i)
                    rotate(i)
                for i in range(4):
                    stream("rv", i)
                    taken("rv", i)
                    r = row_of("rv", i)
                    for t in range(TT):
                        do(V.tensor_tensor(val_r[:, t, i * CW:(i + 1) * CW], psum[2 * (CHUNK["rv", i] % 2) + t][:, :], r, ALU.add), read_dve if t else None)

                def r_output(h):
                    dve.wait_ge(ry_read, h + 1)
                    for t in range(TT):
                        statistics(y[:, t, h * RDV:(h + 1) * RDV], t, h)

                for h in range(HEADS):
                    weigh(HEADS, h, 1.0, lambda h: cst("decay")[:, h * 384:(h + 1) * 384])
                    if h >= 1:
                        r_output(h - 1)
                r_output(HEADS - 1)
                head_norm(2, RDV)
                gated_mixer("rg", 4, 4)
                mixed(T_YR, 0)
                for i in range(2):
                    stream("gr", i)
                    if i:
                        dve.wait_ge(gated, 8 + i)
                    gate_in("gr", i)
                mixed(T_YR + 4, KD)
                for i in range(2):
                    stream("br", i)
                    taken("br", i)
                    dve.wait_ge(gated, 10)
                    for t in range(TT):
                        cs = slice(i * CW, (i + 1) * CW)
                        do(V.tensor_tensor(pre[:, t, :], psum[2 * (CHUNK["br", i] % 2) + t][:, :], gate[:, t, cs], ALU.mult), read_dve if t else None)
                        do(V.tensor_tensor(merged[:, t, cs], merged[:, t, cs], pre[:, t, :], ALU.add), merged_ready if t else None)
                mixed(T_MG, 0)

                def residual(name, i):
                    taken(name, i)
                    for t in range(TT):
                        cs = slice(i * CW, (i + 1) * CW)
                        do(V.tensor_tensor(x[:, t, cs], x[:, t, cs], psum[2 * (CHUNK[name, i] % 2) + t][:, :], ALU.add), read_dve if t else None)

                for i in range(2):
                    stream("out", i)
                    residual("out", i)
                norm(1)
                for half, (one, two) in enumerate((("ffa1", "ffa2"), ("ffb1", "ffb2"))):
                    for i in range(4):
                        stream(one, i)
                        wait_read(dve, CHUNK[one, i])
                        do(V.tensor_tensor(conv[:, :, :], conv[:, :, :], conv[:, :, :], ALU.mult), sq_ready)
                        dve.wait_ge(ff_hi, 4 * half + i + 1)
                        do(V.tensor_tensor(mix_lo[:, 4 * i:4 * i + 4, :], conv[:, :, :], mix_hi[:, 4 * i:4 * i + 4, :].bitcast(F32), ALU.subtract), ff_lo)
                    for i in range(2):
                        stream(two, i)
                        if half:
                            r = row_of(two, i)
                            for t in range(TT):
                                cs = slice(i * CW, (i + 1) * CW)
                                do(V.tensor_tensor(x[:, t, cs], x[:, t, cs], r, ALU.add))
                        residual(two, i)
                norm(2)
                for i in range(2):
                    stream("peg", i)
                    dve.wait_ge(gated, 10 + i + 1)
                    dve.wait_ge(pe_mm, 1)
                    for t in range(TT):
                        cs = slice(i * CW, (i + 1) * CW)
                        do(V.tensor_tensor(pre[:, t, :], psum[4 + 2 * i + t][:, :], gate[:, t, cs], ALU.mult))
                        do(V.tensor_tensor(x[:, t, cs], x[:, t, cs], pre[:, t, :], ALU.add), read_dve if t else None)
                dve.sem_inc(layer_left, 1)
                dve.wait_ge(layer_open, layer + 1)
            do = Order(dve, dve_step)
            dve.wait_ge(final_std, 1)
            do(V.reciprocal(rstd[:, :], rstd[:, :]))
            dve.wait_ge(final_loaded, 16)
            for t in range(TT):
                do(V.tensor_scalar(x[:, t, :], x[:, t, :], rstd[:, t:t + 1], None, ALU.mult))
                do(V.tensor_tensor(x[:, t, :], x[:, t, :], row[:, 0:2, :].rearrange("p a n -> p (a n)"), ALU.mult), x_ready if t else None)
    memory.close()


def second_block(nc, ctx, m, base, erows, ecols, lora_w, side_w, keys, ln_rows, consts_b, out):
    raw, w_hi, w_lo, x, act_hi, act_lo, ident, psum = m.raw, m.w_hi, m.w_lo, m.x, m.act_hi, m.act_lo, m.ident, m.psum
    raw_loaded, hi_ready, lo_ready, tile_used = m.raw_loaded, m.hi_ready, m.lo_ready, m.tile_used
    V, A = nc.vector, nc.scalar
    total = base + TILES_B

    def sb(name, shape, dt=F32, stack=ctx):
        return stack.enter_context(nc.sbuf_tensor(name, shape, dt))

    def sem(name):
        return ctx.enter_context(nc.semaphore(name))

    const_b = sb("const_b", [P, CONSTS_B])

    def cst(name):
        first, n = CONST_B[name]
        return const_b[:, first:first + n]

    small = sb("small", [P, 64])
    even = ExitStack()
    rkv = sb("rkv", [P, 3, FT, S], F32, even)
    sgw = sb("sgw", [P, FT, S], F32, even)
    asig = sb("asig", [P, FT, S], F32, even)
    gnat = sb("gnat", [P, TT, EW], F32, even)
    erow = sb("erow", [P, EROWS], F32, even)
    ecol = sb("ecol", [P, ECOLS], F32, even)
    ymix = sb("ymix", [P, TT, D], F32, even)
    gla = ExitStack()
    lora = sb("lora", [P, LORA], F32, gla)
    side_t = sb("side_t", [P, 2, S], F32, gla)
    sh = sb("sh", [P, FT, S + 1], F32, gla)
    dif = sb("dif", [P, FT, S], F32, gla)
    gqk = sb("gqk", [P, 4, S], F32, gla)
    gv = sb("gv", [P, TT, EW], F32, gla)
    gsil = sb("gsil", [P, TT, EW], F32, gla)
    side_scope = ExitStack()
    side_raw = sb("side_raw", [P, KD, 2 * P], F32, side_scope)
    side_hi = sb("side_hi", [P, KD, 2 * P], F32R, side_scope)
    side_lo = sb("side_lo", [P, KD, 2 * P], F32R, side_scope)
    side_scope.close()
    la = sb("la", [P, GP, S], F32, gla)
    lb = sb("lb", [P, GP, S], F32, gla)
    eb = sb("eb", [P, GP, S], F32, gla)
    en = sb("en", [P, GP, S], F32, gla)
    qin = sb("qin", [P, GP, S], F32, gla)
    kin = sb("kin", [P, GP, S], F32, gla)
    qz = sb("qz", [P, CH, GP, S], F32, gla)
    konat = sb("konat", [P, TT * GP * P], F32, gla)
    attn = sb("attn", [P, 2, TT, GP, P], F32, gla)
    state = sb("state", [P, CH * TT, GP, 2 * P], F32, gla)
    gla.close()
    rw = ExitStack()
    cw = sb("cw", [P, FT, P], F32, rw)
    pinc = sb("pinc", [P, FT, P], F32, rw)
    pinv = sb("pinv", [P, FT, P], F32, rw)
    pm = sb("pm", [P, FT, P], F32, rw)
    kk = sb("kk", [P, FT, P], F32, rw)
    tmp = sb("tmp", [P, FT, P], F32, rw)
    kp = sb("kp", [P, FT, P], F32, rw)
    ar = sb("ar", [P, FT, 2, P], F32, rw)
    bt = sb("bt", [P, FT, P], F32, rw)
    kt = sb("kt", [P, FT, P], F32, rw)
    rz = sb("rz", [P, CH, FT, P], F32, rw)
    lrb = sb("lrb", [P, 2, FT, 2 * P], F32, rw)
    lrk = sb("lrk", [P, 2, FT, 2 * P], F32, rw)
    dd = sb("dd", [P, 2, FT, P], F32, rw)
    dt_ = sb("dt_", [P, 2, FT, P], F32, rw)
    xx = sb("xx", [P, 2, FT, P], F32, rw)
    wv = sb("wv", [P, FT, P], F32, rw)
    tat = sb("tat", [P, FT, P], F32, rw)
    uu = sb("uu", [P, FT, P], F32, rw)
    s_all = sb("s_all", [P, 3, FT, P], F32, rw)
    rkind = sb("rkind", [P, FT, 2], F32, rw)
    bonus = sb("bonus", [P, RH], F32, rw)
    rstat = sb("rstat", [P, RH, 2], F32, rw)
    r6 = sb("r6", [P, 6], F32, rw)
    rw.close()
    even.close()
    nat = {"a": cw, "b": pm, "k": pinv, "v": tmp}
    zz = kk
    ln_row = sb("ln_row", [P, 2, D])
    odd = ExitStack()
    qn = sb("qn", [P, TT, D], F32, odd)
    qin_ = sb("qidx", [P, TT, IH * ID], F32, odd)
    kn = sb("kn", [P, TT, AD], F32, odd)
    vn = sb("vn", [P, TT, AD], F32, odd)
    kid = sb("kid", [P, TT, 2 * ID], F32, odd)
    wi = sb("wi", [P, TT, IH], F32, odd)
    rtmp = sb("rtmp", [P, CW // 2], F32, odd)
    q_t = sb("q_t", [P, AH, S], F32, odd)
    qi_t = sb("qi_t", [P, IH // 2, S], F32, odd)
    k_t = sb("k_t", [P, S], F32, odd)
    kib = sb("kib", [P, 2 * S], F32, odd)
    rel = sb("rel", [P, IH, S], F32, odd)
    score = sb("score", [P, TT, S], F32, odd)
    madd = sb("madd", [P, TT, S], F32, odd)
    logit = sb("logit", [P, AH, S], F32, odd)
    pt = sb("pt", [P, AH, TT, P], F32, odd)
    amax = sb("amax", [P, AH], F32, odd)
    asum = sb("asum", [P, AH], F32, odd)
    top8 = sb("top8", [P, 8], F32, odd)
    odd.close()
    peer = ExitStack()
    hid = sb("hid", [P, JH, S], F32, peer)
    pq, keys_sb = hid[:, JH - 2 * PH:JH - PH, :], hid[:, JH - PH:JH, :]
    ijg = sb("ijg", [P, 3, S], F32, peer)
    hot_i = sb("hot_i", [P, HOT, GT, KEYS], F32, peer)
    hot_j = sb("hot_j", [P, HOT, GT, JH], F32, peer)
    hot = hot_i[:, :, :, :].rearrange("p a t n -> p (a t n)").rearrange("p (h k a) -> p h k a", h=PH, k=PK)
    tops = sb("tops", [P, 2 * PH, PK], F32, peer)
    topi = sb("topi", [P, 2 * PH, PK], U32, peer)
    topf = sb("topf", [P, 2 * PH, PK], F32, peer)
    best = sb("best", [P, TT, PH, PK], F32, peer)
    pos = sb("pos", [P, PH, PK], U32, peer)
    posab = sb("posab", [P, 2, PH * PK], U32, peer)
    posf = sb("posf", [P, 2, PH * PK], F32, peer)
    sel = sb("sel", [P, TT, 3, PH * PK], F32, peer)
    gsum = sb("gsum", [P, TT * PH], F32, peer)
    scores = ExitStack()
    ss1 = sb("ss1", [P, 2 * PH, KEYS], F32, scores)
    staged = ss1[:, :, :].rearrange("p c n -> p (c n)")[:, 0:HOT // 2 * GT * JH].rearrange("p (b t j) -> p b t j", b=HOT // 2, t=GT)
    scores.close()
    ss = (ln_row[:, :, :].rearrange("p a n -> p (a n)").rearrange("p (c n) -> p c n", n=KEYS), ss1)
    c_hi = sb("c_hi", [P, 2, 2 * S], F32R, peer)
    c_lo = sb("c_lo", [P, 2, 2 * S], F32R, peer)
    peer.close()

    act_own, dve_own = sem("b_act_own"), sem("b_dve_own")
    b_const = sem("b_const")
    side_loaded = sem("side_loaded")
    even_loaded = sem("even_loaded")
    ln_loaded = sem("ln_loaded")
    keys_loaded = sem("keys_loaded")
    x_ready = m.x_ready
    tr_done = sem("b_tr_done")
    tr_hi = sem("b_tr_hi")
    tr_lo = sem("b_tr_lo")
    side_hi_ready, side_lo_ready = sem("side_hi_ready"), sem("side_lo_ready")
    read_act, read_dve = sem("b_read_act"), sem("b_read_dve")
    shifted_done = sem("shifted_done")
    even_pe, even_act, even_dve = sem("even_pe"), sem("even_act"), sem("even_dve")
    rw_pe, rw_act, rw_dve = sem("rw_pe"), sem("rw_act"), sem("rw_dve")
    odd_pe, odd_act, odd_dve = sem("odd_pe"), sem("odd_act"), sem("odd_dve")
    att_hi, att_lo = sem("att_hi"), sem("att_lo")
    ln_var, ln_std = sem("ln_var"), sem("ln_std")
    s_done, s_read, s_used = sem("s_done"), sem("s_read"), sem("s_used")
    best_ready, exp_ready, sel_ready = sem("best_ready"), sem("exp_ready"), sem("sel_ready")
    sel_t, ijg_ready = sem("sel_t"), sem("ijg_ready")
    hot_eq = sem("hot_eq")
    hot_ready = sem("hot_ready")
    gates_done = sem("gates_done")
    gates_read = sem("gates_read")
    gated_odd = sem("gated_odd")
    gated_even = sem("gated_even")
    act_pad = sem("act_pad")
    gelu_ready = sem("gelu_ready")
    c_hi_ready, c_lo_ready = sem("c_hi_ready"), sem("c_lo_ready")
    out_stored = m.out_stored

    def wait_read(eng, c):
        by, count = READ_B[c]
        eng.wait_ge(read_act if by == "act" else read_dve, count)

    block = ctx.enter_context(nc.Block())

    @block.sync
    def _(sp):
        with sp.Fori(base // RAW + 1, total // RAW) as n:
            for r in range(RAW):
                sp.wait_ge(lo_ready, n * RAW + (r - RAW + 1))
                sp.dma_start(raw[:, r, :], m.weights[n * RAW + r]).then_inc(raw_loaded[r], 16)
        sp.wait_ge(x_ready, 5)
        sp.dma_start(out, x[:, :, :]).then_inc(out_stored, 16)
        sp.wait_ge(out_stored, 16)

    @block.gpsimd
    def _(pool):
        pool.dma_start(side_raw[:, :, :], side_w).then_inc(side_loaded, 16)
        pool.dma_start(const_b[:, :], consts_b).then_inc(b_const, 16)
        pool.dma_start(lora[:, :], lora_w).then_inc(even_loaded, 16)
        pool.dma_start(ecol[:, :], ecols).then_inc(even_loaded, 16)
        pool.dma_start(erow[:, :], erows.partition_broadcast(P)).then_inc(even_loaded, 16)

        def ln_load(n):
            pool.dma_start(ln_row[:, 0, :], ln_rows[2 * n].partition_broadcast(P)).then_inc(ln_loaded, 16)
            pool.dma_start(ln_row[:, 1, :], ln_rows[2 * n + 1].partition_broadcast(P)).then_inc(ln_loaded, 16)

        pool.wait_ge(tr_lo, 8)
        ln_load(0)
        pool.dma_start(keys_sb, keys[0]).then_inc(keys_loaded, 16)

        def gate(layer):
            for part in range(2):
                done = 2 * layer + part
                g0 = GROUPS * done

                def rows(n, b):
                    pool.wait_ge(hot_eq, n * HOT + (g0 + b + 1))
                    tok = bass.ds(n * HOT * GT + b * GT, GT)
                    at = hot_j[:, b % HOT, :, :]
                    nc.gpsimd.tensor_tensor(at, at, ijg[:, 2, tok].unsqueeze(2).broadcast_to([P, GT, JH]), ALU.mult).then_inc(hot_ready, 1)

                def apply(n, b):
                    pool.wait_ge(gates_read, n * (HOT // 2) + (g0 // 2 + b // 2 + 1))
                    tok = hid[:, :, bass.ds(n * HOT * GT + b * GT, GT)].rearrange("p j t -> p t j")
                    nc.gpsimd.tensor_tensor(tok, tok, staged[:, b // 2, :, :], ALU.mult).then_inc(gated_odd, 1)

                pool.wait_ge(ijg_ready, 2 * layer + 2)
                rows(0, 0)
                rows(0, 1)
                pool.wait_ge(gelu_ready, PAIRS * (done + 1))
                with pool.Fori(0, GROUPS // HOT - 1) as n:
                    for b in range(HOT):
                        rows(n, b + 2)
                        if b % 2:
                            apply(n, b)
                for b in range(HOT):
                    if b + 2 < HOT:
                        rows(GROUPS // HOT - 1, b + 2)
                    if b % 2:
                        apply(GROUPS // HOT - 1, b)

        pool.wait_ge(sel_ready, 2)
        ln_load(1)
        gate(0)
        pool.wait_ge(x_ready, 3)
        ln_load(2)
        pool.wait_ge(att_lo, 2)
        pool.dma_start(keys_sb, keys[1]).then_inc(keys_loaded, 16)
        pool.wait_ge(sel_ready, 4)
        ln_load(3)
        gate(1)

    @block.tensor
    def _(pe):
        mm = nc.tensor.matmul

        def natural(name, i):
            c, k0 = CHUNK_B[name, i], base + TILE_B[name, i]
            if c >= 2:
                wait_read(pe, c - 2)
            for j in range(2):
                k = k0 + j
                pe.wait_ge(lo_ready, k + 1)
                for kk_ in range(KB):
                    ki = j * KB + kk_
                    for t in range(TT):
                        dst = psum[2 * (c % 2) + t][:, :]
                        ws = slice(kk_ * CW, (kk_ + 1) * CW)
                        mm(dst, act_hi[:, ki, HALVES[t]], w_hi[:, k % SPLIT, ws], start=ki == 0, stop=False)
                        mm(dst, act_hi[:, ki, HALVES[t]], w_lo[:, k % SPLIT, ws], start=False, stop=False)
                        last = mm(dst, act_lo[:, ki, HALVES[t]], w_hi[:, k % SPLIT, ws], start=False, stop=ki == KD - 1)
                last.then_inc(tile_used, 1)

        def featured(name, i):
            c, k0 = CHUNK_B[name, i], base + TILE_B[name, i]
            if c >= 2:
                wait_read(pe, c - 2)
            for j in range(2):
                k = k0 + j
                pe.wait_ge(lo_ready, k + 1)
                for f in range(4):
                    for kk_ in range(KB):
                        ki = j * KB + kk_
                        ws = slice(kk_ * CW + f * P, kk_ * CW + (f + 1) * P)
                        dst = psum[2 * (c % 2) + f // 2][:, (f % 2) * S:(f % 2 + 1) * S]
                        wh, wl = w_hi[:, k % SPLIT, ws], w_lo[:, k % SPLIT, ws]
                        mm(dst, wh, act_hi[:, ki, :], start=ki == 0 and f % 2 == 0, stop=False)
                        mm(dst, wh, act_lo[:, ki, :], start=False, stop=False)
                        last = mm(dst, wl, act_hi[:, ki, :], start=False, stop=ki == KD - 1 and f % 2 == 1)
                last.then_inc(tile_used, 1)

        def transposes(src):
            for b in range(KD // 2):
                for k in (2 * b, 2 * b + 1):
                    for t in range(TT):
                        last = nc.tensor.transpose(psum[4 + b][:, (k % 2) * S + t * P:(k % 2) * S + (t + 1) * P],
                                                   src[:, t, k * P:(k + 1) * P], ident)
                last.then_inc(tr_done, 1)

        pe.wait_ge(x_ready, 1)
        transposes(x)
        pe.wait_ge(tr_lo, 4)
        pe.wait_ge(side_lo_ready, 1)
        for g in range(2):
            for k in range(KD):
                dst, ws = psum[4][:, g * S:(g + 1) * S], slice(g * P, (g + 1) * P)
                mm(dst, side_hi[:, k, ws], act_hi[:, k, :], start=k == 0 and g == 0, stop=False)
                mm(dst, side_hi[:, k, ws], act_lo[:, k, :], start=False, stop=False)
                last = mm(dst, side_lo[:, k, ws], act_hi[:, k, :], start=False, stop=k == KD - 1 and g == 1)
        last.then_inc(even_pe, 1)
        featured("gqk", 0)
        pe.wait_ge(even_loaded, 48)
        pe.wait_ge(even_act, EVEN_ACT["gates"])
        for g in range(GP):
            cols = slice(EW + g * P, EW + (g + 1) * P)
            last = mm(psum[5][:, g * S:(g + 1) * S], lora[GA2[0], cols], side_t[GA2[0], 1, :], start=True, stop=True)
        last.then_inc(even_pe, 1)
        for f in range(FT):
            last = mm(psum[6 + f // 2][:, (f % 2) * S:(f % 2 + 1) * S], lora[W2[0], f * P:(f + 1) * P], side_t[W2[0], 0, :],
                      start=True, stop=True)
        last.then_inc(even_pe, 1)
        natural("gv", 0)
        natural("gg", 0)
        pe.wait_ge(even_dve, EVEN_DVE["la"])
        pe.wait_ge(even_act, EVEN_ACT["w"])
        for f in range(FT):
            cols = slice(EW + f * P, EW + (f + 1) * P)
            last = mm(psum[4 + f // 2][:, (f % 2) * S:(f % 2 + 1) * S], lora[A2[0], cols], side_t[A2[0], 1, :], start=True, stop=True)
        last.then_inc(even_pe, 1)
        for t in range(TT):
            last = mm(psum[6 + t][:, :], side_t[G2[0], 0, HALVES[t]], lora[G2[0], G2[1]], start=True, stop=True)
        last.then_inc(even_pe, 1)
        featured("r", 0)
        featured("k", 0)
        featured("v", 0)
        pe.wait_ge(even_dve, EVEN_DVE["decayed"])
        pe.wait_ge(even_act, EVEN_ACT["a"])
        for e in range(2):
            for t in range(TT):
                for g in range(GP):
                    es = slice(e * GDK, (e + 1) * GDK)
                    last = mm(psum[4 + e][:, (t * GP + g) * P:(t * GP + g + 1) * P], kin[es, g, HALVES[t]], qin[es, g, HALVES[t]],
                              start=True, stop=True)
        last.then_inc(even_pe, 1)
        for t in range(TT):
            for g in range(GP):
                last = nc.tensor.transpose(psum[6][:, (t * GP + g) * P:(t * GP + g + 1) * P], en[:, g, HALVES[t]], ident)
        last.then_inc(even_pe, 1)
        wait_read(pe, CHUNK_B["v", 0])
        wait_read(pe, CHUNK_B["k", 0])
        pe.wait_ge(even_act, EVEN_ACT["keys"])
        for t in range(TT):
            for c in range(CH):
                cs = slice(c * CHUNK_T, (c + 1) * CHUNK_T)
                for g in range(GP):
                    last = mm(psum[2 * t + c][:, g * S:(g + 1) * S], konat[cs, (t * GP + g) * P:(t * GP + g + 1) * P],
                              gv[cs, t, g * S:(g + 1) * S], start=True, stop=True)
        last.then_inc(even_pe, 1)
        pe.wait_ge(even_dve, EVEN_DVE["states"])
        for t in range(TT):
            for g in range(GP):
                for c in range(CH):
                    if t or c:
                        mm(psum[6 + t][:, g * S:(g + 1) * S], qz[:, c, g, HALVES[t]], state[:, t * CH + c, g, :],
                           start=g == 0 and c == (0 if t else 1), stop=False)
                for e in range(2):
                    last = mm(psum[6 + t][:, g * S + e * GDV:g * S + (e + 1) * GDV], attn[:, e, t, g, :],
                              gv[:, t, g * S + e * GDV:g * S + (e + 1) * GDV], start=False, stop=g == GP - 1 and e == 1)
        last.then_inc(even_pe, 1)

        pe.wait_ge(even_dve, EVEN_DVE["gla"])
        for t in range(TT):
            by_act = lambda step: pe.wait_ge(rw_act, t * len(RW_ACT) + RW_ACT[step])
            by_dve = lambda step: pe.wait_ge(rw_dve, t * len(RW_DVE) + RW_DVE[step])
            by_dve("bonus")
            for f in range(FT):
                last = mm(psum[1][:, 2 * f:2 * f + 2], kt[:, f, :], rkind[:, f, :], start=True, stop=True)
            last.then_inc(rw_pe, 1)
            last = mm(psum[0][:, :], cst("same_head"), tmp[:, :, :].rearrange("p f s -> p (f s)"), start=True, stop=True)
            last.then_inc(rw_pe, 1)
            by_dve("tilde")
            for n, src in enumerate((ar[:, :, 0, :], bt[:, :, :], kt[:, :, :], rkv[:, 2, :, HALVES[t]])):
                for f in range(FT):
                    last = nc.tensor.transpose(psum[n][:, f * P:(f + 1) * P], src[:, f, :], ident)
                last.then_inc(rw_pe, 1)
            for step, src in (("lb", bt), ("lk", kt)):
                if step == "lk":
                    by_dve("lb")
                for e in range(2):
                    es = slice(e * RN, (e + 1) * RN)
                    for f in range(FT):
                        last = mm(psum[4 + 2 * e + f // 2][:, (f % 2) * S:(f % 2 + 1) * S], src[es, f, :],
                                  ar[es, f, :, :].rearrange("p a s -> p (a s)"), start=True, stop=True)
                last.then_inc(rw_pe, 1)
            by_act("nat3")
            for n in range(LEVELS):
                if n:
                    by_dve(f"d{n - 1}")
                else:
                    by_dve("lk")
                for e in range(2):
                    for f in range(FT):
                        last = mm(psum[e][:, f * P:(f + 1) * P], lrb[:, e, f, 0:P], dd[:, e, f, :], start=True, stop=True)
                last.then_inc(rw_pe, 1)
                by_dve(f"x{n}")
                for e in range(2):
                    for f in range(FT):
                        mm(psum[2 + e][:, f * P:(f + 1) * P], dt_[:, e, f, :], xx[:, e, f, :], start=True, stop=True)
                        last = mm(psum[4 + e][:, f * P:(f + 1) * P], xx[:, e, f, :], dt_[:, e, f, :], start=True, stop=True)
                last.then_inc(rw_pe, 1)
            by_dve(f"d{LEVELS - 1}")
            for f in range(FT):
                for e in range(2):
                    hs = slice((2 * f + e) * RN, (2 * f + e + 1) * RN)
                    vs = slice(e * RN, (e + 1) * RN)
                    last = mm(psum[6][:, hs], lrk[:, e, f, 0:P], nat["v"][:, f, vs], start=True, stop=True)
            last.then_inc(rw_pe, 1)
            by_dve("z")
            for f in range(FT):
                for e in range(2):
                    hs = slice((2 * f + e) * RN, (2 * f + e + 1) * RN)
                    last = mm(psum[7][:, hs], dt_[:, e, f, :], zz[:, f, e * RN:(e + 1) * RN], start=True, stop=True)
            last.then_inc(rw_pe, 1)
            for f in range(FT):
                for e in range(2):
                    es = slice(e * RN, (e + 1) * RN)
                    last = mm(psum[0][es, f * P:(f + 1) * P], nat["a"][:, f, es], dt_[:, e, f, :], start=True, stop=True)
            last.then_inc(rw_pe, 1)
            by_act("ta")
            by_dve("wv")
            for c in range(CH):
                cs = slice(c * CHUNK_T, (c + 1) * CHUNK_T)
                if c:
                    by_dve("s0")
                for f in range(FT):
                    last = mm(psum[2 + c][cs, f * P:(f + 1) * P], tat[:, f, cs], s_all[:, c, f, :], start=True, stop=True)
                last.then_inc(rw_pe, 1)
                by_dve(f"u{c}")
                for f in range(FT):
                    mm(psum[4 + c][:, f * P:(f + 1) * P], nat["b"][cs, f, :], uu[cs, f, :], start=f == 0, stop=False)
                    last = mm(psum[4 + c][:, f * P:(f + 1) * P], nat["k"][cs, f, :], nat["v"][cs, f, :], start=False, stop=f == FT - 1)
                last.then_inc(rw_pe, 1)
            for f in range(FT):
                for c in range(CH):
                    mm(psum[6][:, f * P:(f + 1) * P], rz[:, c, f, :], s_all[:, c, f, :], start=f == 0 and c == 0, stop=False)
                for e in range(2):
                    es = slice(e * RN, (e + 1) * RN)
                    dst = psum[6][:, f * P + e * RN:f * P + (e + 1) * RN]
                    mm(dst, lrb[:, e, f, P:2 * P], uu[:, f, es], start=False, stop=False)
                    last = mm(dst, lrk[:, e, f, P:2 * P], nat["v"][:, f, es], start=False, stop=f == FT - 1 and e == 1)
            last.then_inc(rw_pe, 1)
            by_dve("out")
        transposes(ymix)
        pe.wait_ge(tr_lo, 8)
        natural("eout", 0)
        natural("eout", 1)

        def peer_layer(layer, t_lo):
            pe.wait_ge(x_ready, 2 + 2 * layer)
            transposes(x)
            pe.wait_ge(tr_lo, t_lo)
            featured(f"pq{layer}", 0)
            featured(f"pq{layer}", 1)
            pe.wait_ge(keys_loaded, 16 * (layer + 1))
            wait_read(pe, CHUNK_B[f"pq{layer}", 1])
            for t in range(TT):
                for h in range(PH):
                    last = mm(psum[4 * (1 - t) + h // 2][:, (h % 2) * 2 * KEYS:(h % 2 + 1) * 2 * KEYS], pq[:, h, HALVES[t]], keys_sb[:, h, :],
                              start=True, stop=True)
                last.then_inc(s_done, 1)
            pe.wait_ge(s_read, 2 * layer + 1)
            for part in range(2):
                done = 2 * layer + part
                first, g0 = PAIRS * done, GROUPS * done
                tile = base + PEER_UV[layer] + 2 * PAIRS * part

                def hidden(n, p):
                    k = tile + p
                    pe.wait_ge(lo_ready, n * 2 + (k + 1))
                    if first or p > 1 or not isinstance(n, int):
                        pe.wait_ge(gelu_ready, n * 2 + (first + p - 1))
                    for jj in range(2):
                        dst = psum[4 + p % 2][:, jj * S:(jj + 1) * S]
                        for kk_ in range(KD):
                            ws = slice((2 * kk_ + jj) * P, (2 * kk_ + jj + 1) * P)
                            mm(dst, w_hi[:, k % SPLIT, ws], act_hi[:, kk_, :], start=kk_ == 0 and jj == 0, stop=False)
                            mm(dst, w_hi[:, k % SPLIT, ws], act_lo[:, kk_, :], start=False, stop=False)
                            last = mm(dst, w_lo[:, k % SPLIT, ws], act_hi[:, kk_, :], start=False, stop=kk_ == KD - 1 and jj == 1)
                    last.then_inc(tile_used, 1)

                def gates(n, b):
                    pe.wait_ge(hot_ready, n * HOT + (g0 + b + 1))
                    if g0 or not isinstance(n, int):
                        pe.wait_ge(gates_read if b % 2 else gated_even, n * (HOT // 2) + (g0 // 2 + b // 2 + 1 - HOT // 2))
                    for i in range(GT):
                        last = mm(psum[4 + b][:, i * JH:(i + 1) * JH], hot_i[:, b, i, :], hot_j[:, b, i, :], start=True, stop=True)
                    last.then_inc(gates_done, 1)

                def output(n, p, begin=False, end=False):
                    k = tile + PAIRS + p
                    pe.wait_ge(lo_ready, n * 2 + (k + 1))
                    pe.wait_ge(c_lo_ready, n * 2 + (first + p + 1))
                    for jj in range(2):
                        for t in range(TT):
                            cs = slice(jj * S + t * P, jj * S + (t + 1) * P)
                            for c in range(2):
                                dst, ws = psum[2 * t + c][:, :], slice(jj * D + c * CW, jj * D + (c + 1) * CW)
                                mm(dst, c_hi[:, p % 2, cs], w_hi[:, k % SPLIT, ws], start=begin and jj == 0, stop=False)
                                mm(dst, c_hi[:, p % 2, cs], w_lo[:, k % SPLIT, ws], start=False, stop=False)
                                last = mm(dst, c_lo[:, p % 2, cs], w_hi[:, k % SPLIT, ws], start=False, stop=end and jj == 1)
                    last.then_inc(tile_used, 1)

                hidden(0, 0)
                hidden(0, 1)
                with pe.Fori(1, PAIRS // 2) as q:
                    hidden(q, 0)
                    hidden(q, 1)
                if part == 0:
                    for t in range(TT):
                        pe.wait_ge(sel_ready, 2 * layer + t + 1)
                        for n in range(3):
                            last = nc.tensor.transpose(psum[6 + t][:, n * P:(n + 1) * P], sel[:, t, n, :], ident)
                        last.then_inc(sel_t, 1)
                    pe.wait_ge(ijg_ready, 2 * layer + 2)
                pe.wait_ge(gelu_ready, first + PAIRS)
                for b in range(HOT):
                    gates(0, b)
                with pe.Fori(1, GROUPS // HOT) as n:
                    for b in range(HOT):
                        gates(n, b)
                if part == 0:
                    pe.wait_ge(s_read, 2 * layer + 2)
                output(0, 0, begin=part == 0)
                output(0, 1)
                with pe.Fori(1, PAIRS // 2 - 1) as q:
                    output(q, 0)
                    output(q, 1)
                output(0, PAIRS - 2)
                output(0, PAIRS - 1, end=part == 1)

        peer_layer(0, 12)

        pe.wait_ge(x_ready, 3)
        transposes(x)
        pe.wait_ge(tr_lo, 16)
        for name, i in (("oq", 0), ("oq", 1), ("oqi", 0), ("okv", 0)):
            natural(name, i)
        pe.wait_ge(odd_dve, ODD_DVE["rope"])
        for h in range(AH):
            for t in range(TT):
                last = nc.tensor.transpose(psum[4 + h // 2][:, (h % 2) * S + t * P:(h % 2) * S + (t + 1) * P],
                                           qn[:, t, h * AD:(h + 1) * AD], ident)
        last.then_inc(odd_pe, 1)
        for h in range(IH // 2):
            for t in range(TT):
                last = nc.tensor.transpose(psum[h // 2][:, (h % 2) * S + t * P:(h % 2) * S + (t + 1) * P],
                                           qin_[:, t, h * P:(h + 1) * P], ident)
        for n, src in enumerate((kn, kid)):
            for t in range(TT):
                last = nc.tensor.transpose(psum[2 + n][:, t * P:(t + 1) * P], src[:, t, :], ident)
        last.then_inc(odd_pe, 1)
        pe.wait_ge(odd_act, ODD_ACT["it"])
        pe.wait_ge(odd_dve, ODD_DVE["kib"])
        for t in range(TT):
            for h in range(IH // 2):
                last = mm(psum[4 * t + h][:, :], qi_t[:, h, HALVES[t]], kib[:, :], start=True, stop=True)
            last.then_inc(odd_pe, 1)
        for t in range(TT):
            n = (t + 1) * P
            if t == 0:
                pe.wait_ge(odd_act, ODD_ACT["index1"])
            else:
                pe.wait_ge(att_lo, 1)
            for h in range(AH):
                last = mm(psum[h // 2][:, (h % 2) * S:(h % 2) * S + n], q_t[:, h, HALVES[t]], k_t[:, 0:n], start=True, stop=True)
            last.then_inc(odd_pe, 1)
            pe.wait_ge(odd_dve, ODD_DVE[f"probs{t}"])
            for h in range(AH):
                for s in range(t + 1):
                    last = nc.tensor.transpose(psum[4 + h // 2][:, ((h % 2) * TT + s) * P:((h % 2) * TT + s + 1) * P],
                                               logit[:, h, HALVES[s]], ident)
            last.then_inc(odd_pe, 1)
            pe.wait_ge(odd_act, ODD_ACT[f"pt{t}"])
            for hh in range(2):
                for s in range(t + 1):
                    last = mm(psum[hh][:, :], vn[:, s, :], pt[:, 4 * hh:4 * hh + 4, s, :], start=s == 0, stop=s == t)
            last.then_inc(odd_pe, 1)
        pe.wait_ge(att_lo, TT)
        natural("oout", 0)
        natural("oout", 1)
        peer_layer(1, 20)

    @block.scalar
    def _(act):
        do = Order(act, act_own)

        def split_hi(k):
            if k < total:
                act.wait_ge(raw_loaded[k % RAW], 16 * (k // RAW + 1))
                act.wait_ge(tile_used, k - 1)
                A.activation(w_hi[:, k % SPLIT, :], raw[:, k % RAW, :], ACT.Copy).then_inc(hi_ready, 1)

        def stream(name, i):
            for j in range(2):
                split_hi(base + TILE_B[name, i] + j + SPLIT)

        def taken(name, i):
            act.wait_ge(tile_used, base + TILE_B[name, i] + 2)

        def bank(name, i, t):
            return psum[2 * (CHUNK_B[name, i] % 2) + t]

        def split_t(first):
            for b in range(KD // 2):
                act.wait_ge(tr_done, first + b + 1)
                do(A.activation(act_hi[:, 2 * b:2 * b + 2, :].rearrange("p k s -> p (k s)"), psum[4 + b][:, :], ACT.Copy), tr_hi)

        def layer_norm(n):
            act.wait_ge(ln_var, n + 1)
            do(A.activation(small[:, 32:34], small[:, 24:28].rearrange("p (t k) -> p t k", k=2)[:, :, 1], ACT.Sqrt, bias=cst("ln_eps")), ln_std)

        def ecolumn(name, i):
            return ecol[:, ECOL[name] + i:ECOL[name] + i + 1]

        act.wait_ge(side_loaded, 16)
        do(A.activation(side_hi[:, :, :].rearrange("p k n -> p (k n)"), side_raw[:, :, :].rearrange("p k n -> p (k n)"), ACT.Copy),
           side_hi_ready)
        split_t(0)
        act.wait_ge(b_const, 16)
        act.wait_ge(even_loaded, 48)
        act.wait_ge(even_pe, EVEN_PE["side"])
        do(A.activation(sh[:, 0:2, 1:], psum[4][:, :].rearrange("p (g s) -> p g s", g=2), ACT.Copy), even_act)
        stream("gqk", 0)
        act.wait_ge(even_dve, EVEN_DVE["side"])
        do(A.activation(side_t[W2[0], 0, :], side_t[W2[0], 0, :], ACT.Tanh))
        do(A.activation(side_t[G2[0], 0, :], side_t[G2[0], 0, :], ACT.Sigmoid), even_act)
        taken("gqk", 0)
        for t in range(2):
            do(A.activation(gqk[:, 2 * t:2 * t + 2, :].rearrange("p f s -> p (f s)"), bank("gqk", 0, t)[:, :], ACT.Copy),
               read_act if t else None)
        act.wait_ge(even_pe, EVEN_PE["la"])
        for g in range(GP):
            do(A.activation(lb[:, g, :], psum[5][:, g * S:(g + 1) * S], ACT.Abs, bias=ecolumn("gla_a_b", g)))
        do(A.activation(lb[:, :, :], lb[:, :, :], ACT.Exp, scale=-1.0))
        do(A.activation(lb[:, :, :], lb[:, :, :], ACT.Ln, bias=cst("one")), even_act)
        act.wait_ge(even_pe, EVEN_PE["w"])
        for f in range(FT):
            do(A.activation(sgw[:, f, :], psum[6 + f // 2][:, (f % 2) * S:(f % 2 + 1) * S], ACT.Sigmoid, bias=ecolumn("w0", f)),
               even_act if f == FT - 1 else None)
        stream("gv", 0)
        taken("gv", 0)
        for t in range(TT):
            do(A.activation(gv[:, t, :], bank("gv", 0, t)[:, :], ACT.Copy), read_act if t else None)
        stream("gg", 0)
        taken("gg", 0)
        for t in range(TT):
            do(A.activation(gsil[:, t, :], bank("gg", 0, t)[:, :], ACT.Silu), read_act if t else None)
        act.wait_ge(even_pe, EVEN_PE["g"])
        for f in range(FT):
            do(A.activation(asig[:, f, :], psum[4 + f // 2][:, (f % 2) * S:(f % 2 + 1) * S], ACT.Sigmoid, bias=ecolumn("a0", f)))
        for t in range(TT):
            do(A.activation(gnat[:, t, :], psum[6 + t][:, :], ACT.Copy), even_act if t else None)
        act.wait_ge(even_dve, EVEN_DVE["cumsum"])
        do(A.activation(eb[:, :, :], la[:, :, :], ACT.Exp, scale=1.0 / 16))
        do(A.activation(kin[:, :, :], la[:, :, :], ACT.Exp, scale=-1.0 / 16))
        do(A.activation(en[:, :, :], lb[:, :, :], ACT.Exp, scale=-1.0 / 16), even_act)
        for n, name in enumerate("rkv"):
            stream(name, 0)
            taken(name, 0)
            if n:
                act.wait_ge(shifted_done, n)
            for t in range(2):
                do(A.activation(sh[:, 2 * t:2 * t + 2, 1:], bank(name, 0, t)[:, :].rearrange("p (f s) -> p f s", f=2), ACT.Copy),
                   read_act if t else None)
        act.wait_ge(even_pe, EVEN_PE["keys"])
        do(A.activation(konat[:, :], psum[6][:, :], ACT.Copy), even_act)
        act.wait_ge(even_pe, EVEN_PE["o"])
        for t in range(TT):
            for h in range(GH):
                ins = A.activation(lb[:, 0, 0:GDV], psum[6 + t][:, h * GDV:(h + 1) * GDV], ACT.Square, accum_out=small[:, t * GH + h:t * GH + h + 1])
                do(ins, even_act if t == TT - 1 and h == GH - 1 else None)
        do(A.activation(small[:, 8:16], small[:, 0:8], ACT.Sqrt, scale=1.0 / GDV, bias=cst("ln_eps")), even_act)
        for t in range(TT):
            by_pe = lambda step: act.wait_ge(rw_pe, t * len(RW_PE) + RW_PE[step])
            by_dve = lambda step: act.wait_ge(rw_dve, t * len(RW_DVE) + RW_DVE[step])
            by_dve("cumsum")
            do(A.activation(pinc[:, :, :], cw[:, :, :], ACT.Exp))
            do(A.activation(pinv[:, :, :], cw[:, :, :], ACT.Exp, scale=-1.0))
            do(A.activation(pm[:, :, :], pm[:, :, :], ACT.Exp), rw_act)
            by_pe("kk")
            do(A.activation(xx[:, 0, :, :].rearrange("p f s -> p (f s)"), psum[0][:, :], ACT.Sqrt), rw_act)
            for n, name in enumerate("abkv"):
                by_pe(f"nat{n}")
                do(A.activation(nat[name][:, :, :].rearrange("p f s -> p (f s)"), psum[n][:, :], ACT.Copy), rw_act)
            by_pe("ta")
            do(A.activation(tat[:, :, :].rearrange("p f s -> p (f s)"), psum[0][:, :], ACT.Copy), rw_act)
            by_dve("stats")
            do(A.activation(small[:, 0:8], rstat[:, :, 1], ACT.Sqrt, bias=cst("lnx_eps")), rw_act)
        split_t(4)
        for i in range(2):
            stream("eout", i)
        layer_norm(0)

        def peer_layer(layer, t0):
            split_t(t0)
            for i in range(2):
                stream(f"pq{layer}", i)
                taken(f"pq{layer}", i)
                for t in range(2):
                    do(A.activation(pq[:, 4 * i + 2 * t:4 * i + 2 * t + 2, :].rearrange("p f s -> p (f s)"), bank(f"pq{layer}", i, t)[:, :], ACT.Copy),
                       read_act if t else None)
            for t in range(TT):
                act.wait_ge(s_done, 2 * layer + t + 1)
                for b in range(4):
                    do(A.activation(ss[t][:, 4 * b:4 * b + 4, :].rearrange("p f s -> p (f s)"), psum[4 * (1 - t) + b][:, :], ACT.Copy),
                       s_read if b == 3 else None)
            for part in range(2):
                done = 2 * layer + part
                first = PAIRS * done
                tile = base + PEER_UV[layer] + 2 * PAIRS * part

                def split_tile(n, k):
                    kt_ = tile + k
                    if kt_ >= total:
                        return
                    act.wait_ge(raw_loaded[kt_ % RAW], n * 16 + 16 * (kt_ // RAW + 1))
                    act.wait_ge(tile_used, n * RAW + (kt_ - 1))
                    A.activation(w_hi[:, kt_ % SPLIT, :], raw[:, kt_ % RAW, :], ACT.Copy).then_inc(hi_ready, 1)

                def padded(wait, n):
                    act.wait_ge(wait, n)
                    act.sem_inc(act_pad, 1)

                def pair(ap, n, p):
                    return ap[:, 2 * p:2 * p + 2, :] if isinstance(n, int) else ap[:, bass.ds(n * 2 * RAW + 2 * p, 2), :]

                def gelu(n, p):
                    padded(tile_used, n * RAW + (tile + p + 1))
                    A.activation(pair(hid, n, p), psum[4 + p % 2][:, :].rearrange("p (j s) -> p j s", j=2), ACT.Gelu).then_inc(gelu_ready, 1)

                def upper(n, p):
                    padded(tile_used, n * RAW + (tile + PAIRS + p - 1))
                    A.activation(c_hi[:, p % 2, :].rearrange("p (j s) -> p j s", j=2), pair(hid, n, p), ACT.Copy).then_inc(c_hi_ready, 1)

                if first:
                    act.wait_ge(c_lo_ready, first)
                with act.Fori(0, PAIRS // RAW) as n:
                    for p in range(RAW):
                        split_tile(n, p + 2)
                        gelu(n, p)
                if part == 0:
                    act.wait_ge(best_ready, layer + 1)
                    do(A.activation(best[:, :, :, :], best[:, :, :, :], ACT.Exp), exp_ready)
                    for t in range(TT):
                        act.wait_ge(sel_t, 2 * layer + t + 1)
                        do(A.activation(ijg[:, :, HALVES[t]], psum[6 + t][:, 0:3 * P].rearrange("p (n s) -> p n s", n=3), ACT.Copy), ijg_ready)
                g0 = GROUPS * done

                def stage(n, b):
                    act.wait_ge(gates_done, n * HOT + (g0 + b + 1))
                    if g0 or not isinstance(n, int):
                        act.wait_ge(gated_odd, n * (HOT // 2) + (g0 // 2 + b // 2 + 1 - HOT // 2))
                    A.activation(staged[:, b // 2, :, :].rearrange("p t j -> p (t j)"), psum[4 + b][:, 0:GT * JH], ACT.Copy).then_inc(gates_read, 1)

                for b in range(1, HOT, 2):
                    stage(0, b)
                with act.Fori(1, GROUPS // HOT) as n:
                    for b in range(1, HOT, 2):
                        stage(n, b)
                act.wait_ge(gated_odd, GROUPS // 2 * (done + 1))
                act.wait_ge(gated_even, GROUPS // 2 * (done + 1))
                upper(0, 0)
                upper(0, 1)
                with act.Fori(0, PAIRS // RAW - 1) as n:
                    for p in range(RAW):
                        split_tile(n, PAIRS + p + 2)
                        upper(n, p + 2)
                for p in range(PAIRS - RAW, PAIRS):
                    split_tile(0, PAIRS + p + 2)
                    if p + 2 < PAIRS:
                        upper(0, p + 2)

        peer_layer(0, 8)
        layer_norm(1)
        split_t(12)
        for name, i in (("oq", 0), ("oq", 1), ("oqi", 0), ("okv", 0)):
            stream(name, i)
        act.wait_ge(odd_pe, ODD_PE["qt"])
        for b in range(4):
            do(A.activation(q_t[:, 2 * b:2 * b + 2, :].rearrange("p h s -> p (h s)"), psum[4 + b][:, :], ACT.Copy), odd_act if b == 3 else None)
        act.wait_ge(odd_pe, ODD_PE["it"])
        for b in range(2):
            do(A.activation(qi_t[:, 2 * b:2 * b + 2, :].rearrange("p h s -> p (h s)"), psum[b][:, :], ACT.Copy))
        do(A.activation(k_t[:, :], psum[2][:, 0:S], ACT.Copy), odd_act)
        for t in range(TT):
            act.wait_ge(odd_pe, ODD_PE[f"index{t}"])
            if t:
                act.wait_ge(odd_dve, ODD_DVE["index0"])
            for h in range(IH // 2):
                do(A.activation(rel[:, 2 * h:2 * h + 2, :].rearrange("p h s -> p (h s)"), psum[4 * t + h][:, :], ACT.Relu),
                   odd_act if h == IH // 2 - 1 else None)
        for t in range(TT):
            n = (t + 1) * P
            act.wait_ge(odd_dve, ODD_DVE[f"logits{t}"])
            for h in range(AH):
                do(A.activation(logit[:, h, 0:n], logit[:, h, 0:n], ACT.Exp, bias=amax[:, h:h + 1], accum_out=asum[:, h:h + 1]),
                   odd_act if h == AH - 1 else None)
            act.wait_ge(odd_pe, ODD_PE[f"pt{t}"])
            for b in range(4):
                for s in range(t + 1):
                    do(A.activation(pt[:, 2 * b:2 * b + 2, s, :], psum[4 + b][:, :].rearrange("p (h s k) -> p h s k", h=2, s=TT)[:, :, s, :], ACT.Copy),
                       odd_act if b == 3 and s == t else None)
            act.wait_ge(odd_pe, ODD_PE[f"o{t}"])
            for hh in range(2):
                do(A.activation(act_hi[:, 4 * hh:4 * hh + 4, HALVES[t]], psum[hh][:, :].rearrange("p (h s) -> p h s", h=4), ACT.Copy),
                   att_hi if hh else None)
        for i in range(2):
            stream("oout", i)
        layer_norm(2)
        peer_layer(1, 16)
        layer_norm(3)

    @block.vector
    def _(dve):
        do = Order(dve, dve_own)

        def bcast(ap, shape):
            return ap.broadcast_to(shape)

        def split_lo(k):
            if k < total:
                dve.wait_ge(hi_ready, k + 1)
                V.tensor_tensor(w_lo[:, k % SPLIT, :], raw[:, k % RAW, :], w_hi[:, k % SPLIT, :].bitcast(F32), ALU.subtract).then_inc(lo_ready, 1)

        def stream(name, i):
            for j in range(2):
                split_lo(base + TILE_B[name, i] + j + SPLIT)

        def taken(name, i):
            dve.wait_ge(tile_used, base + TILE_B[name, i] + 2)

        def bank(name, i, t):
            return psum[2 * (CHUNK_B[name, i] % 2) + t]

        def split_t(first):
            for b in range(KD // 2):
                dve.wait_ge(tr_hi, first + b + 1)
                ks = slice(2 * b, 2 * b + 2)
                do(V.tensor_tensor(act_lo[:, ks, :].rearrange("p k s -> p (k s)"), psum[4 + b][:, :],
                                   act_hi[:, ks, :].rearrange("p k s -> p (k s)").bitcast(F32), ALU.subtract), tr_lo)

        def residual(t, n, src):
            xs = x[:, t, n * CW:(n + 1) * CW]
            return V.scalar_tensor_tensor(out=xs, in0=xs, scalar=ALPHA, in1=src, op0=ALU.mult, op1=ALU.add)

        def layer_norm(n):
            for t in range(TT):
                for c in range(2):
                    do(V.bn_stats(small[:, 40 + 6 * c:46 + 6 * c], x[:, t, c * CW:(c + 1) * CW]))
                do(V.bn_aggr(small[:, 24 + 2 * t:26 + 2 * t], small[:, 40:52].rearrange("p (c k) -> p c k", c=2)), ln_var if t else None)
            dve.wait_ge(ln_std, n + 1)
            do(V.reciprocal(small[:, 34:36], small[:, 32:34]))
            dve.wait_ge(ln_loaded, 32 * (n + 1))
            for t in range(TT):
                do(V.tensor_scalar(x[:, t, :], x[:, t, :], small[:, 24 + 2 * t:25 + 2 * t], small[:, 34 + t:35 + t], ALU.subtract, ALU.mult))
                do(V.tensor_tensor(x[:, t, :], x[:, t, :], ln_row[:, 0, :], ALU.mult))
                do(V.tensor_tensor(x[:, t, :], x[:, t, :], ln_row[:, 1, :], ALU.add), x_ready if t else None)

        def ecolumn(name, i):
            return ecol[:, ECOL[name] + i:ECOL[name] + i + 1]

        do(V.memset(sh[:, :, 0:1], 0.0))
        dve.wait_ge(side_hi_ready, 1)
        do(V.tensor_tensor(side_lo[:, :, :].rearrange("p k n -> p (k n)"), side_raw[:, :, :].rearrange("p k n -> p (k n)"),
                           side_hi[:, :, :].rearrange("p k n -> p (k n)").bitcast(F32), ALU.subtract), side_lo_ready)
        split_t(0)
        dve.wait_ge(b_const, 16)
        dve.wait_ge(even_loaded, 48)

        def shift(dst, n, mu, signal):
            do(V.tensor_tensor(dif[:, 0:n, :], sh[:, 0:n, 0:S], sh[:, 0:n, 1:], ALU.subtract))
            for f in range(n):
                do(V.scalar_tensor_tensor(out=dst(f), in0=dif[:, f, :], scalar=mu(f), in1=sh[:, f, 1:], op0=ALU.mult, op1=ALU.add),
                   signal if f == n - 1 else None)

        dve.wait_ge(even_act, EVEN_ACT["side"])
        shift(lambda f: side_t[:, f, :], 2, lambda f: ecolumn("mu_side", f), even_dve)
        stream("gqk", 0)
        dve.wait_ge(even_act, EVEN_ACT["lnexp"])
        for g in range(GP):
            do(V.tensor_scalar(la[:, g, :], psum[5][:, g * S:(g + 1) * S], ecolumn("gla_a_b", g), 0.0, ALU.add, ALU.min))
        do(V.tensor_tensor(la[:, :, :], la[:, :, :], lb[:, :, :], ALU.subtract), even_dve)
        stream("gv", 0)
        for g in range(GP):
            do(V.tensor_tensor_scan(qin[:, g, :], cst("keep"), la[:, g, :], 0.0, ALU.mult, ALU.add))
        do(V.tensor_copy(la[:, :, :], qin[:, :, :]))
        for g in range(GP):
            sums = la[:, g, :].rearrange("p (c s) -> p c s", s=CHUNK_T)
            do(V.tensor_tensor(lb[:, g, :].rearrange("p (c s) -> p c s", s=CHUNK_T), sums,
                               bcast(sums[:, :, CHUNK_T - 1:CHUNK_T], [P, CH * TT, CHUNK_T]), ALU.subtract), even_dve if g else None)
        stream("gg", 0)
        for n, name in enumerate("rkv"):
            stream(name, 0)
            wait_read(dve, CHUNK_B[name, 0])
            shift(lambda f: rkv[:, n, f, :], FT, lambda f: ecolumn("mu", FT * n + f), shifted_done)
        dve.wait_ge(even_act, EVEN_ACT["decays"])
        do(V.scalar_tensor_tensor(out=qin[:, :, :], in0=gqk[:, 0:2, :], scalar=GDK ** -0.5, in1=eb[:, :, :], op0=ALU.mult, op1=ALU.mult))
        do(V.tensor_tensor(kin[:, :, :], kin[:, :, :], gqk[:, 2:4, :], ALU.mult))
        do(V.memset(qz[:, :, :, :], 0.0))
        for c in range(CH):
            for g in range(GP):
                cut = lambda ap: ap.rearrange("p (t c s) -> p t c s", c=CH, s=CHUNK_T)[:, :, c, :]
                do(V.tensor_copy(cut(qz[:, c, g, :]), cut(qin[:, g, :])))
        do(V.tensor_tensor(en[:, :, :], en[:, :, :], gqk[:, 2:4, :], ALU.mult), even_dve)
        upto = cst("strict_upto")[:, P:2 * P]
        dve.wait_ge(even_pe, EVEN_PE["keys"])
        for e in range(2):
            do(V.tensor_tensor(attn[:, e, :, :, :].rearrange("p t g s -> p (t g) s"), psum[4 + e][:, :].rearrange("p (n s) -> p n s", n=TT * GP),
                               bcast(upto.unsqueeze(1), [P, TT * GP, P]), ALU.mult), even_dve if e else None)
        dve.wait_ge(even_pe, EVEN_PE["kv"])
        for c in range(CH * TT - 1):
            for g in range(GP):
                do(V.tensor_tensor(state[:, c + 1, g, :], psum[c][:, g * S:(g + 1) * S], cst("diag2"), ALU.mult))
                if c:
                    do(V.scalar_tensor_tensor(out=state[:, c + 1, g, :], in0=state[:, c, g, :], scalar=eb[:, g, (c + 1) * CHUNK_T - 1:(c + 1) * CHUNK_T],
                                              in1=state[:, c + 1, g, :], op0=ALU.mult, op1=ALU.add),
                       even_dve if c == CH * TT - 2 and g == GP - 1 else None)
        dve.wait_ge(even_act, EVEN_ACT["std"])
        do(V.reciprocal(small[:, 8:16], small[:, 8:16]))
        for t in range(TT):
            for h in range(GH):
                hs = slice(h * GDV, (h + 1) * GDV)
                do(V.scalar_tensor_tensor(out=ymix[:, t, hs], in0=psum[6 + t][:, hs], scalar=small[:, 8 + t * GH + h:9 + t * GH + h],
                                          in1=erow[:, EROW["gla_g"]], op0=ALU.mult, op1=ALU.mult))
            do(V.tensor_tensor(ymix[:, t, 0:EW], ymix[:, t, 0:EW], gsil[:, t, :], ALU.mult), even_dve if t else None)

        flat = lambda ap: ap.rearrange("p f s -> p (f s)")
        dve.wait_ge(tile_used, base + EVEN + 12)
        do(V.memset(s_all[:, 0, :, :], 0.0))
        do(V.memset(rz[:, :, :, :], 0.0))
        for f in range(FT):
            do(V.tensor_scalar(rkind[:, f, :], cst("half"), ecolumn("r_k", f), None, ALU.mult))
        for t in range(TT):
            by_act = lambda step: dve.wait_ge(rw_act, t * len(RW_ACT) + RW_ACT[step])
            by_pe = lambda step: dve.wait_ge(rw_pe, t * len(RW_PE) + RW_PE[step])
            ts = HALVES[t]
            r, k, v = (rkv[:, n, :, ts] for n in range(3))
            if t:
                do(V.tensor_copy(s_all[:, 0, :, :], s_all[:, 2, :, :]))
            do(V.tensor_scalar(tmp[:, :, :], sgw[:, :, ts], -float(np.exp(-0.5)), None, ALU.mult))
            for f in range(FT):
                do(V.tensor_tensor_scan(cw[:, f, :], cst("keep")[:, 0:P], tmp[:, f, :], 0.0, ALU.mult, ALU.add))
            do(V.tensor_tensor(pm[:, :, :], cw[:, :, :], tmp[:, :, :], ALU.subtract), rw_dve)
            for f in range(FT):
                do(V.tensor_scalar(kk[:, f, :], k[:, f, :], ecolumn("k_k", f), None, ALU.mult))
            do(V.tensor_tensor(tmp[:, :, :], kk[:, :, :], kk[:, :, :], ALU.mult), rw_dve)
            for f in range(FT):
                do(V.tensor_scalar(kp[:, f, :], asig[:, f, ts], -1.0, ecolumn("k_a", f), ALU.add, ALU.mult))
            do(V.scalar_tensor_tensor(out=kp[:, :, :], in0=kp[:, :, :], scalar=1.0, in1=k, op0=ALU.add, op1=ALU.mult))
            do(V.tensor_tensor(kt[:, :, :], r, kp[:, :, :], ALU.mult), rw_dve)
            by_pe("bonus")
            do(V.tensor_copy(bonus[:, :], psum[1][:, 0:RH]))
            by_act("norm")
            n0 = xx[:, 0, :, :]
            do(V.tensor_scalar(n0, n0, 1e-12, None, ALU.max))
            do(V.reciprocal(n0, n0))
            do(V.tensor_tensor(kk[:, :, :], kk[:, :, :], n0, ALU.mult))
            do(V.scalar_tensor_tensor(out=ar[:, :, 0, :], in0=kk[:, :, :], scalar=-1.0, in1=pm[:, :, :], op0=ALU.mult, op1=ALU.mult))
            do(V.tensor_tensor(ar[:, :, 1, :], r, pinc[:, :, :], ALU.mult))
            for c in range(CH):
                cs = slice(c * CHUNK_T, (c + 1) * CHUNK_T)
                do(V.tensor_copy(rz[:, c, :, cs], ar[:, :, 1, cs]))
            do(V.tensor_tensor(bt[:, :, :], kk[:, :, :], asig[:, :, ts], ALU.mult))
            do(V.tensor_tensor(bt[:, :, :], bt[:, :, :], pinv[:, :, :], ALU.mult))
            do(V.tensor_tensor(kt[:, :, :], kp[:, :, :], pinv[:, :, :], ALU.mult), rw_dve)
            for step, dst in (("lb", lrb), ("lk", lrk)):
                by_pe(step)
                if step == "lk":
                    for e in range(2):
                        for f in range(FT):
                            do(V.tensor_copy(dd[:, e, f, :], ident))
                            do(V.tensor_copy(dt_[:, e, f, :], ident))
                for b in range(4):
                    do(V.tensor_tensor(dst[:, b // 2, 2 * (b % 2):2 * (b % 2) + 2, :], psum[4 + b][:, :].rearrange("p (f s) -> p f s", f=2),
                                       bcast(cst("strict_upto").unsqueeze(1), [P, 2, 2 * P]), ALU.mult), rw_dve if b == 3 else None)
            for n in range(LEVELS):
                by_pe(f"x{n}")
                level = cst("levels")[:, n * P:(n + 1) * P]
                for e in range(2):
                    do(V.tensor_tensor(xx[:, e, :, :], psum[e][:, :].rearrange("p (f s) -> p f s", f=FT),
                                       bcast(level.unsqueeze(1), [P, FT, P]), ALU.mult), rw_dve if e else None)
                by_pe(f"d{n}")
                for e in range(2):
                    do(V.tensor_tensor(flat(dd[:, e, :, :]), flat(dd[:, e, :, :]), psum[2 + e][:, :], ALU.add))
                    do(V.tensor_tensor(flat(dt_[:, e, :, :]), flat(dt_[:, e, :, :]), psum[4 + e][:, :], ALU.add), rw_dve if e else None)
            by_pe("z")
            do(V.tensor_copy(flat(zz[:, :, :]), psum[6][:, :]), rw_dve)
            by_pe("wv")
            do(V.tensor_copy(flat(wv[:, :, :]), psum[7][:, :]), rw_dve)
            for c in range(CH):
                cs = slice(c * CHUNK_T, (c + 1) * CHUNK_T)
                by_pe(f"u{c}")
                do(V.tensor_tensor(flat(uu[cs, :, :]), psum[2 + c][cs, :], flat(wv[cs, :, :]), ALU.add), rw_dve)
                by_pe(f"s{c}")
                nxt = s_all[:, c + 1, :, :]
                do(V.tensor_tensor(nxt, psum[4 + c][:, :].rearrange("p (f s) -> p f s", f=FT), bcast(cst("same_head").unsqueeze(1), [P, FT, P]), ALU.mult))
                do(V.tensor_tensor(nxt, nxt, s_all[:, c, :, :], ALU.add))
                do(V.tensor_tensor(nxt, nxt, bcast(pinc[:, :, (c + 1) * CHUNK_T - 1:(c + 1) * CHUNK_T], [P, FT, P]), ALU.mult), rw_dve)
            by_pe("y")
            for h in range(RH):
                do(V.bn_stats(r6[:, :], psum[6][:, h * RN:(h + 1) * RN]))
                do(V.bn_aggr(rstat[:, h, :], r6[:, :]), rw_dve if h == RH - 1 else None)
            by_act("std")
            do(V.reciprocal(small[:, 8:16], small[:, 0:8]))
            yo = ymix[:, t, EW:2 * EW]
            for h in range(RH):
                hs = slice(h * RN, (h + 1) * RN)
                do(V.tensor_scalar(yo[:, hs], psum[6][:, hs], rstat[:, h, 0:1], small[:, 8 + h:9 + h], ALU.subtract, ALU.mult))
            do(V.tensor_tensor(yo, yo, erow[:, EROW["lnx_g"]], ALU.mult))
            do(V.tensor_tensor(yo, yo, erow[:, EROW["lnx_b"]], ALU.add))
            for h in range(RH):
                hs = slice(h * RN, (h + 1) * RN)
                do(V.scalar_tensor_tensor(out=yo[:, hs], in0=flat(nat["v"][:, :, :])[:, hs], scalar=bonus[:, h:h + 1], in1=yo[:, hs],
                                          op0=ALU.mult, op1=ALU.add))
            do(V.tensor_tensor(yo, yo, gnat[:, t, :], ALU.mult), rw_dve)
        split_t(4)
        for i in range(2):
            stream("eout", i)
            taken("eout", i)
            for t in range(TT):
                do(residual(t, i, bank("eout", i, t)[:, :]), read_dve if t else None)
        layer_norm(0)

        def peer_layer(layer, t0):
            split_t(t0)
            for i in range(2):
                stream(f"pq{layer}", i)
            def top16(streams):
                for vals, top, _ in streams:
                    do.also(V.max(top[:, 0:8], vals))
                do.settle()
                for vals, top, idx in streams:
                    do.also(V.max_index(idx[:, 0:8], top[:, 0:8], vals))
                do.settle()
                for vals, top, _ in streams:
                    do.also(V.match_replace(out=vals, in_to_replace=top[:, 0:8], in_values=vals, imm_value=-3e38))
                do.settle()
                for vals, top, _ in streams:
                    do.also(V.max(top[:, 8:16], vals))
                do.settle()
                for vals, top, idx in streams:
                    do.also(V.max_index(idx[:, 8:16], top[:, 8:16], vals))
                do.settle()

            def choose(t, split):
                dve.wait_ge(s_read, 2 * layer + t + 1)
                for n in range(0, 2 * PH, 2):
                    top16([(ss[t][:, c, :], tops[:, c, :], topi[:, c, :]) for c in (n, n + 1)])
                    split(n // 2)
                do(V.tensor_copy(topf[:, :, :], topi[:, :, :]))
                cand = ss[t][:, :, :].rearrange("p (h c) n -> p h (c n)", h=PH)
                for h in range(0, PH, 2):
                    for i in (h, h + 1):
                        do.also(V.tensor_tensor(cand[:, i, :].rearrange("p (a b) -> p a b", a=PK), bcast(tops[:, 2 * i, :].unsqueeze(2), [P, PK, PK]),
                                                bcast(tops[:, 2 * i + 1, :].unsqueeze(1), [P, PK, PK]), ALU.add))
                    do.settle()
                    top16([(cand[:, i, :], best[:, t, i, :], pos[:, i, :]) for i in (h, h + 1)])
                    split(PH + h // 2)
                do(V.tensor_copy(gsum[:, 0:PH], best[:, t, :, 0]))
                do(V.tensor_tensor(best[:, t, :, :], best[:, t, :, :], bcast(gsum[:, 0:PH].unsqueeze(2), [P, PH, PK]), ALU.subtract),
                   best_ready if t else None)
                pf = pos[:, :, :].rearrange("p h k -> p (h k)")
                do.also(V.tensor_scalar(posab[:, 0, :], pf, 4, None, ALU.logical_shift_right))
                do(V.tensor_scalar(posab[:, 1, :], pf, PK - 1, None, ALU.bitwise_and))
                do(V.tensor_copy(posf[:, :, :], posab[:, :, :]))
                tf = topf[:, :, :].rearrange("p (h c) k -> p h c k", c=2)
                split(PH + 4)
                for c in range(2):
                    do(V.tensor_tensor(hot.rearrange("p h k a -> p (h k) a"), bcast(posf[:, c, :].unsqueeze(2), [P, PH * PK, PK]),
                                       bcast(cst("iota")[:, 0:PK].unsqueeze(1), [P, PH * PK, PK]), ALU.is_equal))
                    do(V.tensor_tensor(hot, hot, bcast(tf[:, :, c, :].unsqueeze(2), [P, PH, PK, PK]), ALU.mult))
                    do(V.reduce_sum(sel[:, t, c, :], hot.rearrange("p h k a -> p (h k) a"), AXX))
                    split(PH + 5 + c)
                split(PH + 7)

            for part in range(2):
                done = 2 * layer + part
                first, g0 = PAIRS * done, GROUPS * done
                tile = base + PEER_UV[layer] + 2 * PAIRS * part

                def split_tile(n, k):
                    kt_ = tile + k
                    if kt_ >= total:
                        return
                    dve.wait_ge(hi_ready, n * RAW + (kt_ + 1))
                    V.tensor_tensor(w_lo[:, kt_ % SPLIT, :], raw[:, kt_ % RAW, :], w_hi[:, kt_ % SPLIT, :].bitcast(F32), ALU.subtract).then_inc(lo_ready, 1)

                if part == 0:
                    for t in range(TT):
                        choose(t, lambda n: split_tile(0, t * PAIRS // 2 + n + 2))
                    dve.wait_ge(exp_ready, layer + 1)
                    do(V.reduce_sum(gsum[:, :], best[:, :, :, :].rearrange("p t h k -> p (t h) k"), AXX))
                    do(V.reciprocal(gsum[:, :], gsum[:, :]))
                    for t in range(TT):
                        do(V.tensor_tensor(sel[:, t, 2, :].rearrange("p (h k) -> p h k", h=PH), best[:, t, :, :],
                                           bcast(gsum[:, t * PH:(t + 1) * PH].unsqueeze(2), [P, PH, PK]), ALU.mult), sel_ready)
                    dve.wait_ge(ijg_ready, 2 * layer + 2)
                else:
                    with dve.Fori(0, PAIRS // RAW) as n:
                        for p in range(RAW):
                            split_tile(n, p + 2)

                def one_hot(n, b):
                    tok = bass.ds(n * HOT * GT + b * GT, GT)
                    if not isinstance(n, int):
                        dve.wait_ge(gates_done, n * HOT + (g0 + b + 1 - HOT))
                    V.tensor_tensor(hot_j[:, b, :, :], bcast(cst("iota")[:, part * JH:(part + 1) * JH].unsqueeze(1), [P, GT, JH]),
                                    bcast(ijg[:, 1, tok].unsqueeze(2), [P, GT, JH]), ALU.is_equal)
                    V.tensor_tensor(hot_i[:, b, :, :], bcast(cst("iota").unsqueeze(1), [P, GT, KEYS]),
                                    bcast(ijg[:, 0, tok].unsqueeze(2), [P, GT, KEYS]), ALU.is_equal).then_inc(hot_eq, 1)

                def apply(n, b):
                    dve.wait_ge(gates_done, n * HOT + (g0 + b + 1))
                    tok = hid[:, :, bass.ds(n * HOT * GT + b * GT, GT)].rearrange("p j t -> p t j")
                    V.tensor_tensor(tok, tok, psum[4 + b][:, 0:GT * JH].rearrange("p (t j) -> p t j", t=GT), ALU.mult).then_inc(gated_even, 1)

                for b in range(HOT):
                    one_hot(0, b)
                dve.wait_ge(gelu_ready, first + PAIRS)
                with dve.Fori(0, GROUPS // HOT - 1) as n:
                    for b in range(HOT):
                        if b % 2 == 0:
                            apply(n, b)
                        one_hot(n + 1, b)
                for b in range(0, HOT, 2):
                    apply(GROUPS // HOT - 1, b)

                def lower(n, p):
                    dve.wait_ge(c_hi_ready, n * RAW + (first + p + 1))
                    at = slice(2 * p, 2 * p + 2) if isinstance(n, int) else bass.ds(n * 2 * RAW + 2 * p, 2)
                    halves = lambda ap: ap.rearrange("p (j s) -> p j s", j=2)
                    V.tensor_tensor(halves(c_lo[:, p % 2, :]), hid[:, at, :], halves(c_hi[:, p % 2, :]).bitcast(F32), ALU.subtract).then_inc(c_lo_ready, 1)

                lower(0, 0)
                lower(0, 1)
                with dve.Fori(0, PAIRS // RAW - 1) as n:
                    for p in range(RAW):
                        split_tile(n, PAIRS + p + 2)
                        lower(n, p + 2)
                for p in range(PAIRS - RAW, PAIRS):
                    split_tile(0, PAIRS + p + 2)
                    if p + 2 < PAIRS:
                        lower(0, p + 2)
            dve.wait_ge(tile_used, base + PEER_UV[layer] + 4 * PAIRS)
            for t in range(TT):
                for n in range(2):
                    do(residual(t, n, psum[2 * t + n][:, :]))

        peer_layer(0, 8)
        layer_norm(1)
        split_t(12)

        def rope(dst, src, width, t):
            w = width // 2
            heads = dst.shape[1] // width
            cut = lambda ap: ap.rearrange("p (h n) -> p h n", n=width)
            cos = bcast(cst(f"cos{width}")[:, t * w:(t + 1) * w].unsqueeze(1), [P, heads, w])
            sin = bcast(cst(f"sin{width}")[:, t * w:(t + 1) * w].unsqueeze(1), [P, heads, w])
            x1, x2 = cut(src)[:, :, 0:w], cut(src)[:, :, w:width]
            o1, o2 = cut(dst)[:, :, 0:w], cut(dst)[:, :, w:width]
            r1 = rtmp[:, 0:heads * w].rearrange("p (h n) -> p h n", n=w)
            do(V.tensor_tensor(o1, x1, cos, ALU.mult))
            do(V.tensor_tensor(r1, x2, sin, ALU.mult))
            do(V.tensor_tensor(o1, o1, r1, ALU.subtract))
            do(V.tensor_tensor(o2, x2, cos, ALU.mult))
            do(V.tensor_tensor(r1, x1, sin, ALU.mult))
            return V.tensor_tensor(o2, o2, r1, ALU.add)

        for i in range(2):
            stream("oq", i)
            taken("oq", i)
            for t in range(TT):
                do(rope(qn[:, t, i * CW:(i + 1) * CW], bank("oq", i, t)[:, :], AD, t), read_dve if t else None)
        stream("oqi", 0)
        taken("oqi", 0)
        for t in range(TT):
            do(rope(qin_[:, t, :], bank("oqi", 0, t)[:, :], ID, t), read_dve if t else None)
        stream("okv", 0)
        taken("okv", 0)
        for t in range(TT):
            src = bank("okv", 0, t)
            do(rope(kn[:, t, :], src[:, 0:AD], AD, t))
            do(V.tensor_copy(vn[:, t, :], src[:, AD:2 * AD]))
            do(rope(kid[:, t, 0:ID], src[:, 2 * AD:2 * AD + ID], ID, t))
            do(V.tensor_scalar(wi[:, t, :], src[:, 2 * AD + ID:2 * AD + ID + IH], float(IH ** -0.5 * ID ** -0.5), None, ALU.mult), read_dve if t else None)
        do(V.tensor_copy(kid[:, :, ID:2 * ID], kid[:, :, 0:ID]), odd_dve)
        do(V.memset(kib[:, :], 0.0))
        dve.wait_ge(odd_pe, ODD_PE["it"])
        do(V.tensor_copy(kib[0:ID, 0:S], psum[3][0:ID, 0:S]))
        do(V.tensor_copy(kib[ID:P, S:2 * S], psum[3][ID:P, 0:S]), odd_dve)
        for t in range(TT):
            dve.wait_ge(odd_act, ODD_ACT[f"index{t}"])
            for h in range(IH):
                wh = wi[:, t, h:h + 1]
                if h == 0:
                    ins = V.tensor_scalar(score[:, t, :], rel[:, h, :], wh, None, ALU.mult)
                else:
                    ins = V.scalar_tensor_tensor(out=score[:, t, :], in0=rel[:, h, :], scalar=wh, in1=score[:, t, :], op0=ALU.mult, op1=ALU.add)
                do(ins, odd_dve if h == IH - 1 else None)
        for t in range(TT):
            causal, sc, ma = cst("causal")[:, t * S:(t + 1) * S], score[:, t, :], madd[:, t, :]
            do(V.tensor_scalar(ma, causal, -1.0, NEG, ALU.add, ALU.mult))
            do(V.tensor_tensor(sc, sc, causal, ALU.mult))
            do(V.tensor_tensor(sc, sc, ma, ALU.add))
            for n in range(SELECT // 8):
                do(V.max(top8[:, :], sc))
                do(V.match_replace(out=sc, in_to_replace=top8[:, :], in_values=sc, imm_value=-3e38))
            do(V.scalar_tensor_tensor(out=ma, in0=sc, scalar=-2e30, in1=causal, op0=ALU.is_lt, op1=ALU.mult))
            do(V.tensor_scalar(ma, ma, -1.0, NEG, ALU.add, ALU.mult))
        for t in range(TT):
            n = (t + 1) * P
            dve.wait_ge(odd_pe, ODD_PE[f"logits{t}"])
            for b in range(4):
                do(V.scalar_tensor_tensor(out=logit[:, 2 * b:2 * b + 2, 0:n], in0=psum[b][:, :].rearrange("p (h s) -> p h s", h=2)[:, :, 0:n],
                                          scalar=AD ** -0.5, in1=bcast(madd[:, t, 0:n].unsqueeze(1), [P, 2, n]), op0=ALU.mult, op1=ALU.add))
            do(V.reduce_max(amax[:, :], logit[:, :, 0:n], AXX))
            do(V.tensor_scalar(amax[:, :], amax[:, :], -1.0, None, ALU.mult), odd_dve)
            dve.wait_ge(odd_act, ODD_ACT[f"exp{t}"])
            do(V.reciprocal(asum[:, :], asum[:, :]))
            do(V.tensor_tensor(logit[:, :, 0:n], logit[:, :, 0:n], bcast(asum[:, :].unsqueeze(2), [P, AH, n]), ALU.mult), odd_dve)
            dve.wait_ge(att_hi, t + 1)
            for hh in range(2):
                hs = slice(4 * hh, 4 * hh + 4)
                do(V.tensor_tensor(act_lo[:, hs, HALVES[t]], psum[hh][:, :].rearrange("p (h s) -> p h s", h=4),
                                   act_hi[:, hs, HALVES[t]].bitcast(F32), ALU.subtract), att_lo if hh else None)
        for i in range(2):
            stream("oout", i)
            taken("oout", i)
            for t in range(TT):
                do(residual(t, i, bank("oout", i, t)[:, :]), read_dve if t else None)
        layer_norm(2)
        peer_layer(1, 16)
        layer_norm(3)


def program(nc, x_in, weights, rows, cols, bgate, p_t, w_pe, final_row, identity, consts_a, erows, ecols, lora_w, side_w, keys, ln_rows,
            consts_b, out):
    ctx = ExitStack()
    with ctx:
        m = Common(nc, ctx, weights)
        first_block(nc, ctx, m, x_in, rows, cols, bgate, p_t, w_pe, final_row, identity, consts_a)
        second_block(nc, ctx, m, LAYERS * TILES_A, erows, ecols, lora_w, side_w, keys, ln_rows, consts_b, out)


def _weight_tiles(w):
    k, n = w.shape
    return w.reshape(k // (KB * P), KB, P, n // CW, CW).transpose(3, 0, 2, 1, 4).reshape(-1, P, TW)


def _cols(v):
    return v.reshape(-1, P).T


def _constants_a():
    p, t = np.arange(P)[:, None], np.arange(P)[None, :]
    log_gamma = np.log(1.0 - 2.0 ** (-5.0 - np.arange(HEADS)))
    decay = []
    for h in range(HEADS):
        near = np.where(t >= p, np.exp(np.maximum(t - p, 0) * log_gamma[h]), 0.0)
        far = np.exp((t + P - p) * log_gamma[h])
        decay += [near, far, near]
    inv = np.float32(10000.0) ** (-np.arange(0, 256, 2, dtype=np.float32) / np.float32(256))
    ang = inv[:, None] * np.arange(S, dtype=np.float32)[None, :]
    sel = np.zeros((P, HEADS * P))
    for h in range(HEADS):
        sel[h, h * P:(h + 1) * P] = 1.0
    parts = {"cum": t >= p, "ones": np.ones((P, P)), "mask": np.where(t >= p, 0.0, NEG),
             "decay": np.concatenate(decay, 1) / 16.0, "cos": np.cos(ang.astype(np.float64)), "sin": np.sin(ang.astype(np.float64)), "headsel": sel,
             "eps": np.full((P, 1), EPS), "one": np.ones((P, 1))}
    return np.concatenate([np.asarray(parts[n], np.float32) for n in CONST_A], 1)


def _first_block_arrays(i):
    w = []
    rows, cols, bgate = [], [], []
    for l in range(LAYERS):
        w_in, b_in = i["w_in"][l], i["b_in"][l]
        at = {}
        off = 0
        for name, n in (("mq", 1024), ("mk", 1024), ("mv", 1024), ("mo", 1024), ("gates", 8), ("rq", 1024), ("rk", 1024),
                        ("rv", 2048), ("rg", 2048), ("gm", 1024), ("gr", 1024)):
            at[name] = slice(off, off + n)
            off += n
        both = {"mqk": ("mq", "mk"), "rqk": ("rq", "rk")}
        part = lambda name: np.concatenate([w_in[:, at[n]] for n in both.get(name, (name,))], 1)
        ff1, ff2 = i["w_ff1"][l], i["w_ff2"][l]
        ws = {"bm": i["w_bm"][l], "br": i["w_br"][l], "out": i["w_out"][l], "ffa1": ff1[:, :2048], "ffa2": ff2[:2048],
              "ffb1": ff1[:, 2048:], "ffb2": ff2[2048:], "peg": i["w_pe_gate"][l]}
        for name, _, _ in ORDER_A:
            w.append(_weight_tiles(ws[name] if name in ws else part(name)))
        g = {"mo": i["m_norm_g"][l], "rg": i["r_norm_g"][l]}
        for name, n in (("mv", 2), ("mo", 2), ("gm", 2), ("rv", 4), ("rg", 4), ("gr", 2), ("ffb2", 2)):
            b = i["b_ff2"][l] if name == "ffb2" else b_in[at[name]]
            for c in range(n):
                rows.append(b[c * CW:(c + 1) * CW])
                if name in g:
                    rows.append(g[name][c * CW:(c + 1) * CW])
        cat = lambda a, b: np.concatenate([b_in[at[a]], b_in[at[b]]])
        cols.append(np.concatenate(
            [_cols(i[f"norm{n}_g"][l]) for n in (1, 2, 3)] + [_cols(cat("mq", "mk")), _cols(cat("rq", "rk"))]
            + [_cols(i["conv_w"][l][j]) for j in range(4)] + [_cols(i["conv_b"][l]), _cols(i["b_ff1"][l])]
            + [w_in[:, at["gates"]].reshape(KD, P, 8).transpose(1, 0, 2).reshape(P, 64)], 1))
        bgate.append(b_in[at["gates"]])
    return {
        "x_in": i["x"][0].reshape(TT, P, D).transpose(1, 0, 2),
        "rows": np.stack(rows).reshape(LAYERS, ROWS_A, CW),
        "cols": np.stack(cols),
        "bgate": np.stack(bgate),
        "p_t": i["p"][:, 0].reshape(LAYERS, S, 2, P).transpose(0, 3, 2, 1),
        "w_pe": i["w_pe"].reshape(LAYERS, 2, P, D).transpose(0, 2, 1, 3),
        "final_row": i["final_g"],
        "identity": np.eye(P, dtype=np.float32),
        "consts_a": _constants_a(),
    }, w


def _constants_b():
    p, t = np.arange(P)[:, None], np.arange(P)[None, :]
    same = p // CHUNK_T == t // CHUNK_T
    tok = np.arange(S).reshape(TT, P).T
    levels = [(p // (2 << n) == t // (2 << n)) & ((p >> n) % 2 == 1) & ((t >> n) % 2 == 0) for n in range(LEVELS)]

    def angles(dim):
        inv = np.float32(10000.0) ** (-np.arange(0, dim, 2, dtype=np.float32) / np.float32(dim))
        return (tok.astype(np.float32)[:, :, None] * inv).astype(np.float64).reshape(P, -1)

    parts = {"same_head": same, "strict_upto": np.concatenate([(p < t) & same, (p <= t) & same], 1),
             "diag2": p // GDK == np.arange(2 * P)[None, :] // GDV, "levels": np.concatenate(levels, 1),
             "keep": np.broadcast_to(np.arange(S) % CHUNK_T != 0, (P, S)), "half": p // RN == np.arange(2)[None, :],
             "iota": np.broadcast_to(np.arange(P), (P, P)), "causal": (np.arange(S) <= tok[:, :, None]).reshape(P, -1),
             "cos128": np.cos(angles(128)), "sin128": np.sin(angles(128)), "cos64": np.cos(angles(64)), "sin64": np.sin(angles(64)),
             "ln_eps": np.full((P, 1), LN_EPS), "lnx_eps": np.full((P, 1), LNX_EPS), "one": np.ones((P, 1))}
    return np.concatenate([np.asarray(parts[n], np.float32) for n in CONST_B], 1)


def _expert_tiles(u, v):
    u = u.reshape(KEYS, KEYS // 2, 2, KD, P).transpose(1, 4, 3, 2, 0).reshape(KEYS // 2, P, TW)
    v = v.reshape(KEYS, KEYS // 2, 2 * D).transpose(1, 0, 2)
    tiles = []
    for first in range(0, KEYS // 2, PAIRS):
        tiles += [u[first:first + PAIRS], v[first:first + PAIRS]]
    return np.concatenate(tiles, 0)


def _second_block_arrays(i):
    g = lambda name: i[name + "_2"]
    w_in, mu = g("even_w_in")[0], g("rwkv_mu")[0]
    ends = np.cumsum([256, 256, 512, 512, 16, 512, 512, 512, 32, 32, 96])
    gq, gk, gv, gg, gal, r, k, v, wl, al, gl = np.split(w_in, ends[:-1], 1)
    mr, mk, mv, mwl, mal, mgl = np.split(mu, (ends[5:-1] - ends[4]))
    zeros = lambda *s: np.zeros(s, np.float32)
    side = np.concatenate([gl, wl, gal, zeros(D, 16), al, zeros(D, 64)], 1)
    lora = zeros(P, LORA)
    lora[G2], lora[W2], lora[A2] = g("rwkv_g2")[0], g("rwkv_w2")[0], g("rwkv_a2")[0]
    lora[0:16, GA2[1]] = g("gla_a_w2")[0]
    cols = {"mu_side": _cols(np.concatenate([mgl, mwl, zeros(32), mal, zeros(64)])), "mu": _cols(np.concatenate([mr, mk, mv])),
            "gla_a_b": _cols(g("gla_a_b")[0]), "w0": _cols(g("rwkv_w0")[0]), "a0": _cols(g("rwkv_a0")[0]), "k_k": _cols(g("rwkv_k_k")[0]),
            "k_a": _cols(g("rwkv_k_a")[0]), "r_k": _cols(g("rwkv_r_k")[0].reshape(-1))}
    odd = g("odd_w_in")[0]
    okv = np.concatenate([odd[:, 1024:1280], odd[:, 1792:], zeros(D, CW - 256 - 72)], 1)
    keys = zeros(LAYERS, 2, 64, PH, 2, KEYS)
    for c in range(2):
        keys[:, c, :, :, c, :] = g("peer_sub_keys")[:, :, c].transpose(0, 3, 1, 2)
    weights = []
    for layer in range(LAYERS):
        if layer == 0:
            weights += [_weight_tiles(w) for w in (np.concatenate([gq, gk], 1), gv, gg, r, k, v, g("even_w_out")[0])]
        else:
            weights += [_weight_tiles(w) for w in (odd[:, :1024], odd[:, 1280:1792], okv, g("odd_w_out")[0])]
        weights += [_weight_tiles(g("peer_w_q")[layer]), _expert_tiles(g("peer_u")[layer], g("peer_v")[layer])]
    norms = [g(f"{n}_ln_{p}")[layer] for layer in range(LAYERS) for n in ("mix", "ffn") for p in "gb"]
    return {
        "erows": np.concatenate([g("gla_norm_g")[0], g("rwkv_lnx_g")[0], g("rwkv_lnx_b")[0]]),
        "ecols": np.concatenate([cols[n] for n in ECOL], 1),
        "lora_w": lora,
        "side_w": side.reshape(KD, P, 2 * P).transpose(1, 0, 2),
        "keys": keys.reshape(LAYERS, P, PH, 2 * KEYS),
        "ln_rows": np.stack(norms),
        "consts_b": _constants_b(),
    }, weights


def kernel(**inputs):
    import concourse.bacc as bacc
    from concourse.bass_utils import run_bass_kernel_spmd

    i = {name: np.asarray(a) for name, a in inputs.items()}
    arrays, first = _first_block_arrays(i)
    more, second = _second_block_arrays(i)
    arrays.update(more)
    arrays["weights"] = np.concatenate(first + second, 0)
    arrays = {name: np.ascontiguousarray(a) for name, a in arrays.items()}
    nc = bacc.Bacc("TRN2", target_bir_lowering=False, num_devices=1)
    aps = {name: nc.dram_tensor(name, a.shape, mybir.dt.from_np(a.dtype), kind="ExternalInput").ap() for name, a in arrays.items()}
    aps["out"] = nc.dram_tensor("out", (P, TT, D), F32, kind="ExternalOutput").ap()
    program(nc, **aps)
    r = run_bass_kernel_spmd(nc, [arrays], core_ids=[0])
    return r.results[0]["out"].transpose(1, 0, 2).reshape(1, S, D)
```

```python
from contextlib import ExitStack

import numpy as np
import concourse.bass as bass
from concourse import mybir

F32 = mybir.dt.float32
F32R = mybir.dt.float32r
U32 = mybir.dt.uint32
ALU = mybir.AluOpType
ACT = mybir.ActivationFunctionType
AXX = mybir.AxisListType.X

P = 128
D = 1024
S = 256
TT = S // P
KD = D // P
LAYERS = 2
CW = 512
KB = 4
TW = KB * CW
RAW = 4
SPLIT = 2
EPS = 1e-6
HEADS = 4
MDV = 256
RDV = 512
NEG = 1e30

ORDER_A = [("mqk", 4, 2), ("mv", 2, 2), ("mo", 2, 2), ("gm", 2, 2), ("bm", 2, 2), ("rqk", 4, 2), ("rv", 4, 2),
           ("rg", 4, 2), ("gr", 2, 2), ("br", 2, 4), ("out", 2, 2), ("ffa1", 4, 2), ("ffa2", 2, 4),
           ("ffb1", 4, 2), ("ffb2", 2, 4), ("peg", 2, 2)]
CHUNK, TILE = {}, {}
_c = _t = 0
for _name, _n, _per in ORDER_A:
    for _i in range(_n):
        CHUNK[_name, _i] = _c
        TILE[_name, _i] = _t
        _c, _t = _c + 1, _t + _per
CHUNKS_A, TILES_A = _c, _t
PER_CHUNK = {_name: _per for _name, _n, _per in ORDER_A}
assert CHUNKS_A % 2 == 0 and TILES_A % RAW == 0

BY_ACT = ("mqk", "rqk", "ffa1", "ffb1")
TAKEN = []
for _name, _n, _ in ORDER_A:
    for _i in range(_n):
        TAKEN.append((_name in BY_ACT, 1 + sum(a == (_name in BY_ACT) for a, _ in TAKEN)))

ROW_OF = {}
ROW_CHUNK = []
for _name, _n, _gains in (("mv", 2, 0), ("mo", 2, 1), ("gm", 2, 0), ("rv", 4, 0), ("rg", 4, 1), ("gr", 2, 0), ("ffb2", 2, 0)):
    for _i in range(_n):
        ROW_OF[_name, _i] = len(ROW_CHUNK)
        ROW_CHUNK += [CHUNK[_name, _i]] * (1 + _gains)
ROWS_A = len(ROW_CHUNK)
RROW = 4
assert ROWS_A % RROW == 0

COL = {}
_c = 0
for _name, _n in (("norm1", 8), ("norm2", 8), ("norm3", 8), ("bmqk", 16), ("brqk", 16), ("convw", 64), ("convb", 16),
                  ("bff1", 32), ("gatew", 64)):
    COL[_name] = _c
    _c += _n
COLS_A = _c

T_H, T_YM, T_YR, T_MG, T_H2, T_H3, T_ALL = 0, 4, 8, 16, 20, 24, 28

CONST_A = {}
_c = 0
for _name, _n in (("cum", P), ("ones", P), ("mask", P), ("decay", HEADS * 384), ("cos", S), ("sin", S), ("headsel", HEADS * P),
                  ("eps", 1), ("one", 1)):
    CONST_A[_name] = (_c, _n)
    _c += _n
CONSTS_A = _c
CHUNK_T = 64
LEVELS = 6
CONST_B = {}
_c = 0
for _name, _n in (("same_head", P), ("upto", P), ("strict_upto", 2 * CHUNK_T), ("diag2", 2 * P),
                  ("levels", LEVELS * CHUNK_T), ("eye64", CHUNK_T), ("keep", S), ("half", 2),
                  ("iota", P), ("causal", TT * S), ("cos128", TT * 64), ("sin128", TT * 64), ("cos64", TT * 32), ("sin64", TT * 32),
                  ("ln_eps", 1), ("lnx_eps", 1), ("one", 1)):
    CONST_B[_name] = (_c, _n)
    _c += _n
CONSTS_B = _c

B0 = LAYERS * TILES_A
EVEN, EVEN_OUT, ODD, ODD_OUT = 0, 12, 148, 156
PEER_Q, PEER_UV = (16, 160), (20, 164)
TILES_B = 292
ALPHA = (2 * LAYERS) ** 0.25
LN_EPS, LNX_EPS = 1e-5, 64e-5
GH, GDK, GDV = 4, 64, 128
RH, RN = 8, 64
EW = 512
AH, AD = 8, 128
IH, ID = 8, 64
SELECT = 64
KEYS, PH, PK = 128, 8, 16
JH = KEYS // 2
PAIRS = JH // 2
GT = 4
HOT = 4
GROUPS = S // GT
REGATED = GROUPS // 2 // HOT

ECOL = {}
_c = 0
for _name, _n in (("mu_side", 2), ("mu", 12), ("gla_a_b", 2), ("w0", 4), ("a0", 4), ("k_k", 4), ("k_a", 4), ("r_k", 4)):
    ECOL[_name] = _c
    _c += _n
ECOLS = _c

ORDER_B = [("gqk", EVEN, 1, "act"), ("gv", EVEN + 2, 1, "act"), ("gg", EVEN + 4, 1, "act"), ("r", EVEN + 6, 1, "act"),
           ("k", EVEN + 8, 1, "act"), ("v", EVEN + 10, 1, "act"), ("eout", EVEN_OUT, 2, "dve"), ("pq0", PEER_Q[0], 2, "act"),
           ("oq", ODD, 2, "dve"), ("oqi", ODD + 4, 1, "dve"), ("okv", ODD + 6, 1, "dve"), ("oout", ODD_OUT, 2, "dve"),
           ("pq1", PEER_Q[1], 2, "act")]
CHUNK_B, TILE_B, READ_B = {}, {}, []
for _name, _t, _n, _by in ORDER_B:
    for _i in range(_n):
        CHUNK_B[_name, _i] = len(READ_B)
        TILE_B[_name, _i] = _t + 2 * _i
        READ_B.append((_by, 1 + sum(b == _by for b, _ in READ_B)))

LORA = 1024
G2, W2 = (slice(0, 96), slice(0, EW)), (slice(96, 128), slice(0, EW))
GA2, A2 = (slice(0, 32), slice(EW, EW + 256)), (slice(32, 64), slice(EW, 2 * EW))
EROW = {"gla_g": slice(0, GDV), "lnx_g": slice(GDV, GDV + EW), "lnx_b": slice(GDV + EW, GDV + 2 * EW)}
EROWS = GDV + 2 * EW
HALVES = tuple(slice(t * P, (t + 1) * P) for t in range(TT))
FT = EW // P
GP = GH // 2
CH = P // CHUNK_T


def steps(*names):
    return {name: i + 1 for i, name in enumerate(names)}


EVEN_PE = steps("side", "la", "w", "a", "g", "scores", "keys", "kv", "o")
EVEN_ACT = steps("side", "gates", "lnexp", "w", "a", "decays", "keys", "square", "std")
EVEN_DVE = steps("side", "la", "cumsum", "decayed", "scores", "states", "gla")
LEVEL_STEPS = [f"{s}{n}" for n in range(LEVELS) for s in "xd"]
RW_PE = steps("bonus", "nat", "lr", *LEVEL_STEPS, "z", "wv", "y")
RW_ACT = steps("decays", "norm", "nat", "z", "wv", "std")
RW_DVE = steps("cumsum", "bonus", "tilde", "lr", *LEVEL_STEPS, "stats", "out")
ODD_PE = steps("qt", "it", "index0", "index1", "logits0", "pt0", "o0", "logits1", "pt1", "o1")
ODD_ACT = steps("qt", "it", "index0", "index1", "exp0", "pt0", "exp1", "pt1")
ODD_DVE = steps("rope", "kib", "index0", "index1", "logits0", "probs0", "logits1", "probs1")


class Order:

    def __init__(self, eng, own):
        self.eng, self.own, self.count = eng, own, {}

    def __call__(self, ins, signal=None):
        s = self.own if signal is None else signal
        self.count[s] = self.count.get(s, 0) + 1
        ins.then_inc(s, 1)
        self.eng.wait_ge(s, self.count[s])

    def also(self, ins):
        self.count[self.own] = self.count.get(self.own, 0) + 1
        ins.then_inc(self.own, 1)

    def settle(self):
        self.eng.wait_ge(self.own, self.count[self.own])


class Common:

    def __init__(self, nc, ctx, weights):
        def sb(name, shape, dt=F32):
            return ctx.enter_context(nc.sbuf_tensor(name, shape, dt))

        def sem(name):
            return ctx.enter_context(nc.semaphore(name))

        self.weights = weights
        self.raw = sb("raw", [P, RAW, TW])
        self.w_hi = sb("w_hi", [P, SPLIT, TW], F32R)
        self.w_lo = sb("w_lo", [P, SPLIT, TW], F32R)
        self.x = sb("x", [P, TT, D])
        self.act_hi = sb("act_hi", [P, KD, S], F32R)
        self.act_lo = sb("act_lo", [P, KD, S], F32R)
        self.ident_sb = sb("ident_sb", [P, P])
        self.ident = self.ident_sb[:, :]
        self.psum = [ctx.enter_context(nc.psum_tensor(f"bank{b}", [P, CW], F32)) for b in range(8)]
        self.raw_loaded = [sem(f"raw_loaded{r}") for r in range(RAW)]
        self.hi_ready = sem("hi_ready")
        self.lo_ready = sem("lo_ready")
        self.tile_used = sem("tile_used")
        self.x_ready = sem("x_ready")
        self.out_stored = sem("out_stored")


def first_block(nc, ctx, m, x_in, rows, cols, bgate, p_t, w_pe, final_row, identity, consts_a):
    raw, w_hi, w_lo, x, act_hi, act_lo, ident, psum = m.raw, m.w_hi, m.w_lo, m.x, m.act_hi, m.act_lo, m.ident, m.psum
    raw_loaded, hi_ready, lo_ready, tile_used, x_ready = m.raw_loaded, m.hi_ready, m.lo_ready, m.tile_used, m.x_ready

    def sb(name, shape, dt=F32, stack=ctx):
        return stack.enter_context(nc.sbuf_tensor(name, shape, dt))

    def sem(name):
        return ctx.enter_context(nc.semaphore(name))

    memory = ExitStack()
    const_a = sb("const_a", [P, CONSTS_A], F32, memory)

    def cst(name):
        first, n = CONST_A[name]
        return const_a[:, first:first + n]

    eps = cst("eps")
    attention = memory.enter_context(ExitStack())
    qk_t = sb("qk_t", [P, 16, S], F32, attention)
    val = sb("val", [P, TT, HEADS * (RDV + 2)], F32, attention)
    attention.close()
    mix_hi = sb("mix_hi", [P, 16, S], F32R, memory)
    mix_lo = sb("mix_lo", [P, 16, S], F32R, memory)
    pad = sb("pad", [P, 64], F32, memory)
    y = sb("y", [P, TT, HEADS * RDV], F32, memory)
    merged = sb("merged", [P, TT, D], F32, memory)
    gate = sb("gate", [P, TT, D], F32, memory)
    row = sb("row", [P, RROW, CW], F32, memory)
    col = sb("col", [P, COLS_A], F32, memory)
    bgate_row = sb("bgate_row", [P, 8], F32, memory)
    shifted = sb("shifted", [P, 4, S + 3], F32, memory)
    conv = sb("conv", [P, 4, S], F32, memory)
    pre = sb("pre", [P, TT, CW], F32, memory)
    decayed = sb("decayed", [P, HEADS, 3, P], F32, memory)
    weighed = sb("weighed", [P, 2, 3 * P], F32, memory)
    junk = sb("junk", [P, D], F32, memory)
    gw_hi = sb("gw_hi", [P, KD, 8], F32R, memory)
    gw_lo = sb("gw_lo", [P, KD, 8], F32R, memory)
    gz = sb("gz", [P, TT, 8], F32, memory)
    gl = sb("gl", [P, 4, TT, HEADS], F32, memory)
    gi = sb("gi", [P, TT, HEADS], F32, memory)
    grow = sb("grow", [HEADS, S], F32, memory)
    mrow = sb("mrow", [HEADS, S], F32, memory)
    floor = sb("floor", [P, TT, HEADS], F32, memory)
    ssq = sb("ssq", [P, TT], F32, memory)
    rstd = sb("rstd", [P, TT], F32, memory)
    st6 = sb("st6", [P, 6], F32, memory)
    stats = sb("stats", [P, TT, HEADS, 2], F32, memory)
    hstd = sb("hstd", [P, TT, HEADS], F32, memory)
    den = sb("den", [P, 2], F32, memory)
    wpe_sb = y[:, :, :].rearrange("p t n -> p (t n)")[:, 0:2 * D].rearrange("p (k n) -> p k n", k=2)
    pt_sb = y[:, :, :].rearrange("p t n -> p (t n)")[:, 2 * D:2 * D + 2 * S].rearrange("p (k n) -> p k n", k=2)
    val_m = val[:, :, 0:HEADS * (MDV + 1)].rearrange("p t (h n) -> p t h n", h=HEADS)
    val_r = val[:, :, 0:HEADS * RDV]

    const_loaded = sem("const_loaded")
    x_loaded = sem("x_loaded")
    layer_left = sem("layer_left")
    layer_open = sem("layer_open")
    cleared = sem("cleared")
    final_loaded = sem("final_loaded")
    final_std = sem("final_std")
    col_loaded = sem("col_loaded")
    row_loaded = [sem(f"row_loaded{r}") for r in range(RROW)]
    pe_loaded = sem("pe_loaded")

    per_layer = []

    def lsem(name):
        per_layer.append(sem(name))
        return per_layer[-1]

    act_step = lsem("act_step")
    dve_step = lsem("dve_step")
    read_act = lsem("read_act")
    read_dve = lsem("read_dve")
    std_ready = lsem("std_ready")
    xn_ready = lsem("xn_ready")
    trans_done = lsem("trans_done")
    t_hi = lsem("t_hi")
    t_lo = lsem("t_lo")
    gw_split = lsem("gw_split")
    gate_mm = lsem("gate_mm")
    gz_ready = lsem("gz_ready")
    lnf_ready = lsem("lnf_ready")
    lf_ready = lsem("lf_ready")
    gi_ready = lsem("gi_ready")
    m_ready = lsem("m_ready")
    fm_ready = lsem("fm_ready")
    mmask_ready = lsem("mmask_ready")
    decay_ready = lsem("decay_ready")
    floor_ready = lsem("floor_ready")
    conv_done = lsem("conv_done")
    mqk_ready = lsem("mqk_ready")
    rqk_ready = lsem("rqk_ready")
    score_done = lsem("score_done")
    weighed_ready = lsem("weighed_ready")
    y_done = lsem("y_done")
    my_read = lsem("my_read")
    ry_read = lsem("ry_read")
    stats_ready = lsem("stats_ready")
    hstd_ready = lsem("hstd_ready")
    gated = lsem("gated")
    y_ready = lsem("y_ready")
    merged_ready = lsem("merged_ready")
    relu_ready = lsem("relu_ready")
    sq_ready = lsem("sq_ready")
    ff_hi = lsem("ff_hi")
    ff_lo = lsem("ff_lo")
    pe_mm = lsem("pe_mm")

    def wait_read(eng, c):
        by_act, count = TAKEN[c]
        eng.wait_ge(read_act if by_act else read_dve, count)

    with nc.Block() as block:

        @block.sync
        def _(sp):
            for r in range(RAW):
                sp.dma_start(raw[:, r, :], m.weights[r]).then_inc(raw_loaded[r], 16)
            with sp.Fori(1, LAYERS * TILES_A // RAW + 1) as n:
                for r in range(RAW):
                    sp.wait_ge(lo_ready, n * RAW + (r - RAW + 1))
                    sp.dma_start(raw[:, r, :], m.weights[n * RAW + r]).then_inc(raw_loaded[r], 16)

        @block.gpsimd
        def _(pool):
            pool.dma_start(ident, identity).then_inc(const_loaded, 16)
            pool.dma_start(const_a[:, :], consts_a).then_inc(const_loaded, 16)
            pool.dma_start(x[:, :, :], x_in).then_inc(x_loaded, 16)
            with pool.Fori(0, LAYERS) as layer:
                pool.dma_start(col[:, :], cols[layer]).then_inc(col_loaded, 16)
                pool.dma_start(bgate_row[:, :], bgate[layer].partition_broadcast(P)).then_inc(col_loaded, 16)
                for r in range(ROWS_A):
                    if r >= RROW:
                        wait_read(pool, ROW_CHUNK[r - RROW])
                    if r == ROW_OF["ffb2", 0]:
                        pool.wait_ge(t_lo, T_MG)
                        pool.dma_start(wpe_sb, w_pe[layer]).then_inc(pe_loaded, 16)
                        pool.dma_start(pt_sb, p_t[layer]).then_inc(pe_loaded, 16)
                    pool.dma_start(row[:, r % RROW, :], rows[layer, r].partition_broadcast(P)).then_inc(row_loaded[r % RROW], 16)
                pool.wait_ge(layer_left, layer * 3 + 3)
                pool.sem_inc(cleared, 1)
                for s in per_layer:
                    pool.sem_clear(s)
                pool.sem_inc(layer_open, 1)
            pool.dma_start(row[:, 0:2, :].rearrange("p a n -> p (a n)"), final_row.partition_broadcast(P)).then_inc(final_loaded, 16)

        def row_slot(name, i, k=0):
            r = ROW_OF[name, i] + k
            return row[:, r % RROW, :], row_loaded[r % RROW], 16 * (r // RROW + 1)

        @block.tensor
        def _(pe):
            def mm3(dst, lh, ll, rh, rl, first, last):
                nc.tensor.matmul(dst, lh, rh, start=first, stop=False)
                nc.tensor.matmul(dst, lh, rl, start=False, stop=False)
                return nc.tensor.matmul(dst, ll, rh, start=False, stop=last)

            def natural(base, k0, c, per, hi, lo):
                for j in range(per):
                    k = k0 + j
                    pe.wait_ge(lo_ready, base + (k + 1))
                    for kk in range(KB):
                        ki = j * KB + kk
                        for t in range(TT):
                            ts = slice(t * P, (t + 1) * P)
                            ws = slice(kk * CW, (kk + 1) * CW)
                            last = mm3(psum[2 * (c % 2) + t][:, :], hi[:, ki, ts], lo[:, ki, ts], w_hi[:, k % SPLIT, ws],
                                       w_lo[:, k % SPLIT, ws], ki == 0, ki == per * KB - 1)
                    last.then_inc(tile_used, 1)

            def featured(base, k0, c, hi, lo):
                for j in range(2):
                    k = k0 + j
                    pe.wait_ge(lo_ready, base + (k + 1))
                    for f in range(4):
                        for kk in range(KB):
                            ki = j * KB + kk
                            ws = slice(kk * CW + f * P, kk * CW + (f + 1) * P)
                            dst = psum[2 * (c % 2) + f // 2][:, (f % 2) * S:(f % 2 + 1) * S]
                            wh, wl = w_hi[:, k % SPLIT, ws], w_lo[:, k % SPLIT, ws]
                            nc.tensor.matmul(dst, wh, hi[:, ki, :], start=ki == 0 and f % 2 == 0, stop=False)
                            nc.tensor.matmul(dst, wh, lo[:, ki, :], start=False, stop=False)
                            last = nc.tensor.matmul(dst, wl, hi[:, ki, :], start=False, stop=ki == KD - 1 and f % 2 == 1)
                    last.then_inc(tile_used, 1)

            def transposes(src, blocks):
                for b in range(blocks // 2):
                    for k in (2 * b, 2 * b + 1):
                        for t in range(TT):
                            last = nc.tensor.transpose(psum[4 + b][:, (k % 2) * S + t * P:(k % 2) * S + (t + 1) * P],
                                                       src(k, t), ident)
                    last.then_inc(trans_done, 1)

            pe.wait_ge(const_loaded, 32)
            with pe.Fori(0, LAYERS) as layer:
                base = layer * TILES_A

                def bank_free(c):
                    if c >= 2:
                        wait_read(pe, c - 2)

                def nat(name, i, hi, lo):
                    bank_free(CHUNK[name, i])
                    natural(base, TILE[name, i], CHUNK[name, i], PER_CHUNK[name], hi, lo)

                def feat(name, i, hi, lo):
                    bank_free(CHUNK[name, i])
                    featured(base, TILE[name, i], CHUNK[name, i], hi, lo)

                def normed(i):
                    pe.wait_ge(xn_ready, 2 * (i + 1))
                    transposes(lambda k, t: gate[:, t, k * P:(k + 1) * P], KD)

                normed(0)
                pe.wait_ge(t_lo, T_YM)
                pe.wait_ge(gw_split, 2)
                for t in range(TT):
                    for k in range(KD):
                        ts = slice(t * P, (t + 1) * P)
                        last = mm3(psum[6][:, t * 8:t * 8 + 8], act_hi[:, k, ts], act_lo[:, k, ts], gw_hi[:, k, :],
                                   gw_lo[:, k, :], k == 0, k == KD - 1)
                last.then_inc(gate_mm, 1)
                feat("mqk", 0, act_hi, act_lo)
                pe.wait_ge(lf_ready, 1)
                lf = gl[:, 2, :, :]
                nc.tensor.matmul(psum[7][:, 0:HEADS], cst("cum"), lf[:, 0, :], start=True, stop=True)
                nc.tensor.matmul(psum[7][:, HEADS:2 * HEADS], cst("ones"), lf[:, 0, :], start=True, stop=False)
                nc.tensor.matmul(psum[7][:, HEADS:2 * HEADS], cst("cum"), lf[:, 1, :], start=False, stop=True).then_inc(gate_mm, 1)
                feat("mqk", 1, act_hi, act_lo)
                pe.wait_ge(gi_ready, 1)
                for t in range(TT):
                    last = nc.tensor.transpose(psum[6][0:HEADS, t * P:(t + 1) * P], gi[:, t, :], ident)
                last.then_inc(gate_mm, 1)
                feat("mqk", 2, act_hi, act_lo)
                pe.wait_ge(m_ready, 1)
                for t in range(TT):
                    last = nc.tensor.transpose(psum[7][:, 8 + t * HEADS:8 + (t + 1) * HEADS], mrow[:, t * P:(t + 1) * P],
                                               ident[0:HEADS, 0:HEADS])
                last.then_inc(gate_mm, 1)
                for h in range(HEADS):
                    sel = cst("headsel")[0:HEADS, h * P:(h + 1) * P]
                    last = nc.tensor.matmul(psum[4 + h // 2][:, (h % 2) * S:(h % 2 + 1) * S], sel, mrow[:, :], start=True, stop=True)
                last.then_inc(gate_mm, 1)
                feat("mqk", 3, act_hi, act_lo)
                nat("mv", 0, act_hi, act_lo)
                nat("mv", 1, act_hi, act_lo)

                def attend(h0, width, values, qk_ready, v_chunk, y_read):
                    def outputs(h):
                        pe.wait_ge(weighed_ready, h0 + h + 1)
                        if h >= 1:
                            pe.wait_ge(y_read, h)
                        if h == 0:
                            wait_read(pe, v_chunk)
                        w = weighed[:, h % 2, :]
                        nc.tensor.matmul(psum[6][:, 0:width], w[:, 0:P], values(0, h), start=True, stop=True)
                        nc.tensor.matmul(psum[7][:, 0:width], w[:, P:2 * P], values(0, h), start=True, stop=False)
                        nc.tensor.matmul(psum[7][:, 0:width], w[:, 2 * P:3 * P], values(1, h), start=False, stop=True).then_inc(y_done, 1)

                    pe.wait_ge(qk_ready, 4)
                    for h in range(HEADS):
                        if h >= 2:
                            pe.wait_ge(weighed_ready, h0 + h - 1)
                        bank = psum[4 + h % 2]
                        for d in range(2):
                            nc.tensor.matmul(bank[:, 0:S], qk_t[:, 8 + 2 * h + d, 0:P], qk_t[:, 2 * h + d, :], start=d == 0, stop=d == 1)
                        for d in range(2):
                            last = nc.tensor.matmul(bank[:, S:S + P], qk_t[:, 8 + 2 * h + d, P:S], qk_t[:, 2 * h + d, P:S],
                                                    start=d == 0, stop=d == 1)
                        last.then_inc(score_done, 1)
                        if h >= 1:
                            outputs(h - 1)
                    outputs(HEADS - 1)

                pe.wait_ge(mmask_ready, HEADS)
                attend(0, MDV + 1, lambda t, h: val_m[:, t, h, :], mqk_ready, CHUNK["mv", 1], my_read)
                nat("mo", 0, act_hi, act_lo)
                nat("mo", 1, act_hi, act_lo)
                pe.wait_ge(y_ready, 2)
                transposes(lambda k, t: y[:, t, k * P:(k + 1) * P], KD)
                nat("gm", 0, act_hi, act_lo)
                nat("gm", 1, act_hi, act_lo)
                pe.wait_ge(t_lo, T_YR)
                nat("bm", 0, mix_hi, mix_lo)
                nat("bm", 1, mix_hi, mix_lo)
                for i in range(4):
                    feat("rqk", i, act_hi, act_lo)
                for i in range(4):
                    nat("rv", i, act_hi, act_lo)
                attend(HEADS, RDV, lambda t, h: val_r[:, t, h * RDV:(h + 1) * RDV], rqk_ready, CHUNK["rv", 3], ry_read)
                for i in range(4):
                    nat("rg", i, act_hi, act_lo)
                pe.wait_ge(y_ready, 6)
                transposes(lambda k, t: y[:, t, k * P:(k + 1) * P], KD)
                nat("gr", 0, act_hi, act_lo)
                nat("gr", 1, act_hi, act_lo)
                pe.wait_ge(t_lo, T_YR + 4)
                transposes(lambda k, t: y[:, t, D + k * P:D + (k + 1) * P], KD)
                pe.wait_ge(t_lo, T_MG)
                nat("br", 0, mix_hi, mix_lo)
                nat("br", 1, mix_hi, mix_lo)
                pe.wait_ge(merged_ready, 2)
                transposes(lambda k, t: merged[:, t, k * P:(k + 1) * P], KD)
                pe.wait_ge(t_lo, T_H2)
                nat("out", 0, mix_hi, mix_lo)
                nat("out", 1, mix_hi, mix_lo)
                normed(1)
                pe.wait_ge(t_lo, T_H3)
                for half, (one, two) in enumerate((("ffa1", "ffa2"), ("ffb1", "ffb2"))):
                    for i in range(4):
                        feat(one, i, act_hi, act_lo)
                    pe.wait_ge(ff_lo, 4 * half + 4)
                    for i in range(2):
                        nat(two, i, mix_hi, mix_lo)
                normed(2)
                pe.wait_ge(t_lo, T_ALL)
                pe.wait_ge(pe_loaded, layer * 32 + 32)
                for i in range(2):
                    for t in range(TT):
                        for k in range(2):
                            last = nc.tensor.matmul(psum[4 + 2 * i + t][:, :], pt_sb[:, k, t * P:(t + 1) * P],
                                                    wpe_sb[:, k, i * CW:(i + 1) * CW], start=k == 0, stop=k == 1)
                last.then_inc(pe_mm, 1)
                nat("peg", 0, act_hi, act_lo)
                nat("peg", 1, act_hi, act_lo)
                wait_read(pe, CHUNKS_A - 1)
                pe.sem_inc(layer_left, 1)
                pe.wait_ge(layer_open, layer + 1)

        @block.scalar
        def _(act):
            def split_hi(base, k, free=True):
                act.wait_ge(raw_loaded[k % RAW], base * (16 // RAW) + 16 * (k // RAW + 1))
                if free:
                    act.wait_ge(tile_used, base + (k - 1))
                nc.scalar.activation(w_hi[:, k % SPLIT, :], raw[:, k % RAW, :], ACT.Copy).then_inc(hi_ready, 1)

            for k in range(SPLIT):
                split_hi(0, k, free=False)
            act.wait_ge(const_loaded, 32)
            act.wait_ge(x_loaded, 16)
            with act.Fori(0, LAYERS) as layer:
                base = layer * TILES_A
                do = Order(act, act_step)

                def stream(name, i):
                    for j in range(PER_CHUNK[name]):
                        split_hi(base, TILE[name, i] + j + SPLIT)

                def taken(name, i):
                    act.wait_ge(tile_used, base + (TILE[name, i] + PER_CHUNK[name]))

                def norm(i, c):
                    if c is not None:
                        wait_read(act, c)
                    for t in range(TT):
                        do(nc.scalar.activation(junk[:, :], x[:, t, :], ACT.Square, accum_out=ssq[:, t:t + 1]))
                    do(nc.scalar.activation(rstd[:, :], ssq[:, :], ACT.Sqrt, bias=eps, scale=1.0 / D), std_ready)
                    g0 = COL[f"norm{i + 1}"]
                    first = (T_H, T_H2, T_H3)[i]
                    for b in range(KD // 2):
                        act.wait_ge(trans_done, first + b + 1)
                        for k in (2 * b, 2 * b + 1):
                            ins = nc.scalar.activation(act_hi[:, k, :], psum[4 + b][:, (k % 2) * S:(k % 2 + 1) * S], ACT.Copy,
                                                       scale=col[:, g0 + k:g0 + k + 1])
                            do(ins, t_hi if k % 2 else None)

                def mixed(first, k0):
                    for b in range(KD // 2):
                        act.wait_ge(trans_done, first + b + 1)
                        do(nc.scalar.activation(mix_hi[:, k0 + 2 * b:k0 + 2 * b + 2, :].rearrange("p k s -> p (k s)"),
                                                psum[4 + b][:, :], ACT.Copy), t_hi)

                act.wait_ge(col_loaded, layer * 32 + 32)
                do(nc.scalar.activation(gw_hi[:, :, :].rearrange("p k n -> p (k n)"), col[:, COL["gatew"]:COL["gatew"] + 64], ACT.Copy), gw_split)
                norm(0, None)
                act.wait_ge(gz_ready, 1)
                do(nc.scalar.activation(gl[:, 0, :, :], gz[:, :, 4:8], ACT.Abs))
                do(nc.scalar.activation(gl[:, 0, :, :], gl[:, 0, :, :], ACT.Exp, scale=-1.0))
                do(nc.scalar.activation(gl[:, 1, :, :], gl[:, 0, :, :], ACT.Ln, bias=cst("one")), lnf_ready)

                def biased(name, i, bias):
                    taken(name, i)
                    for f in range(4):
                        n = bias + 4 * i + f
                        do(nc.scalar.activation(shifted[:, f, 3:], psum[2 * (CHUNK[name, i] % 2) + f // 2][:, (f % 2) * S:(f % 2 + 1) * S],
                                                ACT.Identity, bias=col[:, n:n + 1]), read_act if f == 3 else None)

                def silu(i):
                    act.wait_ge(conv_done, i + 1)
                    do(nc.scalar.activation(qk_t[:, 4 * i:4 * i + 4, :], conv[:, :, :], ACT.Silu), mqk_ready)

                for i in range(4):
                    stream("mqk", i)
                    if i >= 1:
                        act.wait_ge(conv_done, i)
                    biased("mqk", i, COL["bmqk"])
                    if i >= 1:
                        silu(i - 1)
                act.wait_ge(fm_ready, 1)
                do(nc.scalar.activation(floor[:, :, :], gl[:, 0, :, :], ACT.Exp, scale=-1.0), floor_ready)
                for h in range(HEADS):
                    act.wait_ge(mmask_ready, h + 1)
                    do(nc.scalar.activation(decayed[:, h, 0:2, :], decayed[:, h, 0:2, :], ACT.Exp, bias=gi[:, 0, h:h + 1], scale=-1.0))
                    do(nc.scalar.activation(decayed[:, h, 2, :], decayed[:, h, 2, :], ACT.Exp, bias=gi[:, 1, h:h + 1], scale=-1.0), decay_ready)
                stream("mv", 0)
                silu(3)
                stream("mv", 1)

                def head_std(n):
                    act.wait_ge(stats_ready, n)
                    do(nc.scalar.activation(hstd[:, :, :], stats[:, :, :, 1], ACT.Sqrt, bias=eps), hstd_ready)

                head_std(1)

                def gates(name, i, func, dst):
                    stream(name, i)
                    wait_read(act, CHUNK[name, i])
                    do(nc.scalar.activation(dst, pre[:, :, :], func), gated)

                for i in range(2):
                    gates("mo", i, ACT.Sigmoid, pre[:, :, :])
                mixed(T_YM, 0)
                for i in range(2):
                    gates("gm", i, ACT.Sigmoid, gate[:, :, i * CW:(i + 1) * CW])
                for i in range(2):
                    stream("bm", i)
                for i in range(4):
                    stream("rqk", i)
                    if i >= 1:
                        act.wait_ge(rqk_ready, i)
                    biased("rqk", i, COL["brqk"])
                for i in range(4):
                    stream("rv", i)
                for h in range(HEADS):
                    act.wait_ge(y_done, HEADS + h + 1)
                    for t in range(TT):
                        do(nc.scalar.activation(y[:, t, h * RDV:(h + 1) * RDV], psum[6 + t][:, :], ACT.Copy), ry_read if t == 1 else None)
                head_std(2)
                for i in range(4):
                    gates("rg", i, ACT.Silu, pre[:, :, :])
                mixed(T_YR, 0)
                for i in range(2):
                    gates("gr", i, ACT.Sigmoid, gate[:, :, i * CW:(i + 1) * CW])
                mixed(T_YR + 4, KD)
                for i in range(2):
                    stream("br", i)
                mixed(T_MG, 0)
                for i in range(2):
                    stream("out", i)
                norm(1, CHUNK["out", 1])
                for half, (one, two) in enumerate((("ffa1", "ffa2"), ("ffb1", "ffb2"))):
                    for i in range(4):
                        stream(one, i)
                        taken(one, i)
                        if 4 * half + i >= 1:
                            act.wait_ge(ff_lo, 4 * half + i)
                        for f in range(4):
                            n = COL["bff1"] + 16 * half + 4 * i + f
                            do(nc.scalar.activation(conv[:, f, :], psum[2 * (CHUNK[one, i] % 2) + f // 2][:, (f % 2) * S:(f % 2 + 1) * S],
                                                    ACT.Relu, bias=col[:, n:n + 1]), read_act if f == 3 else None)
                        act.wait_ge(sq_ready, 4 * half + i + 1)
                        do(nc.scalar.activation(mix_hi[:, 4 * i:4 * i + 4, :], conv[:, :, :], ACT.Copy), ff_hi)
                    for i in range(2):
                        stream(two, i)
                norm(2, CHUNK["ffb2", 1])
                for i in range(2):
                    stream("peg", i)
                    taken("peg", i)
                    c = CHUNK["peg", i]
                    for t in range(TT):
                        do(nc.scalar.activation(gate[:, t, i * CW:(i + 1) * CW], psum[2 * (c % 2) + t][:, :], ACT.Sigmoid), gated if t else None)
                act.sem_inc(layer_left, 1)
                act.wait_ge(layer_open, layer + 1)
            do = Order(act, act_step)
            for t in range(TT):
                do(nc.scalar.activation(junk[:, :], x[:, t, :], ACT.Square, accum_out=ssq[:, t:t + 1]))
            do(nc.scalar.activation(rstd[:, :], ssq[:, :], ACT.Sqrt, bias=eps, scale=1.0 / D), final_std)

        @block.vector
        def _(dve):
            def split_lo(base, k):
                dve.wait_ge(hi_ready, base + (k + 1))
                nc.vector.tensor_tensor(w_lo[:, k % SPLIT, :], raw[:, k % RAW, :], w_hi[:, k % SPLIT, :].bitcast(F32), ALU.subtract).then_inc(lo_ready, 1)

            for k in range(SPLIT):
                split_lo(0, k)
            dve.wait_ge(const_loaded, 32)
            dve.wait_ge(x_loaded, 16)
            with dve.Fori(0, LAYERS) as layer:
                base = layer * TILES_A
                do = Order(dve, dve_step)
                V = nc.vector

                def stream(name, i):
                    for j in range(PER_CHUNK[name]):
                        split_lo(base, TILE[name, i] + j + SPLIT)

                def taken(name, i):
                    dve.wait_ge(tile_used, base + (TILE[name, i] + PER_CHUNK[name]))

                def row_of(name, i, k=0):
                    ap, s, n = row_slot(name, i, k)
                    dve.wait_ge(s, layer * (16 * ROWS_A // RROW) + n)
                    return ap

                def norm(i):
                    dve.wait_ge(std_ready, i + 1)
                    do(V.reciprocal(rstd[:, :], rstd[:, :]))
                    for t in range(TT):
                        do(V.tensor_scalar(gate[:, t, :], x[:, t, :], rstd[:, t:t + 1], None, ALU.mult), xn_ready)
                    g0 = COL[f"norm{i + 1}"]
                    first = (T_H, T_H2, T_H3)[i]
                    for b in range(KD // 2):
                        dve.wait_ge(t_hi, first + b + 1)
                        for k in (2 * b, 2 * b + 1):
                            do(V.scalar_tensor_tensor(out=act_lo[:, k, :], in0=psum[4 + b][:, (k % 2) * S:(k % 2 + 1) * S],
                                                      scalar=col[:, g0 + k:g0 + k + 1], in1=act_hi[:, k, :].bitcast(F32),
                                                      op0=ALU.mult, op1=ALU.subtract), t_lo if k % 2 else None)

                def mixed(first, k0):
                    for b in range(KD // 2):
                        dve.wait_ge(t_hi, first + b + 1)
                        ks = slice(k0 + 2 * b, k0 + 2 * b + 2)
                        do(V.tensor_tensor(mix_lo[:, ks, :].rearrange("p k s -> p (k s)"), psum[4 + b][:, :],
                                           mix_hi[:, ks, :].rearrange("p k s -> p (k s)").bitcast(F32), ALU.subtract), t_lo)

                dve.wait_ge(col_loaded, layer * 32 + 32)
                dve.wait_ge(gw_split, 1)
                do(V.memset(shifted[:, :, 0:3], 0.0))
                do(V.memset(val_m[:, :, :, MDV:MDV + 1], 1.0))
                gwl = V.tensor_tensor(gw_lo[:, :, :].rearrange("p k n -> p (k n)"), col[:, COL["gatew"]:COL["gatew"] + 64],
                                      gw_hi[:, :, :].rearrange("p k n -> p (k n)").bitcast(F32), ALU.subtract)
                gwl.then_inc(gw_split, 1)
                norm(0)
                dve.wait_ge(gate_mm, 1)
                for t in range(TT):
                    do(V.tensor_tensor(gz[:, t, :], psum[6][:, t * 8:t * 8 + 8], bgate_row[:, :], ALU.add), gz_ready if t else None)
                dve.wait_ge(lnf_ready, 1)
                do(V.scalar_tensor_tensor(out=gl[:, 2, :, :], in0=gz[:, :, 4:8], scalar=0.0, in1=gl[:, 1, :, :], op0=ALU.min, op1=ALU.subtract), lf_ready)

                def convolve(i):
                    wait_read(dve, CHUNK["mqk", i])
                    if i >= 1:
                        dve.wait_ge(mqk_ready, i)
                    for j in range(4):
                        for f in range(4):
                            w = COL["convw"] + 16 * j + 4 * i + f
                            b = COL["convb"] + 4 * i + f
                            if j == 0:
                                ins = V.tensor_scalar(conv[:, f, :], shifted[:, f, 0:S], col[:, w:w + 1], col[:, b:b + 1], ALU.mult, ALU.add)
                            else:
                                ins = V.scalar_tensor_tensor(out=conv[:, f, :], in0=shifted[:, f, j:j + S], scalar=col[:, w:w + 1],
                                                             in1=conv[:, f, :], op0=ALU.mult, op1=ALU.add)
                            do(ins, conv_done if j == 3 and f == 3 else None)

                stream("mqk", 0)
                convolve(0)
                dve.wait_ge(gate_mm, 2)
                do(V.tensor_copy(gl[:, 3, :, :].rearrange("p t h -> p (t h)"), psum[7][:, 0:2 * HEADS]))
                do(V.tensor_tensor(gi[:, :, :], gz[:, :, 0:4], gl[:, 3, :, :], ALU.subtract), gi_ready)
                stream("mqk", 1)
                convolve(1)
                dve.wait_ge(gate_mm, 3)
                do(V.tensor_copy(grow[:, :], psum[6][0:HEADS, 0:S]))
                do(V.tensor_tensor_scan(mrow[:, :], grow[:, :], grow[:, :], 0.0, ALU.max, ALU.max), m_ready)
                stream("mqk", 2)
                convolve(2)
                dve.wait_ge(gate_mm, 4)
                do(V.tensor_tensor(gl[:, 0, :, :].rearrange("p t h -> p (t h)"), gl[:, 3, :, :].rearrange("p t h -> p (t h)"),
                                   psum[7][:, 8:8 + 2 * HEADS], ALU.add), fm_ready)
                dve.wait_ge(gate_mm, 5)
                for h in range(HEADS):
                    m = psum[4 + h // 2][:, (h % 2) * S:(h % 2 + 1) * S]
                    for b, t, masked in ((0, 0, 1), (1, 1, 0), (2, 1, 1)):
                        dst, src = decayed[:, h, b, :], m[:, t * P:(t + 1) * P]
                        ins = V.tensor_tensor(dst, src, cst("mask"), ALU.add) if masked else V.tensor_copy(dst, src)
                        do(ins, mmask_ready if b == 2 else None)
                stream("mqk", 3)
                convolve(3)
                for i in range(2):
                    stream("mv", i)
                    taken("mv", i)
                    r = row_of("mv", i)
                    for t in range(TT):
                        do(V.tensor_tensor(val_m[:, t, 2 * i:2 * i + 2, 0:MDV], psum[2 * (CHUNK["mv", i] % 2) + t][:, :].rearrange("p (h n) -> p h n", h=2),
                                           r.rearrange("p (h n) -> p h n", h=2), ALU.add), read_dve if t else None)

                def weigh(h0, h, scale, weights_of):
                    dve.wait_ge(score_done, h0 + h + 1)
                    if h >= 2:
                        dve.wait_ge(y_done, h0 + h - 1)
                    do(V.scalar_tensor_tensor(out=weighed[:, h % 2, :], in0=psum[4 + h % 2][:, 0:3 * P], scalar=scale, in1=weights_of(h),
                                              op0=ALU.mult, op1=ALU.mult), weighed_ready)

                def statistics(src, t, h):
                    do(V.bn_stats(st6[:, :], src))
                    do(V.bn_aggr(stats[:, t, h, :], st6[:, :]), stats_ready if (t, h) == (TT - 1, HEADS - 1) else None)

                def head_norm(n, width):
                    dve.wait_ge(hstd_ready, n)
                    do(V.reciprocal(hstd[:, :, :], hstd[:, :, :]))
                    for h in range(HEADS):
                        for t in range(TT):
                            ys = y[:, t, h * width:(h + 1) * width]
                            do(V.tensor_scalar(ys, ys, stats[:, t, h, 0:1], hstd[:, t, h:h + 1], ALU.subtract, ALU.mult))

                def m_output(h):
                    dve.wait_ge(y_done, h + 1)
                    for t in range(TT):
                        total = psum[6 + t][:, MDV:MDV + 1]
                        do(V.scalar_tensor_tensor(out=den[:, 0:1], in0=total, scalar=-1.0, in1=floor[:, t, h:h + 1], op0=ALU.mult, op1=ALU.max))
                        do(V.tensor_tensor(den[:, 0:1], den[:, 0:1], total, ALU.max))
                        do(V.reciprocal(den[:, 1:2], den[:, 0:1]))
                        do(V.tensor_scalar(y[:, t, h * MDV:(h + 1) * MDV], psum[6 + t][:, 0:MDV], den[:, 1:2], None, ALU.mult), my_read if t else None)
                        statistics(y[:, t, h * MDV:(h + 1) * MDV], t, h)

                dve.wait_ge(floor_ready, 1)
                for h in range(HEADS):
                    dve.wait_ge(decay_ready, h + 1)
                    weigh(0, h, MDV ** -0.5, lambda h: decayed[:, h, :, :].rearrange("p b s -> p (b s)"))
                    if h >= 1:
                        m_output(h - 1)
                m_output(HEADS - 1)
                head_norm(1, MDV)

                def gate_in(name, i, c0=None):
                    taken(name, i)
                    r = row_of(name, i)
                    for t in range(TT):
                        do(V.tensor_tensor(pre[:, t, :], psum[2 * (CHUNK[name, i] % 2) + t][:, :], r, ALU.add), read_dve if t else None)

                def gated_mixer(name, n, ready0):
                    for i in range(n):
                        stream(name, i)
                        g = row_of(name, i, 1)
                        for t in range(TT):
                            ys = y[:, t, i * CW:(i + 1) * CW]
                            do(V.tensor_tensor(ys, ys, g, ALU.mult))
                        gate_in(name, i)
                        dve.wait_ge(gated, ready0 + i + 1)
                        for t in range(TT):
                            ys = y[:, t, i * CW:(i + 1) * CW]
                            do(V.tensor_tensor(ys, ys, pre[:, t, :], ALU.mult), y_ready if t else None)

                gated_mixer("mo", 2, 0)
                mixed(T_YM, 0)
                for i in range(2):
                    stream("gm", i)
                    if i:
                        dve.wait_ge(gated, 2 + i)
                    gate_in("gm", i)
                for i in range(2):
                    stream("bm", i)
                    taken("bm", i)
                    dve.wait_ge(gated, 4)
                    for t in range(TT):
                        cs = slice(i * CW, (i + 1) * CW)
                        do(V.tensor_tensor(merged[:, t, cs], psum[2 * (CHUNK["bm", i] % 2) + t][:, :], gate[:, t, cs], ALU.mult), read_dve if t else None)

                def rotate(i):
                    wait_read(dve, CHUNK["rqk", i])
                    for a in range(2):
                        x1, x2 = shifted[:, 2 * a, 3:], shifted[:, 2 * a + 1, 3:]
                        o1, o2 = qk_t[:, 4 * i + 2 * a, :], qk_t[:, 4 * i + 2 * a + 1, :]
                        do(V.tensor_tensor(o1, x1, cst("cos"), ALU.mult))
                        do(V.tensor_tensor(o2, x1, cst("sin"), ALU.mult))
                        do(V.tensor_tensor(conv[:, 0, :], x2, cst("sin"), ALU.mult))
                        do(V.tensor_tensor(conv[:, 1, :], x2, cst("cos"), ALU.mult))
                        do(V.tensor_tensor(o1, o1, conv[:, 0, :], ALU.subtract))
                        do(V.tensor_tensor(o2, o2, conv[:, 1, :], ALU.add), rqk_ready if a else None)

                for i in range(4):
                    stream("rqk", i)
                    rotate(i)
                for i in range(4):
                    stream("rv", i)
                    taken("rv", i)
                    r = row_of("rv", i)
                    for t in range(TT):
                        do(V.tensor_tensor(val_r[:, t, i * CW:(i + 1) * CW], psum[2 * (CHUNK["rv", i] % 2) + t][:, :], r, ALU.add), read_dve if t else None)

                def r_output(h):
                    dve.wait_ge(ry_read, h + 1)
                    for t in range(TT):
                        statistics(y[:, t, h * RDV:(h + 1) * RDV], t, h)

                for h in range(HEADS):
                    weigh(HEADS, h, 1.0, lambda h: cst("decay")[:, h * 384:(h + 1) * 384])
                    if h >= 1:
                        r_output(h - 1)
                r_output(HEADS - 1)
                head_norm(2, RDV)
                gated_mixer("rg", 4, 4)
                mixed(T_YR, 0)
                for i in range(2):
                    stream("gr", i)
                    if i:
                        dve.wait_ge(gated, 8 + i)
                    gate_in("gr", i)
                mixed(T_YR + 4, KD)
                for i in range(2):
                    stream("br", i)
                    taken("br", i)
                    dve.wait_ge(gated, 10)
                    for t in range(TT):
                        cs = slice(i * CW, (i + 1) * CW)
                        do(V.tensor_tensor(pre[:, t, :], psum[2 * (CHUNK["br", i] % 2) + t][:, :], gate[:, t, cs], ALU.mult), read_dve if t else None)
                        do(V.tensor_tensor(merged[:, t, cs], merged[:, t, cs], pre[:, t, :], ALU.add), merged_ready if t else None)
                mixed(T_MG, 0)

                def residual(name, i):
                    taken(name, i)
                    for t in range(TT):
                        cs = slice(i * CW, (i + 1) * CW)
                        do(V.tensor_tensor(x[:, t, cs], x[:, t, cs], psum[2 * (CHUNK[name, i] % 2) + t][:, :], ALU.add), read_dve if t else None)

                for i in range(2):
                    stream("out", i)
                    residual("out", i)
                norm(1)
                for half, (one, two) in enumerate((("ffa1", "ffa2"), ("ffb1", "ffb2"))):
                    for i in range(4):
                        stream(one, i)
                        wait_read(dve, CHUNK[one, i])
                        do(V.tensor_tensor(conv[:, :, :], conv[:, :, :], conv[:, :, :], ALU.mult), sq_ready)
                        dve.wait_ge(ff_hi, 4 * half + i + 1)
                        do(V.tensor_tensor(mix_lo[:, 4 * i:4 * i + 4, :], conv[:, :, :], mix_hi[:, 4 * i:4 * i + 4, :].bitcast(F32), ALU.subtract), ff_lo)
                    for i in range(2):
                        stream(two, i)
                        if half:
                            r = row_of(two, i)
                            for t in range(TT):
                                cs = slice(i * CW, (i + 1) * CW)
                                do(V.tensor_tensor(x[:, t, cs], x[:, t, cs], r, ALU.add))
                        residual(two, i)
                norm(2)
                for i in range(2):
                    stream("peg", i)
                    dve.wait_ge(gated, 10 + i + 1)
                    dve.wait_ge(pe_mm, 1)
                    for t in range(TT):
                        cs = slice(i * CW, (i + 1) * CW)
                        do(V.tensor_tensor(pre[:, t, :], psum[4 + 2 * i + t][:, :], gate[:, t, cs], ALU.mult))
                        do(V.tensor_tensor(x[:, t, cs], x[:, t, cs], pre[:, t, :], ALU.add), read_dve if t else None)
                dve.sem_inc(layer_left, 1)
                dve.wait_ge(layer_open, layer + 1)
            do = Order(dve, dve_step)
            dve.wait_ge(final_std, 1)
            do(V.reciprocal(rstd[:, :], rstd[:, :]))
            dve.wait_ge(final_loaded, 16)
            for t in range(TT):
                do(V.tensor_scalar(x[:, t, :], x[:, t, :], rstd[:, t:t + 1], None, ALU.mult))
                do(V.tensor_tensor(x[:, t, :], x[:, t, :], row[:, 0:2, :].rearrange("p a n -> p (a n)"), ALU.mult), x_ready if t else None)
    memory.close()


def second_block(nc, ctx, m, base, erows, ecols, lora_w, side_w, keys, ln_rows, consts_b, spill, out):
    raw, w_hi, w_lo, x, act_hi, act_lo, ident, psum = m.raw, m.w_hi, m.w_lo, m.x, m.act_hi, m.act_lo, m.ident, m.psum
    raw_loaded, hi_ready, lo_ready, tile_used = m.raw_loaded, m.hi_ready, m.lo_ready, m.tile_used
    V, A = nc.vector, nc.scalar
    total = base + TILES_B

    def sb(name, shape, dt=F32, stack=ctx):
        return stack.enter_context(nc.sbuf_tensor(name, shape, dt))

    def sem(name):
        return ctx.enter_context(nc.semaphore(name))

    const_b = sb("const_b", [P, CONSTS_B])

    def cst(name):
        first, n = CONST_B[name]
        return const_b[:, first:first + n]

    small = sb("small", [P, 64])
    even = ExitStack()
    rkv = sb("rkv", [P, 3, FT, S], F32, even)
    sgw = sb("sgw", [P, FT, S], F32, even)
    asig = sb("asig", [P, FT, S], F32, even)
    gnat = sb("gnat", [P, TT, EW], F32, even)
    erow = sb("erow", [P, EROWS], F32, even)
    ecol = sb("ecol", [P, ECOLS], F32, even)
    ymix = sb("ymix", [P, TT, D], F32, even)
    gla = ExitStack()
    lora = sb("lora", [P, LORA], F32, gla)
    side_t = sb("side_t", [P, 2, S], F32, gla)
    sh = sb("sh", [P, FT, S + 1], F32, gla)
    dif = sb("dif", [P, FT, S], F32, gla)
    gqk = sb("gqk", [P, 4, S], F32, gla)
    gv = sb("gv", [P, TT, EW], F32, gla)
    gsil = sb("gsil", [P, TT, EW], F32, gla)
    side_scope = ExitStack()
    side_raw = sb("side_raw", [P, KD, 2 * P], F32, side_scope)
    side_hi = sb("side_hi", [P, KD, 2 * P], F32R, side_scope)
    side_lo = sb("side_lo", [P, KD, 2 * P], F32R, side_scope)
    side_scope.close()
    la = sb("la", [P, GP, S], F32, gla)
    lb = sb("lb", [P, GP, S], F32, gla)
    eb = sb("eb", [P, GP, S], F32, gla)
    en = sb("en", [P, GP, S], F32, gla)
    qin = sb("qin", [P, GP, S], F32, gla)
    kin = sb("kin", [P, GP, S], F32, gla)
    qz = sb("qz", [P, CH, GP, S], F32, gla)
    konat = sb("konat", [P, TT * GP * P], F32, gla)
    attn = sb("attn", [P, 2, TT, GP, P], F32, gla)
    state = sb("state", [P, CH * TT, GP, 2 * P], F32, gla)
    gla.close()
    rw = ExitStack()
    cw = sb("cw", [P, FT, S], F32, rw)
    pinc = sb("pinc", [P, FT, S], F32, rw)
    pinv = sb("pinv", [P, FT, S], F32, rw)
    pm = sb("pm", [P, FT, S], F32, rw)
    kk = sb("kk", [P, FT, S], F32, rw)
    kp = sb("kp", [P, FT, S], F32, rw)
    bt = sb("bt", [P, FT, S], F32, rw)
    kt = sb("kt", [P, FT, S], F32, rw)
    ar = sb("ar", [P, FT, 2, S], F32, rw)
    lrb = sb("lrb", [P, TT, 2, FT, 2, CHUNK_T], F32, rw)
    lrk = sb("lrk", [P, TT, 2, FT, 2, CHUNK_T], F32, rw)
    dt_ = sb("dt_", [P, TT, 2, FT, CHUNK_T], F32, rw)
    s_all = sb("s_all", [P, TT * CH + 1, FT, P], F32, rw)
    rkind = sb("rkind", [P, FT, 2], F32, rw)
    bonus = sb("bonus", [P, TT, RH], F32, rw)
    rstat = sb("rstat", [P, TT, RH, 2], F32, rw)
    r6 = sb("r6", [P, 6], F32, rw)
    rw.close()
    even.close()

    def by_half(buf):
        return buf[:, :, :].rearrange("p f s -> p (f s)").rearrange("p (t e f s) -> p t e f s", t=TT, e=2, f=FT)

    def nat_of(buf):
        return buf[:, :, :].rearrange("p f s -> p (f s)").rearrange("p (t n) -> p t n", t=TT)

    sq = sgw
    nat = {"a": nat_of(cw), "b": nat_of(pm), "k": nat_of(pinv), "v": nat_of(sgw)}
    dd, xx = by_half(asig), by_half(kk)
    zz, wv, tat, uu = nat_of(asig), nat_of(kp), bt, nat_of(kt)
    norm = nat_of(dt_[:, :, :, :, :].rearrange("p t e f s -> p (t e f s)").rearrange("p (f s) -> p f s", f=FT))
    ln_row = sb("ln_row", [P, 2, D])
    odd = ExitStack()
    qn = sb("qn", [P, TT, D], F32, odd)
    qin_ = sb("qidx", [P, TT, IH * ID], F32, odd)
    kn = sb("kn", [P, TT, AD], F32, odd)
    vn = sb("vn", [P, TT, AD], F32, odd)
    kid = sb("kid", [P, TT, 2 * ID], F32, odd)
    wi = sb("wi", [P, TT, IH], F32, odd)
    rtmp = sb("rtmp", [P, CW // 2], F32, odd)
    q_t = sb("q_t", [P, AH, S], F32, odd)
    qi_t = sb("qi_t", [P, IH // 2, S], F32, odd)
    k_t = sb("k_t", [P, S], F32, odd)
    kib = sb("kib", [P, 2 * S], F32, odd)
    rel = sb("rel", [P, IH, S], F32, odd)
    score = sb("score", [P, TT, S], F32, odd)
    madd = sb("madd", [P, TT, S], F32, odd)
    logit = sb("logit", [P, AH, S], F32, odd)
    pt = sb("pt", [P, AH, TT, P], F32, odd)
    amax = sb("amax", [P, AH], F32, odd)
    asum = sb("asum", [P, AH], F32, odd)
    top8 = sb("top8", [P, 8], F32, odd)
    odd.close()
    peer = ExitStack()
    hid = sb("hid", [P, JH, S], F32, peer)
    pq, keys_sb = hid[:, JH - 2 * PH:JH - PH, :], hid[:, JH - PH:JH, :]
    ijg = sb("ijg", [P, 3, S], F32, peer)
    hot_i = sb("hot_i", [P, HOT, GT, KEYS], F32, peer)
    hot_j = sb("hot_j", [P, HOT, GT, KEYS], F32, peer)
    hot = hot_i[:, :, :, :].rearrange("p a t n -> p (a t n)").rearrange("p (h k a) -> p h k a", h=PH, k=PK)
    tops = sb("tops", [P, 2 * PH, PK], F32, peer)
    topi = sb("topi", [P, 2 * PH, PK], U32, peer)
    topf = sb("topf", [P, 2 * PH, PK], F32, peer)
    best = sb("best", [P, TT, PH, PK], F32, peer)
    pos = sb("pos", [P, PH, PK], U32, peer)
    posab = sb("posab", [P, 2, PH * PK], U32, peer)
    posf = sb("posf", [P, 2, PH * PK], F32, peer)
    sel = sb("sel", [P, TT, 3, PH * PK], F32, peer)
    gsum = sb("gsum", [P, TT * PH], F32, peer)
    scores = ExitStack()
    ss1 = sb("ss1", [P, 2 * PH, KEYS], F32, scores)
    flat1 = ss1[:, :, :].rearrange("p c n -> p (c n)")
    staged = flat1.rearrange("p (b h t j) -> p b h t j", b=HOT, h=2, t=GT)
    reload = flat1.rearrange("p (b g t j) -> p b (g t) j", b=HOT, g=2, t=GT)
    scores.close()
    ss = (ln_row[:, :, :].rearrange("p a n -> p (a n)").rearrange("p (c n) -> p c n", n=KEYS), ss1)
    c_hi = sb("c_hi", [P, 2, 2 * S], F32R, peer)
    c_lo = sb("c_lo", [P, 2, 2 * S], F32R, peer)
    peer.close()

    act_own, dve_own = sem("b_act_own"), sem("b_dve_own")
    b_const = sem("b_const")
    side_loaded = sem("side_loaded")
    even_loaded = sem("even_loaded")
    ln_loaded = sem("ln_loaded")
    keys_loaded = sem("keys_loaded")
    x_ready = m.x_ready
    tr_done = sem("b_tr_done")
    tr_hi = sem("b_tr_hi")
    tr_lo = sem("b_tr_lo")
    side_hi_ready, side_lo_ready = sem("side_hi_ready"), sem("side_lo_ready")
    read_act, read_dve = sem("b_read_act"), sem("b_read_dve")
    shifted_done = sem("shifted_done")
    even_pe, even_act, even_dve = sem("even_pe"), sem("even_act"), sem("even_dve")
    rw_pe, rw_act, rw_dve = sem("rw_pe"), sem("rw_act"), sem("rw_dve")
    chain_pe, chain_dve = sem("chain_pe"), sem("chain_dve")
    odd_pe, odd_act, odd_dve = sem("odd_pe"), sem("odd_act"), sem("odd_dve")
    att_hi, att_lo = sem("att_hi"), sem("att_lo")
    ln_var, ln_std = sem("ln_var"), sem("ln_std")
    s_done, s_read, s_used = sem("s_done"), sem("s_read"), sem("s_used")
    best_ready, exp_ready, sel_ready = sem("best_ready"), sem("exp_ready"), sem("sel_ready")
    sel_t, ijg_ready = sem("sel_t"), sem("ijg_ready")
    hot_eq = sem("hot_eq")
    hot_ready = sem("hot_ready")
    gates_done = sem("gates_done")
    gates_read = sem("gates_read")
    spilled = [sem(f"spilled{b}") for b in range(HOT)]
    reloaded = [sem(f"reloaded{b}") for b in range(HOT)]
    gated_odd = sem("gated_odd")
    gated_even = sem("gated_even")
    regated_pool = sem("regated_pool")
    regated_dve = sem("regated_dve")
    act_pad = sem("act_pad")
    gelu_ready = sem("gelu_ready")
    c_hi_ready, c_lo_ready = sem("c_hi_ready"), sem("c_lo_ready")
    out_stored = m.out_stored

    def wait_read(eng, c):
        by, count = READ_B[c]
        eng.wait_ge(read_act if by == "act" else read_dve, count)

    block = ctx.enter_context(nc.Block())

    @block.sync
    def _(sp):
        def stream(first, end):
            with sp.Fori(first // RAW, end // RAW) as n:
                for r in range(RAW):
                    sp.wait_ge(lo_ready, n * RAW + (r - RAW + 1))
                    sp.dma_start(raw[:, r, :], m.weights[n * RAW + r]).then_inc(raw_loaded[r], 16)

        at = base + RAW
        for layer in range(LAYERS):
            first = base + PEER_UV[layer]
            stream(at, first + PAIRS + RAW)
            with sp.Fori(0, GROUPS // HOT) as n:
                for b in range(HOT):
                    sp.wait_ge(gates_read, n * HOT + (GROUPS * layer + b + 1))
                    sp.dma_start(spill[n * HOT + b], staged[:, b, 1, :, :].rearrange("p t j -> p (t j)")).then_inc(spilled[b], 16)
            stream(first + PAIRS + RAW, first + 3 * PAIRS + RAW)
            for b in range(HOT):
                sp.wait_ge(spilled[b], 16 * (GROUPS // HOT) * (layer + 1))
            sp.wait_ge(tile_used, first + 2 * PAIRS)

            def again(n, b):
                sp.dma_start(reload[:, b, :, :].rearrange("p (g t) j -> p g (t j)", g=2),
                             spill[bass.ds(n * 2 * HOT + 2 * b, 2)].rearrange("g p n -> p g n")).then_inc(reloaded[b], 16)

            for b in range(HOT):
                again(0, b)
            with sp.Fori(1, REGATED) as n:
                for b in range(HOT):
                    if b < HOT - 1:
                        sp.wait_ge(regated_dve, n * (HOT - 1) + ((HOT - 1) * (REGATED * layer - 1) + b + 1))
                    else:
                        sp.wait_ge(regated_pool, n + REGATED * layer)
                    again(n, b)
            at = first + 3 * PAIRS + RAW
        stream(at, total)
        sp.wait_ge(x_ready, 5)
        sp.dma_start(out, x[:, :, :]).then_inc(out_stored, 16)
        sp.wait_ge(out_stored, 16)

    @block.gpsimd
    def _(pool):
        pool.dma_start(side_raw[:, :, :], side_w).then_inc(side_loaded, 16)
        pool.dma_start(const_b[:, :], consts_b).then_inc(b_const, 16)
        pool.dma_start(lora[:, :], lora_w).then_inc(even_loaded, 16)
        pool.dma_start(ecol[:, :], ecols).then_inc(even_loaded, 16)
        pool.dma_start(erow[:, :], erows.partition_broadcast(P)).then_inc(even_loaded, 16)

        def ln_load(n):
            pool.dma_start(ln_row[:, 0, :], ln_rows[2 * n].partition_broadcast(P)).then_inc(ln_loaded, 16)
            pool.dma_start(ln_row[:, 1, :], ln_rows[2 * n + 1].partition_broadcast(P)).then_inc(ln_loaded, 16)

        pool.wait_ge(tr_lo, 8)
        ln_load(0)
        pool.dma_start(keys_sb, keys[0]).then_inc(keys_loaded, 16)

        def gate(layer):
            g0 = GROUPS * layer

            def rows(n, b):
                pool.wait_ge(hot_eq, n * HOT + (g0 + b + 1))
                tok = bass.ds(n * HOT * GT + b * GT, GT)
                at = hot_j[:, b % HOT, :, :]
                nc.gpsimd.tensor_tensor(at, at, ijg[:, 2, tok].unsqueeze(2).broadcast_to([P, GT, KEYS]), ALU.mult).then_inc(hot_ready, 1)

            def apply(n, b):
                pool.wait_ge(gates_read, n * HOT + (g0 + b + 1))
                tok = hid[:, :, bass.ds(n * HOT * GT + b * GT, GT)].rearrange("p j t -> p t j")
                nc.gpsimd.tensor_tensor(tok, tok, staged[:, b, 0, :, :], ALU.mult).then_inc(gated_odd, 1)

            pool.wait_ge(ijg_ready, 2 * layer + 2)
            rows(0, 0)
            rows(0, 1)
            pool.wait_ge(gelu_ready, PAIRS * (2 * layer + 1))
            with pool.Fori(0, GROUPS // HOT - 1) as n:
                for b in range(HOT):
                    rows(n, b + 2)
                    if b % 2:
                        apply(n, b)
            for b in range(HOT):
                if b + 2 < HOT:
                    rows(GROUPS // HOT - 1, b + 2)
                if b % 2:
                    apply(GROUPS // HOT - 1, b)
            pool.wait_ge(gelu_ready, PAIRS * (2 * layer + 2))
            with pool.Fori(0, REGATED) as n:
                b = HOT - 1
                pool.wait_ge(reloaded[b], n * 16 + 16 * (REGATED * layer + 1))
                tok = hid[:, :, bass.ds((n * HOT + b) * (2 * GT), 2 * GT)].rearrange("p j t -> p t j")
                nc.gpsimd.tensor_tensor(tok, tok, reload[:, b, :, :], ALU.mult).then_inc(regated_pool, 1)

        pool.wait_ge(sel_ready, 2)
        ln_load(1)
        gate(0)
        pool.wait_ge(x_ready, 3)
        ln_load(2)
        pool.wait_ge(att_lo, 2)
        pool.dma_start(keys_sb, keys[1]).then_inc(keys_loaded, 16)
        pool.wait_ge(sel_ready, 4)
        ln_load(3)
        gate(1)

    @block.tensor
    def _(pe):
        mm = nc.tensor.matmul

        def natural(name, i):
            c, k0 = CHUNK_B[name, i], base + TILE_B[name, i]
            if c >= 2:
                wait_read(pe, c - 2)
            for j in range(2):
                k = k0 + j
                pe.wait_ge(lo_ready, k + 1)
                for kk_ in range(KB):
                    ki = j * KB + kk_
                    for t in range(TT):
                        dst = psum[2 * (c % 2) + t][:, :]
                        ws = slice(kk_ * CW, (kk_ + 1) * CW)
                        mm(dst, act_hi[:, ki, HALVES[t]], w_hi[:, k % SPLIT, ws], start=ki == 0, stop=False)
                        mm(dst, act_hi[:, ki, HALVES[t]], w_lo[:, k % SPLIT, ws], start=False, stop=False)
                        last = mm(dst, act_lo[:, ki, HALVES[t]], w_hi[:, k % SPLIT, ws], start=False, stop=ki == KD - 1)
                last.then_inc(tile_used, 1)

        def featured(name, i):
            c, k0 = CHUNK_B[name, i], base + TILE_B[name, i]
            if c >= 2:
                wait_read(pe, c - 2)
            for j in range(2):
                k = k0 + j
                pe.wait_ge(lo_ready, k + 1)
                for f in range(4):
                    for kk_ in range(KB):
                        ki = j * KB + kk_
                        ws = slice(kk_ * CW + f * P, kk_ * CW + (f + 1) * P)
                        dst = psum[2 * (c % 2) + f // 2][:, (f % 2) * S:(f % 2 + 1) * S]
                        wh, wl = w_hi[:, k % SPLIT, ws], w_lo[:, k % SPLIT, ws]
                        mm(dst, wh, act_hi[:, ki, :], start=ki == 0 and f % 2 == 0, stop=False)
                        mm(dst, wh, act_lo[:, ki, :], start=False, stop=False)
                        last = mm(dst, wl, act_hi[:, ki, :], start=False, stop=ki == KD - 1 and f % 2 == 1)
                last.then_inc(tile_used, 1)

        def transposes(src):
            for b in range(KD // 2):
                for k in (2 * b, 2 * b + 1):
                    for t in range(TT):
                        last = nc.tensor.transpose(psum[4 + b][:, (k % 2) * S + t * P:(k % 2) * S + (t + 1) * P],
                                                   src[:, t, k * P:(k + 1) * P], ident)
                last.then_inc(tr_done, 1)

        pe.wait_ge(x_ready, 1)
        transposes(x)
        pe.wait_ge(tr_lo, 4)
        pe.wait_ge(side_lo_ready, 1)
        for g in range(2):
            for k in range(KD):
                dst, ws = psum[4][:, g * S:(g + 1) * S], slice(g * P, (g + 1) * P)
                mm(dst, side_hi[:, k, ws], act_hi[:, k, :], start=k == 0 and g == 0, stop=False)
                mm(dst, side_hi[:, k, ws], act_lo[:, k, :], start=False, stop=False)
                last = mm(dst, side_lo[:, k, ws], act_hi[:, k, :], start=False, stop=k == KD - 1 and g == 1)
        last.then_inc(even_pe, 1)
        featured("gqk", 0)
        pe.wait_ge(even_loaded, 48)
        pe.wait_ge(even_act, EVEN_ACT["gates"])
        for g in range(GP):
            cols = slice(EW + g * P, EW + (g + 1) * P)
            last = mm(psum[5][:, g * S:(g + 1) * S], lora[GA2[0], cols], side_t[GA2[0], 1, :], start=True, stop=True)
        last.then_inc(even_pe, 1)
        for f in range(FT):
            last = mm(psum[6 + f // 2][:, (f % 2) * S:(f % 2 + 1) * S], lora[W2[0], f * P:(f + 1) * P], side_t[W2[0], 0, :],
                      start=True, stop=True)
        last.then_inc(even_pe, 1)
        natural("gv", 0)
        natural("gg", 0)
        pe.wait_ge(even_dve, EVEN_DVE["la"])
        pe.wait_ge(even_act, EVEN_ACT["w"])
        for f in range(FT):
            cols = slice(EW + f * P, EW + (f + 1) * P)
            last = mm(psum[4 + f // 2][:, (f % 2) * S:(f % 2 + 1) * S], lora[A2[0], cols], side_t[A2[0], 1, :], start=True, stop=True)
        last.then_inc(even_pe, 1)
        for t in range(TT):
            last = mm(psum[6 + t][:, :], side_t[G2[0], 0, HALVES[t]], lora[G2[0], G2[1]], start=True, stop=True)
        last.then_inc(even_pe, 1)
        featured("r", 0)
        featured("k", 0)
        featured("v", 0)
        pe.wait_ge(even_dve, EVEN_DVE["decayed"])
        pe.wait_ge(even_act, EVEN_ACT["a"])
        for e in range(2):
            for t in range(TT):
                for g in range(GP):
                    es = slice(e * GDK, (e + 1) * GDK)
                    last = mm(psum[4 + e][:, (t * GP + g) * P:(t * GP + g + 1) * P], kin[es, g, HALVES[t]], qin[es, g, HALVES[t]],
                              start=True, stop=True)
        last.then_inc(even_pe, 1)
        for t in range(TT):
            for g in range(GP):
                last = nc.tensor.transpose(psum[6][:, (t * GP + g) * P:(t * GP + g + 1) * P], en[:, g, HALVES[t]], ident)
        last.then_inc(even_pe, 1)
        wait_read(pe, CHUNK_B["v", 0])
        wait_read(pe, CHUNK_B["k", 0])
        pe.wait_ge(even_act, EVEN_ACT["keys"])
        for t in range(TT):
            for c in range(CH):
                cs = slice(c * CHUNK_T, (c + 1) * CHUNK_T)
                for g in range(GP):
                    last = mm(psum[2 * t + c][:, g * S:(g + 1) * S], konat[cs, (t * GP + g) * P:(t * GP + g + 1) * P],
                              gv[cs, t, g * S:(g + 1) * S], start=True, stop=True)
        last.then_inc(even_pe, 1)
        pe.wait_ge(even_dve, EVEN_DVE["states"])
        for t in range(TT):
            for g in range(GP):
                for c in range(CH):
                    if t or c:
                        mm(psum[6 + t][:, g * S:(g + 1) * S], qz[:, c, g, HALVES[t]], state[:, t * CH + c, g, :],
                           start=g == 0 and c == (0 if t else 1), stop=False)
                for e in range(2):
                    last = mm(psum[6 + t][:, g * S + e * GDV:g * S + (e + 1) * GDV], attn[:, e, t, g, :],
                              gv[:, t, g * S + e * GDV:g * S + (e + 1) * GDV], start=False, stop=g == GP - 1 and e == 1)
        last.then_inc(even_pe, 1)

        pe.wait_ge(even_dve, EVEN_DVE["gla"])

        def by_act(step, t):
            pe.wait_ge(rw_act, TT * RW_ACT[step] - TT + t + 1)

        def by_dve(step, t):
            pe.wait_ge(rw_dve, TT * RW_DVE[step] - TT + t + 1)

        chunks = [slice(c * CHUNK_T, (c + 1) * CHUNK_T) for c in range(CH)]
        heads = [(e, f) for e in range(2) for f in range(FT)]
        for t in range(TT):
            by_dve("bonus", t)
            for f in range(FT):
                mm(psum[4 * t + 1][:, 2 * f:2 * f + 2], kt[:, f, HALVES[t]], rkind[:, f, :], start=True, stop=True)
            for f in range(FT):
                last = mm(psum[4 * t][:, f * P:(f + 1) * P], cst("same_head"), sq[:, f, HALVES[t]], start=True, stop=True)
            last.then_inc(rw_pe, 1)
        for t in range(TT):
            by_dve("tilde", t)
            for n, src in enumerate((ar[:, :, 0, HALVES[t]], bt[:, :, HALVES[t]], kt[:, :, HALVES[t]], rkv[:, 2, :, HALVES[t]])):
                for f in range(FT):
                    last = nc.tensor.transpose(psum[4 * t + n][:, f * P:(f + 1) * P], src[:, f, :], ident)
            last.then_inc(rw_pe, 1)
        for t in range(TT):
            by_act("nat", t)
            for n, src in enumerate((bt, kt)):
                for f in range(FT):
                    for c in range(CH):
                        at = slice(t * P + c * CHUNK_T, t * P + (c + 1) * CHUNK_T)
                        for e in range(2):
                            es = slice(e * RN, (e + 1) * RN)
                            last = mm(psum[4 * t + 2 * n + e][chunks[c], f * P:(f + 1) * P], src[es, f, at], ar[es, f, :, at], start=True, stop=True)
            last.then_inc(rw_pe, 1)
        for n in range(LEVELS):
            for t in range(TT):
                by_dve(f"d{n - 1}" if n else "lr", t)
                for e, f in heads:
                    hs = slice((e * FT + f) * CHUNK_T, (e * FT + f + 1) * CHUNK_T)
                    for cs in chunks:
                        last = mm(psum[4 * t][cs, hs], lrb[cs, t, e, f, 0, :], dd[cs, t, e, f, :], start=True, stop=True)
                last.then_inc(rw_pe, 1)
            for t in range(TT):
                by_dve(f"x{n}", t)
                for e, f in heads:
                    hs = slice((e * FT + f) * CHUNK_T, (e * FT + f + 1) * CHUNK_T)
                    for cs in chunks:
                        last = mm(psum[4 * t + 2][cs, hs], xx[cs, t, e, f, :], dt_[cs, t, e, f, :], start=True, stop=True)
                        if n < LEVELS - 1:
                            last = mm(psum[4 * t + 1][cs, hs], dt_[cs, t, e, f, :], xx[cs, t, e, f, :], start=True, stop=True)
                last.then_inc(rw_pe, 1)
        for t in range(TT):
            by_dve(f"d{LEVELS - 1}", t)
            for f in range(FT):
                for e in range(2):
                    hs, es = slice((2 * f + e) * RN, (2 * f + e + 1) * RN), slice(e * RN, (e + 1) * RN)
                    for c, cs in enumerate(chunks):
                        mm(psum[4 * t][cs, hs], lrk[cs, t, e, f, 0, :], nat["v"][cs, t, hs], start=True, stop=True)
                        last = mm(psum[4 * t + 2 + c][es, f * CHUNK_T:(f + 1) * CHUNK_T], nat["a"][cs, t, hs], dt_[cs, t, e, f, :],
                                  start=True, stop=True)
            last.then_inc(rw_pe, 1)
        for t in range(TT):
            by_act("z", t)
            for f in range(FT):
                for e in range(2):
                    hs = slice((2 * f + e) * RN, (2 * f + e + 1) * RN)
                    for cs in chunks:
                        last = mm(psum[4 * t + 1][cs, hs], dt_[cs, t, e, f, :], zz[cs, t, hs], start=True, stop=True)
            last.then_inc(rw_pe, 1)
        for t in range(TT):
            by_act("wv", t)
            for c, cs in enumerate(chunks):
                n = t * CH + c
                if n:
                    pe.wait_ge(chain_dve, 2 * n)
                at = slice(t * P + c * CHUNK_T, t * P + (c + 1) * CHUNK_T)
                for f in range(FT):
                    last = mm(psum[4 * t + c][cs, f * P:(f + 1) * P], tat[:, f, at], s_all[:, n, f, :], start=True, stop=True)
                last.then_inc(chain_pe, 1)
                pe.wait_ge(chain_dve, 2 * n + 1)
                for f in range(FT):
                    fs = slice(f * P, (f + 1) * P)
                    mm(psum[4 * t + 2 + c][:, fs], nat["b"][cs, t, fs], uu[cs, t, fs], start=f == 0, stop=False)
                    last = mm(psum[4 * t + 2 + c][:, fs], nat["k"][cs, t, fs], nat["v"][cs, t, fs], start=False, stop=f == FT - 1)
                last.then_inc(chain_pe, 1)
            for c, cs in enumerate(chunks):
                at = slice(t * P + c * CHUNK_T, t * P + (c + 1) * CHUNK_T)
                for f in range(FT):
                    mm(psum[4 * t][cs, f * P:(f + 1) * P], ar[:, f, 1, at], s_all[:, t * CH + c, f, :], start=f == 0, stop=False)
                    for e in range(2):
                        hs = slice((2 * f + e) * RN, (2 * f + e + 1) * RN)
                        mm(psum[4 * t][cs, hs], lrb[cs, t, e, f, 1, :], uu[cs, t, hs], start=False, stop=False)
                        last = mm(psum[4 * t][cs, hs], lrk[cs, t, e, f, 1, :], nat["v"][cs, t, hs], start=False, stop=f == FT - 1 and e == 1)
            last.then_inc(rw_pe, 1)
        by_dve("out", TT - 1)
        transposes(ymix)
        pe.wait_ge(tr_lo, 8)
        natural("eout", 0)
        natural("eout", 1)

        def peer_layer(layer, t_lo):
            pe.wait_ge(x_ready, 2 + 2 * layer)
            transposes(x)
            pe.wait_ge(tr_lo, t_lo)
            featured(f"pq{layer}", 0)
            featured(f"pq{layer}", 1)
            pe.wait_ge(keys_loaded, 16 * (layer + 1))
            wait_read(pe, CHUNK_B[f"pq{layer}", 1])
            for t in range(TT):
                for h in range(PH):
                    last = mm(psum[4 * (1 - t) + h // 2][:, (h % 2) * 2 * KEYS:(h % 2 + 1) * 2 * KEYS], pq[:, h, HALVES[t]], keys_sb[:, h, :],
                              start=True, stop=True)
                last.then_inc(s_done, 1)
            pe.wait_ge(s_read, 2 * layer + 1)
            for part in range(2):
                done = 2 * layer + part
                first, g0 = PAIRS * done, GROUPS * layer
                tile = base + PEER_UV[layer] + 2 * PAIRS * part

                def hidden(n, p):
                    k = tile + p
                    pe.wait_ge(lo_ready, n * 2 + (k + 1))
                    if first or p > 1 or not isinstance(n, int):
                        pe.wait_ge(gelu_ready, n * 2 + (first + p - 1))
                    for jj in range(2):
                        dst = psum[4 + p % 2][:, jj * S:(jj + 1) * S]
                        for kk_ in range(KD):
                            ws = slice((2 * kk_ + jj) * P, (2 * kk_ + jj + 1) * P)
                            mm(dst, w_hi[:, k % SPLIT, ws], act_hi[:, kk_, :], start=kk_ == 0 and jj == 0, stop=False)
                            mm(dst, w_hi[:, k % SPLIT, ws], act_lo[:, kk_, :], start=False, stop=False)
                            last = mm(dst, w_lo[:, k % SPLIT, ws], act_hi[:, kk_, :], start=False, stop=kk_ == KD - 1 and jj == 1)
                    last.then_inc(tile_used, 1)

                def gates(n, b):
                    pe.wait_ge(hot_ready, n * HOT + (g0 + b + 1))
                    if g0 or not isinstance(n, int):
                        pe.wait_ge(gates_read, n * HOT + (g0 + b + 1 - HOT))
                    for i in range(GT):
                        last = mm(psum[4 + b][:, i * KEYS:(i + 1) * KEYS], hot_i[:, b, i, :], hot_j[:, b, i, :], start=True, stop=True)
                    last.then_inc(gates_done, 1)

                def output(n, p, begin=False, end=False):
                    k = tile + PAIRS + p
                    pe.wait_ge(lo_ready, n * 2 + (k + 1))
                    pe.wait_ge(c_lo_ready, n * 2 + (first + p + 1))
                    for jj in range(2):
                        for t in range(TT):
                            cs = slice(jj * S + t * P, jj * S + (t + 1) * P)
                            for c in range(2):
                                dst, ws = psum[2 * t + c][:, :], slice(jj * D + c * CW, jj * D + (c + 1) * CW)
                                mm(dst, c_hi[:, p % 2, cs], w_hi[:, k % SPLIT, ws], start=begin and jj == 0, stop=False)
                                mm(dst, c_hi[:, p % 2, cs], w_lo[:, k % SPLIT, ws], start=False, stop=False)
                                last = mm(dst, c_lo[:, p % 2, cs], w_hi[:, k % SPLIT, ws], start=False, stop=end and jj == 1)
                    last.then_inc(tile_used, 1)

                hidden(0, 0)
                hidden(0, 1)
                with pe.Fori(1, PAIRS // 2) as q:
                    hidden(q, 0)
                    hidden(q, 1)
                if part == 0:
                    for t in range(TT):
                        pe.wait_ge(sel_ready, 2 * layer + t + 1)
                        for n in range(3):
                            last = nc.tensor.transpose(psum[6 + t][:, n * P:(n + 1) * P], sel[:, t, n, :], ident)
                        last.then_inc(sel_t, 1)
                    pe.wait_ge(ijg_ready, 2 * layer + 2)
                    pe.wait_ge(gelu_ready, first + PAIRS)
                    for b in range(HOT):
                        gates(0, b)
                    with pe.Fori(1, GROUPS // HOT) as n:
                        for b in range(HOT):
                            gates(n, b)
                if part == 0:
                    pe.wait_ge(s_read, 2 * layer + 2)
                output(0, 0, begin=part == 0)
                output(0, 1)
                with pe.Fori(1, PAIRS // 2 - 1) as q:
                    output(q, 0)
                    output(q, 1)
                output(0, PAIRS - 2)
                output(0, PAIRS - 1, end=part == 1)

        peer_layer(0, 12)

        pe.wait_ge(x_ready, 3)
        transposes(x)
        pe.wait_ge(tr_lo, 16)
        for name, i in (("oq", 0), ("oq", 1), ("oqi", 0), ("okv", 0)):
            natural(name, i)
        pe.wait_ge(odd_dve, ODD_DVE["rope"])
        for h in range(AH):
            for t in range(TT):
                last = nc.tensor.transpose(psum[4 + h // 2][:, (h % 2) * S + t * P:(h % 2) * S + (t + 1) * P],
                                           qn[:, t, h * AD:(h + 1) * AD], ident)
        last.then_inc(odd_pe, 1)
        for h in range(IH // 2):
            for t in range(TT):
                last = nc.tensor.transpose(psum[h // 2][:, (h % 2) * S + t * P:(h % 2) * S + (t + 1) * P],
                                           qin_[:, t, h * P:(h + 1) * P], ident)
        for n, src in enumerate((kn, kid)):
            for t in range(TT):
                last = nc.tensor.transpose(psum[2 + n][:, t * P:(t + 1) * P], src[:, t, :], ident)
        last.then_inc(odd_pe, 1)
        pe.wait_ge(odd_act, ODD_ACT["it"])
        pe.wait_ge(odd_dve, ODD_DVE["kib"])
        for t in range(TT):
            for h in range(IH // 2):
                last = mm(psum[4 * t + h][:, :], qi_t[:, h, HALVES[t]], kib[:, :], start=True, stop=True)
            last.then_inc(odd_pe, 1)
        for t in range(TT):
            n = (t + 1) * P
            if t == 0:
                pe.wait_ge(odd_act, ODD_ACT["index1"])
            else:
                pe.wait_ge(att_lo, 1)
            for h in range(AH):
                last = mm(psum[h // 2][:, (h % 2) * S:(h % 2) * S + n], q_t[:, h, HALVES[t]], k_t[:, 0:n], start=True, stop=True)
            last.then_inc(odd_pe, 1)
            pe.wait_ge(odd_dve, ODD_DVE[f"probs{t}"])
            for h in range(AH):
                for s in range(t + 1):
                    last = nc.tensor.transpose(psum[4 + h // 2][:, ((h % 2) * TT + s) * P:((h % 2) * TT + s + 1) * P],
                                               logit[:, h, HALVES[s]], ident)
            last.then_inc(odd_pe, 1)
            pe.wait_ge(odd_act, ODD_ACT[f"pt{t}"])
            for hh in range(2):
                for s in range(t + 1):
                    last = mm(psum[hh][:, :], vn[:, s, :], pt[:, 4 * hh:4 * hh + 4, s, :], start=s == 0, stop=s == t)
            last.then_inc(odd_pe, 1)
        pe.wait_ge(att_lo, TT)
        natural("oout", 0)
        natural("oout", 1)
        peer_layer(1, 20)

    @block.scalar
    def _(act):
        do = Order(act, act_own)

        def split_hi(k):
            if k < total:
                act.wait_ge(raw_loaded[k % RAW], 16 * (k // RAW + 1))
                act.wait_ge(tile_used, k - 1)
                A.activation(w_hi[:, k % SPLIT, :], raw[:, k % RAW, :], ACT.Copy).then_inc(hi_ready, 1)

        def stream(name, i):
            for j in range(2):
                split_hi(base + TILE_B[name, i] + j + SPLIT)

        def taken(name, i):
            act.wait_ge(tile_used, base + TILE_B[name, i] + 2)

        def bank(name, i, t):
            return psum[2 * (CHUNK_B[name, i] % 2) + t]

        def split_t(first):
            for b in range(KD // 2):
                act.wait_ge(tr_done, first + b + 1)
                do(A.activation(act_hi[:, 2 * b:2 * b + 2, :].rearrange("p k s -> p (k s)"), psum[4 + b][:, :], ACT.Copy), tr_hi)

        def layer_norm(n):
            act.wait_ge(ln_var, n + 1)
            do(A.activation(small[:, 32:34], small[:, 24:28].rearrange("p (t k) -> p t k", k=2)[:, :, 1], ACT.Sqrt, bias=cst("ln_eps")), ln_std)

        def ecolumn(name, i):
            return ecol[:, ECOL[name] + i:ECOL[name] + i + 1]

        act.wait_ge(side_loaded, 16)
        do(A.activation(side_hi[:, :, :].rearrange("p k n -> p (k n)"), side_raw[:, :, :].rearrange("p k n -> p (k n)"), ACT.Copy),
           side_hi_ready)
        split_t(0)
        act.wait_ge(b_const, 16)
        act.wait_ge(even_loaded, 48)
        act.wait_ge(even_pe, EVEN_PE["side"])
        do(A.activation(sh[:, 0:2, 1:], psum[4][:, :].rearrange("p (g s) -> p g s", g=2), ACT.Copy), even_act)
        stream("gqk", 0)
        act.wait_ge(even_dve, EVEN_DVE["side"])
        do(A.activation(side_t[W2[0], 0, :], side_t[W2[0], 0, :], ACT.Tanh))
        do(A.activation(side_t[G2[0], 0, :], side_t[G2[0], 0, :], ACT.Sigmoid), even_act)
        taken("gqk", 0)
        for t in range(2):
            do(A.activation(gqk[:, 2 * t:2 * t + 2, :].rearrange("p f s -> p (f s)"), bank("gqk", 0, t)[:, :], ACT.Copy),
               read_act if t else None)
        act.wait_ge(even_pe, EVEN_PE["la"])
        for g in range(GP):
            do(A.activation(lb[:, g, :], psum[5][:, g * S:(g + 1) * S], ACT.Abs, bias=ecolumn("gla_a_b", g)))
        do(A.activation(lb[:, :, :], lb[:, :, :], ACT.Exp, scale=-1.0))
        do(A.activation(lb[:, :, :], lb[:, :, :], ACT.Ln, bias=cst("one")), even_act)
        act.wait_ge(even_pe, EVEN_PE["w"])
        for f in range(FT):
            do(A.activation(sgw[:, f, :], psum[6 + f // 2][:, (f % 2) * S:(f % 2 + 1) * S], ACT.Sigmoid, bias=ecolumn("w0", f)),
               even_act if f == FT - 1 else None)
        stream("gv", 0)
        taken("gv", 0)
        for t in range(TT):
            do(A.activation(gv[:, t, :], bank("gv", 0, t)[:, :], ACT.Copy), read_act if t else None)
        stream("gg", 0)
        taken("gg", 0)
        for t in range(TT):
            do(A.activation(gsil[:, t, :], bank("gg", 0, t)[:, :], ACT.Silu), read_act if t else None)
        act.wait_ge(even_pe, EVEN_PE["g"])
        for f in range(FT):
            do(A.activation(asig[:, f, :], psum[4 + f // 2][:, (f % 2) * S:(f % 2 + 1) * S], ACT.Sigmoid, bias=ecolumn("a0", f)))
        for t in range(TT):
            do(A.activation(gnat[:, t, :], psum[6 + t][:, :], ACT.Copy), even_act if t else None)
        act.wait_ge(even_dve, EVEN_DVE["cumsum"])
        do(A.activation(eb[:, :, :], la[:, :, :], ACT.Exp, scale=1.0 / 16))
        do(A.activation(kin[:, :, :], la[:, :, :], ACT.Exp, scale=-1.0 / 16))
        do(A.activation(en[:, :, :], lb[:, :, :], ACT.Exp, scale=-1.0 / 16), even_act)
        for n, name in enumerate("rkv"):
            stream(name, 0)
            taken(name, 0)
            if n:
                act.wait_ge(shifted_done, n)
            for t in range(2):
                do(A.activation(sh[:, 2 * t:2 * t + 2, 1:], bank(name, 0, t)[:, :].rearrange("p (f s) -> p f s", f=2), ACT.Copy),
                   read_act if t else None)
        act.wait_ge(even_pe, EVEN_PE["keys"])
        do(A.activation(konat[:, :], psum[6][:, :], ACT.Copy), even_act)
        act.wait_ge(even_pe, EVEN_PE["o"])
        for t in range(TT):
            for h in range(GH):
                ins = A.activation(lb[:, 0, 0:GDV], psum[6 + t][:, h * GDV:(h + 1) * GDV], ACT.Square, accum_out=small[:, t * GH + h:t * GH + h + 1])
                do(ins, even_act if t == TT - 1 and h == GH - 1 else None)
        do(A.activation(small[:, 8:16], small[:, 0:8], ACT.Sqrt, scale=1.0 / GDV, bias=cst("ln_eps")), even_act)
        def by_pe(step, t):
            act.wait_ge(rw_pe, TT * RW_PE[step] - TT + t + 1)

        def by_dve(step, t):
            act.wait_ge(rw_dve, TT * RW_DVE[step] - TT + t + 1)

        for t in range(TT):
            by_dve("cumsum", t)
            ts = HALVES[t]
            do(A.activation(pinc[:, :, ts], cw[:, :, ts], ACT.Exp))
            do(A.activation(pinv[:, :, ts], cw[:, :, ts], ACT.Exp, scale=-1.0))
            do(A.activation(pm[:, :, ts], pm[:, :, ts], ACT.Exp), rw_act)
        for t in range(TT):
            by_pe("bonus", t)
            do(A.activation(norm[:, t, :], psum[4 * t][:, :], ACT.Sqrt), rw_act)
        by_dve("tilde", TT - 1)
        for t in range(TT):
            by_pe("nat", t)
            for n, name in enumerate("abkv"):
                do(A.activation(nat[name][:, t, :], psum[4 * t + n][:, :], ACT.Copy), rw_act if n == 3 else None)
        for t in range(TT):
            by_pe("z", t)
            if t == 0:
                by_dve(f"d{LEVELS - 1}", TT - 1)
            do(A.activation(zz[:, t, :], psum[4 * t][:, :], ACT.Copy))
            for c in range(CH):
                at = slice(t * P + c * CHUNK_T, t * P + (c + 1) * CHUNK_T)
                do(A.activation(tat[:, :, at], psum[4 * t + 2 + c][:, 0:FT * CHUNK_T].rearrange("p (f s) -> p f s", f=FT), ACT.Copy),
                   rw_act if c == CH - 1 else None)
        for t in range(TT):
            by_pe("wv", t)
            do(A.activation(wv[:, t, :], psum[4 * t + 1][:, :], ACT.Copy), rw_act)
        for t in range(TT):
            by_dve("stats", t)
            do(A.activation(small[:, 8 * t:8 * t + 8], rstat[:, t, :, 1], ACT.Sqrt, bias=cst("lnx_eps")), rw_act)
        split_t(4)
        for i in range(2):
            stream("eout", i)
        layer_norm(0)

        def peer_layer(layer, t0):
            split_t(t0)
            for i in range(2):
                stream(f"pq{layer}", i)
                taken(f"pq{layer}", i)
                for t in range(2):
                    do(A.activation(pq[:, 4 * i + 2 * t:4 * i + 2 * t + 2, :].rearrange("p f s -> p (f s)"), bank(f"pq{layer}", i, t)[:, :], ACT.Copy),
                       read_act if t else None)
            for t in range(TT):
                act.wait_ge(s_done, 2 * layer + t + 1)
                for b in range(4):
                    do(A.activation(ss[t][:, 4 * b:4 * b + 4, :].rearrange("p f s -> p (f s)"), psum[4 * (1 - t) + b][:, :], ACT.Copy),
                       s_read if b == 3 else None)
            for part in range(2):
                done = 2 * layer + part
                first = PAIRS * done
                tile = base + PEER_UV[layer] + 2 * PAIRS * part

                def split_tile(n, k):
                    kt_ = tile + k
                    if kt_ >= total:
                        return
                    act.wait_ge(raw_loaded[kt_ % RAW], n * 16 + 16 * (kt_ // RAW + 1))
                    act.wait_ge(tile_used, n * RAW + (kt_ - 1))
                    A.activation(w_hi[:, kt_ % SPLIT, :], raw[:, kt_ % RAW, :], ACT.Copy).then_inc(hi_ready, 1)

                def padded(wait, n):
                    act.wait_ge(wait, n)
                    act.sem_inc(act_pad, 1)

                def pair(ap, n, p):
                    return ap[:, 2 * p:2 * p + 2, :] if isinstance(n, int) else ap[:, bass.ds(n * 2 * RAW + 2 * p, 2), :]

                def gelu(n, p):
                    padded(tile_used, n * RAW + (tile + p + 1))
                    A.activation(pair(hid, n, p), psum[4 + p % 2][:, :].rearrange("p (j s) -> p j s", j=2), ACT.Gelu).then_inc(gelu_ready, 1)

                def upper(n, p):
                    padded(tile_used, n * RAW + (tile + PAIRS + p - 1))
                    A.activation(c_hi[:, p % 2, :].rearrange("p (j s) -> p j s", j=2), pair(hid, n, p), ACT.Copy).then_inc(c_hi_ready, 1)

                if first:
                    act.wait_ge(c_lo_ready, first)
                with act.Fori(0, PAIRS // RAW) as n:
                    for p in range(RAW):
                        split_tile(n, p + 2)
                        gelu(n, p)
                if part == 0:
                    act.wait_ge(best_ready, layer + 1)
                    do(A.activation(best[:, :, :, :], best[:, :, :, :], ACT.Exp), exp_ready)
                    for t in range(TT):
                        act.wait_ge(sel_t, 2 * layer + t + 1)
                        do(A.activation(ijg[:, :, HALVES[t]], psum[6 + t][:, 0:3 * P].rearrange("p (n s) -> p n s", n=3), ACT.Copy), ijg_ready)
                g0 = GROUPS * layer

                def stage(n, b):
                    act.wait_ge(gates_done, n * HOT + (g0 + b + 1))
                    if not isinstance(n, int):
                        act.wait_ge(gated_odd if b % 2 else gated_even, n * (HOT // 2) + (g0 // 2 + b // 2 + 1 - HOT // 2))
                        act.wait_ge(spilled[b], n * 16 + 16 * (GROUPS // HOT) * layer)
                    A.activation(staged[:, b, :, :, :].rearrange("p h t j -> p t h j"), psum[4 + b][:, :].rearrange("p (t h j) -> p t h j", t=GT, h=2),
                                 ACT.Copy).then_inc(gates_read, 1)

                if part == 0:
                    for b in range(HOT):
                        stage(0, b)
                    with act.Fori(1, GROUPS // HOT) as n:
                        for b in range(HOT):
                            stage(n, b)
                if part == 0:
                    act.wait_ge(gated_odd, GROUPS // 2 * (layer + 1))
                    act.wait_ge(gated_even, GROUPS // 2 * (layer + 1))
                else:
                    act.wait_ge(regated_pool, REGATED * (layer + 1))
                    act.wait_ge(regated_dve, (HOT - 1) * REGATED * (layer + 1))
                if part == 0:
                    for b in range(HOT):
                        act.wait_ge(spilled[b], 16 * (GROUPS // HOT) * (layer + 1))
                upper(0, 0)
                upper(0, 1)
                with act.Fori(0, PAIRS // RAW - 1) as n:
                    for p in range(RAW):
                        split_tile(n, PAIRS + p + 2)
                        upper(n, p + 2)
                for p in range(PAIRS - RAW, PAIRS):
                    split_tile(0, PAIRS + p + 2)
                    if p + 2 < PAIRS:
                        upper(0, p + 2)

        peer_layer(0, 8)
        layer_norm(1)
        split_t(12)
        for name, i in (("oq", 0), ("oq", 1), ("oqi", 0), ("okv", 0)):
            stream(name, i)
        act.wait_ge(odd_pe, ODD_PE["qt"])
        for b in range(4):
            do(A.activation(q_t[:, 2 * b:2 * b + 2, :].rearrange("p h s -> p (h s)"), psum[4 + b][:, :], ACT.Copy), odd_act if b == 3 else None)
        act.wait_ge(odd_pe, ODD_PE["it"])
        for b in range(2):
            do(A.activation(qi_t[:, 2 * b:2 * b + 2, :].rearrange("p h s -> p (h s)"), psum[b][:, :], ACT.Copy))
        do(A.activation(k_t[:, :], psum[2][:, 0:S], ACT.Copy), odd_act)
        for t in range(TT):
            act.wait_ge(odd_pe, ODD_PE[f"index{t}"])
            if t:
                act.wait_ge(odd_dve, ODD_DVE["index0"])
            for h in range(IH // 2):
                do(A.activation(rel[:, 2 * h:2 * h + 2, :].rearrange("p h s -> p (h s)"), psum[4 * t + h][:, :], ACT.Relu),
                   odd_act if h == IH // 2 - 1 else None)
        for t in range(TT):
            n = (t + 1) * P
            act.wait_ge(odd_dve, ODD_DVE[f"logits{t}"])
            for h in range(AH):
                do(A.activation(logit[:, h, 0:n], logit[:, h, 0:n], ACT.Exp, bias=amax[:, h:h + 1], accum_out=asum[:, h:h + 1]),
                   odd_act if h == AH - 1 else None)
            act.wait_ge(odd_pe, ODD_PE[f"pt{t}"])
            for b in range(4):
                for s in range(t + 1):
                    do(A.activation(pt[:, 2 * b:2 * b + 2, s, :], psum[4 + b][:, :].rearrange("p (h s k) -> p h s k", h=2, s=TT)[:, :, s, :], ACT.Copy),
                       odd_act if b == 3 and s == t else None)
            act.wait_ge(odd_pe, ODD_PE[f"o{t}"])
            for hh in range(2):
                do(A.activation(act_hi[:, 4 * hh:4 * hh + 4, HALVES[t]], psum[hh][:, :].rearrange("p (h s) -> p h s", h=4), ACT.Copy),
                   att_hi if hh else None)
        for i in range(2):
            stream("oout", i)
        layer_norm(2)
        peer_layer(1, 16)
        layer_norm(3)

    @block.vector
    def _(dve):
        do = Order(dve, dve_own)

        def bcast(ap, shape):
            return ap.broadcast_to(shape)

        def split_lo(k):
            if k < total:
                dve.wait_ge(hi_ready, k + 1)
                V.tensor_tensor(w_lo[:, k % SPLIT, :], raw[:, k % RAW, :], w_hi[:, k % SPLIT, :].bitcast(F32), ALU.subtract).then_inc(lo_ready, 1)

        def stream(name, i):
            for j in range(2):
                split_lo(base + TILE_B[name, i] + j + SPLIT)

        def taken(name, i):
            dve.wait_ge(tile_used, base + TILE_B[name, i] + 2)

        def bank(name, i, t):
            return psum[2 * (CHUNK_B[name, i] % 2) + t]

        def split_t(first):
            for b in range(KD // 2):
                dve.wait_ge(tr_hi, first + b + 1)
                ks = slice(2 * b, 2 * b + 2)
                do(V.tensor_tensor(act_lo[:, ks, :].rearrange("p k s -> p (k s)"), psum[4 + b][:, :],
                                   act_hi[:, ks, :].rearrange("p k s -> p (k s)").bitcast(F32), ALU.subtract), tr_lo)

        def residual(t, n, src):
            xs = x[:, t, n * CW:(n + 1) * CW]
            return V.scalar_tensor_tensor(out=xs, in0=xs, scalar=ALPHA, in1=src, op0=ALU.mult, op1=ALU.add)

        def layer_norm(n):
            for t in range(TT):
                for c in range(2):
                    do(V.bn_stats(small[:, 40 + 6 * c:46 + 6 * c], x[:, t, c * CW:(c + 1) * CW]))
                do(V.bn_aggr(small[:, 24 + 2 * t:26 + 2 * t], small[:, 40:52].rearrange("p (c k) -> p c k", c=2)), ln_var if t else None)
            dve.wait_ge(ln_std, n + 1)
            do(V.reciprocal(small[:, 34:36], small[:, 32:34]))
            dve.wait_ge(ln_loaded, 32 * (n + 1))
            for t in range(TT):
                do(V.tensor_scalar(x[:, t, :], x[:, t, :], small[:, 24 + 2 * t:25 + 2 * t], small[:, 34 + t:35 + t], ALU.subtract, ALU.mult))
                do(V.tensor_tensor(x[:, t, :], x[:, t, :], ln_row[:, 0, :], ALU.mult))
                do(V.tensor_tensor(x[:, t, :], x[:, t, :], ln_row[:, 1, :], ALU.add), x_ready if t else None)

        def ecolumn(name, i):
            return ecol[:, ECOL[name] + i:ECOL[name] + i + 1]

        do(V.memset(sh[:, :, 0:1], 0.0))
        dve.wait_ge(side_hi_ready, 1)
        do(V.tensor_tensor(side_lo[:, :, :].rearrange("p k n -> p (k n)"), side_raw[:, :, :].rearrange("p k n -> p (k n)"),
                           side_hi[:, :, :].rearrange("p k n -> p (k n)").bitcast(F32), ALU.subtract), side_lo_ready)
        split_t(0)
        dve.wait_ge(b_const, 16)
        dve.wait_ge(even_loaded, 48)

        def shift(dst, n, mu, signal):
            do(V.tensor_tensor(dif[:, 0:n, :], sh[:, 0:n, 0:S], sh[:, 0:n, 1:], ALU.subtract))
            for f in range(n):
                do(V.scalar_tensor_tensor(out=dst(f), in0=dif[:, f, :], scalar=mu(f), in1=sh[:, f, 1:], op0=ALU.mult, op1=ALU.add),
                   signal if f == n - 1 else None)

        dve.wait_ge(even_act, EVEN_ACT["side"])
        shift(lambda f: side_t[:, f, :], 2, lambda f: ecolumn("mu_side", f), even_dve)
        stream("gqk", 0)
        dve.wait_ge(even_act, EVEN_ACT["lnexp"])
        for g in range(GP):
            do(V.tensor_scalar(la[:, g, :], psum[5][:, g * S:(g + 1) * S], ecolumn("gla_a_b", g), 0.0, ALU.add, ALU.min))
        do(V.tensor_tensor(la[:, :, :], la[:, :, :], lb[:, :, :], ALU.subtract), even_dve)
        stream("gv", 0)
        for g in range(GP):
            do(V.tensor_tensor_scan(qin[:, g, :], cst("keep"), la[:, g, :], 0.0, ALU.mult, ALU.add))
        do(V.tensor_copy(la[:, :, :], qin[:, :, :]))
        for g in range(GP):
            sums = la[:, g, :].rearrange("p (c s) -> p c s", s=CHUNK_T)
            do(V.tensor_tensor(lb[:, g, :].rearrange("p (c s) -> p c s", s=CHUNK_T), sums,
                               bcast(sums[:, :, CHUNK_T - 1:CHUNK_T], [P, CH * TT, CHUNK_T]), ALU.subtract), even_dve if g else None)
        stream("gg", 0)
        for n, name in enumerate("rkv"):
            stream(name, 0)
            wait_read(dve, CHUNK_B[name, 0])
            shift(lambda f: rkv[:, n, f, :], FT, lambda f: ecolumn("mu", FT * n + f), shifted_done)
        dve.wait_ge(even_act, EVEN_ACT["decays"])
        do(V.scalar_tensor_tensor(out=qin[:, :, :], in0=gqk[:, 0:2, :], scalar=GDK ** -0.5, in1=eb[:, :, :], op0=ALU.mult, op1=ALU.mult))
        do(V.tensor_tensor(kin[:, :, :], kin[:, :, :], gqk[:, 2:4, :], ALU.mult))
        do(V.memset(qz[:, :, :, :], 0.0))
        for c in range(CH):
            for g in range(GP):
                cut = lambda ap: ap.rearrange("p (t c s) -> p t c s", c=CH, s=CHUNK_T)[:, :, c, :]
                do(V.tensor_copy(cut(qz[:, c, g, :]), cut(qin[:, g, :])))
        do(V.tensor_tensor(en[:, :, :], en[:, :, :], gqk[:, 2:4, :], ALU.mult), even_dve)
        upto = cst("upto")
        dve.wait_ge(even_pe, EVEN_PE["keys"])
        for e in range(2):
            do(V.tensor_tensor(attn[:, e, :, :, :].rearrange("p t g s -> p (t g) s"), psum[4 + e][:, :].rearrange("p (n s) -> p n s", n=TT * GP),
                               bcast(upto.unsqueeze(1), [P, TT * GP, P]), ALU.mult), even_dve if e else None)
        dve.wait_ge(even_pe, EVEN_PE["kv"])
        for c in range(CH * TT - 1):
            for g in range(GP):
                do(V.tensor_tensor(state[:, c + 1, g, :], psum[c][:, g * S:(g + 1) * S], cst("diag2"), ALU.mult))
                if c:
                    do(V.scalar_tensor_tensor(out=state[:, c + 1, g, :], in0=state[:, c, g, :], scalar=eb[:, g, (c + 1) * CHUNK_T - 1:(c + 1) * CHUNK_T],
                                              in1=state[:, c + 1, g, :], op0=ALU.mult, op1=ALU.add),
                       even_dve if c == CH * TT - 2 and g == GP - 1 else None)
        dve.wait_ge(even_act, EVEN_ACT["std"])
        do(V.reciprocal(small[:, 8:16], small[:, 8:16]))
        for t in range(TT):
            for h in range(GH):
                hs = slice(h * GDV, (h + 1) * GDV)
                do(V.scalar_tensor_tensor(out=ymix[:, t, hs], in0=psum[6 + t][:, hs], scalar=small[:, 8 + t * GH + h:9 + t * GH + h],
                                          in1=erow[:, EROW["gla_g"]], op0=ALU.mult, op1=ALU.mult))
            do(V.tensor_tensor(ymix[:, t, 0:EW], ymix[:, t, 0:EW], gsil[:, t, :], ALU.mult), even_dve if t else None)

        flat = lambda ap: ap.rearrange("p f s -> p (f s)")
        do(V.memset(s_all[:, 0, :, :], 0.0))
        for f in range(FT):
            do(V.tensor_scalar(rkind[:, f, :], cst("half"), ecolumn("r_k", f), None, ALU.mult))

        def by_act(step, t):
            dve.wait_ge(rw_act, TT * RW_ACT[step] - TT + t + 1)

        def by_pe(step, t):
            dve.wait_ge(rw_pe, TT * RW_PE[step] - TT + t + 1)

        r, k = rkv[:, 0, :, :], rkv[:, 1, :, :]
        for t in range(TT):
            ts = HALVES[t]
            do(V.tensor_scalar(sgw[:, :, ts], sgw[:, :, ts], -float(np.exp(-0.5)), None, ALU.mult))
            for f in range(FT):
                do.also(V.tensor_tensor_scan(cw[:, f, ts], cst("keep")[:, 0:P], sgw[:, f, ts], 0.0, ALU.mult, ALU.add))
            do.settle()
            do(V.tensor_tensor(pm[:, :, ts], cw[:, :, ts], sgw[:, :, ts], ALU.subtract), rw_dve)
        for t in range(TT):
            ts = HALVES[t]
            for f in range(FT):
                do.also(V.tensor_scalar(kk[:, f, ts], k[:, f, ts], ecolumn("k_k", f), None, ALU.mult))
                do.also(V.tensor_scalar(kp[:, f, ts], asig[:, f, ts], -1.0, ecolumn("k_a", f), ALU.add, ALU.mult))
            do.settle()
            do.also(V.tensor_tensor(sq[:, :, ts], kk[:, :, ts], kk[:, :, ts], ALU.mult))
            do(V.scalar_tensor_tensor(out=kp[:, :, ts], in0=kp[:, :, ts], scalar=1.0, in1=k[:, :, ts], op0=ALU.add, op1=ALU.mult))
            do(V.tensor_tensor(kt[:, :, ts], r[:, :, ts], kp[:, :, ts], ALU.mult), rw_dve)
        for t in range(TT):
            ts = HALVES[t]
            by_act("decays", t)
            do.also(V.tensor_tensor(ar[:, :, 1, ts], r[:, :, ts], pinc[:, :, ts], ALU.mult))
            by_act("norm", t)
            do.also(V.tensor_copy(bonus[:, t, :], psum[4 * t + 1][:, 0:RH]))
            n0 = norm[:, t, :]
            do(V.tensor_scalar(n0, n0, 1e-12, None, ALU.max))
            do(V.reciprocal(n0, n0))
            do(V.tensor_tensor(kk[:, :, ts], kk[:, :, ts], n0.rearrange("p (f s) -> p f s", f=FT), ALU.mult))
            do.also(V.scalar_tensor_tensor(out=ar[:, :, 0, ts], in0=kk[:, :, ts], scalar=-1.0, in1=pm[:, :, ts], op0=ALU.mult, op1=ALU.mult))
            do(V.tensor_tensor(bt[:, :, ts], kk[:, :, ts], asig[:, :, ts], ALU.mult))
            do.also(V.tensor_tensor(bt[:, :, ts], bt[:, :, ts], pinv[:, :, ts], ALU.mult))
            do.settle()
            do(V.tensor_tensor(kt[:, :, ts], kp[:, :, ts], pinv[:, :, ts], ALU.mult), rw_dve)
        eye = cst("eye64")
        for t in range(TT):
            for buf in (dd, dt_):
                do.also(V.tensor_copy(buf[:, t, :, :, :].rearrange("p e f s -> p (e f) s"), bcast(eye.unsqueeze(1), [P, RH, CHUNK_T])))
        do.settle()
        for t in range(TT):
            by_pe("lr", t)
            for n, dst in enumerate((lrb, lrk)):
                for e in range(2):
                    ins = V.tensor_tensor(dst[:, t, e, :, :, :].rearrange("p f a s -> p f (a s)"), psum[4 * t + 2 * n + e][:, :].rearrange("p (f s) -> p f s", f=FT),
                                          bcast(cst("strict_upto").unsqueeze(1), [P, FT, P]), ALU.mult)
                    do.also(ins) if n == 0 or e == 0 else do(ins, rw_dve)
        for n in range(LEVELS):
            level = cst("levels")[:, n * CHUNK_T:(n + 1) * CHUNK_T]
            for t in range(TT):
                by_pe(f"x{n}", t)
                do(V.tensor_tensor(xx[:, t, :, :, :].rearrange("p e f s -> p (e f) s"), psum[4 * t][:, :].rearrange("p (h s) -> p h s", h=RH),
                                   bcast(level.unsqueeze(1), [P, RH, CHUNK_T]), ALU.mult), rw_dve)
            for t in range(TT):
                by_pe(f"d{n}", t)
                all_of = lambda buf: buf[:, t, :, :, :].rearrange("p e f s -> p (e f s)")
                if n < LEVELS - 1:
                    do.also(V.tensor_tensor(all_of(dd), all_of(dd), psum[4 * t + 1][:, :], ALU.add))
                do(V.tensor_tensor(all_of(dt_), all_of(dt_), psum[4 * t + 2][:, :], ALU.add), rw_dve)
        do.settle()
        for t in range(TT):
            by_act("wv", t)
            for c in range(CH):
                n = t * CH + c
                cs = slice(c * CHUNK_T, (c + 1) * CHUNK_T)
                dve.wait_ge(chain_pe, 2 * n + 1)
                do(V.tensor_tensor(uu[cs, t, :], psum[4 * t + c][cs, :], wv[cs, t, :], ALU.add), chain_dve)
                dve.wait_ge(chain_pe, 2 * n + 2)
                nxt, end = s_all[:, n + 1, :, :], t * P + (c + 1) * CHUNK_T - 1
                do(V.tensor_tensor(nxt, psum[4 * t + 2 + c][:, :].rearrange("p (f s) -> p f s", f=FT), bcast(cst("same_head").unsqueeze(1), [P, FT, P]), ALU.mult))
                do(V.tensor_tensor(nxt, nxt, s_all[:, n, :, :], ALU.add))
                do(V.tensor_tensor(nxt, nxt, bcast(pinc[:, :, end:end + 1], [P, FT, P]), ALU.mult), chain_dve)
        for t in range(TT):
            by_pe("y", t)
            for h in range(RH):
                do(V.bn_stats(r6[:, :], psum[4 * t][:, h * RN:(h + 1) * RN]))
                do(V.bn_aggr(rstat[:, t, h, :], r6[:, :]), rw_dve if h == RH - 1 else None)
        for t in range(TT):
            by_act("std", t)
            do(V.reciprocal(small[:, 16 + 8 * t:24 + 8 * t], small[:, 8 * t:8 * t + 8]))
            yo = ymix[:, t, EW:2 * EW]
            for h in range(RH):
                hs = slice(h * RN, (h + 1) * RN)
                do.also(V.tensor_scalar(yo[:, hs], psum[4 * t][:, hs], rstat[:, t, h, 0:1], small[:, 16 + 8 * t + h:17 + 8 * t + h],
                                        ALU.subtract, ALU.mult))
            do.settle()
            do(V.tensor_tensor(yo, yo, erow[:, EROW["lnx_g"]], ALU.mult))
            do(V.tensor_tensor(yo, yo, erow[:, EROW["lnx_b"]], ALU.add))
            for h in range(RH):
                hs = slice(h * RN, (h + 1) * RN)
                do.also(V.scalar_tensor_tensor(out=yo[:, hs], in0=nat["v"][:, t, hs], scalar=bonus[:, t, h:h + 1], in1=yo[:, hs],
                                               op0=ALU.mult, op1=ALU.add))
            do.settle()
            do(V.tensor_tensor(yo, yo, gnat[:, t, :], ALU.mult), rw_dve)
        split_t(4)
        for i in range(2):
            stream("eout", i)
            taken("eout", i)
            for t in range(TT):
                do(residual(t, i, bank("eout", i, t)[:, :]), read_dve if t else None)
        layer_norm(0)

        def peer_layer(layer, t0):
            split_t(t0)
            for i in range(2):
                stream(f"pq{layer}", i)
            def top16(streams):
                for vals, top, _ in streams:
                    do.also(V.max(top[:, 0:8], vals))
                do.settle()
                for vals, top, idx in streams:
                    do.also(V.max_index(idx[:, 0:8], top[:, 0:8], vals))
                do.settle()
                for vals, top, _ in streams:
                    do.also(V.match_replace(out=vals, in_to_replace=top[:, 0:8], in_values=vals, imm_value=-3e38))
                do.settle()
                for vals, top, _ in streams:
                    do.also(V.max(top[:, 8:16], vals))
                do.settle()
                for vals, top, idx in streams:
                    do.also(V.max_index(idx[:, 8:16], top[:, 8:16], vals))
                do.settle()

            def choose(t, split):
                dve.wait_ge(s_read, 2 * layer + t + 1)
                for n in range(0, 2 * PH, 2):
                    top16([(ss[t][:, c, :], tops[:, c, :], topi[:, c, :]) for c in (n, n + 1)])
                    split(n // 2)
                do(V.tensor_copy(topf[:, :, :], topi[:, :, :]))
                cand = ss[t][:, :, :].rearrange("p (h c) n -> p h (c n)", h=PH)
                for h in range(0, PH, 2):
                    for i in (h, h + 1):
                        do.also(V.tensor_tensor(cand[:, i, :].rearrange("p (a b) -> p a b", a=PK), bcast(tops[:, 2 * i, :].unsqueeze(2), [P, PK, PK]),
                                                bcast(tops[:, 2 * i + 1, :].unsqueeze(1), [P, PK, PK]), ALU.add))
                    do.settle()
                    top16([(cand[:, i, :], best[:, t, i, :], pos[:, i, :]) for i in (h, h + 1)])
                    split(PH + h // 2)
                do(V.tensor_copy(gsum[:, 0:PH], best[:, t, :, 0]))
                do(V.tensor_tensor(best[:, t, :, :], best[:, t, :, :], bcast(gsum[:, 0:PH].unsqueeze(2), [P, PH, PK]), ALU.subtract),
                   best_ready if t else None)
                pf = pos[:, :, :].rearrange("p h k -> p (h k)")
                do.also(V.tensor_scalar(posab[:, 0, :], pf, 4, None, ALU.logical_shift_right))
                do(V.tensor_scalar(posab[:, 1, :], pf, PK - 1, None, ALU.bitwise_and))
                do(V.tensor_copy(posf[:, :, :], posab[:, :, :]))
                tf = topf[:, :, :].rearrange("p (h c) k -> p h c k", c=2)
                split(PH + 4)
                for c in range(2):
                    do(V.tensor_tensor(hot.rearrange("p h k a -> p (h k) a"), bcast(posf[:, c, :].unsqueeze(2), [P, PH * PK, PK]),
                                       bcast(cst("iota")[:, 0:PK].unsqueeze(1), [P, PH * PK, PK]), ALU.is_equal))
                    do(V.tensor_tensor(hot, hot, bcast(tf[:, :, c, :].unsqueeze(2), [P, PH, PK, PK]), ALU.mult))
                    do(V.reduce_sum(sel[:, t, c, :], hot.rearrange("p h k a -> p (h k) a"), AXX))
                    split(PH + 5 + c)
                split(PH + 7)

            for part in range(2):
                done = 2 * layer + part
                first, g0 = PAIRS * done, GROUPS * layer
                tile = base + PEER_UV[layer] + 2 * PAIRS * part

                def split_tile(n, k):
                    kt_ = tile + k
                    if kt_ >= total:
                        return
                    dve.wait_ge(hi_ready, n * RAW + (kt_ + 1))
                    V.tensor_tensor(w_lo[:, kt_ % SPLIT, :], raw[:, kt_ % RAW, :], w_hi[:, kt_ % SPLIT, :].bitcast(F32), ALU.subtract).then_inc(lo_ready, 1)

                if part == 0:
                    for t in range(TT):
                        choose(t, lambda n: split_tile(0, t * PAIRS // 2 + n + 2))
                    dve.wait_ge(exp_ready, layer + 1)
                    do(V.reduce_sum(gsum[:, :], best[:, :, :, :].rearrange("p t h k -> p (t h) k"), AXX))
                    do(V.reciprocal(gsum[:, :], gsum[:, :]))
                    for t in range(TT):
                        do(V.tensor_tensor(sel[:, t, 2, :].rearrange("p (h k) -> p h k", h=PH), best[:, t, :, :],
                                           bcast(gsum[:, t * PH:(t + 1) * PH].unsqueeze(2), [P, PH, PK]), ALU.mult), sel_ready)
                    dve.wait_ge(ijg_ready, 2 * layer + 2)
                else:
                    with dve.Fori(0, PAIRS // RAW) as n:
                        for p in range(RAW):
                            split_tile(n, p + 2)

                def one_hot(n, b):
                    tok = bass.ds(n * HOT * GT + b * GT, GT)
                    if not isinstance(n, int):
                        dve.wait_ge(gates_done, n * HOT + (g0 + b + 1 - HOT))
                    for keys_at, dst in ((1, hot_j), (0, hot_i)):
                        ins = V.tensor_tensor(dst[:, b, :, :], bcast(cst("iota").unsqueeze(1), [P, GT, KEYS]),
                                              bcast(ijg[:, keys_at, tok].unsqueeze(2), [P, GT, KEYS]), ALU.is_equal)
                    ins.then_inc(hot_eq, 1)

                def apply(n, b):
                    dve.wait_ge(gates_read, n * HOT + (g0 + b + 1))
                    tok = hid[:, :, bass.ds(n * HOT * GT + b * GT, GT)].rearrange("p j t -> p t j")
                    V.tensor_tensor(tok, tok, staged[:, b, 0, :, :], ALU.mult).then_inc(gated_even, 1)

                if part == 0:
                    for b in range(HOT):
                        one_hot(0, b)
                    dve.wait_ge(gelu_ready, first + PAIRS)
                    with dve.Fori(0, GROUPS // HOT - 1) as n:
                        for b in range(HOT):
                            one_hot(n + 1, b)
                            if b % 2 == 0:
                                apply(n, b)
                    for b in range(0, HOT, 2):
                        apply(GROUPS // HOT - 1, b)
                else:
                    dve.wait_ge(gelu_ready, first + PAIRS)
                    with dve.Fori(0, REGATED) as n:
                        for b in range(HOT - 1):
                            dve.wait_ge(reloaded[b], n * 16 + 16 * (REGATED * layer + 1))
                            tok = hid[:, :, bass.ds((n * HOT + b) * (2 * GT), 2 * GT)].rearrange("p j t -> p t j")
                            V.tensor_tensor(tok, tok, reload[:, b, :, :], ALU.mult).then_inc(regated_dve, 1)

                def lower(n, p):
                    dve.wait_ge(c_hi_ready, n * RAW + (first + p + 1))
                    at = slice(2 * p, 2 * p + 2) if isinstance(n, int) else bass.ds(n * 2 * RAW + 2 * p, 2)
                    halves = lambda ap: ap.rearrange("p (j s) -> p j s", j=2)
                    V.tensor_tensor(halves(c_lo[:, p % 2, :]), hid[:, at, :], halves(c_hi[:, p % 2, :]).bitcast(F32), ALU.subtract).then_inc(c_lo_ready, 1)

                lower(0, 0)
                lower(0, 1)
                with dve.Fori(0, PAIRS // RAW - 1) as n:
                    for p in range(RAW):
                        split_tile(n, PAIRS + p + 2)
                        lower(n, p + 2)
                for p in range(PAIRS - RAW, PAIRS):
                    split_tile(0, PAIRS + p + 2)
                    if p + 2 < PAIRS:
                        lower(0, p + 2)
            dve.wait_ge(tile_used, base + PEER_UV[layer] + 4 * PAIRS)
            for t in range(TT):
                for n in range(2):
                    do(residual(t, n, psum[2 * t + n][:, :]))

        peer_layer(0, 8)
        layer_norm(1)
        split_t(12)

        def rope(dst, src, width, t):
            w = width // 2
            heads = dst.shape[1] // width
            cut = lambda ap: ap.rearrange("p (h n) -> p h n", n=width)
            cos = bcast(cst(f"cos{width}")[:, t * w:(t + 1) * w].unsqueeze(1), [P, heads, w])
            sin = bcast(cst(f"sin{width}")[:, t * w:(t + 1) * w].unsqueeze(1), [P, heads, w])
            x1, x2 = cut(src)[:, :, 0:w], cut(src)[:, :, w:width]
            o1, o2 = cut(dst)[:, :, 0:w], cut(dst)[:, :, w:width]
            r1 = rtmp[:, 0:heads * w].rearrange("p (h n) -> p h n", n=w)
            do(V.tensor_tensor(o1, x1, cos, ALU.mult))
            do(V.tensor_tensor(r1, x2, sin, ALU.mult))
            do(V.tensor_tensor(o1, o1, r1, ALU.subtract))
            do(V.tensor_tensor(o2, x2, cos, ALU.mult))
            do(V.tensor_tensor(r1, x1, sin, ALU.mult))
            return V.tensor_tensor(o2, o2, r1, ALU.add)

        for i in range(2):
            stream("oq", i)
            taken("oq", i)
            for t in range(TT):
                do(rope(qn[:, t, i * CW:(i + 1) * CW], bank("oq", i, t)[:, :], AD, t), read_dve if t else None)
        stream("oqi", 0)
        taken("oqi", 0)
        for t in range(TT):
            do(rope(qin_[:, t, :], bank("oqi", 0, t)[:, :], ID, t), read_dve if t else None)
        stream("okv", 0)
        taken("okv", 0)
        for t in range(TT):
            src = bank("okv", 0, t)
            do(rope(kn[:, t, :], src[:, 0:AD], AD, t))
            do(V.tensor_copy(vn[:, t, :], src[:, AD:2 * AD]))
            do(rope(kid[:, t, 0:ID], src[:, 2 * AD:2 * AD + ID], ID, t))
            do(V.tensor_scalar(wi[:, t, :], src[:, 2 * AD + ID:2 * AD + ID + IH], float(IH ** -0.5 * ID ** -0.5), None, ALU.mult), read_dve if t else None)
        do(V.tensor_copy(kid[:, :, ID:2 * ID], kid[:, :, 0:ID]), odd_dve)
        do(V.memset(kib[:, :], 0.0))
        dve.wait_ge(odd_pe, ODD_PE["it"])
        do(V.tensor_copy(kib[0:ID, 0:S], psum[3][0:ID, 0:S]))
        do(V.tensor_copy(kib[ID:P, S:2 * S], psum[3][ID:P, 0:S]), odd_dve)
        for t in range(TT):
            dve.wait_ge(odd_act, ODD_ACT[f"index{t}"])
            for h in range(IH):
                wh = wi[:, t, h:h + 1]
                if h == 0:
                    ins = V.tensor_scalar(score[:, t, :], rel[:, h, :], wh, None, ALU.mult)
                else:
                    ins = V.scalar_tensor_tensor(out=score[:, t, :], in0=rel[:, h, :], scalar=wh, in1=score[:, t, :], op0=ALU.mult, op1=ALU.add)
                do(ins, odd_dve if h == IH - 1 else None)
        for t in range(TT):
            causal, sc, ma = cst("causal")[:, t * S:(t + 1) * S], score[:, t, :], madd[:, t, :]
            do(V.tensor_scalar(ma, causal, -1.0, NEG, ALU.add, ALU.mult))
            do(V.tensor_tensor(sc, sc, causal, ALU.mult))
            do(V.tensor_tensor(sc, sc, ma, ALU.add))
            for n in range(SELECT // 8):
                do(V.max(top8[:, :], sc))
                do(V.match_replace(out=sc, in_to_replace=top8[:, :], in_values=sc, imm_value=-3e38))
            do(V.scalar_tensor_tensor(out=ma, in0=sc, scalar=-2e30, in1=causal, op0=ALU.is_lt, op1=ALU.mult))
            do(V.tensor_scalar(ma, ma, -1.0, NEG, ALU.add, ALU.mult))
        for t in range(TT):
            n = (t + 1) * P
            dve.wait_ge(odd_pe, ODD_PE[f"logits{t}"])
            for b in range(4):
                do(V.scalar_tensor_tensor(out=logit[:, 2 * b:2 * b + 2, 0:n], in0=psum[b][:, :].rearrange("p (h s) -> p h s", h=2)[:, :, 0:n],
                                          scalar=AD ** -0.5, in1=bcast(madd[:, t, 0:n].unsqueeze(1), [P, 2, n]), op0=ALU.mult, op1=ALU.add))
            do(V.reduce_max(amax[:, :], logit[:, :, 0:n], AXX))
            do(V.tensor_scalar(amax[:, :], amax[:, :], -1.0, None, ALU.mult), odd_dve)
            dve.wait_ge(odd_act, ODD_ACT[f"exp{t}"])
            do(V.reciprocal(asum[:, :], asum[:, :]))
            do(V.tensor_tensor(logit[:, :, 0:n], logit[:, :, 0:n], bcast(asum[:, :].unsqueeze(2), [P, AH, n]), ALU.mult), odd_dve)
            dve.wait_ge(att_hi, t + 1)
            for hh in range(2):
                hs = slice(4 * hh, 4 * hh + 4)
                do(V.tensor_tensor(act_lo[:, hs, HALVES[t]], psum[hh][:, :].rearrange("p (h s) -> p h s", h=4),
                                   act_hi[:, hs, HALVES[t]].bitcast(F32), ALU.subtract), att_lo if hh else None)
        for i in range(2):
            stream("oout", i)
            taken("oout", i)
            for t in range(TT):
                do(residual(t, i, bank("oout", i, t)[:, :]), read_dve if t else None)
        layer_norm(2)
        peer_layer(1, 16)
        layer_norm(3)


def program(nc, x_in, weights, rows, cols, bgate, p_t, w_pe, final_row, identity, consts_a, erows, ecols, lora_w, side_w, keys, ln_rows,
            consts_b, out):
    ctx = ExitStack()
    with ctx:
        m = Common(nc, ctx, weights)
        spill = nc.dram_tensor("spill", (GROUPS, P, GT * JH), F32, kind="Internal").ap()
        first_block(nc, ctx, m, x_in, rows, cols, bgate, p_t, w_pe, final_row, identity, consts_a)
        second_block(nc, ctx, m, LAYERS * TILES_A, erows, ecols, lora_w, side_w, keys, ln_rows, consts_b, spill, out)


def _weight_tiles(w):
    k, n = w.shape
    return w.reshape(k // (KB * P), KB, P, n // CW, CW).transpose(3, 0, 2, 1, 4).reshape(-1, P, TW)


def _cols(v):
    return v.reshape(-1, P).T


def _constants_a():
    p, t = np.arange(P)[:, None], np.arange(P)[None, :]
    log_gamma = np.log(1.0 - 2.0 ** (-5.0 - np.arange(HEADS)))
    decay = []
    for h in range(HEADS):
        near = np.where(t >= p, np.exp(np.maximum(t - p, 0) * log_gamma[h]), 0.0)
        far = np.exp((t + P - p) * log_gamma[h])
        decay += [near, far, near]
    inv = np.float32(10000.0) ** (-np.arange(0, 256, 2, dtype=np.float32) / np.float32(256))
    ang = inv[:, None] * np.arange(S, dtype=np.float32)[None, :]
    sel = np.zeros((P, HEADS * P))
    for h in range(HEADS):
        sel[h, h * P:(h + 1) * P] = 1.0
    parts = {"cum": t >= p, "ones": np.ones((P, P)), "mask": np.where(t >= p, 0.0, NEG),
             "decay": np.concatenate(decay, 1) / 16.0, "cos": np.cos(ang.astype(np.float64)), "sin": np.sin(ang.astype(np.float64)), "headsel": sel,
             "eps": np.full((P, 1), EPS), "one": np.ones((P, 1))}
    return np.concatenate([np.asarray(parts[n], np.float32) for n in CONST_A], 1)


def _first_block_arrays(i):
    w = []
    rows, cols, bgate = [], [], []
    for l in range(LAYERS):
        w_in, b_in = i["w_in"][l], i["b_in"][l]
        at = {}
        off = 0
        for name, n in (("mq", 1024), ("mk", 1024), ("mv", 1024), ("mo", 1024), ("gates", 8), ("rq", 1024), ("rk", 1024),
                        ("rv", 2048), ("rg", 2048), ("gm", 1024), ("gr", 1024)):
            at[name] = slice(off, off + n)
            off += n
        both = {"mqk": ("mq", "mk"), "rqk": ("rq", "rk")}
        part = lambda name: np.concatenate([w_in[:, at[n]] for n in both.get(name, (name,))], 1)
        ff1, ff2 = i["w_ff1"][l], i["w_ff2"][l]
        ws = {"bm": i["w_bm"][l], "br": i["w_br"][l], "out": i["w_out"][l], "ffa1": ff1[:, :2048], "ffa2": ff2[:2048],
              "ffb1": ff1[:, 2048:], "ffb2": ff2[2048:], "peg": i["w_pe_gate"][l]}
        for name, _, _ in ORDER_A:
            w.append(_weight_tiles(ws[name] if name in ws else part(name)))
        g = {"mo": i["m_norm_g"][l], "rg": i["r_norm_g"][l]}
        for name, n in (("mv", 2), ("mo", 2), ("gm", 2), ("rv", 4), ("rg", 4), ("gr", 2), ("ffb2", 2)):
            b = i["b_ff2"][l] if name == "ffb2" else b_in[at[name]]
            for c in range(n):
                rows.append(b[c * CW:(c + 1) * CW])
                if name in g:
                    rows.append(g[name][c * CW:(c + 1) * CW])
        cat = lambda a, b: np.concatenate([b_in[at[a]], b_in[at[b]]])
        cols.append(np.concatenate(
            [_cols(i[f"norm{n}_g"][l]) for n in (1, 2, 3)] + [_cols(cat("mq", "mk")), _cols(cat("rq", "rk"))]
            + [_cols(i["conv_w"][l][j]) for j in range(4)] + [_cols(i["conv_b"][l]), _cols(i["b_ff1"][l])]
            + [w_in[:, at["gates"]].reshape(KD, P, 8).transpose(1, 0, 2).reshape(P, 64)], 1))
        bgate.append(b_in[at["gates"]])
    return {
        "x_in": i["x"][0].reshape(TT, P, D).transpose(1, 0, 2),
        "rows": np.stack(rows).reshape(LAYERS, ROWS_A, CW),
        "cols": np.stack(cols),
        "bgate": np.stack(bgate),
        "p_t": i["p"][:, 0].reshape(LAYERS, S, 2, P).transpose(0, 3, 2, 1),
        "w_pe": i["w_pe"].reshape(LAYERS, 2, P, D).transpose(0, 2, 1, 3),
        "final_row": i["final_g"],
        "identity": np.eye(P, dtype=np.float32),
        "consts_a": _constants_a(),
    }, w


def _constants_b():
    p, t = np.arange(P)[:, None], np.arange(P)[None, :]
    same = p // CHUNK_T == t // CHUNK_T
    tok = np.arange(S).reshape(TT, P).T
    q, u = p % CHUNK_T, np.arange(CHUNK_T)[None, :]
    levels = [(q // (2 << n) == u // (2 << n)) & ((q >> n) % 2 == 1) & ((u >> n) % 2 == 0) for n in range(LEVELS)]

    def angles(dim):
        inv = np.float32(10000.0) ** (-np.arange(0, dim, 2, dtype=np.float32) / np.float32(dim))
        return (tok.astype(np.float32)[:, :, None] * inv).astype(np.float64).reshape(P, -1)

    parts = {"same_head": same, "upto": (p <= t) & same, "strict_upto": np.concatenate([q < u, q <= u], 1),
             "diag2": p // GDK == np.arange(2 * P)[None, :] // GDV, "levels": np.concatenate(levels, 1), "eye64": q == u,
             "keep": np.broadcast_to(np.arange(S) % CHUNK_T != 0, (P, S)), "half": p // RN == np.arange(2)[None, :],
             "iota": np.broadcast_to(np.arange(P), (P, P)), "causal": (np.arange(S) <= tok[:, :, None]).reshape(P, -1),
             "cos128": np.cos(angles(128)), "sin128": np.sin(angles(128)), "cos64": np.cos(angles(64)), "sin64": np.sin(angles(64)),
             "ln_eps": np.full((P, 1), LN_EPS), "lnx_eps": np.full((P, 1), LNX_EPS), "one": np.ones((P, 1))}
    return np.concatenate([np.asarray(parts[n], np.float32) for n in CONST_B], 1)


def _expert_tiles(u, v):
    u = u.reshape(KEYS, KEYS // 2, 2, KD, P).transpose(1, 4, 3, 2, 0).reshape(KEYS // 2, P, TW)
    v = v.reshape(KEYS, KEYS // 2, 2 * D).transpose(1, 0, 2)
    tiles = []
    for first in range(0, KEYS // 2, PAIRS):
        tiles += [u[first:first + PAIRS], v[first:first + PAIRS]]
    return np.concatenate(tiles, 0)


def _second_block_arrays(i):
    g = lambda name: i[name + "_2"]
    w_in, mu = g("even_w_in")[0], g("rwkv_mu")[0]
    ends = np.cumsum([256, 256, 512, 512, 16, 512, 512, 512, 32, 32, 96])
    gq, gk, gv, gg, gal, r, k, v, wl, al, gl = np.split(w_in, ends[:-1], 1)
    mr, mk, mv, mwl, mal, mgl = np.split(mu, (ends[5:-1] - ends[4]))
    zeros = lambda *s: np.zeros(s, np.float32)
    side = np.concatenate([gl, wl, gal, zeros(D, 16), al, zeros(D, 64)], 1)
    lora = zeros(P, LORA)
    lora[G2], lora[W2], lora[A2] = g("rwkv_g2")[0], g("rwkv_w2")[0], g("rwkv_a2")[0]
    lora[0:16, GA2[1]] = g("gla_a_w2")[0]
    cols = {"mu_side": _cols(np.concatenate([mgl, mwl, zeros(32), mal, zeros(64)])), "mu": _cols(np.concatenate([mr, mk, mv])),
            "gla_a_b": _cols(g("gla_a_b")[0]), "w0": _cols(g("rwkv_w0")[0]), "a0": _cols(g("rwkv_a0")[0]), "k_k": _cols(g("rwkv_k_k")[0]),
            "k_a": _cols(g("rwkv_k_a")[0]), "r_k": _cols(g("rwkv_r_k")[0].reshape(-1))}
    odd = g("odd_w_in")[0]
    okv = np.concatenate([odd[:, 1024:1280], odd[:, 1792:], zeros(D, CW - 256 - 72)], 1)
    keys = zeros(LAYERS, 2, 64, PH, 2, KEYS)
    for c in range(2):
        keys[:, c, :, :, c, :] = g("peer_sub_keys")[:, :, c].transpose(0, 3, 1, 2)
    weights = []
    for layer in range(LAYERS):
        if layer == 0:
            weights += [_weight_tiles(w) for w in (np.concatenate([gq, gk], 1), gv, gg, r, k, v, g("even_w_out")[0])]
        else:
            weights += [_weight_tiles(w) for w in (odd[:, :1024], odd[:, 1280:1792], okv, g("odd_w_out")[0])]
        weights += [_weight_tiles(g("peer_w_q")[layer]), _expert_tiles(g("peer_u")[layer], g("peer_v")[layer])]
    norms = [g(f"{n}_ln_{p}")[layer] for layer in range(LAYERS) for n in ("mix", "ffn") for p in "gb"]
    return {
        "erows": np.concatenate([g("gla_norm_g")[0], g("rwkv_lnx_g")[0], g("rwkv_lnx_b")[0]]),
        "ecols": np.concatenate([cols[n] for n in ECOL], 1),
        "lora_w": lora,
        "side_w": side.reshape(KD, P, 2 * P).transpose(1, 0, 2),
        "keys": keys.reshape(LAYERS, P, PH, 2 * KEYS),
        "ln_rows": np.stack(norms),
        "consts_b": _constants_b(),
    }, weights


def kernel(**inputs):
    import concourse.bacc as bacc
    from concourse.bass_utils import run_bass_kernel_spmd

    i = {name: np.asarray(a) for name, a in inputs.items()}
    arrays, first = _first_block_arrays(i)
    more, second = _second_block_arrays(i)
    arrays.update(more)
    arrays["weights"] = np.concatenate(first + second, 0)
    arrays = {name: np.ascontiguousarray(a) for name, a in arrays.items()}
    nc = bacc.Bacc("TRN2", target_bir_lowering=False, num_devices=1)
    aps = {name: nc.dram_tensor(name, a.shape, mybir.dt.from_np(a.dtype), kind="ExternalInput").ap() for name, a in arrays.items()}
    aps["out"] = nc.dram_tensor("out", (P, TT, D), F32, kind="ExternalOutput").ap()
    program(nc, **aps)
    r = run_bass_kernel_spmd(nc, [arrays], core_ids=[0])
    return r.results[0]["out"].transpose(1, 0, 2).reshape(1, S, D)
```

```python
from contextlib import ExitStack

import numpy as np
import concourse.bass as bass
from concourse import mybir

F32 = mybir.dt.float32
F32R = mybir.dt.float32r
U32 = mybir.dt.uint32
ALU = mybir.AluOpType
ACT = mybir.ActivationFunctionType
AXX = mybir.AxisListType.X

P = 128
D = 1024
S = 256
TT = S // P
KD = D // P
LAYERS = 2
CW = 512
KB = 4
TW = KB * CW
RAW = 4
SPLIT = 2
EPS = 1e-6
HEADS = 4
MDV = 256
RDV = 512
NEG = 1e30

ORDER_A = [("mqk", 4, 2), ("mv", 2, 2), ("mo", 2, 2), ("gm", 2, 2), ("bm", 2, 2), ("rqk", 4, 2), ("rv", 4, 2),
           ("rg", 4, 2), ("gr", 2, 2), ("br", 2, 4), ("out", 2, 2), ("ffa1", 4, 2), ("ffa2", 2, 4),
           ("ffb1", 4, 2), ("ffb2", 2, 4), ("peg", 2, 2)]
CHUNK, TILE = {}, {}
_c = _t = 0
for _name, _n, _per in ORDER_A:
    for _i in range(_n):
        CHUNK[_name, _i] = _c
        TILE[_name, _i] = _t
        _c, _t = _c + 1, _t + _per
CHUNKS_A, TILES_A = _c, _t
PER_CHUNK = {_name: _per for _name, _n, _per in ORDER_A}
assert CHUNKS_A % 2 == 0 and TILES_A % RAW == 0

BY_ACT = ("mqk", "rqk", "ffa1", "ffb1")
TAKEN = []
for _name, _n, _ in ORDER_A:
    for _i in range(_n):
        TAKEN.append((_name in BY_ACT, 1 + sum(a == (_name in BY_ACT) for a, _ in TAKEN)))

ROW_OF = {}
ROW_CHUNK = []
for _name, _n, _gains in (("mv", 2, 0), ("mo", 2, 1), ("gm", 2, 0), ("rv", 4, 0), ("rg", 4, 1), ("gr", 2, 0), ("ffb2", 2, 0)):
    for _i in range(_n):
        ROW_OF[_name, _i] = len(ROW_CHUNK)
        ROW_CHUNK += [CHUNK[_name, _i]] * (1 + _gains)
ROWS_A = len(ROW_CHUNK)
GAIN_ROWS = {ROW_OF[_name, _i] + 1: _n + _i + 1 for _name, _n, _of in (("mo", 0, 2), ("rg", 2, 4)) for _i in range(_of)}
RROW = 4
assert ROWS_A % RROW == 0

COL = {}
_c = 0
for _name, _n in (("norm1", 8), ("norm2", 8), ("norm3", 8), ("bmqk", 16), ("brqk", 16), ("convw", 64), ("convb", 16),
                  ("bff1", 32), ("gatew", 64)):
    COL[_name] = _c
    _c += _n
COLS_A = _c

T_H, T_YM, T_YR, T_MG, T_H2, T_H3 = 0, 4, 8, 16, 20, 24

CONST_A = {}
_c = 0
for _name, _n in (("cum", P), ("ones", P), ("mask", P), ("decay", HEADS * 384), ("cos", S), ("sin", S), ("headsel", HEADS * P),
                  ("eps", 1), ("one", 1)):
    CONST_A[_name] = (_c, _n)
    _c += _n
CONSTS_A = _c
CHUNK_T = 64
LEVELS = 6
CONST_B = {}
_c = 0
for _name, _n in (("same_head", P), ("upto", P), ("strict_upto", 2 * CHUNK_T), ("diag2", 2 * P),
                  ("levels", LEVELS * CHUNK_T), ("eye64", CHUNK_T), ("level0_t", CHUNK_T), ("keep", S), ("half", 2),
                  ("iota", P), ("causal", TT * S), ("cos128", TT * 64), ("sin128", TT * 64), ("cos64", TT * 32), ("sin64", TT * 32),
                  ("ln_eps", 1), ("lnx_eps", 1), ("one", 1)):
    CONST_B[_name] = (_c, _n)
    _c += _n
CONSTS_B = _c

EVEN, EVEN_OUT, ODD, ODD_OUT = 0, 12, 148, 156
PEER_Q, PEER_UV = (16, 160), (20, 164)
TILES_B = 292
ALPHA = (2 * LAYERS) ** 0.25
LN_EPS, LNX_EPS = 1e-5, 64e-5
GH, GDK, GDV = 4, 64, 128
RH, RN = 8, 64
EW = 512
AH, AD = 8, 128
IH, ID = 8, 64
SELECT = 64
KEYS, PH, PK = 128, 8, 16
JH = KEYS // 2
PAIRS = JH // 2
GT = 4
HOT = 4
GROUPS = S // GT
RELOAD = 4 * HOT
REGATED = GROUPS // 2 // RELOAD

ECOL = {}
_c = 0
for _name, _n in (("mu_side", 2), ("mu", 12), ("gla_a_b", 2), ("w0", 4), ("a0", 4), ("k_k", 4), ("k_a", 4), ("r_k", 4)):
    ECOL[_name] = _c
    _c += _n
ECOLS = _c

ORDER_B = [("gqk", EVEN, 1, "act"), ("gv", EVEN + 2, 1, "act"), ("gg", EVEN + 4, 1, "act"), ("r", EVEN + 6, 1, "act"),
           ("k", EVEN + 8, 1, "act"), ("v", EVEN + 10, 1, "act"), ("eout", EVEN_OUT, 2, "dve"), ("pq0", PEER_Q[0], 2, "act"),
           ("oqi", ODD, 1, "dve"), ("okv", ODD + 2, 1, "dve"), ("oq", ODD + 4, 2, "dve"), ("oout", ODD_OUT, 2, "dve"),
           ("pq1", PEER_Q[1], 2, "act")]
CHUNK_B, TILE_B, READ_B = {}, {}, []
for _name, _t, _n, _by in ORDER_B:
    for _i in range(_n):
        CHUNK_B[_name, _i] = len(READ_B)
        TILE_B[_name, _i] = _t + 2 * _i
        READ_B.append((_by, 1 + sum(b == _by for b, _ in READ_B)))

LORA = 1024
G2, W2 = (slice(0, 96), slice(0, EW)), (slice(96, 128), slice(0, EW))
GA2, A2 = (slice(0, 32), slice(EW, EW + 256)), (slice(32, 64), slice(EW, 2 * EW))
EROW = {"gla_g": slice(0, GDV), "lnx_g": slice(GDV, GDV + EW), "lnx_b": slice(GDV + EW, GDV + 2 * EW)}
EROWS = GDV + 2 * EW
HALVES = tuple(slice(t * P, (t + 1) * P) for t in range(TT))
FT = EW // P
GP = GH // 2
CH = P // CHUNK_T


def steps(*names):
    return {name: i + 1 for i, name in enumerate(names)}


EVEN_PE = steps("side", "la", "w", "a", "g", "scores", "keys", "kv", "o")
EVEN_ACT = steps("side", "gates", "lnexp", "w", "a", "decays", "keys", "square", "std")
EVEN_DVE = steps("side", "la", "cumsum", "decayed", "scores", "states", "gla")
LEVEL_STEPS = [f"{s}{n}" for n in range(LEVELS) for s in "xd"]
RW_PE = steps("bonus", "nat", "lr", "x0", *LEVEL_STEPS[2:], "z", "wv", "y")
RW_ACT = steps("decays", "norm", "nat", "z", "wv", "std")
RW_DVE = steps("cumsum", "bonus", "tilde", "lr", *LEVEL_STEPS, "stats", "out")
ODD_PE = steps("it", "index0", "index1", "qt", "logits0", "pt0", "o0", "logits1", "pt1", "o1")
ODD_ACT = steps("it", "index0", "index1", "qt", "exp0", "pt0", "exp1", "pt1")
ODD_DVE = steps("turned", "kib", "rope", "logits0", "probs0", "logits1", "probs1")


class Order:

    def __init__(self, eng, own):
        self.eng, self.own, self.count = eng, own, {}

    def __call__(self, ins, signal=None):
        s = self.own if signal is None else signal
        self.count[s] = self.count.get(s, 0) + 1
        ins.then_inc(s, 1)
        self.eng.wait_ge(s, self.count[s])

    def also(self, ins):
        self.count[self.own] = self.count.get(self.own, 0) + 1
        ins.then_inc(self.own, 1)

    def settle(self):
        self.eng.wait_ge(self.own, self.count[self.own])


class Common:

    def __init__(self, nc, ctx, weights):
        def sb(name, shape, dt=F32):
            return ctx.enter_context(nc.sbuf_tensor(name, shape, dt))

        def sem(name):
            return ctx.enter_context(nc.semaphore(name))

        self.weights = weights
        self.raw = sb("raw", [P, RAW, TW])
        self.w_hi = sb("w_hi", [P, SPLIT, TW], F32R)
        self.w_lo = sb("w_lo", [P, SPLIT, TW], F32R)
        self.x = sb("x", [P, TT, D])
        self.act_hi = sb("act_hi", [P, KD, S], F32R)
        self.act_lo = sb("act_lo", [P, KD, S], F32R)
        self.ident_sb = sb("ident_sb", [P, P])
        self.ident = self.ident_sb[:, :]
        self.psum = [ctx.enter_context(nc.psum_tensor(f"bank{b}", [P, CW], F32)) for b in range(8)]
        self.raw_loaded = [sem(f"raw_loaded{r}") for r in range(RAW)]
        self.hi_ready = sem("hi_ready")
        self.lo_ready = sem("lo_ready")
        self.tile_used = sem("tile_used")
        self.x_ready = sem("x_ready")
        self.out_stored = sem("out_stored")


def first_block(nc, ctx, m, x_in, rows, cols, bgate, p_t, w_pe, final_row, identity, consts_a):
    raw, w_hi, w_lo, x, act_hi, act_lo, ident, psum = m.raw, m.w_hi, m.w_lo, m.x, m.act_hi, m.act_lo, m.ident, m.psum
    raw_loaded, hi_ready, lo_ready, tile_used, x_ready = m.raw_loaded, m.hi_ready, m.lo_ready, m.tile_used, m.x_ready

    def sb(name, shape, dt=F32, stack=ctx):
        return stack.enter_context(nc.sbuf_tensor(name, shape, dt))

    def sem(name):
        return ctx.enter_context(nc.semaphore(name))

    memory = ExitStack()
    const_a = sb("const_a", [P, CONSTS_A], F32, memory)

    def cst(name):
        first, n = CONST_A[name]
        return const_a[:, first:first + n]

    eps = cst("eps")
    attention = memory.enter_context(ExitStack())
    qk_t = sb("qk_t", [P, 16, S], F32, attention)
    val = sb("val", [P, TT, HEADS * (RDV + 2)], F32, attention)
    attention.close()
    mix_hi = sb("mix_hi", [P, 16, S], F32R, memory)
    mix_lo = sb("mix_lo", [P, 16, S], F32R, memory)
    pad = sb("pad", [P, 64], F32, memory)
    y = sb("y", [P, TT, HEADS * RDV], F32, memory)
    merged = sb("merged", [P, TT, D], F32, memory)
    gate = sb("gate", [P, TT, D], F32, memory)
    row = sb("row", [P, RROW, CW], F32, memory)
    col = sb("col", [P, COLS_A], F32, memory)
    bgate_row = sb("bgate_row", [P, 8], F32, memory)
    shifted = sb("shifted", [P, 4, S + 3], F32, memory)
    conv = sb("conv", [P, 4, S], F32, memory)
    pre = sb("pre", [P, TT, CW], F32, memory)
    decayed = sb("decayed", [P, HEADS, 3, P], F32, memory)
    weighed = sb("weighed", [P, 2, 3 * P], F32, memory)
    junk = sb("junk", [P, D], F32, memory)
    gw_hi = sb("gw_hi", [P, KD, 8], F32R, memory)
    gw_lo = sb("gw_lo", [P, KD, 8], F32R, memory)
    gz = sb("gz", [P, TT, 8], F32, memory)
    gl = sb("gl", [P, 4, TT, HEADS], F32, memory)
    gi = sb("gi", [P, TT, HEADS], F32, memory)
    grow = sb("grow", [HEADS, S], F32, memory)
    mrow = sb("mrow", [HEADS, S], F32, memory)
    floor = sb("floor", [P, TT, HEADS], F32, memory)
    ssq = sb("ssq", [P, TT], F32, memory)
    rstd = sb("rstd", [P, TT], F32, memory)
    st6 = sb("st6", [P, 6], F32, memory)
    stats = sb("stats", [P, TT, HEADS, 2], F32, memory)
    hstd = sb("hstd", [P, TT, HEADS], F32, memory)
    den = sb("den", [P, 2], F32, memory)
    wpe_sb = y[:, :, :].rearrange("p t n -> p (t n)")[:, 0:2 * D].rearrange("p (k n) -> p k n", k=2)
    pt_sb = y[:, :, :].rearrange("p t n -> p (t n)")[:, 2 * D:2 * D + 2 * S].rearrange("p (k n) -> p k n", k=2)
    val_m = val[:, :, 0:HEADS * (MDV + 1)].rearrange("p t (h n) -> p t h n", h=HEADS)
    val_r = val[:, :, 0:HEADS * RDV]

    const_loaded = sem("const_loaded")
    x_loaded = sem("x_loaded")
    layer_left = sem("layer_left")
    layer_open = sem("layer_open")
    cleared = sem("cleared")
    final_loaded = sem("final_loaded")
    final_std = sem("final_std")
    col_loaded = sem("col_loaded")
    row_loaded = [sem(f"row_loaded{r}") for r in range(RROW)]
    pe_loaded = sem("pe_loaded")

    per_layer = []

    def lsem(name):
        per_layer.append(sem(name))
        return per_layer[-1]

    act_step = lsem("act_step")
    dve_step = lsem("dve_step")
    read_act = lsem("read_act")
    read_dve = lsem("read_dve")
    std_ready = lsem("std_ready")
    half_done = lsem("half_done")
    half_added = lsem("half_added")
    xn_ready = lsem("xn_ready")
    trans_done = lsem("trans_done")
    t_hi = lsem("t_hi")
    t_lo = lsem("t_lo")
    gw_split = lsem("gw_split")
    gate_mm = lsem("gate_mm")
    gz_ready = lsem("gz_ready")
    lnf_ready = lsem("lnf_ready")
    lf_ready = lsem("lf_ready")
    gi_ready = lsem("gi_ready")
    m_ready = lsem("m_ready")
    fm_ready = lsem("fm_ready")
    mmask_ready = lsem("mmask_ready")
    decay_ready = lsem("decay_ready")
    floor_ready = lsem("floor_ready")
    tap_ready = lsem("tap_ready")
    conv_done = lsem("conv_done")
    mqk_ready = lsem("mqk_ready")
    rqk_ready = lsem("rqk_ready")
    score_done = lsem("score_done")
    weighed_ready = lsem("weighed_ready")
    y_done = lsem("y_done")
    my_read = lsem("my_read")
    ry_read = lsem("ry_read")
    stats_ready = lsem("stats_ready")
    hstd_ready = lsem("hstd_ready")
    gated = lsem("gated")
    y_ready = lsem("y_ready")
    merged_ready = lsem("merged_ready")
    sq_ready = lsem("sq_ready")
    ff_hi = lsem("ff_hi")
    ff_lo = lsem("ff_lo")
    pe_mm = lsem("pe_mm")

    def wait_read(eng, c):
        by_act, count = TAKEN[c]
        eng.wait_ge(read_act if by_act else read_dve, count)

    with nc.Block() as block:

        @block.sync
        def _(sp):
            sp.dma_start(x[:, :, :], x_in).then_inc(x_loaded, 16)
            for r in range(RAW):
                sp.dma_start(raw[:, r, :], m.weights[r]).then_inc(raw_loaded[r], 16)
            with sp.Fori(1, LAYERS * TILES_A // RAW + 1) as n:
                for r in range(RAW):
                    sp.wait_ge(lo_ready, n * RAW + (r - RAW + 1))
                    sp.dma_start(raw[:, r, :], m.weights[n * RAW + r]).then_inc(raw_loaded[r], 16)

        @block.gpsimd
        def _(pool):
            pool.dma_start(ident, identity).then_inc(const_loaded, 16)
            pool.dma_start(const_a[:, :], consts_a).then_inc(const_loaded, 16)
            with pool.Fori(0, LAYERS) as layer:
                pool.dma_start(col[:, :], cols[layer]).then_inc(col_loaded, 16)
                pool.dma_start(bgate_row[:, :], bgate[layer].partition_broadcast(P)).then_inc(col_loaded, 16)
                for r in range(ROWS_A):
                    if r >= RROW:
                        if r - RROW in GAIN_ROWS:
                            pool.wait_ge(y_ready, GAIN_ROWS[r - RROW])
                        else:
                            wait_read(pool, ROW_CHUNK[r - RROW])
                    if r == ROW_OF["ffb2", 0]:
                        pool.wait_ge(t_lo, T_MG)
                        pool.dma_start(wpe_sb, w_pe[layer]).then_inc(pe_loaded, 16)
                        pool.dma_start(pt_sb, p_t[layer]).then_inc(pe_loaded, 16)
                    pool.dma_start(row[:, r % RROW, :], rows[layer, r].partition_broadcast(P)).then_inc(row_loaded[r % RROW], 16)
                pool.wait_ge(layer_left, layer * 3 + 3)
                pool.sem_inc(cleared, 1)
                for s in per_layer:
                    pool.sem_clear(s)
                pool.sem_inc(layer_open, 1)
            pool.dma_start(row[:, 0:2, :].rearrange("p a n -> p (a n)"), final_row.partition_broadcast(P)).then_inc(final_loaded, 16)

        def row_slot(name, i, k=0):
            r = ROW_OF[name, i] + k
            return row[:, r % RROW, :], row_loaded[r % RROW], 16 * (r // RROW + 1)

        @block.tensor
        def _(pe):
            def mm3(dst, lh, ll, rh, rl, first, last):
                nc.tensor.matmul(dst, lh, rh, start=first, stop=False)
                nc.tensor.matmul(dst, lh, rl, start=False, stop=False)
                return nc.tensor.matmul(dst, ll, rh, start=False, stop=last)

            def natural(base, k0, c, per, hi, lo, ready, tiles, half):
                for j in range(per) if tiles is None else tiles:
                    k = k0 + j
                    pe.wait_ge(lo_ready, base + (k + 1))
                    if ready is not None:
                        ready(j)
                    apart = half is not None and j == per - 1
                    for kk, t in [(n, t) for t in range(TT) for n in range(KB)] if apart else [(n, t) for n in range(KB) for t in range(TT)]:
                        ki = j * KB + kk
                        ts = slice(t * P, (t + 1) * P)
                        ws = slice(kk * CW, (kk + 1) * CW)
                        last = mm3(psum[2 * (c % 2) + t][:, :], hi[:, ki, ts], lo[:, ki, ts], w_hi[:, k % SPLIT, ws],
                                   w_lo[:, k % SPLIT, ws], ki == 0, ki == per * KB - 1)
                        if apart and t == 0 and kk == KB - 1:
                            last.then_inc(half, 1)
                    last.then_inc(tile_used, 1)

            def featured(base, k0, c, hi, lo, ready):
                for j in range(2):
                    k = k0 + j
                    pe.wait_ge(lo_ready, base + (k + 1))
                    if ready is not None:
                        ready(j)
                    for f in range(4):
                        for kk in range(KB):
                            ki = j * KB + kk
                            ws = slice(kk * CW + f * P, kk * CW + (f + 1) * P)
                            dst = psum[2 * (c % 2) + f // 2][:, (f % 2) * S:(f % 2 + 1) * S]
                            wh, wl = w_hi[:, k % SPLIT, ws], w_lo[:, k % SPLIT, ws]
                            nc.tensor.matmul(dst, wh, hi[:, ki, :], start=ki == 0 and f % 2 == 0, stop=False)
                            nc.tensor.matmul(dst, wh, lo[:, ki, :], start=False, stop=False)
                            last = nc.tensor.matmul(dst, wl, hi[:, ki, :], start=False, stop=ki == KD - 1 and f % 2 == 1)
                    last.then_inc(tile_used, 1)

            def transposes(src, blocks, first=0):
                for b in range(first // 2, (first + blocks) // 2):
                    for k in (2 * b, 2 * b + 1):
                        for t in range(TT):
                            last = nc.tensor.transpose(psum[4 + b][:, (k % 2) * S + t * P:(k % 2) * S + (t + 1) * P],
                                                       src(k, t), ident)
                    last.then_inc(trans_done, 1)

            pe.wait_ge(const_loaded, 32)
            with pe.Fori(0, LAYERS) as layer:
                base = layer * TILES_A

                def bank_free(c):
                    if c >= 2:
                        wait_read(pe, c - 2)

                def nat(name, i, hi, lo, ready=None, tiles=None, half=None):
                    if tiles is None or 0 in tiles:
                        bank_free(CHUNK[name, i])
                    natural(base, TILE[name, i], CHUNK[name, i], PER_CHUNK[name], hi, lo, ready, tiles, half)

                def feat(name, i, hi, lo, ready=None):
                    bank_free(CHUNK[name, i])
                    featured(base, TILE[name, i], CHUNK[name, i], hi, lo, ready)

                def by_tile(first):
                    return lambda j: pe.wait_ge(t_lo, first + 2 * (j + 1))

                def normed(i):
                    for t in range(TT):
                        pe.wait_ge(xn_ready, TT * i + t + 1)
                        for k in range(KD):
                            last = nc.tensor.transpose(psum[4 + k // 2][:, (k % 2) * S + t * P:(k % 2) * S + (t + 1) * P],
                                                       gate[:, t, k * P:(k + 1) * P], ident)
                            if t == TT - 1 and k % 2:
                                last.then_inc(trans_done, 1)

                normed(0)

                def input_gates(j):
                    by_tile(T_H)(j)
                    if j == 0:
                        return
                    pe.wait_ge(gw_split, 2)
                    for t in range(TT):
                        for k in range(KD):
                            ts = slice(t * P, (t + 1) * P)
                            last = mm3(psum[6][:, t * 8:t * 8 + 8], act_hi[:, k, ts], act_lo[:, k, ts], gw_hi[:, k, :],
                                       gw_lo[:, k, :], k == 0, k == KD - 1)
                    last.then_inc(gate_mm, 1)

                feat("mqk", 0, act_hi, act_lo, input_gates)
                pe.wait_ge(lf_ready, 1)
                lf = gl[:, 2, :, :]
                nc.tensor.matmul(psum[7][:, 0:HEADS], cst("cum"), lf[:, 0, :], start=True, stop=True)
                nc.tensor.matmul(psum[7][:, HEADS:2 * HEADS], cst("ones"), lf[:, 0, :], start=True, stop=False)
                nc.tensor.matmul(psum[7][:, HEADS:2 * HEADS], cst("cum"), lf[:, 1, :], start=False, stop=True).then_inc(gate_mm, 1)
                feat("mqk", 1, act_hi, act_lo)
                pe.wait_ge(gi_ready, 1)
                for t in range(TT):
                    last = nc.tensor.transpose(psum[6][0:HEADS, t * P:(t + 1) * P], gi[:, t, :], ident)
                last.then_inc(gate_mm, 1)
                feat("mqk", 2, act_hi, act_lo)
                pe.wait_ge(m_ready, 1)
                for t in range(TT):
                    last = nc.tensor.transpose(psum[7][:, 8 + t * HEADS:8 + (t + 1) * HEADS], mrow[:, t * P:(t + 1) * P],
                                               ident[0:HEADS, 0:HEADS])
                last.then_inc(gate_mm, 1)
                for h in range(HEADS):
                    sel = cst("headsel")[0:HEADS, h * P:(h + 1) * P]
                    last = nc.tensor.matmul(psum[4 + h // 2][:, (h % 2) * S:(h % 2 + 1) * S], sel, mrow[:, :], start=True, stop=True)
                last.then_inc(gate_mm, 1)
                feat("mqk", 3, act_hi, act_lo)
                nat("mv", 0, act_hi, act_lo)
                nat("mv", 1, act_hi, act_lo)

                def attend(h0, width, values, qk_ready, v_chunk, y_read, between):
                    def outputs(h):
                        pe.wait_ge(weighed_ready, h0 + h + 1)
                        if h >= 1:
                            pe.wait_ge(y_read, h)
                        if h == 0:
                            wait_read(pe, v_chunk)
                        w = weighed[:, h % 2, :]
                        nc.tensor.matmul(psum[6][:, 0:width], w[:, 0:P], values(0, h), start=True, stop=True)
                        nc.tensor.matmul(psum[7][:, 0:width], w[:, P:2 * P], values(0, h), start=True, stop=False)
                        nc.tensor.matmul(psum[7][:, 0:width], w[:, 2 * P:3 * P], values(1, h), start=False, stop=True).then_inc(y_done, 1)

                    def scores(h):
                        if h >= 2:
                            pe.wait_ge(weighed_ready, h0 + h - 1)
                        bank = psum[4 + h % 2]
                        for d in range(2):
                            nc.tensor.matmul(bank[:, 0:S], qk_t[:, 8 + 2 * h + d, 0:P], qk_t[:, 2 * h + d, :], start=d == 0, stop=d == 1)
                        for d in range(2):
                            last = nc.tensor.matmul(bank[:, S:S + P], qk_t[:, 8 + 2 * h + d, P:S], qk_t[:, 2 * h + d, P:S],
                                                    start=d == 0, stop=d == 1)
                        last.then_inc(score_done, 1)

                    pe.wait_ge(qk_ready, 4)
                    scores(0)
                    scores(1)
                    between(0, 0)
                    outputs(0)
                    scores(2)
                    between(0, 1)
                    outputs(1)
                    scores(3)
                    between(1, 0)
                    outputs(2)
                    between(1, 1)
                    outputs(3)

                pe.wait_ge(mmask_ready, HEADS)
                attend(0, MDV + 1, lambda t, h: val_m[:, t, h, :], mqk_ready, CHUNK["mv", 1], my_read,
                       lambda i, j: nat("mo", i, act_hi, act_lo, tiles=(j,)))
                nat("gm", 0, act_hi, act_lo)
                nat("gm", 1, act_hi, act_lo, tiles=(0,))
                pe.wait_ge(y_ready, 2)
                transposes(lambda k, t: y[:, t, k * P:(k + 1) * P], KD)
                nat("gm", 1, act_hi, act_lo, tiles=(1,))
                nat("bm", 0, mix_hi, mix_lo, by_tile(T_YM))
                nat("bm", 1, mix_hi, mix_lo)
                for i in range(4):
                    feat("rqk", i, act_hi, act_lo)
                for i in range(4):
                    nat("rv", i, act_hi, act_lo)
                attend(HEADS, RDV, lambda t, h: val_r[:, t, h * RDV:(h + 1) * RDV], rqk_ready, CHUNK["rv", 3], ry_read,
                       lambda i, j: nat("rg", i, act_hi, act_lo, tiles=(j,)))
                for i in range(2, 4):
                    nat("rg", i, act_hi, act_lo)
                nat("gr", 0, act_hi, act_lo)
                pe.wait_ge(y_ready, 6)
                transposes(lambda k, t: y[:, t, k * P:(k + 1) * P], KD)
                nat("gr", 1, act_hi, act_lo)
                pe.wait_ge(t_lo, T_YR + 4)
                transposes(lambda k, t: y[:, t, D + k * P:D + (k + 1) * P], KD)
                nat("br", 0, mix_hi, mix_lo, by_tile(T_YR))
                nat("br", 1, mix_hi, mix_lo, tiles=(0, 1, 2))
                pe.wait_ge(merged_ready, 1)
                transposes(lambda k, t: merged[:, t, k * P:(k + 1) * P], KB)
                nat("br", 1, mix_hi, mix_lo, tiles=(3,))
                nat("out", 0, mix_hi, mix_lo, by_tile(T_MG), tiles=(0,))
                pe.wait_ge(merged_ready, 2)
                transposes(lambda k, t: merged[:, t, k * P:(k + 1) * P], KB, KB)
                nat("out", 0, mix_hi, mix_lo, by_tile(T_MG), tiles=(1,))
                nat("out", 1, mix_hi, mix_lo, half=half_done)
                normed(1)
                for half, (one, two) in enumerate((("ffa1", "ffa2"), ("ffb1", "ffb2"))):
                    for i in range(4):
                        feat(one, i, act_hi, act_lo, by_tile(T_H2) if half == 0 and i == 0 else None)
                    for i in range(2):
                        nat(two, i, mix_hi, mix_lo, lambda j: pe.wait_ge(ff_lo, 4 * half + j + 1), half=half_done if half and i else None)
                normed(2)
                nat("peg", 0, act_hi, act_lo, by_tile(T_H3))
                pe.wait_ge(pe_loaded, layer * 32 + 32)
                for i in range(2):
                    for t in range(TT):
                        for k in range(2):
                            last = nc.tensor.matmul(psum[4 + 2 * i + t][:, :], pt_sb[:, k, t * P:(t + 1) * P],
                                                    wpe_sb[:, k, i * CW:(i + 1) * CW], start=k == 0, stop=k == 1)
                last.then_inc(pe_mm, 1)
                nat("peg", 1, act_hi, act_lo, half=half_done)
                wait_read(pe, CHUNKS_A - 1)
                pe.sem_inc(layer_left, 1)
                pe.wait_ge(layer_open, layer + 1)

        @block.scalar
        def _(act):
            def split_hi(base, k, free=True):
                act.wait_ge(raw_loaded[k % RAW], base * (16 // RAW) + 16 * (k // RAW + 1))
                if free:
                    act.wait_ge(tile_used, base + (k - 1))
                nc.scalar.activation(w_hi[:, k % SPLIT, :], raw[:, k % RAW, :], ACT.Copy).then_inc(hi_ready, 1)

            for k in range(SPLIT):
                split_hi(0, k, free=False)
            act.wait_ge(const_loaded, 32)
            act.wait_ge(x_loaded, 16)
            with act.Fori(0, LAYERS) as layer:
                base = layer * TILES_A
                do = Order(act, act_step)

                def stream(name, i, left=0):
                    for j in range(PER_CHUNK[name] - left):
                        split_hi(base, TILE[name, i] + j + SPLIT)

                def taken(name, i):
                    act.wait_ge(tile_used, base + (TILE[name, i] + PER_CHUNK[name]))

                def norm(i):
                    for t in range(TT):
                        if i:
                            act.wait_ge(half_added, TT * (i - 1) + t + 1)
                        do(nc.scalar.activation(junk[:, :], x[:, t, :], ACT.Square, accum_out=ssq[:, t:t + 1]))
                        do(nc.scalar.activation(rstd[:, t:t + 1], ssq[:, t:t + 1], ACT.Sqrt, bias=eps, scale=1.0 / D), std_ready)
                    if i == 0:
                        act.wait_ge(col_loaded, layer * 32 + 32)
                        do(nc.scalar.activation(gw_hi[:, :, :].rearrange("p k n -> p (k n)"), col[:, COL["gatew"]:COL["gatew"] + 64], ACT.Copy), gw_split)
                    g0 = COL[f"norm{i + 1}"]
                    first = (T_H, T_H2, T_H3)[i]
                    for b in range(KD // 2):
                        act.wait_ge(trans_done, first + b + 1)
                        for k in (2 * b, 2 * b + 1):
                            ins = nc.scalar.activation(act_hi[:, k, :], psum[4 + b][:, (k % 2) * S:(k % 2 + 1) * S], ACT.Copy,
                                                       scale=col[:, g0 + k:g0 + k + 1])
                            do(ins, t_hi if k % 2 else None)

                def mixed(first, k0, banks=range(KD // 2)):
                    for b in banks:
                        act.wait_ge(trans_done, first + b + 1)
                        do(nc.scalar.activation(mix_hi[:, k0 + 2 * b:k0 + 2 * b + 2, :].rearrange("p k s -> p (k s)"),
                                                psum[4 + b][:, :], ACT.Copy), t_hi)

                norm(0)
                act.wait_ge(gz_ready, 1)
                do(nc.scalar.activation(gl[:, 0, :, :], gz[:, :, 4:8], ACT.Abs))
                do(nc.scalar.activation(gl[:, 0, :, :], gl[:, 0, :, :], ACT.Exp, scale=-1.0))
                do(nc.scalar.activation(gl[:, 1, :, :], gl[:, 0, :, :], ACT.Ln, bias=cst("one")), lnf_ready)

                def biased(name, i, bias):
                    taken(name, i)
                    for f in range(4):
                        n = bias + 4 * i + f
                        do(nc.scalar.activation(shifted[:, f, 3:], psum[2 * (CHUNK[name, i] % 2) + f // 2][:, (f % 2) * S:(f % 2 + 1) * S],
                                                ACT.Identity, bias=col[:, n:n + 1]), read_act if f == 3 else None)

                def silu(i):
                    act.wait_ge(conv_done, i + 1)
                    do(nc.scalar.activation(qk_t[:, 4 * i:4 * i + 4, :], conv[:, :, :], ACT.Silu), mqk_ready)

                for i in range(4):
                    stream("mqk", i)
                    if i >= 1:
                        act.wait_ge(conv_done, i)
                    biased("mqk", i, COL["bmqk"])
                    if i >= 1:
                        silu(i - 1)
                    for f in range(4):
                        w, b = COL["convw"] + 4 * i + f, COL["convb"] + 4 * i + f
                        do(nc.scalar.activation(conv[:, f, :], shifted[:, f, 0:S], ACT.Identity, bias=col[:, b:b + 1], scale=col[:, w:w + 1]),
                           tap_ready if f == 3 else None)
                act.wait_ge(fm_ready, 1)
                do(nc.scalar.activation(floor[:, :, :], gl[:, 0, :, :], ACT.Exp, scale=-1.0), floor_ready)
                for h in range(HEADS):
                    act.wait_ge(mmask_ready, h + 1)
                    do(nc.scalar.activation(decayed[:, h, 0:2, :], decayed[:, h, 0:2, :], ACT.Exp, bias=gi[:, 0, h:h + 1], scale=-1.0))
                    do(nc.scalar.activation(decayed[:, h, 2, :], decayed[:, h, 2, :], ACT.Exp, bias=gi[:, 1, h:h + 1], scale=-1.0), decay_ready)
                stream("mv", 0)
                silu(3)
                stream("mv", 1)

                def head_std(n):
                    act.wait_ge(stats_ready, n)
                    do(nc.scalar.activation(hstd[:, :, :], stats[:, :, :, 1], ACT.Sqrt, bias=eps), hstd_ready)

                def gates(name, i, func, dst, src=None):
                    stream(name, i)
                    wait_read(act, CHUNK[name, i])
                    do(nc.scalar.activation(dst, pre[:, :, :] if src is None else src, func), gated)

                for i in range(2):
                    held = merged[:, :, i * CW:(i + 1) * CW]
                    gates("mo", i, ACT.Sigmoid, held, held)
                head_std(1)
                gates("gm", 0, ACT.Sigmoid, gate[:, :, 0:CW])
                mixed(T_YM, 0)
                gates("gm", 1, ACT.Sigmoid, gate[:, :, CW:D])
                for i in range(2):
                    stream("bm", i)
                for i in range(4):
                    stream("rqk", i)
                    if i >= 1:
                        act.wait_ge(rqk_ready, i)
                    biased("rqk", i, COL["brqk"])
                for i in range(4):
                    stream("rv", i)
                def r_outputs(h):
                    act.wait_ge(y_done, HEADS + h + 1)
                    for t in range(TT):
                        do(nc.scalar.activation(y[:, t, h * RDV:(h + 1) * RDV], psum[6 + t][:, :], ACT.Copy), ry_read if t == 1 else None)

                def held_gate(i):
                    wait_read(act, CHUNK["rg", i])
                    held = gate[:, :, i * CW:(i + 1) * CW]
                    do(nc.scalar.activation(held, held, ACT.Silu), gated)

                first_tile = TILE["rg", 0]
                split_hi(base, first_tile + SPLIT)
                r_outputs(0)
                split_hi(base, first_tile + 1 + SPLIT)
                r_outputs(1)
                held_gate(0)
                split_hi(base, first_tile + 2 + SPLIT)
                r_outputs(2)
                split_hi(base, first_tile + 3 + SPLIT)
                r_outputs(3)
                held_gate(1)
                head_std(2)
                for i in range(2, 4):
                    gates("rg", i, ACT.Silu, pre[:, :, :])
                gates("gr", 0, ACT.Sigmoid, gate[:, :, 0:CW])
                mixed(T_YR, 0)
                gates("gr", 1, ACT.Sigmoid, gate[:, :, CW:D])
                mixed(T_YR + 4, KD)
                stream("br", 0)
                stream("br", 1, left=1)
                mixed(T_MG, 0, (0, 1))
                split_hi(base, TILE["out", 0] + 1)
                mixed(T_MG, 0, (2, 3))
                stream("out", 0)
                stream("out", 1, left=1)
                norm(1)
                split_hi(base, TILE["ffa1", 0] + 1)
                for half, (one, two) in enumerate((("ffa1", "ffa2"), ("ffb1", "ffb2"))):
                    for i in range(4):
                        stream(one, i)
                        taken(one, i)
                        if 4 * half + i >= 1:
                            act.wait_ge(ff_lo, 4 * half + i)
                        for f in range(4):
                            n = COL["bff1"] + 16 * half + 4 * i + f
                            do(nc.scalar.activation(conv[:, f, :], psum[2 * (CHUNK[one, i] % 2) + f // 2][:, (f % 2) * S:(f % 2 + 1) * S],
                                                    ACT.Relu, bias=col[:, n:n + 1]), read_act if f == 3 else None)
                        act.wait_ge(sq_ready, 4 * half + i + 1)
                        do(nc.scalar.activation(mix_hi[:, 4 * i:4 * i + 4, :], conv[:, :, :], ACT.Copy), ff_hi)
                    for i in range(2):
                        stream(two, i, left=1 if half and i else 0)
                norm(2)
                split_hi(base, TILE["peg", 0] + 1)
                for i in range(2):
                    stream("peg", i, left=i)
                    c = CHUNK["peg", i]
                    for t in range(TT):
                        if i and t == 0:
                            act.wait_ge(half_done, 3)
                        else:
                            taken("peg", i)
                        do(nc.scalar.activation(gate[:, t, i * CW:(i + 1) * CW], psum[2 * (c % 2) + t][:, :], ACT.Sigmoid), gated)
                act.sem_inc(layer_left, 1)
                split_hi(base, TILE["peg", 1] + 1 + SPLIT)
                act.wait_ge(layer_open, layer + 1)
            do = Order(act, act_step)
            for t in range(TT):
                do(nc.scalar.activation(junk[:, :], x[:, t, :], ACT.Square, accum_out=ssq[:, t:t + 1]))
                do(nc.scalar.activation(rstd[:, t:t + 1], ssq[:, t:t + 1], ACT.Sqrt, bias=eps, scale=1.0 / D), final_std)

        @block.vector
        def _(dve):
            def split_lo(base, k):
                dve.wait_ge(hi_ready, base + (k + 1))
                nc.vector.tensor_tensor(w_lo[:, k % SPLIT, :], raw[:, k % RAW, :], w_hi[:, k % SPLIT, :].bitcast(F32), ALU.subtract).then_inc(lo_ready, 1)

            for k in range(SPLIT):
                split_lo(0, k)
            dve.wait_ge(const_loaded, 32)
            dve.wait_ge(x_loaded, 16)
            with dve.Fori(0, LAYERS) as layer:
                base = layer * TILES_A
                do = Order(dve, dve_step)
                V = nc.vector

                def stream(name, i, left=0):
                    for j in range(PER_CHUNK[name] - left):
                        split_lo(base, TILE[name, i] + j + SPLIT)

                def taken(name, i):
                    dve.wait_ge(tile_used, base + (TILE[name, i] + PER_CHUNK[name]))

                def row_of(name, i, k=0):
                    ap, s, n = row_slot(name, i, k)
                    dve.wait_ge(s, layer * (16 * ROWS_A // RROW) + n)
                    return ap

                def norm(i, name=None):
                    for t in range(TT):
                        if i:
                            if t == 0:
                                dve.wait_ge(half_done, i)
                            else:
                                taken(name, 1)
                            add(name, 1, t, half_added)
                            if t:
                                dve.sem_inc(read_dve, 1)
                        dve.wait_ge(std_ready, TT * i + t + 1)
                        do(V.reciprocal(rstd[:, t:t + 1], rstd[:, t:t + 1]))
                        do(V.tensor_scalar(gate[:, t, :], x[:, t, :], rstd[:, t:t + 1], None, ALU.mult), xn_ready)
                    if i == 0:
                        dve.wait_ge(col_loaded, layer * 32 + 32)
                        dve.wait_ge(gw_split, 1)
                        V.tensor_tensor(gw_lo[:, :, :].rearrange("p k n -> p (k n)"), col[:, COL["gatew"]:COL["gatew"] + 64],
                                        gw_hi[:, :, :].rearrange("p k n -> p (k n)").bitcast(F32), ALU.subtract).then_inc(gw_split, 1)
                    g0 = COL[f"norm{i + 1}"]
                    first = (T_H, T_H2, T_H3)[i]
                    for b in range(KD // 2):
                        dve.wait_ge(t_hi, first + b + 1)
                        for k in (2 * b, 2 * b + 1):
                            do(V.scalar_tensor_tensor(out=act_lo[:, k, :], in0=psum[4 + b][:, (k % 2) * S:(k % 2 + 1) * S],
                                                      scalar=col[:, g0 + k:g0 + k + 1], in1=act_hi[:, k, :].bitcast(F32),
                                                      op0=ALU.mult, op1=ALU.subtract), t_lo if k % 2 else None)

                def mixed(first, k0, banks=range(KD // 2)):
                    for b in banks:
                        dve.wait_ge(t_hi, first + b + 1)
                        ks = slice(k0 + 2 * b, k0 + 2 * b + 2)
                        do(V.tensor_tensor(mix_lo[:, ks, :].rearrange("p k s -> p (k s)"), psum[4 + b][:, :],
                                           mix_hi[:, ks, :].rearrange("p k s -> p (k s)").bitcast(F32), ALU.subtract), t_lo)

                do(V.memset(shifted[:, :, 0:3], 0.0))
                do(V.memset(val_m[:, :, :, MDV:MDV + 1], 1.0))
                norm(0)
                dve.wait_ge(gate_mm, 1)
                for t in range(TT):
                    do(V.tensor_tensor(gz[:, t, :], psum[6][:, t * 8:t * 8 + 8], bgate_row[:, :], ALU.add), gz_ready if t else None)
                dve.wait_ge(lnf_ready, 1)
                do(V.scalar_tensor_tensor(out=gl[:, 2, :, :], in0=gz[:, :, 4:8], scalar=0.0, in1=gl[:, 1, :, :], op0=ALU.min, op1=ALU.subtract), lf_ready)

                def convolve(i):
                    dve.wait_ge(tap_ready, i + 1)
                    for j in range(1, 4):
                        for f in range(4):
                            w = COL["convw"] + 16 * j + 4 * i + f
                            ins = V.scalar_tensor_tensor(out=conv[:, f, :], in0=shifted[:, f, j:j + S], scalar=col[:, w:w + 1],
                                                         in1=conv[:, f, :], op0=ALU.mult, op1=ALU.add)
                            do(ins, conv_done if j == 3 and f == 3 else None)

                stream("mqk", 0)
                convolve(0)
                dve.wait_ge(gate_mm, 2)
                do(V.tensor_copy(gl[:, 3, :, :].rearrange("p t h -> p (t h)"), psum[7][:, 0:2 * HEADS]))
                do(V.tensor_tensor(gi[:, :, :], gz[:, :, 0:4], gl[:, 3, :, :], ALU.subtract), gi_ready)
                stream("mqk", 1)
                convolve(1)
                dve.wait_ge(gate_mm, 3)
                do(V.tensor_copy(grow[:, :], psum[6][0:HEADS, 0:S]))
                do(V.tensor_tensor_scan(mrow[:, :], grow[:, :], grow[:, :], 0.0, ALU.max, ALU.max), m_ready)
                stream("mqk", 2)
                convolve(2)
                dve.wait_ge(gate_mm, 4)
                do(V.tensor_tensor(gl[:, 0, :, :].rearrange("p t h -> p (t h)"), gl[:, 3, :, :].rearrange("p t h -> p (t h)"),
                                   psum[7][:, 8:8 + 2 * HEADS], ALU.add), fm_ready)
                dve.wait_ge(gate_mm, 5)
                for h in range(HEADS):
                    m = psum[4 + h // 2][:, (h % 2) * S:(h % 2 + 1) * S]
                    for b, t, masked in ((0, 0, 1), (1, 1, 0), (2, 1, 1)):
                        dst, src = decayed[:, h, b, :], m[:, t * P:(t + 1) * P]
                        ins = V.tensor_tensor(dst, src, cst("mask"), ALU.add) if masked else V.tensor_copy(dst, src)
                        do(ins, mmask_ready if b == 2 else None)
                    if h % 2:
                        split_lo(base, TILE["mqk", 3] + h // 2 + SPLIT)
                convolve(3)
                for i in range(2):
                    stream("mv", i)
                    taken("mv", i)
                    r = row_of("mv", i)
                    for t in range(TT):
                        do(V.tensor_tensor(val_m[:, t, 2 * i:2 * i + 2, 0:MDV], psum[2 * (CHUNK["mv", i] % 2) + t][:, :].rearrange("p (h n) -> p h n", h=2),
                                           r.rearrange("p (h n) -> p h n", h=2), ALU.add), read_dve if t else None)

                def weigh(h0, h, scale, weights_of):
                    dve.wait_ge(score_done, h0 + h + 1)
                    if h >= 2:
                        dve.wait_ge(y_done, h0 + h - 1)
                    do(V.scalar_tensor_tensor(out=weighed[:, h % 2, :], in0=psum[4 + h % 2][:, 0:3 * P], scalar=scale, in1=weights_of(h),
                                              op0=ALU.mult, op1=ALU.mult), weighed_ready)

                def statistics(src, t, h):
                    do(V.bn_stats(st6[:, :], src))
                    do(V.bn_aggr(stats[:, t, h, :], st6[:, :]), stats_ready if (t, h) == (TT - 1, HEADS - 1) else None)

                def head_norm(n, width):
                    dve.wait_ge(hstd_ready, n)
                    do(V.reciprocal(hstd[:, :, :], hstd[:, :, :]))
                    for h in range(HEADS):
                        for t in range(TT):
                            ys = y[:, t, h * width:(h + 1) * width]
                            do(V.tensor_scalar(ys, ys, stats[:, t, h, 0:1], hstd[:, t, h:h + 1], ALU.subtract, ALU.mult))

                def m_output(h):
                    dve.wait_ge(y_done, h + 1)
                    for t in range(TT):
                        total = psum[6 + t][:, MDV:MDV + 1]
                        do(V.scalar_tensor_tensor(out=den[:, 0:1], in0=total, scalar=-1.0, in1=floor[:, t, h:h + 1], op0=ALU.mult, op1=ALU.max))
                        do(V.tensor_tensor(den[:, 0:1], den[:, 0:1], total, ALU.max))
                        do(V.reciprocal(den[:, 1:2], den[:, 0:1]))
                        do(V.tensor_scalar(y[:, t, h * MDV:(h + 1) * MDV], psum[6 + t][:, 0:MDV], den[:, 1:2], None, ALU.mult), my_read if t else None)
                        statistics(y[:, t, h * MDV:(h + 1) * MDV], t, h)

                def m_weigh(h):
                    dve.wait_ge(decay_ready, h + 1)
                    weigh(0, h, MDV ** -0.5, lambda h: decayed[:, h, :, :].rearrange("p b s -> p (b s)"))

                def gate_in(name, i, dst):
                    taken(name, i)
                    r = row_of(name, i)
                    for t in range(TT):
                        do(V.tensor_tensor(dst[:, t, :], psum[2 * (CHUNK[name, i] % 2) + t][:, :], r, ALU.add), read_dve if t else None)

                def gating(name, i, count, held):
                    g = row_of(name, i, 1)
                    for t in range(TT):
                        do.also(V.tensor_tensor(y[:, t, i * CW:(i + 1) * CW], y[:, t, i * CW:(i + 1) * CW], g, ALU.mult))
                    do.settle()
                    dve.wait_ge(gated, count)
                    for t in range(TT):
                        ys = y[:, t, i * CW:(i + 1) * CW]
                        do(V.tensor_tensor(ys, ys, held[:, t, :], ALU.mult), y_ready if t else None)

                dve.wait_ge(floor_ready, 1)
                first_tile = TILE["mo", 0]
                m_weigh(0)
                m_weigh(1)
                split_lo(base, first_tile + SPLIT)
                m_output(0)
                m_weigh(2)
                split_lo(base, first_tile + 1 + SPLIT)
                m_output(1)
                gate_in("mo", 0, merged[:, :, 0:CW])
                m_weigh(3)
                split_lo(base, first_tile + 2 + SPLIT)
                m_output(2)
                split_lo(base, first_tile + 3 + SPLIT)
                gate_in("mo", 1, merged[:, :, CW:D])
                m_output(3)
                head_norm(1, MDV)
                split_lo(base, TILE["gm", 0] + SPLIT)
                gating("mo", 0, 1, merged[:, :, 0:CW])
                split_lo(base, TILE["gm", 0] + 1 + SPLIT)
                gating("mo", 1, 2, merged[:, :, CW:D])
                gate_in("gm", 0, pre)
                mixed(T_YM, 0)
                stream("gm", 1)
                dve.wait_ge(gated, 3)
                gate_in("gm", 1, pre)
                for i in range(2):
                    stream("bm", i)
                    taken("bm", i)
                    dve.wait_ge(gated, 4)
                    for t in range(TT):
                        cs = slice(i * CW, (i + 1) * CW)
                        do(V.tensor_tensor(merged[:, t, cs], psum[2 * (CHUNK["bm", i] % 2) + t][:, :], gate[:, t, cs], ALU.mult), read_dve if t else None)

                def rotate(i):
                    wait_read(dve, CHUNK["rqk", i])
                    for a in range(2):
                        x1, x2 = shifted[:, 2 * a, 3:], shifted[:, 2 * a + 1, 3:]
                        o1, o2 = qk_t[:, 4 * i + 2 * a, :], qk_t[:, 4 * i + 2 * a + 1, :]
                        do(V.tensor_tensor(o1, x1, cst("cos"), ALU.mult))
                        do(V.tensor_tensor(o2, x1, cst("sin"), ALU.mult))
                        do(V.tensor_tensor(conv[:, 0, :], x2, cst("sin"), ALU.mult))
                        do(V.tensor_tensor(conv[:, 1, :], x2, cst("cos"), ALU.mult))
                        do(V.tensor_tensor(o1, o1, conv[:, 0, :], ALU.subtract))
                        do(V.tensor_tensor(o2, o2, conv[:, 1, :], ALU.add), rqk_ready if a else None)

                for i in range(4):
                    stream("rqk", i)
                    rotate(i)
                for i in range(4):
                    stream("rv", i)
                    taken("rv", i)
                    r = row_of("rv", i)
                    for t in range(TT):
                        do(V.tensor_tensor(val_r[:, t, i * CW:(i + 1) * CW], psum[2 * (CHUNK["rv", i] % 2) + t][:, :], r, ALU.add), read_dve if t else None)

                def r_output(h):
                    dve.wait_ge(ry_read, h + 1)
                    for t in range(TT):
                        statistics(y[:, t, h * RDV:(h + 1) * RDV], t, h)

                r_weigh = lambda h: weigh(HEADS, h, 1.0, lambda h: cst("decay")[:, h * 384:(h + 1) * 384])
                first_tile = TILE["rg", 0]
                r_weigh(0)
                r_weigh(1)
                split_lo(base, first_tile + SPLIT)
                r_output(0)
                r_weigh(2)
                split_lo(base, first_tile + 1 + SPLIT)
                r_output(1)
                gate_in("rg", 0, gate[:, :, 0:CW])
                r_weigh(3)
                split_lo(base, first_tile + 2 + SPLIT)
                r_output(2)
                split_lo(base, first_tile + 3 + SPLIT)
                gate_in("rg", 1, gate[:, :, CW:D])
                r_output(3)
                head_norm(2, RDV)
                for i in range(2, 4):
                    split_lo(base, TILE["rg", i] + SPLIT)
                    gating("rg", i - 2, 4 + i - 1, gate[:, :, (i - 2) * CW:(i - 1) * CW])
                    split_lo(base, TILE["rg", i] + 1 + SPLIT)
                    if i == 3:
                        gating("rg", 2, 4 + 3, pre)
                    gate_in("rg", i, pre)
                gating("rg", 3, 4 + 4, pre)
                stream("gr", 0)
                gate_in("gr", 0, pre)
                mixed(T_YR, 0)
                stream("gr", 1)
                dve.wait_ge(gated, 9)
                gate_in("gr", 1, pre)
                mixed(T_YR + 4, KD)
                for i in range(2):
                    stream("br", i, left=i)
                    if i:
                        mixed(T_MG, 0, (0, 1))
                    taken("br", i)
                    dve.wait_ge(gated, 10)
                    for t in range(TT):
                        cs = slice(i * CW, (i + 1) * CW)
                        do(V.tensor_tensor(pre[:, t, :], psum[2 * (CHUNK["br", i] % 2) + t][:, :], gate[:, t, cs], ALU.mult), read_dve if t else None)
                        do(V.tensor_tensor(merged[:, t, cs], merged[:, t, cs], pre[:, t, :], ALU.add), merged_ready if t else None)
                split_lo(base, TILE["out", 0] + 1)
                mixed(T_MG, 0, (2, 3))

                def add(name, i, t, signal):
                    cs = slice(i * CW, (i + 1) * CW)
                    do(V.tensor_tensor(x[:, t, cs], x[:, t, cs], psum[2 * (CHUNK[name, i] % 2) + t][:, :], ALU.add), signal)

                def residual(name, i):
                    taken(name, i)
                    for t in range(TT):
                        add(name, i, t, read_dve if t else None)

                stream("out", 0)
                residual("out", 0)
                stream("out", 1, left=1)
                norm(1, "out")
                split_lo(base, TILE["ffa1", 0] + 1)
                for half, (one, two) in enumerate((("ffa1", "ffa2"), ("ffb1", "ffb2"))):
                    for i in range(4):
                        stream(one, i)
                        wait_read(dve, CHUNK[one, i])
                        do(V.tensor_tensor(conv[:, :, :], conv[:, :, :], conv[:, :, :], ALU.mult), sq_ready)
                        dve.wait_ge(ff_hi, 4 * half + i + 1)
                        do(V.tensor_tensor(mix_lo[:, 4 * i:4 * i + 4, :], conv[:, :, :], mix_hi[:, 4 * i:4 * i + 4, :].bitcast(F32), ALU.subtract), ff_lo)
                    for i in range(2):
                        stream(two, i, left=1 if half and i else 0)
                        if half:
                            r = row_of(two, i)
                            for t in range(TT):
                                cs = slice(i * CW, (i + 1) * CW)
                                do(V.tensor_tensor(x[:, t, cs], x[:, t, cs], r, ALU.add))
                        if not half or i == 0:
                            residual(two, i)
                norm(2, "ffb2")
                split_lo(base, TILE["peg", 0] + 1)
                for i in range(2):
                    stream("peg", i, left=i)
                    dve.wait_ge(pe_mm, 1)
                    for t in range(TT):
                        dve.wait_ge(gated, 10 + TT * i + t + 1)
                        cs = slice(i * CW, (i + 1) * CW)
                        do(V.tensor_tensor(pre[:, t, :], psum[4 + 2 * i + t][:, :], gate[:, t, cs], ALU.mult))
                        do(V.tensor_tensor(x[:, t, cs], x[:, t, cs], pre[:, t, :], ALU.add), read_dve if t else None)
                dve.sem_inc(layer_left, 1)
                split_lo(base, TILE["peg", 1] + 1 + SPLIT)
                dve.wait_ge(layer_open, layer + 1)
            do = Order(dve, dve_step)
            dve.wait_ge(final_loaded, 16)
            for t in range(TT):
                dve.wait_ge(final_std, t + 1)
                do(V.reciprocal(rstd[:, t:t + 1], rstd[:, t:t + 1]))
                do(V.scalar_tensor_tensor(out=x[:, t, :], in0=x[:, t, :], scalar=rstd[:, t:t + 1], in1=row[:, 0:2, :].rearrange("p a n -> p (a n)"),
                                          op0=ALU.mult, op1=ALU.mult), x_ready if t else None)
    memory.close()


def second_block(nc, ctx, m, base, erows, ecols, lora_w, side_w, keys, ln_rows, consts_b, spill, out):
    raw, w_hi, w_lo, x, act_hi, act_lo, ident, psum = m.raw, m.w_hi, m.w_lo, m.x, m.act_hi, m.act_lo, m.ident, m.psum
    raw_loaded, hi_ready, lo_ready, tile_used = m.raw_loaded, m.hi_ready, m.lo_ready, m.tile_used
    V, A = nc.vector, nc.scalar
    total = base + TILES_B

    def sb(name, shape, dt=F32, stack=ctx):
        return stack.enter_context(nc.sbuf_tensor(name, shape, dt))

    def sem(name):
        return ctx.enter_context(nc.semaphore(name))

    const_b = sb("const_b", [P, CONSTS_B])

    def cst(name):
        first, n = CONST_B[name]
        return const_b[:, first:first + n]

    small = sb("small", [P, 64])
    even = ExitStack()
    rkv = sb("rkv", [P, 3, FT, S], F32, even)
    sgw = sb("sgw", [P, FT, S], F32, even)
    asig = sb("asig", [P, FT, S], F32, even)
    gnat = sb("gnat", [P, TT, EW], F32, even)
    erow = sb("erow", [P, EROWS], F32, even)
    ecol = sb("ecol", [P, ECOLS], F32, even)
    ymix = sb("ymix", [P, TT, D], F32, even)
    gla = ExitStack()
    lora = sb("lora", [P, LORA], F32, gla)
    side_t = sb("side_t", [P, 2, S], F32, gla)
    sh = sb("sh", [P, FT, S + 1], F32, gla)
    dif = sb("dif", [P, FT, S], F32, gla)
    gqk = sb("gqk", [P, 4, S], F32, gla)
    side_scope = ExitStack()
    side_raw = sb("side_raw", [P, KD, 2 * P], F32, side_scope)
    side_hi = sb("side_hi", [P, KD, 2 * P], F32R, side_scope)
    side_lo = sb("side_lo", [P, KD, 2 * P], F32R, side_scope)
    side_scope.close()
    la = sb("la", [P, GP, S], F32, gla)
    lb = sb("lb", [P, GP, S], F32, gla)
    eb = sb("eb", [P, GP, S], F32, gla)
    en = sb("en", [P, GP, S], F32, gla)
    qin = sb("qin", [P, GP, S], F32, gla)
    kin = sb("kin", [P, GP, S], F32, gla)
    konat = sb("konat", [P, TT * GP * P], F32, gla)
    attn = sb("attn", [P, 2, TT, GP, P], F32, gla)
    state = sb("state", [P, CH * TT, GP, 2 * P], F32, gla)
    qz = sb("qz", [P, CH, GP, S], F32, gla)
    gv = sb("gv", [P, TT, EW], F32, gla)
    gsil = sb("gsil", [P, TT, EW], F32, gla)
    gla.close()
    rw = ExitStack()
    cw = sb("cw", [P, FT, S], F32, rw)
    pinc = sb("pinc", [P, FT, S], F32, rw)
    pinv = sb("pinv", [P, FT, S], F32, rw)
    pm = sb("pm", [P, FT, S], F32, rw)
    kk = sb("kk", [P, FT, S], F32, rw)
    kp = sb("kp", [P, FT, S], F32, rw)
    bt = sb("bt", [P, FT, S], F32, rw)
    kt = sb("kt", [P, FT, S], F32, rw)
    ar = sb("ar", [P, FT, 2, S], F32, rw)
    lrb = sb("lrb", [P, TT, 2, FT, 2, CHUNK_T], F32, rw)
    lrk = sb("lrk", [P, TT, 2, FT, 2, CHUNK_T], F32, rw)
    rstat = sb("rstat", [P, TT, RH, 2], F32, rw)
    dt_ = sb("dt_", [P, TT, 2, FT, CHUNK_T], F32, rw)
    s_all = sb("s_all", [P, TT * CH + 1, FT, P], F32, rw)
    rkind = sb("rkind", [P, FT, 2], F32, rw)
    bonus = sb("bonus", [P, TT, RH], F32, rw)
    r6 = sb("r6", [P, RH, 6], F32, rw)
    rw.close()
    even.close()

    def by_half(buf):
        return buf[:, :, :].rearrange("p f s -> p (f s)").rearrange("p (t e f s) -> p t e f s", t=TT, e=2, f=FT)

    def nat_of(buf):
        return buf[:, :, :].rearrange("p f s -> p (f s)").rearrange("p (t n) -> p t n", t=TT)

    sq = sgw
    nat = {"a": nat_of(cw), "b": nat_of(pm), "k": nat_of(pinv), "v": nat_of(sgw)}
    dd, xx = by_half(asig), by_half(kk)
    zz, wv, tat, uu = nat_of(asig), nat_of(kp), bt, nat_of(kt)
    norm = nat_of(dt_[:, :, :, :, :].rearrange("p t e f s -> p (t e f s)").rearrange("p (f s) -> p f s", f=FT))
    ln_row = sb("ln_row", [P, 2, D])
    odd = ExitStack()
    qn = sb("qn", [P, TT, D], F32, odd)
    qin_ = sb("qidx", [P, TT, IH * ID], F32, odd)
    kn = sb("kn", [P, TT, AD], F32, odd)
    vn = sb("vn", [P, TT, AD], F32, odd)
    kid = sb("kid", [P, TT, 2 * ID], F32, odd)
    wi = sb("wi", [P, TT, IH], F32, odd)
    rtmp = sb("rtmp", [P, 2, CW // 2], F32, odd)
    q_t = sb("q_t", [P, AH, S], F32, odd)
    qi_t = sb("qi_t", [P, IH // 2, S], F32, odd)
    k_t = sb("k_t", [P, S], F32, odd)
    kib = sb("kib", [P, 2 * S], F32, odd)
    rel = sb("rel", [P, TT, IH, S], F32, odd)
    score = sb("score", [P, TT, S], F32, odd)
    madd = sb("madd", [P, TT, S], F32, odd)
    logit = sb("logit", [P, AH, S], F32, odd)
    pt = sb("pt", [P, AH, TT, P], F32, odd)
    amax = sb("amax", [P, AH], F32, odd)
    asum = sb("asum", [P, AH], F32, odd)
    top8 = sb("top8", [P, 8], F32, odd)
    odd.close()
    peer = ExitStack()
    hid = sb("hid", [P, JH, S], F32, peer)
    pq, keys_sb = hid[:, JH - 2 * PH:JH - PH, :], hid[:, JH - PH:JH, :]
    ijg = sb("ijg", [P, 3, S], F32, peer)
    hot_i = sb("hot_i", [P, HOT, GT, KEYS], F32, peer)
    hot_j = sb("hot_j", [P, HOT, GT, KEYS], F32, peer)
    hot = hot_i[:, :, :, :].rearrange("p a t n -> p (a t n)").rearrange("p (h k a) -> p h k a", h=PH, k=PK)
    tops = sb("tops", [P, 2 * PH, PK], F32, peer)
    topi = sb("topi", [P, 2 * PH, PK], U32, peer)
    topf = sb("topf", [P, 2 * PH, PK], F32, peer)
    best = sb("best", [P, TT, PH, PK], F32, peer)
    pos = sb("pos", [P, PH, PK], U32, peer)
    posab = sb("posab", [P, 2, PH * PK], U32, peer)
    posf = sb("posf", [P, 2, PH * PK], F32, peer)
    sel = sb("sel", [P, TT, 3, PH * PK], F32, peer)
    gsum = sb("gsum", [P, TT * PH], F32, peer)
    scores = ExitStack()
    ss1 = sb("ss1", [P, 2 * PH, KEYS], F32, scores)
    flat1 = ss1[:, :, :].rearrange("p c n -> p (c n)")
    staged = flat1.rearrange("p (b h t j) -> p b h t j", b=HOT, h=2, t=GT)
    scores.close()
    ss = (ln_row[:, :, :].rearrange("p a n -> p (a n)").rearrange("p (c n) -> p c n", n=KEYS), ss1)
    reload = [flat.rearrange("p (b g t j) -> p b (g t) j", b=HOT, g=2, t=GT)[:, b, :, :]
              for flat in (hot_i[:, :, :, :].rearrange("p a t n -> p (a t n)"), hot_j[:, :, :, :].rearrange("p a t n -> p (a t n)"),
                           ln_row[:, :, :].rearrange("p a n -> p (a n)"), flat1) for b in range(HOT)]
    c_hi = sb("c_hi", [P, 2, 2 * S], F32R, peer)
    c_lo = sb("c_lo", [P, 2, 2 * S], F32R, peer)
    peer.close()

    act_own, dve_own = sem("b_act_own"), sem("b_dve_own")
    b_const = sem("b_const")
    side_loaded = sem("side_loaded")
    even_loaded = sem("even_loaded")
    ln_loaded = sem("ln_loaded")
    keys_loaded = sem("keys_loaded")
    x_ready = m.x_ready
    tr_done = sem("b_tr_done")
    tr_hi = sem("b_tr_hi")
    tr_lo = sem("b_tr_lo")
    half_done = sem("b_half_done")
    side_hi_ready, side_lo_ready = sem("side_hi_ready"), sem("side_lo_ready")
    read_act, read_dve = sem("b_read_act"), sem("b_read_dve")
    shifted_done = sem("shifted_done")
    even_pe, even_act, even_dve = sem("even_pe"), sem("even_act"), sem("even_dve")
    rw_pe, rw_act, rw_dve = sem("rw_pe"), sem("rw_act"), sem("rw_dve")
    chain_pe, chain_dve = sem("chain_pe"), sem("chain_dve")
    odd_pe, odd_act, odd_dve = sem("odd_pe"), sem("odd_act"), sem("odd_dve")
    att_hi, att_lo = sem("att_hi"), sem("att_lo")
    ln_var, ln_std = sem("ln_var"), sem("ln_std")
    s_done, s_read = sem("s_done"), sem("s_read")
    best_ready = sem("best_ready")
    exp_ready = sem("exp_ready")
    sel_ready = sem("sel_ready")
    sel_t, ijg_ready = sem("sel_t"), sem("ijg_ready")
    hot_eq = sem("hot_eq")
    hot_ready = sem("hot_ready")
    gates_done = sem("gates_done")
    gates_read = sem("gates_read")
    spilled = [sem(f"spilled{b}") for b in range(HOT)]
    reloaded = [sem(f"reloaded{b}") for b in range(RELOAD)]
    gated_odd = sem("gated_odd")
    gated_even = sem("gated_even")
    regated_pool = sem("regated_pool")
    regated_dve = sem("regated_dve")
    act_pad = sem("act_pad")
    gelu_ready = sem("gelu_ready")
    c_hi_ready, c_lo_ready = sem("c_hi_ready"), sem("c_lo_ready")
    out_stored = m.out_stored

    def normed(n, t):
        return 1 + TT * n + t + 1

    def wait_read(eng, c):
        by, count = READ_B[c]
        eng.wait_ge(read_act if by == "act" else read_dve, count)

    block = ctx.enter_context(nc.Block())

    @block.sync
    def _(sp):
        def stream(first, end):
            with sp.Fori(first // RAW, end // RAW) as n:
                for r in range(RAW):
                    sp.wait_ge(lo_ready, n * RAW + (r - RAW + 1))
                    sp.dma_start(raw[:, r, :], m.weights[n * RAW + r]).then_inc(raw_loaded[r], 16)

        at = base + RAW
        for layer in range(LAYERS):
            first = base + PEER_UV[layer]
            stream(at, first + PAIRS + RAW)
            with sp.Fori(0, GROUPS // HOT) as n:
                for b in range(HOT):
                    sp.wait_ge(gates_read, n * HOT + (GROUPS * layer + b + 1))
                    sp.dma_start(spill[n * HOT + b], staged[:, b, 1, :, :].rearrange("p t j -> p (t j)")).then_inc(spilled[b], 16)
            stream(first + PAIRS + RAW, first + 2 * PAIRS + 2 * RAW)
            for b in range(HOT):
                sp.wait_ge(spilled[b], 16 * (GROUPS // HOT) * (layer + 1))
            sp.wait_ge(tile_used, first + 2 * PAIRS)

            def again(n, b):
                sp.dma_start(reload[b].rearrange("p (g t) j -> p g (t j)", g=2),
                             spill[2 * (n * RELOAD + b):2 * (n * RELOAD + b) + 2].rearrange("g p n -> p g n")).then_inc(reloaded[b], 16)

            for b in range(RELOAD):
                again(0, b)
                if b % HOT == HOT - 1:
                    k = first + 2 * PAIRS + (2 + b // HOT) * RAW
                    stream(k, k + RAW)
            stream(first + 2 * PAIRS + (2 + RELOAD // HOT) * RAW, first + 3 * PAIRS + RAW)
            for n in range(1, REGATED):
                for b in range(RELOAD):
                    if b % HOT < HOT - 1:
                        sp.wait_ge(regated_dve, (RELOAD - RELOAD // HOT) * (REGATED * layer + n - 1) + (HOT - 1) * (b // HOT) + b % HOT + 1)
                    else:
                        sp.wait_ge(regated_pool, RELOAD // HOT * (REGATED * layer + n - 1) + b // HOT + 1)
                    again(n, b)
            at = first + 3 * PAIRS + RAW
        stream(at, total)
        for t in range(TT):
            sp.wait_ge(x_ready, normed(2 * LAYERS - 1, t))
            sp.dma_start(out[:, t, :], x[:, t, :]).then_inc(out_stored, 16)
        sp.wait_ge(out_stored, 16 * TT)

    @block.gpsimd
    def _(pool):
        pool.dma_start(side_raw[:, :, :], side_w).then_inc(side_loaded, 16)
        pool.dma_start(const_b[:, :], consts_b).then_inc(b_const, 16)
        pool.dma_start(lora[:, :], lora_w).then_inc(even_loaded, 16)
        pool.dma_start(ecol[:, :], ecols).then_inc(even_loaded, 16)
        pool.dma_start(erow[:, :], erows.partition_broadcast(P)).then_inc(even_loaded, 16)

        def ln_load(n):
            pool.dma_start(ln_row[:, 0, :], ln_rows[2 * n].partition_broadcast(P)).then_inc(ln_loaded, 16)
            pool.dma_start(ln_row[:, 1, :], ln_rows[2 * n + 1].partition_broadcast(P)).then_inc(ln_loaded, 16)

        pool.wait_ge(tr_lo, 8)
        ln_load(0)
        pool.dma_start(keys_sb, keys[0]).then_inc(keys_loaded, 16)

        def gate(layer):
            g0 = GROUPS * layer

            def rows(n, b):
                pool.wait_ge(hot_eq, n * HOT + (g0 + b + 1))
                tok = bass.ds(n * HOT * GT + b * GT, GT)
                at = hot_j[:, b % HOT, :, :]
                nc.gpsimd.tensor_tensor(at, at, ijg[:, 2, tok].unsqueeze(2).broadcast_to([P, GT, KEYS]), ALU.mult).then_inc(hot_ready, 1)

            def apply(n, b):
                pool.wait_ge(gates_read, n * HOT + (g0 + b + 1))
                tok = hid[:, :, bass.ds(n * HOT * GT + b * GT, GT)].rearrange("p j t -> p t j")
                nc.gpsimd.tensor_tensor(tok, tok, staged[:, b, 0, :, :], ALU.mult).then_inc(gated_odd, 1)

            pool.wait_ge(ijg_ready, 2 * layer + 2)
            rows(0, 0)
            rows(0, 1)
            pool.wait_ge(gelu_ready, PAIRS * (2 * layer + 1))
            with pool.Fori(0, GROUPS // HOT - 1) as n:
                for b in range(HOT):
                    rows(n, b + 2)
                    if b % 2:
                        apply(n, b)
            for b in range(HOT):
                if b + 2 < HOT:
                    rows(GROUPS // HOT - 1, b + 2)
                if b % 2:
                    apply(GROUPS // HOT - 1, b)
            pool.wait_ge(gelu_ready, PAIRS * (2 * layer + 2))
            with pool.Fori(0, REGATED) as n:
                for b in range(HOT - 1, RELOAD, HOT):
                    pool.wait_ge(reloaded[b], n * 16 + 16 * (REGATED * layer + 1))
                    tok = hid[:, :, bass.ds(n * RELOAD * 2 * GT + b * 2 * GT, 2 * GT)].rearrange("p j t -> p t j")
                    nc.gpsimd.tensor_tensor(tok, tok, reload[b], ALU.mult).then_inc(regated_pool, 1)
            pool.wait_ge(regated_pool, RELOAD // HOT * REGATED * (layer + 1))
            pool.wait_ge(regated_dve, (RELOAD - RELOAD // HOT) * REGATED * (layer + 1))
            ln_load(2 * layer + 1)

        gate(0)
        pool.wait_ge(x_ready, normed(1, TT - 1))
        ln_load(2)
        pool.wait_ge(att_lo, 2)
        pool.dma_start(keys_sb, keys[1]).then_inc(keys_loaded, 16)
        gate(1)

    @block.tensor
    def _(pe):
        mm = nc.tensor.matmul

        def halves_of(ki, split):
            if split is not None and ki % 2 == 0:
                pe.wait_ge(tr_lo, split + ki // 2 + 1)

        def natural(name, i, tiles=(0, 1), split=None, half=None):
            c, k0 = CHUNK_B[name, i], base + TILE_B[name, i]
            if c >= 2:
                wait_read(pe, c - 2)
            for j in tiles:
                k = k0 + j
                pe.wait_ge(lo_ready, k + 1)
                apart = half is not None and j == 1
                for kk_, t in [(n, t) for t in range(TT) for n in range(KB)] if apart else [(n, t) for n in range(KB) for t in range(TT)]:
                    ki = j * KB + kk_
                    if t == 0:
                        halves_of(ki, split)
                    dst = psum[2 * (c % 2) + t][:, :]
                    ws = slice(kk_ * CW, (kk_ + 1) * CW)
                    mm(dst, act_hi[:, ki, HALVES[t]], w_hi[:, k % SPLIT, ws], start=ki == 0, stop=False)
                    mm(dst, act_hi[:, ki, HALVES[t]], w_lo[:, k % SPLIT, ws], start=False, stop=False)
                    last = mm(dst, act_lo[:, ki, HALVES[t]], w_hi[:, k % SPLIT, ws], start=False, stop=ki == KD - 1)
                    if apart and t == 0 and ki == KD - 1:
                        last.then_inc(half, 1)
                last.then_inc(tile_used, 1)

        def featured(name, i, split=None):
            c, k0 = CHUNK_B[name, i], base + TILE_B[name, i]
            if c >= 2:
                wait_read(pe, c - 2)
            for j in range(2):
                k = k0 + j
                pe.wait_ge(lo_ready, k + 1)
                for f in range(4):
                    for kk_ in range(KB):
                        ki = j * KB + kk_
                        if f == 0:
                            halves_of(ki, split)
                        ws = slice(kk_ * CW + f * P, kk_ * CW + (f + 1) * P)
                        dst = psum[2 * (c % 2) + f // 2][:, (f % 2) * S:(f % 2 + 1) * S]
                        wh, wl = w_hi[:, k % SPLIT, ws], w_lo[:, k % SPLIT, ws]
                        mm(dst, wh, act_hi[:, ki, :], start=ki == 0 and f % 2 == 0, stop=False)
                        mm(dst, wh, act_lo[:, ki, :], start=False, stop=False)
                        last = mm(dst, wl, act_hi[:, ki, :], start=False, stop=ki == KD - 1 and f % 2 == 1)
                last.then_inc(tile_used, 1)

        def transposes(src, ready=None):
            for t in range(TT):
                if ready is not None:
                    pe.wait_ge(x_ready, normed(ready, t))
                for k in range(KD):
                    last = nc.tensor.transpose(psum[4 + k // 2][:, (k % 2) * S + t * P:(k % 2) * S + (t + 1) * P],
                                               src[:, t, k * P:(k + 1) * P], ident)
                    if t == TT - 1 and k % 2:
                        last.then_inc(tr_done, 1)

        pe.wait_ge(x_ready, 1)
        transposes(x)
        featured("gqk", 0, split=0)
        pe.wait_ge(side_lo_ready, 1)
        for g in range(2):
            for k in range(KD):
                dst, ws = psum[4][:, g * S:(g + 1) * S], slice(g * P, (g + 1) * P)
                mm(dst, side_hi[:, k, ws], act_hi[:, k, :], start=k == 0 and g == 0, stop=False)
                mm(dst, side_hi[:, k, ws], act_lo[:, k, :], start=False, stop=False)
                last = mm(dst, side_lo[:, k, ws], act_hi[:, k, :], start=False, stop=k == KD - 1 and g == 1)
        last.then_inc(even_pe, 1)
        natural("gv", 0)
        pe.wait_ge(even_loaded, 48)
        pe.wait_ge(even_act, EVEN_ACT["gates"])
        for g in range(GP):
            cols = slice(EW + g * P, EW + (g + 1) * P)
            last = mm(psum[5][:, g * S:(g + 1) * S], lora[GA2[0], cols], side_t[GA2[0], 1, :], start=True, stop=True)
        last.then_inc(even_pe, 1)
        for f in range(FT):
            last = mm(psum[6 + f // 2][:, (f % 2) * S:(f % 2 + 1) * S], lora[W2[0], f * P:(f + 1) * P], side_t[W2[0], 0, :],
                      start=True, stop=True)
        last.then_inc(even_pe, 1)
        natural("gg", 0)
        pe.wait_ge(even_dve, EVEN_DVE["la"])
        pe.wait_ge(even_act, EVEN_ACT["w"])
        for f in range(FT):
            cols = slice(EW + f * P, EW + (f + 1) * P)
            last = mm(psum[4 + f // 2][:, (f % 2) * S:(f % 2 + 1) * S], lora[A2[0], cols], side_t[A2[0], 1, :], start=True, stop=True)
        last.then_inc(even_pe, 1)
        for t in range(TT):
            last = mm(psum[6 + t][:, :], side_t[G2[0], 0, HALVES[t]], lora[G2[0], G2[1]], start=True, stop=True)
        last.then_inc(even_pe, 1)
        featured("r", 0)
        pe.wait_ge(even_dve, EVEN_DVE["decayed"])
        pe.wait_ge(even_act, EVEN_ACT["a"])
        for e in range(2):
            for t in range(TT):
                for g in range(GP):
                    es = slice(e * GDK, (e + 1) * GDK)
                    last = mm(psum[4 + e][:, (t * GP + g) * P:(t * GP + g + 1) * P], kin[es, g, HALVES[t]], qin[es, g, HALVES[t]],
                              start=True, stop=True)
        last.then_inc(even_pe, 1)
        for t in range(TT):
            for g in range(GP):
                last = nc.tensor.transpose(psum[6][:, (t * GP + g) * P:(t * GP + g + 1) * P], en[:, g, HALVES[t]], ident)
        last.then_inc(even_pe, 1)
        featured("k", 0)
        featured("v", 0)
        wait_read(pe, CHUNK_B["v", 0])
        wait_read(pe, CHUNK_B["k", 0])
        pe.wait_ge(even_act, EVEN_ACT["keys"])
        for t in range(TT):
            for c in range(CH):
                cs = slice(c * CHUNK_T, (c + 1) * CHUNK_T)
                for g in range(GP):
                    last = mm(psum[2 * t + c][:, g * S:(g + 1) * S], konat[cs, (t * GP + g) * P:(t * GP + g + 1) * P],
                              gv[cs, t, g * S:(g + 1) * S], start=True, stop=True)
        last.then_inc(even_pe, 1)
        pe.wait_ge(even_dve, EVEN_DVE["states"])
        for t in range(TT):
            for g in range(GP):
                for c in range(CH):
                    if t or c:
                        mm(psum[6 + t][:, g * S:(g + 1) * S], qz[:, c, g, HALVES[t]], state[:, t * CH + c, g, :],
                           start=g == 0 and c == (0 if t else 1), stop=False)
                for e in range(2):
                    last = mm(psum[6 + t][:, g * S + e * GDV:g * S + (e + 1) * GDV], attn[:, e, t, g, :],
                              gv[:, t, g * S + e * GDV:g * S + (e + 1) * GDV], start=False, stop=g == GP - 1 and e == 1)
        last.then_inc(even_pe, 1)

        def by_act(step, t):
            pe.wait_ge(rw_act, TT * RW_ACT[step] - TT + t + 1)

        def by_dve(step, t):
            pe.wait_ge(rw_dve, TT * RW_DVE[step] - TT + t + 1)

        chunks = [slice(c * CHUNK_T, (c + 1) * CHUNK_T) for c in range(CH)]
        heads = [(e, f) for e in range(2) for f in range(FT)]
        for t in range(TT):
            by_dve("bonus", t)
            for f in range(FT):
                mm(psum[4 * t + 1][:, 2 * f:2 * f + 2], kt[:, f, HALVES[t]], rkind[:, f, :], start=True, stop=True)
            for f in range(FT):
                last = mm(psum[4 * t][:, f * P:(f + 1) * P], cst("same_head"), sq[:, f, HALVES[t]], start=True, stop=True)
            last.then_inc(rw_pe, 1)
        for t in range(TT):
            if t:
                pe.wait_ge(even_dve, EVEN_DVE["gla"])
            by_dve("tilde", t)
            for n, src in enumerate((ar[:, :, 0, HALVES[t]], bt[:, :, HALVES[t]], kt[:, :, HALVES[t]], rkv[:, 2, :, HALVES[t]])):
                for f in range(FT):
                    last = nc.tensor.transpose(psum[4 * t + n][:, f * P:(f + 1) * P], src[:, f, :], ident)
            last.then_inc(rw_pe, 1)
        for t in range(TT):
            by_act("nat", t)
            for n, src in enumerate((bt, kt)):
                for f in range(FT):
                    for c in range(CH):
                        at = slice(t * P + c * CHUNK_T, t * P + (c + 1) * CHUNK_T)
                        for e in range(2):
                            es = slice(e * RN, (e + 1) * RN)
                            last = mm(psum[4 * t + 2 * n + e][chunks[c], f * P:(f + 1) * P], src[es, f, at], ar[es, f, :, at], start=True, stop=True)
            last.then_inc(rw_pe, 1)
        for n in range(LEVELS):
            for t in range(TT):
                by_dve(f"d{n - 1}" if n else "lr", t)
                for e, f in heads:
                    hs = slice((e * FT + f) * CHUNK_T, (e * FT + f + 1) * CHUNK_T)
                    for cs in chunks:
                        last = mm(psum[4 * t][cs, hs], lrb[cs, t, e, f, 0, :], dd[cs, t, e, f, :], start=True, stop=True)
                last.then_inc(rw_pe, 1)
            for t in range(TT):
                if n == 0:
                    break
                by_dve(f"x{n}", t)
                for e, f in heads:
                    hs = slice((e * FT + f) * CHUNK_T, (e * FT + f + 1) * CHUNK_T)
                    for cs in chunks:
                        last = mm(psum[4 * t + 2][cs, hs], xx[cs, t, e, f, :], dt_[cs, t, e, f, :], start=True, stop=True)
                        if n < LEVELS - 1:
                            last = mm(psum[4 * t + 1][cs, hs], dt_[cs, t, e, f, :], xx[cs, t, e, f, :], start=True, stop=True)
                last.then_inc(rw_pe, 1)
        for t in range(TT):
            by_dve(f"d{LEVELS - 1}", t)
            for f in range(FT):
                for e in range(2):
                    hs, es = slice((2 * f + e) * RN, (2 * f + e + 1) * RN), slice(e * RN, (e + 1) * RN)
                    for c, cs in enumerate(chunks):
                        mm(psum[4 * t][cs, hs], lrk[cs, t, e, f, 0, :], nat["v"][cs, t, hs], start=True, stop=True)
                        last = mm(psum[4 * t + 2 + c][es, f * CHUNK_T:(f + 1) * CHUNK_T], nat["a"][cs, t, hs], dt_[cs, t, e, f, :],
                                  start=True, stop=True)
            last.then_inc(rw_pe, 1)
        for t in range(TT):
            by_act("z", t)
            for f in range(FT):
                for e in range(2):
                    hs = slice((2 * f + e) * RN, (2 * f + e + 1) * RN)
                    for cs in chunks:
                        last = mm(psum[4 * t + 1][cs, hs], dt_[cs, t, e, f, :], zz[cs, t, hs], start=True, stop=True)
            last.then_inc(rw_pe, 1)
        for t in range(TT):
            by_act("wv", t)
            for c, cs in enumerate(chunks):
                n = t * CH + c
                if n:
                    pe.wait_ge(chain_dve, 2 * n)
                at = slice(t * P + c * CHUNK_T, t * P + (c + 1) * CHUNK_T)
                for f in range(FT):
                    last = mm(psum[4 * t + c][cs, f * P:(f + 1) * P], tat[:, f, at], s_all[:, n, f, :], start=True, stop=True)
                last.then_inc(chain_pe, 1)
                pe.wait_ge(chain_dve, 2 * n + 1)
                for f in range(FT):
                    fs = slice(f * P, (f + 1) * P)
                    mm(psum[4 * t + 2 + c][:, fs], nat["b"][cs, t, fs], uu[cs, t, fs], start=f == 0, stop=False)
                    last = mm(psum[4 * t + 2 + c][:, fs], nat["k"][cs, t, fs], nat["v"][cs, t, fs], start=False, stop=f == FT - 1)
                last.then_inc(chain_pe, 1)
            for c, cs in enumerate(chunks):
                at = slice(t * P + c * CHUNK_T, t * P + (c + 1) * CHUNK_T)
                for f in range(FT):
                    mm(psum[4 * t][cs, f * P:(f + 1) * P], ar[:, f, 1, at], s_all[:, t * CH + c, f, :], start=f == 0, stop=False)
                    for e in range(2):
                        hs = slice((2 * f + e) * RN, (2 * f + e + 1) * RN)
                        mm(psum[4 * t][cs, hs], lrb[cs, t, e, f, 1, :], uu[cs, t, hs], start=False, stop=False)
                        last = mm(psum[4 * t][cs, hs], lrk[cs, t, e, f, 1, :], nat["v"][cs, t, hs], start=False, stop=f == FT - 1 and e == 1)
            last.then_inc(rw_pe, 1)
        by_dve("out", TT - 1)
        transposes(ymix)
        natural("eout", 0, split=4)
        natural("eout", 1, half=half_done)

        def peer_layer(layer, split):
            transposes(x, 2 * layer)
            featured(f"pq{layer}", 0, split=split)
            featured(f"pq{layer}", 1)
            pe.wait_ge(keys_loaded, 16 * (layer + 1))
            wait_read(pe, CHUNK_B[f"pq{layer}", 1])
            for t in range(TT):
                for h in range(PH):
                    last = mm(psum[4 * (1 - t) + h // 2][:, (h % 2) * 2 * KEYS:(h % 2 + 1) * 2 * KEYS], pq[:, h, HALVES[t]], keys_sb[:, h, :],
                              start=True, stop=True)
                last.then_inc(s_done, 1)
            pe.wait_ge(s_read, 2 * layer + 1)
            for part in range(2):
                done = 2 * layer + part
                first, g0 = PAIRS * done, GROUPS * layer
                tile = base + PEER_UV[layer] + 2 * PAIRS * part

                def hidden(n, p):
                    k = tile + p
                    pe.wait_ge(lo_ready, n * 2 + (k + 1))
                    if first or p > 1 or not isinstance(n, int):
                        pe.wait_ge(gelu_ready, n * 2 + (first + p - 1))
                    for jj in range(2):
                        dst = psum[4 + p % 2][:, jj * S:(jj + 1) * S]
                        for kk_ in range(KD):
                            ws = slice((2 * kk_ + jj) * P, (2 * kk_ + jj + 1) * P)
                            mm(dst, w_hi[:, k % SPLIT, ws], act_hi[:, kk_, :], start=kk_ == 0 and jj == 0, stop=False)
                            mm(dst, w_hi[:, k % SPLIT, ws], act_lo[:, kk_, :], start=False, stop=False)
                            last = mm(dst, w_lo[:, k % SPLIT, ws], act_hi[:, kk_, :], start=False, stop=kk_ == KD - 1 and jj == 1)
                    last.then_inc(tile_used, 1)

                def gates(n, b):
                    pe.wait_ge(hot_ready, n * HOT + (g0 + b + 1))
                    if g0 or not isinstance(n, int):
                        pe.wait_ge(gates_read, n * HOT + (g0 + b + 1 - HOT))
                    for i in range(GT):
                        last = mm(psum[4 + b][:, i * KEYS:(i + 1) * KEYS], hot_i[:, b, i, :], hot_j[:, b, i, :], start=True, stop=True)
                    last.then_inc(gates_done, 1)

                def output(n, p, begin=False, end=False):
                    k = tile + PAIRS + p
                    pe.wait_ge(lo_ready, n * 2 + (k + 1))
                    pe.wait_ge(c_lo_ready, n * 2 + (first + p + 1))
                    for t in range(TT):
                        for jj in range(2):
                            cs = slice(jj * S + t * P, jj * S + (t + 1) * P)
                            for c in range(2):
                                dst, ws = psum[2 * t + c][:, :], slice(jj * D + c * CW, jj * D + (c + 1) * CW)
                                mm(dst, c_hi[:, p % 2, cs], w_hi[:, k % SPLIT, ws], start=begin and jj == 0, stop=False)
                                mm(dst, c_hi[:, p % 2, cs], w_lo[:, k % SPLIT, ws], start=False, stop=False)
                                last = mm(dst, c_lo[:, p % 2, cs], w_hi[:, k % SPLIT, ws], start=False, stop=end and jj == 1)
                        if end and t == 0:
                            last.then_inc(half_done, 1)
                    last.then_inc(tile_used, 1)

                hidden(0, 0)
                hidden(0, 1)
                with pe.Fori(1, PAIRS // 2) as q:
                    hidden(q, 0)
                    hidden(q, 1)
                if part == 0:
                    for t in range(TT):
                        pe.wait_ge(sel_ready, 2 * layer + t + 1)
                        for n in range(3):
                            last = nc.tensor.transpose(psum[6 + t][:, n * P:(n + 1) * P], sel[:, t, n, :], ident)
                        last.then_inc(sel_t, 1)
                    pe.wait_ge(ijg_ready, 2 * layer + 2)
                    pe.wait_ge(gelu_ready, first + PAIRS)
                    for b in range(HOT):
                        gates(0, b)
                    with pe.Fori(1, GROUPS // HOT) as n:
                        for b in range(HOT):
                            gates(n, b)
                if part == 0:
                    pe.wait_ge(s_read, 2 * layer + 2)
                output(0, 0, begin=part == 0)
                output(0, 1)
                with pe.Fori(1, PAIRS // 2 - 1) as q:
                    output(q, 0)
                    output(q, 1)
                output(0, PAIRS - 2)
                output(0, PAIRS - 1, end=part == 1)

        peer_layer(0, 8)

        transposes(x, 1)
        natural("oqi", 0, split=12)
        natural("okv", 0)
        natural("oq", 0, (0,))
        pe.wait_ge(odd_dve, ODD_DVE["turned"])
        for h in range(IH // 2):
            for t in range(TT):
                last = nc.tensor.transpose(psum[4 + h // 2][:, (h % 2) * S + t * P:(h % 2) * S + (t + 1) * P],
                                           qin_[:, t, h * P:(h + 1) * P], ident)
        for n, src in enumerate((kn, kid)):
            for t in range(TT):
                last = nc.tensor.transpose(psum[6 + n][:, t * P:(t + 1) * P], src[:, t, :], ident)
        last.then_inc(odd_pe, 1)
        natural("oq", 0, (1,))
        pe.wait_ge(odd_act, ODD_ACT["it"])
        pe.wait_ge(odd_dve, ODD_DVE["kib"])
        for t in range(TT):
            if t:
                natural("oq", 1, (0,))
                pe.wait_ge(odd_act, ODD_ACT["index0"])
            for h in range(IH // 2):
                last = mm(psum[4 + h][:, :], qi_t[:, h, HALVES[t]], kib[:, :], start=True, stop=True)
            last.then_inc(odd_pe, 1)
        natural("oq", 1, (1,))
        pe.wait_ge(odd_dve, ODD_DVE["rope"])
        for h in range(AH):
            for t in range(TT):
                last = nc.tensor.transpose(psum[h // 2][:, (h % 2) * S + t * P:(h % 2) * S + (t + 1) * P],
                                           qn[:, t, h * AD:(h + 1) * AD], ident)
        last.then_inc(odd_pe, 1)
        for t in range(TT):
            n = (t + 1) * P
            if t == 0:
                pe.wait_ge(odd_act, ODD_ACT["qt"])
            else:
                pe.wait_ge(att_lo, 1)
            for h in range(AH):
                last = mm(psum[h // 2][:, (h % 2) * S:(h % 2) * S + n], q_t[:, h, HALVES[t]], k_t[:, 0:n], start=True, stop=True)
            last.then_inc(odd_pe, 1)
            pe.wait_ge(odd_dve, ODD_DVE[f"probs{t}"])
            for h in range(AH):
                for s in range(t + 1):
                    last = nc.tensor.transpose(psum[4 + h // 2][:, ((h % 2) * TT + s) * P:((h % 2) * TT + s + 1) * P],
                                               logit[:, h, HALVES[s]], ident)
            last.then_inc(odd_pe, 1)
            pe.wait_ge(odd_act, ODD_ACT[f"pt{t}"])
            for hh in range(2):
                for s in range(t + 1):
                    last = mm(psum[hh][:, :], vn[:, s, :], pt[:, 4 * hh:4 * hh + 4, s, :], start=s == 0, stop=s == t)
            last.then_inc(odd_pe, 1)
        pe.wait_ge(att_lo, TT)
        natural("oout", 0)
        natural("oout", 1, half=half_done)
        peer_layer(1, 16)

    @block.scalar
    def _(act):
        do = Order(act, act_own)

        def split_hi(k):
            if k < total:
                act.wait_ge(raw_loaded[k % RAW], 16 * (k // RAW + 1))
                act.wait_ge(tile_used, k - 1)
                A.activation(w_hi[:, k % SPLIT, :], raw[:, k % RAW, :], ACT.Copy).then_inc(hi_ready, 1)

        def stream(name, i, tiles=(0, 1)):
            for j in tiles:
                split_hi(base + TILE_B[name, i] + j + SPLIT)

        def taken(name, i):
            act.wait_ge(tile_used, base + TILE_B[name, i] + 2)

        def bank(name, i, t):
            return psum[2 * (CHUNK_B[name, i] % 2) + t]

        def split_t(first):
            for b in range(KD // 2):
                act.wait_ge(tr_done, first + b + 1)
                do(A.activation(act_hi[:, 2 * b:2 * b + 2, :].rearrange("p k s -> p (k s)"), psum[4 + b][:, :], ACT.Copy), tr_hi)

        def layer_norm(n):
            for t in range(TT):
                act.wait_ge(ln_var, TT * n + t + 1)
                do(A.activation(small[:, 32 + t:33 + t], small[:, 25 + 2 * t:26 + 2 * t], ACT.Sqrt, bias=cst("ln_eps")), ln_std)

        def ecolumn(name, i):
            return ecol[:, ECOL[name] + i:ECOL[name] + i + 1]

        split_t(0)
        stream("gqk", 0, (0,))
        act.wait_ge(side_loaded, 16)
        do(A.activation(side_hi[:, :, :].rearrange("p k n -> p (k n)"), side_raw[:, :, :].rearrange("p k n -> p (k n)"), ACT.Copy),
           side_hi_ready)
        stream("gqk", 0, (1,))
        taken("gqk", 0)
        for t in range(2):
            do(A.activation(gqk[:, 2 * t:2 * t + 2, :].rearrange("p f s -> p (f s)"), bank("gqk", 0, t)[:, :], ACT.Copy),
               read_act if t else None)
        act.wait_ge(b_const, 16)
        act.wait_ge(even_loaded, 48)
        act.wait_ge(even_pe, EVEN_PE["side"])
        do(A.activation(sh[:, 0:2, 1:], psum[4][:, :].rearrange("p (g s) -> p g s", g=2), ACT.Copy), even_act)
        act.wait_ge(even_dve, EVEN_DVE["side"])
        do(A.activation(side_t[W2[0], 0, :], side_t[W2[0], 0, :], ACT.Tanh))
        do(A.activation(side_t[G2[0], 0, :], side_t[G2[0], 0, :], ACT.Sigmoid), even_act)
        stream("gv", 0)
        act.wait_ge(even_pe, EVEN_PE["la"])
        for g in range(GP):
            do(A.activation(lb[:, g, :], psum[5][:, g * S:(g + 1) * S], ACT.Abs, bias=ecolumn("gla_a_b", g)))
        do(A.activation(lb[:, :, :], lb[:, :, :], ACT.Exp, scale=-1.0))
        do(A.activation(lb[:, :, :], lb[:, :, :], ACT.Ln, bias=cst("one")), even_act)
        act.wait_ge(even_pe, EVEN_PE["w"])
        for f in range(FT):
            do(A.activation(sgw[:, f, :], psum[6 + f // 2][:, (f % 2) * S:(f % 2 + 1) * S], ACT.Sigmoid, bias=ecolumn("w0", f)),
               even_act if f == FT - 1 else None)
        taken("gv", 0)
        for t in range(TT):
            do(A.activation(gv[:, t, :], bank("gv", 0, t)[:, :], ACT.Copy), read_act if t else None)
        stream("gg", 0)
        taken("gg", 0)
        for t in range(TT):
            do(A.activation(gsil[:, t, :], bank("gg", 0, t)[:, :], ACT.Silu), read_act if t else None)
        act.wait_ge(even_pe, EVEN_PE["g"])
        for f in range(FT):
            do(A.activation(asig[:, f, :], psum[4 + f // 2][:, (f % 2) * S:(f % 2 + 1) * S], ACT.Sigmoid, bias=ecolumn("a0", f)))
        for t in range(TT):
            do(A.activation(gnat[:, t, :], psum[6 + t][:, :], ACT.Copy), even_act if t else None)
        act.wait_ge(even_dve, EVEN_DVE["cumsum"])
        do(A.activation(eb[:, :, :], la[:, :, :], ACT.Exp, scale=1.0 / 16))
        do(A.activation(kin[:, :, :], la[:, :, :], ACT.Exp, scale=-1.0 / 16))
        do(A.activation(en[:, :, :], lb[:, :, :], ACT.Exp, scale=-1.0 / 16), even_act)
        for n, name in enumerate("rkv"):
            stream(name, 0)
            taken(name, 0)
            if n:
                act.wait_ge(shifted_done, n)
            for t in range(2):
                do(A.activation(sh[:, 2 * t:2 * t + 2, 1:], bank(name, 0, t)[:, :].rearrange("p (f s) -> p f s", f=2), ACT.Copy),
                   read_act if t else None)
            if n == 0:
                act.wait_ge(even_pe, EVEN_PE["keys"])
                do(A.activation(konat[:, :], psum[6][:, :], ACT.Copy), even_act)
        act.wait_ge(even_pe, EVEN_PE["o"])
        for t in range(TT):
            for h in range(GH):
                ins = A.activation(en[:, 0, 0:GDV], psum[6 + t][:, h * GDV:(h + 1) * GDV], ACT.Square, accum_out=small[:, t * GH + h:t * GH + h + 1])
                do(ins, even_act if t == TT - 1 and h == GH - 1 else None)
        do(A.activation(small[:, 8:16], small[:, 0:8], ACT.Sqrt, scale=1.0 / GDV, bias=cst("ln_eps")), even_act)
        def by_pe(step, t):
            act.wait_ge(rw_pe, TT * RW_PE[step] - TT + t + 1)

        def by_dve(step, t):
            act.wait_ge(rw_dve, TT * RW_DVE[step] - TT + t + 1)

        for t in range(TT):
            by_dve("cumsum", t)
            ts = HALVES[t]
            do(A.activation(pinc[:, :, ts], cw[:, :, ts], ACT.Exp))
            do(A.activation(pinv[:, :, ts], cw[:, :, ts], ACT.Exp, scale=-1.0))
            do(A.activation(pm[:, :, ts], pm[:, :, ts], ACT.Exp), rw_act)
        for t in range(TT):
            by_pe("bonus", t)
            do(A.activation(norm[:, t, :], psum[4 * t][:, :], ACT.Sqrt), rw_act)
        by_dve("tilde", TT - 1)
        for t in range(TT):
            by_pe("nat", t)
            for n, name in enumerate("abkv"):
                do(A.activation(nat[name][:, t, :], psum[4 * t + n][:, :], ACT.Copy), rw_act if n == 3 else None)
        for t in range(TT):
            by_pe("z", t)
            if t == 0:
                by_dve(f"d{LEVELS - 1}", TT - 1)
            do(A.activation(zz[:, t, :], psum[4 * t][:, :], ACT.Copy))
            for c in range(CH):
                at = slice(t * P + c * CHUNK_T, t * P + (c + 1) * CHUNK_T)
                do(A.activation(tat[:, :, at], psum[4 * t + 2 + c][:, 0:FT * CHUNK_T].rearrange("p (f s) -> p f s", f=FT), ACT.Copy),
                   rw_act if c == CH - 1 else None)
        for t in range(TT):
            by_pe("wv", t)
            do(A.activation(wv[:, t, :], psum[4 * t + 1][:, :], ACT.Copy), rw_act)
        for t in range(TT):
            by_dve("stats", t)
            do(A.activation(small[:, 8 * t:8 * t + 8], rstat[:, t, :, 1], ACT.Sqrt, bias=cst("lnx_eps")), rw_act)
        split_t(4)
        stream("eout", 0)
        stream("eout", 1, (0,))
        layer_norm(0)

        def peer_layer(layer, t0):
            split_t(t0)
            split_hi(base + PEER_Q[layer] + 1)
            for i in range(2):
                stream(f"pq{layer}", i)
                taken(f"pq{layer}", i)
                for t in range(2):
                    do(A.activation(pq[:, 4 * i + 2 * t:4 * i + 2 * t + 2, :].rearrange("p f s -> p (f s)"), bank(f"pq{layer}", i, t)[:, :], ACT.Copy),
                       read_act if t else None)
            for t in range(TT):
                act.wait_ge(s_done, 2 * layer + t + 1)
                for b in range(4):
                    do(A.activation(ss[t][:, 4 * b:4 * b + 4, :].rearrange("p f s -> p (f s)"), psum[4 * (1 - t) + b][:, :], ACT.Copy),
                       s_read if b == 3 else None)
            for part in range(2):
                done = 2 * layer + part
                first = PAIRS * done
                tile = base + PEER_UV[layer] + 2 * PAIRS * part

                def split_tile(n, k):
                    kt_ = tile + k
                    if kt_ >= total:
                        return
                    act.wait_ge(raw_loaded[kt_ % RAW], n * 16 + 16 * (kt_ // RAW + 1))
                    act.wait_ge(tile_used, n * RAW + (kt_ - 1))
                    A.activation(w_hi[:, kt_ % SPLIT, :], raw[:, kt_ % RAW, :], ACT.Copy).then_inc(hi_ready, 1)

                def padded(wait, n):
                    act.wait_ge(wait, n)
                    act.sem_inc(act_pad, 1)

                def pair(ap, n, p):
                    return ap[:, 2 * p:2 * p + 2, :] if isinstance(n, int) else ap[:, bass.ds(n * 2 * RAW + 2 * p, 2), :]

                def gelu(n, p):
                    padded(tile_used, n * RAW + (tile + p + 1))
                    A.activation(pair(hid, n, p), psum[4 + p % 2][:, :].rearrange("p (j s) -> p j s", j=2), ACT.Gelu).then_inc(gelu_ready, 1)

                def upper(n, p):
                    padded(tile_used, n * RAW + (tile + PAIRS + p - 1))
                    A.activation(c_hi[:, p % 2, :].rearrange("p (j s) -> p j s", j=2), pair(hid, n, p), ACT.Copy).then_inc(c_hi_ready, 1)

                if first:
                    act.wait_ge(c_lo_ready, first)
                with act.Fori(0, PAIRS // RAW) as n:
                    for p in range(RAW):
                        split_tile(n, p + 2)
                        gelu(n, p)
                if part == 0:
                    act.wait_ge(best_ready, layer + 1)
                    do(A.activation(best[:, :, :, :], best[:, :, :, :], ACT.Exp), exp_ready)
                    for t in range(TT):
                        act.wait_ge(sel_t, 2 * layer + t + 1)
                        do(A.activation(ijg[:, :, HALVES[t]], psum[6 + t][:, 0:3 * P].rearrange("p (n s) -> p n s", n=3), ACT.Copy), ijg_ready)
                g0 = GROUPS * layer

                def stage(n, b):
                    act.wait_ge(gates_done, n * HOT + (g0 + b + 1))
                    if not isinstance(n, int):
                        act.wait_ge(gated_odd if b % 2 else gated_even, n * (HOT // 2) + (g0 // 2 + b // 2 + 1 - HOT // 2))
                        act.wait_ge(spilled[b], n * 16 + 16 * (GROUPS // HOT) * layer)
                    A.activation(staged[:, b, :, :, :].rearrange("p h t j -> p t h j"), psum[4 + b][:, :].rearrange("p (t h j) -> p t h j", t=GT, h=2),
                                 ACT.Copy).then_inc(gates_read, 1)

                if part == 0:
                    for b in range(HOT):
                        stage(0, b)
                    with act.Fori(1, GROUPS // HOT) as n:
                        for b in range(HOT):
                            stage(n, b)
                if part == 0:
                    act.wait_ge(gated_odd, GROUPS // 2 * (layer + 1))
                    act.wait_ge(gated_even, GROUPS // 2 * (layer + 1))
                else:
                    act.wait_ge(regated_pool, RELOAD // HOT * REGATED * (layer + 1))
                    act.wait_ge(regated_dve, (RELOAD - RELOAD // HOT) * REGATED * (layer + 1))
                if part == 0:
                    for b in range(HOT):
                        act.wait_ge(spilled[b], 16 * (GROUPS // HOT) * (layer + 1))
                upper(0, 0)
                upper(0, 1)
                with act.Fori(0, PAIRS // RAW - 1) as n:
                    for p in range(RAW):
                        split_tile(n, PAIRS + p + 2)
                        upper(n, p + 2)
                for p in range(PAIRS - RAW, PAIRS):
                    if part == 0 or p < PAIRS - 1:
                        split_tile(0, PAIRS + p + 2)
                    if p + 2 < PAIRS:
                        upper(0, p + 2)

        peer_layer(0, 8)
        layer_norm(1)
        split_t(12)
        split_hi(base + ODD + 1)
        stream("oqi", 0)
        stream("okv", 0)
        stream("oq", 0, (0,))
        act.wait_ge(odd_pe, ODD_PE["it"])
        for b in range(2):
            do(A.activation(qi_t[:, 2 * b:2 * b + 2, :].rearrange("p h s -> p (h s)"), psum[4 + b][:, :], ACT.Copy))
        do(A.activation(k_t[:, :], psum[6][:, 0:S], ACT.Copy), odd_act)
        stream("oq", 0, (1,))
        for t in range(TT):
            act.wait_ge(odd_pe, ODD_PE[f"index{t}"])
            for h in range(IH // 2):
                do(A.activation(rel[:, t, 2 * h:2 * h + 2, :].rearrange("p h s -> p (h s)"), psum[4 + h][:, :], ACT.Relu),
                   odd_act if h == IH // 2 - 1 else None)
            stream("oq", 1, (t,))
        act.wait_ge(odd_pe, ODD_PE["qt"])
        for b in range(4):
            do(A.activation(q_t[:, 2 * b:2 * b + 2, :].rearrange("p h s -> p (h s)"), psum[b][:, :], ACT.Copy), odd_act if b == 3 else None)
        for t in range(TT):
            n = (t + 1) * P
            act.wait_ge(odd_dve, ODD_DVE[f"logits{t}"])
            for h in range(AH):
                do(A.activation(logit[:, h, 0:n], logit[:, h, 0:n], ACT.Exp, bias=amax[:, h:h + 1], accum_out=asum[:, h:h + 1]),
                   odd_act if h == AH - 1 else None)
            act.wait_ge(odd_pe, ODD_PE[f"pt{t}"])
            for b in range(4):
                for s in range(t + 1):
                    do(A.activation(pt[:, 2 * b:2 * b + 2, s, :], psum[4 + b][:, :].rearrange("p (h s k) -> p h s k", h=2, s=TT)[:, :, s, :], ACT.Copy),
                       odd_act if b == 3 and s == t else None)
            act.wait_ge(odd_pe, ODD_PE[f"o{t}"])
            for hh in range(2):
                do(A.activation(act_hi[:, 4 * hh:4 * hh + 4, HALVES[t]], psum[hh][:, :].rearrange("p (h s) -> p h s", h=4), ACT.Copy),
                   att_hi if hh else None)
        stream("oout", 0)
        stream("oout", 1, (0,))
        layer_norm(2)
        peer_layer(1, 16)
        layer_norm(3)

    @block.vector
    def _(dve):
        do = Order(dve, dve_own)

        def bcast(ap, shape):
            return ap.broadcast_to(shape)

        def split_lo(k):
            if k < total:
                dve.wait_ge(hi_ready, k + 1)
                V.tensor_tensor(w_lo[:, k % SPLIT, :], raw[:, k % RAW, :], w_hi[:, k % SPLIT, :].bitcast(F32), ALU.subtract).then_inc(lo_ready, 1)

        def stream(name, i, tiles=(0, 1)):
            for j in tiles:
                split_lo(base + TILE_B[name, i] + j + SPLIT)

        def taken(name, i):
            dve.wait_ge(tile_used, base + TILE_B[name, i] + 2)

        def bank(name, i, t):
            return psum[2 * (CHUNK_B[name, i] % 2) + t]

        def split_t(first):
            for b in range(KD // 2):
                dve.wait_ge(tr_hi, first + b + 1)
                ks = slice(2 * b, 2 * b + 2)
                do(V.tensor_tensor(act_lo[:, ks, :].rearrange("p k s -> p (k s)"), psum[4 + b][:, :],
                                   act_hi[:, ks, :].rearrange("p k s -> p (k s)").bitcast(F32), ALU.subtract), tr_lo)

        def residual(t, n, src, signal=None):
            xs = x[:, t, n * CW:(n + 1) * CW]
            do(V.scalar_tensor_tensor(out=xs, in0=xs, scalar=ALPHA, in1=src, op0=ALU.mult, op1=ALU.add), signal)
            do.also(V.bn_stats(small[:, 40 + 12 * t + 6 * n:46 + 12 * t + 6 * n], xs))

        def layer_norm(n, done, inputs):
            dve.wait_ge(ln_loaded, 32 * (n + 1))
            for t in range(TT):
                if t == 0:
                    dve.wait_ge(half_done, n + 1)
                else:
                    dve.wait_ge(tile_used, done)
                inputs(t)
                do.settle()
                st = small[:, 40 + 12 * t:52 + 12 * t].rearrange("p (c k) -> p c k", c=2)
                do(V.bn_aggr(small[:, 24 + 2 * t:26 + 2 * t], st), ln_var)
                do.also(V.scalar_tensor_tensor(out=x[:, t, :], in0=x[:, t, :], scalar=small[:, 24 + 2 * t:25 + 2 * t], in1=ln_row[:, 0, :],
                                               op0=ALU.subtract, op1=ALU.mult))
                dve.wait_ge(ln_std, TT * n + t + 1)
                do.also(V.reciprocal(small[:, 34 + t:35 + t], small[:, 32 + t:33 + t]))
                do.settle()
                do(V.scalar_tensor_tensor(out=x[:, t, :], in0=x[:, t, :], scalar=small[:, 34 + t:35 + t], in1=ln_row[:, 1, :],
                                          op0=ALU.mult, op1=ALU.add), x_ready)

        def ecolumn(name, i):
            return ecol[:, ECOL[name] + i:ECOL[name] + i + 1]

        split_t(0)
        stream("gqk", 0, (0,))
        dve.wait_ge(side_hi_ready, 1)
        do(V.tensor_tensor(side_lo[:, :, :].rearrange("p k n -> p (k n)"), side_raw[:, :, :].rearrange("p k n -> p (k n)"),
                           side_hi[:, :, :].rearrange("p k n -> p (k n)").bitcast(F32), ALU.subtract), side_lo_ready)
        stream("gqk", 0, (1,))
        do(V.memset(sh[:, :, 0:1], 0.0))
        dve.wait_ge(b_const, 16)
        dve.wait_ge(even_loaded, 48)

        def shift(dst, n, mu, signal):
            do(V.tensor_tensor(dif[:, 0:n, :], sh[:, 0:n, 0:S], sh[:, 0:n, 1:], ALU.subtract))
            for f in range(n):
                do(V.scalar_tensor_tensor(out=dst(f), in0=dif[:, f, :], scalar=mu(f), in1=sh[:, f, 1:], op0=ALU.mult, op1=ALU.add),
                   signal if f == n - 1 else None)

        dve.wait_ge(even_act, EVEN_ACT["side"])
        shift(lambda f: side_t[:, f, :], 2, lambda f: ecolumn("mu_side", f), even_dve)
        stream("gv", 0)
        dve.wait_ge(even_act, EVEN_ACT["lnexp"])
        for g in range(GP):
            do(V.tensor_scalar(la[:, g, :], psum[5][:, g * S:(g + 1) * S], ecolumn("gla_a_b", g), 0.0, ALU.add, ALU.min))
        do(V.tensor_tensor(la[:, :, :], la[:, :, :], lb[:, :, :], ALU.subtract), even_dve)
        for g in range(GP):
            do(V.tensor_tensor_scan(qin[:, g, :], cst("keep"), la[:, g, :], 0.0, ALU.mult, ALU.add))
        do(V.tensor_copy(la[:, :, :], qin[:, :, :]))
        for g in range(GP):
            sums = la[:, g, :].rearrange("p (c s) -> p c s", s=CHUNK_T)
            do(V.tensor_tensor(lb[:, g, :].rearrange("p (c s) -> p c s", s=CHUNK_T), sums,
                               bcast(sums[:, :, CHUNK_T - 1:CHUNK_T], [P, CH * TT, CHUNK_T]), ALU.subtract), even_dve if g else None)
        stream("gg", 0)
        dve.wait_ge(even_act, EVEN_ACT["decays"])
        do(V.scalar_tensor_tensor(out=qin[:, :, :], in0=gqk[:, 0:2, :], scalar=GDK ** -0.5, in1=eb[:, :, :], op0=ALU.mult, op1=ALU.mult))
        do(V.tensor_tensor(kin[:, :, :], kin[:, :, :], gqk[:, 2:4, :], ALU.mult))
        do(V.memset(qz[:, :, :, :], 0.0))
        for c in range(CH):
            for g in range(GP):
                cut = lambda ap: ap.rearrange("p (t c s) -> p t c s", c=CH, s=CHUNK_T)[:, :, c, :]
                do(V.tensor_copy(cut(qz[:, c, g, :]), cut(qin[:, g, :])))
        do(V.tensor_tensor(en[:, :, :], en[:, :, :], gqk[:, 2:4, :], ALU.mult), even_dve)
        for n, name in enumerate("rkv"):
            stream(name, 0)
            wait_read(dve, CHUNK_B[name, 0])
            shift(lambda f: rkv[:, n, f, :], FT, lambda f: ecolumn("mu", FT * n + f), shifted_done)
            if n == 0:
                upto = cst("upto")
                dve.wait_ge(even_pe, EVEN_PE["keys"])
                for e in range(2):
                    do(V.tensor_tensor(attn[:, e, :, :, :].rearrange("p t g s -> p (t g) s"), psum[4 + e][:, :].rearrange("p (n s) -> p n s", n=TT * GP),
                                       bcast(upto.unsqueeze(1), [P, TT * GP, P]), ALU.mult), even_dve if e else None)
        dve.wait_ge(even_pe, EVEN_PE["kv"])
        for c in range(CH * TT - 1):
            for g in range(GP):
                do(V.tensor_tensor(state[:, c + 1, g, :], psum[c][:, g * S:(g + 1) * S], cst("diag2"), ALU.mult))
                if c:
                    do(V.scalar_tensor_tensor(out=state[:, c + 1, g, :], in0=state[:, c, g, :], scalar=eb[:, g, (c + 1) * CHUNK_T - 1:(c + 1) * CHUNK_T],
                                              in1=state[:, c + 1, g, :], op0=ALU.mult, op1=ALU.add),
                       even_dve if c == CH * TT - 2 and g == GP - 1 else None)
        flat = lambda ap: ap.rearrange("p f s -> p (f s)")
        do(V.memset(s_all[:, 0, :, :], 0.0))
        for f in range(FT):
            do(V.tensor_scalar(rkind[:, f, :], cst("half"), ecolumn("r_k", f), None, ALU.mult))

        def by_act(step, t):
            dve.wait_ge(rw_act, TT * RW_ACT[step] - TT + t + 1)

        def by_pe(step, t):
            dve.wait_ge(rw_pe, TT * RW_PE[step] - TT + t + 1)

        r, k = rkv[:, 0, :, :], rkv[:, 1, :, :]
        for t in range(TT):
            ts = HALVES[t]
            do(V.tensor_scalar(sgw[:, :, ts], sgw[:, :, ts], -float(np.exp(-0.5)), None, ALU.mult))
            for f in range(FT):
                do.also(V.tensor_tensor_scan(cw[:, f, ts], cst("keep")[:, 0:P], sgw[:, f, ts], 0.0, ALU.mult, ALU.add))
            do.settle()
            do(V.tensor_tensor(pm[:, :, ts], cw[:, :, ts], sgw[:, :, ts], ALU.subtract), rw_dve)
        for t in range(TT):
            ts = HALVES[t]
            for f in range(FT):
                do.also(V.tensor_scalar(kk[:, f, ts], k[:, f, ts], ecolumn("k_k", f), None, ALU.mult))
                do.also(V.tensor_scalar(kp[:, f, ts], asig[:, f, ts], -1.0, ecolumn("k_a", f), ALU.add, ALU.mult))
            do.settle()
            do.also(V.tensor_tensor(sq[:, :, ts], kk[:, :, ts], kk[:, :, ts], ALU.mult))
            do(V.scalar_tensor_tensor(out=kp[:, :, ts], in0=kp[:, :, ts], scalar=1.0, in1=k[:, :, ts], op0=ALU.add, op1=ALU.mult))
            do(V.tensor_tensor(kt[:, :, ts], r[:, :, ts], kp[:, :, ts], ALU.mult), rw_dve)
        def gla_out():
            dve.wait_ge(even_act, EVEN_ACT["std"])
            do(V.reciprocal(small[:, 8:16], small[:, 8:16]))
            for t in range(TT):
                for h in range(GH):
                    hs = slice(h * GDV, (h + 1) * GDV)
                    do(V.scalar_tensor_tensor(out=ymix[:, t, hs], in0=psum[6 + t][:, hs], scalar=small[:, 8 + t * GH + h:9 + t * GH + h],
                                              in1=erow[:, EROW["gla_g"]], op0=ALU.mult, op1=ALU.mult))
                do(V.tensor_tensor(ymix[:, t, 0:EW], ymix[:, t, 0:EW], gsil[:, t, :], ALU.mult), even_dve if t else None)

        for t in range(TT):
            ts = HALVES[t]
            if t:
                gla_out()
            by_act("decays", t)
            do.also(V.tensor_tensor(ar[:, :, 1, ts], r[:, :, ts], pinc[:, :, ts], ALU.mult))
            by_act("norm", t)
            do.also(V.tensor_copy(bonus[:, t, :], psum[4 * t + 1][:, 0:RH]))
            n0 = norm[:, t, :]
            do(V.tensor_scalar(n0, n0, 1e-12, None, ALU.max))
            do(V.reciprocal(n0, n0))
            do(V.tensor_tensor(kk[:, :, ts], kk[:, :, ts], n0.rearrange("p (f s) -> p f s", f=FT), ALU.mult))
            do.also(V.scalar_tensor_tensor(out=ar[:, :, 0, ts], in0=kk[:, :, ts], scalar=-1.0, in1=pm[:, :, ts], op0=ALU.mult, op1=ALU.mult))
            do(V.tensor_tensor(bt[:, :, ts], kk[:, :, ts], asig[:, :, ts], ALU.mult))
            do.also(V.tensor_tensor(bt[:, :, ts], bt[:, :, ts], pinv[:, :, ts], ALU.mult))
            do.settle()
            do(V.tensor_tensor(kt[:, :, ts], kp[:, :, ts], pinv[:, :, ts], ALU.mult), rw_dve)
        eye = cst("eye64")
        for t in range(TT):
            for buf in (dd, dt_):
                do.also(V.tensor_copy(buf[:, t, :, :, :].rearrange("p e f s -> p (e f) s"), bcast(eye.unsqueeze(1), [P, RH, CHUNK_T])))
        do.settle()
        for t in range(TT):
            by_pe("lr", t)
            for n, dst in enumerate((lrb, lrk)):
                for e in range(2):
                    ins = V.tensor_tensor(dst[:, t, e, :, :, :].rearrange("p f a s -> p f (a s)"), psum[4 * t + 2 * n + e][:, :].rearrange("p (f s) -> p f s", f=FT),
                                          bcast(cst("strict_upto").unsqueeze(1), [P, FT, P]), ALU.mult)
                    do.also(ins) if n == 0 or e == 0 else do(ins, rw_dve)
        for n in range(LEVELS):
            level = cst("levels")[:, n * CHUNK_T:(n + 1) * CHUNK_T]
            for t in range(TT):
                by_pe(f"x{n}", t)
                do(V.tensor_tensor(xx[:, t, :, :, :].rearrange("p e f s -> p (e f) s"), psum[4 * t][:, :].rearrange("p (h s) -> p h s", h=RH),
                                   bcast(level.unsqueeze(1), [P, RH, CHUNK_T]), ALU.mult), rw_dve)
            for t in range(TT):
                all_of = lambda buf: buf[:, t, :, :, :].rearrange("p e f s -> p (e f s)")
                if n == 0:
                    do(V.tensor_tensor(all_of(dd), all_of(dd), all_of(xx), ALU.add))
                    first = lrb[:, t, :, :, 0, :].rearrange("p e f s -> p (e f) s")
                    heads_of = dt_[:, t, :, :, :].rearrange("p e f s -> p (e f) s")
                    do(V.tensor_tensor(all_of(xx).rearrange("p (h s) -> p h s", h=RH), first, bcast(cst("level0_t").unsqueeze(1), [P, RH, CHUNK_T]), ALU.mult))
                    do(V.tensor_tensor(heads_of, heads_of, all_of(xx).rearrange("p (h s) -> p h s", h=RH), ALU.add), rw_dve)
                    continue
                by_pe(f"d{n}", t)
                if n < LEVELS - 1:
                    do.also(V.tensor_tensor(all_of(dd), all_of(dd), psum[4 * t + 1][:, :], ALU.add))
                do(V.tensor_tensor(all_of(dt_), all_of(dt_), psum[4 * t + 2][:, :], ALU.add), rw_dve)
        do.settle()
        for t in range(TT):
            by_act("wv", t)
            for c in range(CH):
                n = t * CH + c
                cs = slice(c * CHUNK_T, (c + 1) * CHUNK_T)
                dve.wait_ge(chain_pe, 2 * n + 1)
                do(V.tensor_tensor(uu[cs, t, :], psum[4 * t + c][cs, :], wv[cs, t, :], ALU.add), chain_dve)
                dve.wait_ge(chain_pe, 2 * n + 2)
                nxt, end = s_all[:, n + 1, :, :], t * P + (c + 1) * CHUNK_T - 1
                do(V.tensor_tensor(nxt, psum[4 * t + 2 + c][:, :].rearrange("p (f s) -> p f s", f=FT), bcast(cst("same_head").unsqueeze(1), [P, FT, P]), ALU.mult))
                do(V.tensor_tensor(nxt, nxt, s_all[:, n, :, :], ALU.add))
                do(V.tensor_tensor(nxt, nxt, bcast(pinc[:, :, end:end + 1], [P, FT, P]), ALU.mult), chain_dve)
        for t in range(TT):
            by_pe("y", t)
            for h in range(RH):
                do.also(V.bn_stats(r6[:, h, :], psum[4 * t][:, h * RN:(h + 1) * RN]))
            do.settle()
            for h in range(RH):
                ins = V.bn_aggr(rstat[:, t, h, :], r6[:, h, :])
                do.also(ins) if h < RH - 1 else do(ins, rw_dve)
            do.settle()
        for t in range(TT):
            by_act("std", t)
            do(V.reciprocal(small[:, 16 + 8 * t:24 + 8 * t], small[:, 8 * t:8 * t + 8]))
            yo = ymix[:, t, EW:2 * EW]
            for h in range(RH):
                hs = slice(h * RN, (h + 1) * RN)
                do.also(V.tensor_scalar(yo[:, hs], psum[4 * t][:, hs], rstat[:, t, h, 0:1], small[:, 16 + 8 * t + h:17 + 8 * t + h],
                                        ALU.subtract, ALU.mult))
            do.settle()
            do(V.tensor_tensor(yo, yo, erow[:, EROW["lnx_g"]], ALU.mult))
            do(V.tensor_tensor(yo, yo, erow[:, EROW["lnx_b"]], ALU.add))
            for h in range(RH):
                hs = slice(h * RN, (h + 1) * RN)
                do.also(V.scalar_tensor_tensor(out=yo[:, hs], in0=nat["v"][:, t, hs], scalar=bonus[:, t, h:h + 1], in1=yo[:, hs],
                                               op0=ALU.mult, op1=ALU.add))
            do.settle()
            do(V.tensor_tensor(yo, yo, gnat[:, t, :], ALU.mult), rw_dve)
        split_t(4)
        stream("eout", 0)
        taken("eout", 0)
        for t in range(TT):
            residual(t, 0, bank("eout", 0, t)[:, :], read_dve if t else None)
        stream("eout", 1, (0,))
        layer_norm(0, base + TILE_B["eout", 1] + 2,
                   lambda t: residual(t, 1, bank("eout", 1, t)[:, :], read_dve if t else None))

        def peer_layer(layer, t0):
            split_t(t0)
            split_lo(base + PEER_Q[layer] + 1)
            for i in range(2):
                stream(f"pq{layer}", i)
            def top16(streams):
                for vals, top, _ in streams:
                    do.also(V.max(top[:, 0:8], vals))
                do.settle()
                for vals, top, idx in streams:
                    do.also(V.max_index(idx[:, 0:8], top[:, 0:8], vals))
                do.settle()
                for vals, top, _ in streams:
                    do.also(V.match_replace(out=vals, in_to_replace=top[:, 0:8], in_values=vals, imm_value=-3e38))
                do.settle()
                for vals, top, _ in streams:
                    do.also(V.max(top[:, 8:16], vals))
                do.settle()
                for vals, top, idx in streams:
                    do.also(V.max_index(idx[:, 8:16], top[:, 8:16], vals))
                do.settle()

            def choose(t, split):
                dve.wait_ge(s_read, 2 * layer + t + 1)
                for n in range(0, 2 * PH, 2):
                    top16([(ss[t][:, c, :], tops[:, c, :], topi[:, c, :]) for c in (n, n + 1)])
                    split(n // 2)
                do(V.tensor_copy(topf[:, :, :], topi[:, :, :]))
                cand = ss[t][:, :, :].rearrange("p (h c) n -> p h (c n)", h=PH)
                for h in range(0, PH, 2):
                    for i in (h, h + 1):
                        do.also(V.tensor_tensor(cand[:, i, :].rearrange("p (a b) -> p a b", a=PK), bcast(tops[:, 2 * i, :].unsqueeze(2), [P, PK, PK]),
                                                bcast(tops[:, 2 * i + 1, :].unsqueeze(1), [P, PK, PK]), ALU.add))
                    do.settle()
                    top16([(cand[:, i, :], best[:, t, i, :], pos[:, i, :]) for i in (h, h + 1)])
                    split(PH + h // 2)
                do(V.tensor_copy(gsum[:, 0:PH], best[:, t, :, 0]))
                do(V.tensor_tensor(best[:, t, :, :], best[:, t, :, :], bcast(gsum[:, 0:PH].unsqueeze(2), [P, PH, PK]), ALU.subtract),
                   best_ready if t else None)
                pf = pos[:, :, :].rearrange("p h k -> p (h k)")
                do.also(V.tensor_scalar(posab[:, 0, :], pf, 4, None, ALU.logical_shift_right))
                do(V.tensor_scalar(posab[:, 1, :], pf, PK - 1, None, ALU.bitwise_and))
                do(V.tensor_copy(posf[:, :, :], posab[:, :, :]))
                tf = topf[:, :, :].rearrange("p (h c) k -> p h c k", c=2)
                split(PH + 4)
                for c in range(2):
                    do(V.tensor_tensor(hot.rearrange("p h k a -> p (h k) a"), bcast(posf[:, c, :].unsqueeze(2), [P, PH * PK, PK]),
                                       bcast(cst("iota")[:, 0:PK].unsqueeze(1), [P, PH * PK, PK]), ALU.is_equal))
                    do(V.tensor_tensor(hot, hot, bcast(tf[:, :, c, :].unsqueeze(2), [P, PH, PK, PK]), ALU.mult))
                    do(V.reduce_sum(sel[:, t, c, :], hot.rearrange("p h k a -> p (h k) a"), AXX))
                    split(PH + 5 + c)
                split(PH + 7)

            for part in range(2):
                done = 2 * layer + part
                first, g0 = PAIRS * done, GROUPS * layer
                tile = base + PEER_UV[layer] + 2 * PAIRS * part

                def split_tile(n, k):
                    kt_ = tile + k
                    if kt_ >= total:
                        return
                    dve.wait_ge(hi_ready, n * RAW + (kt_ + 1))
                    V.tensor_tensor(w_lo[:, kt_ % SPLIT, :], raw[:, kt_ % RAW, :], w_hi[:, kt_ % SPLIT, :].bitcast(F32), ALU.subtract).then_inc(lo_ready, 1)

                if part == 0:
                    for t in range(TT):
                        choose(t, lambda n: split_tile(0, t * PAIRS // 2 + n + 2))
                    dve.wait_ge(exp_ready, layer + 1)
                    do(V.reduce_sum(gsum[:, :], best[:, :, :, :].rearrange("p t h k -> p (t h) k"), AXX))
                    do(V.reciprocal(gsum[:, :], gsum[:, :]))
                    for t in range(TT):
                        do(V.tensor_tensor(sel[:, t, 2, :].rearrange("p (h k) -> p h k", h=PH), best[:, t, :, :],
                                           bcast(gsum[:, t * PH:(t + 1) * PH].unsqueeze(2), [P, PH, PK]), ALU.mult), sel_ready)
                    dve.wait_ge(ijg_ready, 2 * layer + 2)
                else:
                    with dve.Fori(0, PAIRS // RAW) as n:
                        for p in range(RAW):
                            split_tile(n, p + 2)

                def one_hot(n, b):
                    tok = bass.ds(n * HOT * GT + b * GT, GT)
                    if not isinstance(n, int):
                        dve.wait_ge(gates_done, n * HOT + (g0 + b + 1 - HOT))
                    for keys_at, dst in ((1, hot_j), (0, hot_i)):
                        ins = V.tensor_tensor(dst[:, b, :, :], bcast(cst("iota").unsqueeze(1), [P, GT, KEYS]),
                                              bcast(ijg[:, keys_at, tok].unsqueeze(2), [P, GT, KEYS]), ALU.is_equal)
                    ins.then_inc(hot_eq, 1)

                def apply(n, b):
                    dve.wait_ge(gates_read, n * HOT + (g0 + b + 1))
                    tok = hid[:, :, bass.ds(n * HOT * GT + b * GT, GT)].rearrange("p j t -> p t j")
                    V.tensor_tensor(tok, tok, staged[:, b, 0, :, :], ALU.mult).then_inc(gated_even, 1)

                if part == 0:
                    for b in range(HOT):
                        one_hot(0, b)
                    dve.wait_ge(gelu_ready, first + PAIRS)
                    with dve.Fori(0, GROUPS // HOT - 1) as n:
                        for b in range(HOT):
                            one_hot(n + 1, b)
                            if b % 2 == 0:
                                apply(n, b)
                    for b in range(0, HOT, 2):
                        apply(GROUPS // HOT - 1, b)
                else:
                    dve.wait_ge(gelu_ready, first + PAIRS)
                    with dve.Fori(0, REGATED) as n:
                        for b in range(RELOAD):
                            if b % HOT < HOT - 1:
                                dve.wait_ge(reloaded[b], n * 16 + 16 * (REGATED * layer + 1))
                                tok = hid[:, :, bass.ds(n * RELOAD * 2 * GT + b * 2 * GT, 2 * GT)].rearrange("p j t -> p t j")
                                V.tensor_tensor(tok, tok, reload[b], ALU.mult).then_inc(regated_dve, 1)

                def lower(n, p):
                    dve.wait_ge(c_hi_ready, n * RAW + (first + p + 1))
                    at = slice(2 * p, 2 * p + 2) if isinstance(n, int) else bass.ds(n * 2 * RAW + 2 * p, 2)
                    halves = lambda ap: ap.rearrange("p (j s) -> p j s", j=2)
                    V.tensor_tensor(halves(c_lo[:, p % 2, :]), hid[:, at, :], halves(c_hi[:, p % 2, :]).bitcast(F32), ALU.subtract).then_inc(c_lo_ready, 1)

                lower(0, 0)
                lower(0, 1)
                with dve.Fori(0, PAIRS // RAW - 1) as n:
                    for p in range(RAW):
                        split_tile(n, PAIRS + p + 2)
                        lower(n, p + 2)
                for p in range(PAIRS - RAW, PAIRS):
                    if part == 0 or p < PAIRS - 1:
                        split_tile(0, PAIRS + p + 2)
                    if p + 2 < PAIRS:
                        lower(0, p + 2)

        def both_chunks(t):
            for n in range(2):
                residual(t, n, psum[2 * t + n][:, :])

        peer_layer(0, 8)
        layer_norm(1, base + PEER_UV[0] + 4 * PAIRS, both_chunks)
        split_t(12)
        split_lo(base + ODD + 1)

        def rope(dst, src, width, t, signal=None):
            w = width // 2
            heads = dst.shape[1] // width
            cut = lambda ap: ap.rearrange("p (h n) -> p h n", n=width)
            cos = bcast(cst(f"cos{width}")[:, t * w:(t + 1) * w].unsqueeze(1), [P, heads, w])
            sin = bcast(cst(f"sin{width}")[:, t * w:(t + 1) * w].unsqueeze(1), [P, heads, w])
            x1, x2 = cut(src)[:, :, 0:w], cut(src)[:, :, w:width]
            o1, o2 = cut(dst)[:, :, 0:w], cut(dst)[:, :, w:width]
            r1, r2 = (rtmp[:, n, 0:heads * w].rearrange("p (h n) -> p h n", n=w) for n in range(2))
            do.also(V.tensor_tensor(o1, x1, cos, ALU.mult))
            do.also(V.tensor_tensor(r1, x2, sin, ALU.mult))
            do.also(V.tensor_tensor(o2, x2, cos, ALU.mult))
            do.also(V.tensor_tensor(r2, x1, sin, ALU.mult))
            do.settle()
            do.also(V.tensor_tensor(o1, o1, r1, ALU.subtract))
            do(V.tensor_tensor(o2, o2, r2, ALU.add), signal)
            do.settle()

        def turn_q(i):
            taken("oq", i)
            for t in range(TT):
                rope(qn[:, t, i * CW:(i + 1) * CW], bank("oq", i, t)[:, :], AD, t, read_dve if t else None)

        def index_score(t):
            dve.wait_ge(odd_act, ODD_ACT[f"index{t}"])
            for h in range(IH):
                wh = wi[:, t, h:h + 1]
                if h == 0:
                    do(V.tensor_scalar(score[:, t, :], rel[:, t, h, :], wh, None, ALU.mult))
                else:
                    do(V.scalar_tensor_tensor(out=score[:, t, :], in0=rel[:, t, h, :], scalar=wh, in1=score[:, t, :], op0=ALU.mult, op1=ALU.add))

        def select(t):
            causal, sc, ma = cst("causal")[:, t * S:(t + 1) * S], score[:, t, :], madd[:, t, :]
            do(V.tensor_scalar(ma, causal, -1.0, NEG, ALU.add, ALU.mult))
            do(V.tensor_tensor(sc, sc, causal, ALU.mult))
            do(V.tensor_tensor(sc, sc, ma, ALU.add))
            for n in range(SELECT // 8):
                do(V.max(top8[:, :], sc))
                do(V.match_replace(out=sc, in_to_replace=top8[:, :], in_values=sc, imm_value=-3e38))
            do(V.scalar_tensor_tensor(out=ma, in0=sc, scalar=-2e30, in1=causal, op0=ALU.is_lt, op1=ALU.mult))
            do(V.tensor_scalar(ma, ma, -1.0, NEG, ALU.add, ALU.mult))

        stream("oqi", 0)
        taken("oqi", 0)
        for t in range(TT):
            rope(qin_[:, t, :], bank("oqi", 0, t)[:, :], ID, t, read_dve if t else None)
        do(V.memset(kib[:, :], 0.0))
        stream("okv", 0)
        taken("okv", 0)
        for t in range(TT):
            src = bank("okv", 0, t)
            rope(kn[:, t, :], src[:, 0:AD], AD, t)
            rope(kid[:, t, 0:ID], src[:, 2 * AD:2 * AD + ID], ID, t)
        do(V.tensor_copy(kid[:, :, ID:2 * ID], kid[:, :, 0:ID]), odd_dve)
        for t in range(TT):
            src = bank("okv", 0, t)
            do(V.tensor_copy(vn[:, t, :], src[:, AD:2 * AD]))
            do(V.tensor_scalar(wi[:, t, :], src[:, 2 * AD + ID:2 * AD + ID + IH], float(IH ** -0.5 * ID ** -0.5), None, ALU.mult), read_dve if t else None)
        stream("oq", 0, (0,))
        dve.wait_ge(odd_pe, ODD_PE["it"])
        do(V.tensor_copy(kib[0:ID, 0:S], psum[7][0:ID, 0:S]))
        do(V.tensor_copy(kib[ID:P, S:2 * S], psum[7][ID:P, 0:S]), odd_dve)
        stream("oq", 0, (1,))
        turn_q(0)
        index_score(0)
        stream("oq", 1)
        turn_q(1)
        dve.sem_inc(odd_dve, 1)
        select(0)
        for t in range(TT):
            n = (t + 1) * P
            dve.wait_ge(odd_pe, ODD_PE[f"logits{t}"])
            for b in range(4):
                do(V.scalar_tensor_tensor(out=logit[:, 2 * b:2 * b + 2, 0:n], in0=psum[b][:, :].rearrange("p (h s) -> p h s", h=2)[:, :, 0:n],
                                          scalar=AD ** -0.5, in1=bcast(madd[:, t, 0:n].unsqueeze(1), [P, 2, n]), op0=ALU.mult, op1=ALU.add))
            do(V.reduce_max(amax[:, :], logit[:, :, 0:n], AXX))
            do(V.tensor_scalar(amax[:, :], amax[:, :], -1.0, None, ALU.mult), odd_dve)
            if t == 0:
                index_score(1)
            dve.wait_ge(odd_act, ODD_ACT[f"exp{t}"])
            do(V.reciprocal(asum[:, :], asum[:, :]))
            do(V.tensor_tensor(logit[:, :, 0:n], logit[:, :, 0:n], bcast(asum[:, :].unsqueeze(2), [P, AH, n]), ALU.mult), odd_dve)
            if t == 0:
                select(1)
            dve.wait_ge(att_hi, t + 1)
            for hh in range(2):
                hs = slice(4 * hh, 4 * hh + 4)
                do(V.tensor_tensor(act_lo[:, hs, HALVES[t]], psum[hh][:, :].rearrange("p (h s) -> p h s", h=4),
                                   act_hi[:, hs, HALVES[t]].bitcast(F32), ALU.subtract), att_lo if hh else None)
        stream("oout", 0)
        taken("oout", 0)
        for t in range(TT):
            residual(t, 0, bank("oout", 0, t)[:, :], read_dve if t else None)
        stream("oout", 1, (0,))
        layer_norm(2, base + TILE_B["oout", 1] + 2,
                   lambda t: residual(t, 1, bank("oout", 1, t)[:, :], read_dve if t else None))
        peer_layer(1, 16)
        layer_norm(3, base + PEER_UV[1] + 4 * PAIRS, both_chunks)


def program(nc, x_in, weights, rows, cols, bgate, p_t, w_pe, final_row, identity, consts_a, erows, ecols, lora_w, side_w, keys, ln_rows,
            consts_b, out):
    ctx = ExitStack()
    with ctx:
        m = Common(nc, ctx, weights)
        spill = nc.dram_tensor("spill", (GROUPS, P, GT * JH), F32, kind="Internal").ap()
        first_block(nc, ctx, m, x_in, rows, cols, bgate, p_t, w_pe, final_row, identity, consts_a)
        second_block(nc, ctx, m, LAYERS * TILES_A, erows, ecols, lora_w, side_w, keys, ln_rows, consts_b, spill, out)


def _weight_tiles(w):
    k, n = w.shape
    return w.reshape(k // (KB * P), KB, P, n // CW, CW).transpose(3, 0, 2, 1, 4).reshape(-1, P, TW)


def _cols(v):
    return v.reshape(-1, P).T


def _constants_a():
    p, t = np.arange(P)[:, None], np.arange(P)[None, :]
    log_gamma = np.log(1.0 - 2.0 ** (-5.0 - np.arange(HEADS)))
    decay = []
    for h in range(HEADS):
        near = np.where(t >= p, np.exp(np.maximum(t - p, 0) * log_gamma[h]), 0.0)
        far = np.exp((t + P - p) * log_gamma[h])
        decay += [near, far, near]
    inv = np.float32(10000.0) ** (-np.arange(0, 256, 2, dtype=np.float32) / np.float32(256))
    ang = inv[:, None] * np.arange(S, dtype=np.float32)[None, :]
    sel = np.zeros((P, HEADS * P))
    for h in range(HEADS):
        sel[h, h * P:(h + 1) * P] = 1.0
    parts = {"cum": t >= p, "ones": np.ones((P, P)), "mask": np.where(t >= p, 0.0, NEG),
             "decay": np.concatenate(decay, 1) / 16.0, "cos": np.cos(ang.astype(np.float64)), "sin": np.sin(ang.astype(np.float64)), "headsel": sel,
             "eps": np.full((P, 1), EPS), "one": np.ones((P, 1))}
    return np.concatenate([np.asarray(parts[n], np.float32) for n in CONST_A], 1)


def _first_block_arrays(i):
    w = []
    rows, cols, bgate = [], [], []
    for l in range(LAYERS):
        w_in, b_in = i["w_in"][l], i["b_in"][l]
        at = {}
        off = 0
        for name, n in (("mq", 1024), ("mk", 1024), ("mv", 1024), ("mo", 1024), ("gates", 8), ("rq", 1024), ("rk", 1024),
                        ("rv", 2048), ("rg", 2048), ("gm", 1024), ("gr", 1024)):
            at[name] = slice(off, off + n)
            off += n
        both = {"mqk": ("mq", "mk"), "rqk": ("rq", "rk")}
        part = lambda name: np.concatenate([w_in[:, at[n]] for n in both.get(name, (name,))], 1)
        ff1, ff2 = i["w_ff1"][l], i["w_ff2"][l]
        ws = {"bm": i["w_bm"][l], "br": i["w_br"][l], "out": i["w_out"][l], "ffa1": ff1[:, :2048], "ffa2": ff2[:2048],
              "ffb1": ff1[:, 2048:], "ffb2": ff2[2048:], "peg": i["w_pe_gate"][l]}
        for name, _, _ in ORDER_A:
            w.append(_weight_tiles(ws[name] if name in ws else part(name)))
        g = {"mo": i["m_norm_g"][l], "rg": i["r_norm_g"][l]}
        for name, n in (("mv", 2), ("mo", 2), ("gm", 2), ("rv", 4), ("rg", 4), ("gr", 2), ("ffb2", 2)):
            b = i["b_ff2"][l] if name == "ffb2" else b_in[at[name]]
            for c in range(n):
                rows.append(b[c * CW:(c + 1) * CW])
                if name in g:
                    rows.append(g[name][c * CW:(c + 1) * CW])
        cat = lambda a, b: np.concatenate([b_in[at[a]], b_in[at[b]]])
        cols.append(np.concatenate(
            [_cols(i[f"norm{n}_g"][l]) for n in (1, 2, 3)] + [_cols(cat("mq", "mk")), _cols(cat("rq", "rk"))]
            + [_cols(i["conv_w"][l][j]) for j in range(4)] + [_cols(i["conv_b"][l]), _cols(i["b_ff1"][l])]
            + [w_in[:, at["gates"]].reshape(KD, P, 8).transpose(1, 0, 2).reshape(P, 64)], 1))
        bgate.append(b_in[at["gates"]])
    return {
        "x_in": i["x"][0].reshape(TT, P, D).transpose(1, 0, 2),
        "rows": np.stack(rows).reshape(LAYERS, ROWS_A, CW),
        "cols": np.stack(cols),
        "bgate": np.stack(bgate),
        "p_t": i["p"][:, 0].reshape(LAYERS, S, 2, P).transpose(0, 3, 2, 1),
        "w_pe": i["w_pe"].reshape(LAYERS, 2, P, D).transpose(0, 2, 1, 3),
        "final_row": i["final_g"],
        "identity": np.eye(P, dtype=np.float32),
        "consts_a": _constants_a(),
    }, w


def _constants_b():
    p, t = np.arange(P)[:, None], np.arange(P)[None, :]
    same = p // CHUNK_T == t // CHUNK_T
    tok = np.arange(S).reshape(TT, P).T
    q, u = p % CHUNK_T, np.arange(CHUNK_T)[None, :]
    levels = [(q // (2 << n) == u // (2 << n)) & ((q >> n) % 2 == 1) & ((u >> n) % 2 == 0) for n in range(LEVELS)]

    def angles(dim):
        inv = np.float32(10000.0) ** (-np.arange(0, dim, 2, dtype=np.float32) / np.float32(dim))
        return (tok.astype(np.float32)[:, :, None] * inv).astype(np.float64).reshape(P, -1)

    parts = {"same_head": same, "upto": (p <= t) & same, "strict_upto": np.concatenate([q < u, q <= u], 1),
             "diag2": p // GDK == np.arange(2 * P)[None, :] // GDV, "levels": np.concatenate(levels, 1), "eye64": q == u, "level0_t": (q % 2 == 0) & (u == q + 1),
             "keep": np.broadcast_to(np.arange(S) % CHUNK_T != 0, (P, S)), "half": p // RN == np.arange(2)[None, :],
             "iota": np.broadcast_to(np.arange(P), (P, P)), "causal": (np.arange(S) <= tok[:, :, None]).reshape(P, -1),
             "cos128": np.cos(angles(128)), "sin128": np.sin(angles(128)), "cos64": np.cos(angles(64)), "sin64": np.sin(angles(64)),
             "ln_eps": np.full((P, 1), LN_EPS), "lnx_eps": np.full((P, 1), LNX_EPS), "one": np.ones((P, 1))}
    return np.concatenate([np.asarray(parts[n], np.float32) for n in CONST_B], 1)


def _expert_tiles(u, v):
    u = u.reshape(KEYS, KEYS // 2, 2, KD, P).transpose(1, 4, 3, 2, 0).reshape(KEYS // 2, P, TW)
    v = v.reshape(KEYS, KEYS // 2, 2 * D).transpose(1, 0, 2)
    tiles = []
    for first in range(0, KEYS // 2, PAIRS):
        tiles += [u[first:first + PAIRS], v[first:first + PAIRS]]
    return np.concatenate(tiles, 0)


def _second_block_arrays(i):
    g = lambda name: i[name + "_2"]
    w_in, mu = g("even_w_in")[0], g("rwkv_mu")[0]
    ends = np.cumsum([256, 256, 512, 512, 16, 512, 512, 512, 32, 32, 96])
    gq, gk, gv, gg, gal, r, k, v, wl, al, gl = np.split(w_in, ends[:-1], 1)
    mr, mk, mv, mwl, mal, mgl = np.split(mu, (ends[5:-1] - ends[4]))
    zeros = lambda *s: np.zeros(s, np.float32)
    side = np.concatenate([gl, wl, gal, zeros(D, 16), al, zeros(D, 64)], 1)
    lora = zeros(P, LORA)
    lora[G2], lora[W2], lora[A2] = g("rwkv_g2")[0], g("rwkv_w2")[0], g("rwkv_a2")[0]
    lora[0:16, GA2[1]] = g("gla_a_w2")[0]
    cols = {"mu_side": _cols(np.concatenate([mgl, mwl, zeros(32), mal, zeros(64)])), "mu": _cols(np.concatenate([mr, mk, mv])),
            "gla_a_b": _cols(g("gla_a_b")[0]), "w0": _cols(g("rwkv_w0")[0]), "a0": _cols(g("rwkv_a0")[0]), "k_k": _cols(g("rwkv_k_k")[0]),
            "k_a": _cols(g("rwkv_k_a")[0]), "r_k": _cols(g("rwkv_r_k")[0].reshape(-1))}
    odd = g("odd_w_in")[0]
    okv = np.concatenate([odd[:, 1024:1280], odd[:, 1792:], zeros(D, CW - 256 - 72)], 1)
    keys = zeros(LAYERS, 2, 64, PH, 2, KEYS)
    for c in range(2):
        keys[:, c, :, :, c, :] = g("peer_sub_keys")[:, :, c].transpose(0, 3, 1, 2)
    weights = []
    for layer in range(LAYERS):
        if layer == 0:
            weights += [_weight_tiles(w) for w in (np.concatenate([gq, gk], 1), gv, gg, r, k, v, g("even_w_out")[0])]
        else:
            weights += [_weight_tiles(w) for w in (odd[:, 1280:1792], okv, odd[:, :1024], g("odd_w_out")[0])]
        weights += [_weight_tiles(g("peer_w_q")[layer]), _expert_tiles(g("peer_u")[layer], g("peer_v")[layer])]
    norms = [g(f"{n}_ln_{p}")[layer] for layer in range(LAYERS) for n in ("mix", "ffn") for p in "gb"]
    return {
        "erows": np.concatenate([g("gla_norm_g")[0], g("rwkv_lnx_g")[0], g("rwkv_lnx_b")[0]]),
        "ecols": np.concatenate([cols[n] for n in ECOL], 1),
        "lora_w": lora,
        "side_w": side.reshape(KD, P, 2 * P).transpose(1, 0, 2),
        "keys": keys.reshape(LAYERS, P, PH, 2 * KEYS),
        "ln_rows": np.stack(norms),
        "consts_b": _constants_b(),
    }, weights


def kernel(**inputs):
    import concourse.bacc as bacc
    from concourse.bass_utils import run_bass_kernel_spmd

    i = {name: np.asarray(a) for name, a in inputs.items()}
    arrays, first = _first_block_arrays(i)
    more, second = _second_block_arrays(i)
    arrays.update(more)
    arrays["weights"] = np.concatenate(first + second, 0)
    arrays = {name: np.ascontiguousarray(a) for name, a in arrays.items()}
    nc = bacc.Bacc("TRN2", target_bir_lowering=False, num_devices=1)
    aps = {name: nc.dram_tensor(name, a.shape, mybir.dt.from_np(a.dtype), kind="ExternalInput").ap() for name, a in arrays.items()}
    aps["out"] = nc.dram_tensor("out", (P, TT, D), F32, kind="ExternalOutput").ap()
    program(nc, **aps)
    r = run_bass_kernel_spmd(nc, [arrays], core_ids=[0])
    return r.results[0]["out"].transpose(1, 0, 2).reshape(1, S, D)
```
